# Optimizing a Trainium2 kernel written in Bass

```python
import jax, jax.numpy as jnp
from jax import lax
import numpy as np
import math
import jax
import jax.numpy as jnp

D_MODEL = 1024
BATCH = 1
SEQ = 256
DEPTH = 2

D_FF = 2816
CHUNK = 128
A_GROUPS = 4
A_GROUP_CH = 128
A_HALF = A_GROUPS * A_GROUP_CH
N_HEADS = 8
HEAD_DIM = 64
ATT_W = N_HEADS * HEAD_DIM
IDX_HEADS = 8
IDX_DIM = 64
TOPK_MAX = 256
Q_BLOCK = 128
ROPE_THETA = 10000.0
EPS = 1e-6

SPLIT_SIZES = (A_HALF, A_HALF, ATT_W, ATT_W, ATT_W, IDX_HEADS * IDX_DIM, IDX_DIM, IDX_HEADS, D_MODEL, D_MODEL)
SPLIT_POINTS = tuple(int(v) for v in np.cumsum(SPLIT_SIZES)[:-1])
N_IN = int(sum(SPLIT_SIZES))


def _rms_norm(x, g):
    xf = x.astype(jnp.float32)
    y = xf * lax.rsqrt(jnp.mean(xf * xf, axis=-1, keepdims=True) + EPS)
    return (y * g.astype(jnp.float32)).astype(x.dtype)

def _layer_norm(x, g, b):
    xf = x.astype(jnp.float32)
    mu = jnp.mean(xf, axis=-1, keepdims=True)
    var = jnp.mean(jnp.square(xf - mu), axis=-1, keepdims=True)
    y = (xf - mu) * lax.rsqrt(var + EPS)
    return (y * g.astype(jnp.float32) + b.astype(jnp.float32)).astype(x.dtype)

def _swiglu(h, w_gu, w_down):
    gate, up = jnp.split(h @ w_gu, 2, axis=-1)
    return (jax.nn.silu(gate) * up) @ w_down

def _rope(x, pos):
    d = x.shape[-1]
    inv = ROPE_THETA ** (-jnp.arange(0, d, 2, dtype=jnp.float32) / d)
    ang = pos.astype(jnp.float32)[:, None] * inv[None, :]
    cos = jnp.cos(ang)[None, :, None, :].astype(x.dtype)
    sin = jnp.sin(ang)[None, :, None, :].astype(x.dtype)
    x1, x2 = x[..., : d // 2], x[..., d // 2:]
    return jnp.concatenate([x1 * cos - x2 * sin, x2 * cos + x1 * sin], axis=-1)

def _gmlp_spatial(u, v, ln_g, ln_b, w_s, b_s):
    B, T, _ = u.shape
    u = jax.nn.gelu(u)
    v = _layer_norm(jax.nn.gelu(v), ln_g, ln_b)
    vb = v.reshape(B, T // CHUNK, CHUNK, A_GROUPS, A_GROUP_CH)
    mask = jnp.tril(jnp.ones((CHUNK, CHUNK), dtype=bool))
    ws = jnp.where(mask[None], w_s, jnp.zeros((), w_s.dtype))
    mixed = jnp.einsum('gts,bnsgc->bntgc', ws, vb) + b_s.T[:, :, None]
    return u * mixed.reshape(B, T, A_HALF)

def _dsa_attention(q, k, v, q_idx, k_idx, w_idx):
    B, T, H, Dh = q.shape
    L = k.shape[1]
    topk = min(TOPK_MAX, L // 4)
    nb = T // Q_BLOCK
    idx_scale = (IDX_DIM ** -0.5) * (IDX_HEADS ** -0.5)
    att_scale = HEAD_DIM ** -0.5
    kpos = jnp.arange(L, dtype=jnp.int32)
    qpos = jnp.arange(T, dtype=jnp.int32).reshape(nb, Q_BLOCK)
    gather = jax.vmap(lambda a, i: a[i])

    def to_blocks(a):
        return a.reshape((B, nb, Q_BLOCK) + a.shape[2:]).swapaxes(0, 1)

    def one_block(args):
        qb, qib, wb, pb = args
        logits = jnp.einsum('bqhd,bsd->bqhs', qib, k_idx).astype(jnp.float32)
        score = jnp.einsum('bqhs,bqh->bqs', jax.nn.relu(logits), wb.astype(jnp.float32)) * idx_scale
        causal = kpos[None, :] <= pb[:, None]
        score = jnp.where(causal[None], score, -jnp.inf)
        _, sel = lax.top_k(score, topk)
        k_sel = gather(k, sel)
        v_sel = gather(v, sel)
        s = jnp.einsum('bqhd,bqkhd->bhqk', qb, k_sel).astype(jnp.float32) * att_scale
        valid = sel <= pb[None, :, None]
        s = jnp.where(valid[:, None], s, -jnp.inf)
        p = jax.nn.softmax(s, axis=-1).astype(v.dtype)
        return jnp.einsum('bhqk,bqkhd->bqhd', p, v_sel)

    out = lax.map(one_block, (to_blocks(q), to_blocks(q_idx), to_blocks(w_idx), qpos))
    return out.swapaxes(0, 1).reshape(B, T, H * Dh)

def _hybrid_mixer(h, w_in, b_gate, gmlp_ln_g, gmlp_ln_b, gmlp_w_s, gmlp_b_s, w_pa, w_pb, w_out):
    B, T, _ = h.shape
    proj = h @ w_in
    u, va, q, k, v, qi, ki, wi, g_a, g_b = jnp.split(proj, SPLIT_POINTS, axis=-1)
    pos = jnp.arange(T, dtype=jnp.int32)
    y_a = _gmlp_spatial(u, va, gmlp_ln_g, gmlp_ln_b, gmlp_w_s, gmlp_b_s) @ w_pa
    q = _rope(q.reshape(B, T, N_HEADS, HEAD_DIM), pos)
    k = _rope(k.reshape(B, T, N_HEADS, HEAD_DIM), pos)
    v = v.reshape(B, T, N_HEADS, HEAD_DIM)
    qi = _rope(qi.reshape(B, T, IDX_HEADS, IDX_DIM), pos)
    ki = _rope(ki[:, :, None, :], pos)[:, :, 0, :]
    y_b = _dsa_attention(q, k, v, qi, ki, wi) @ w_pb
    gates = jax.nn.sigmoid(jnp.concatenate([g_a, g_b], axis=-1) + b_gate)
    gate_a, gate_b = jnp.split(gates, 2, axis=-1)
    return (gate_a * y_a + gate_b * y_b) @ w_out

def first_inputs(seed: int = 0) -> dict:
    key = jax.random.key(seed)
    ks = jax.random.split(key, 20)
    f32 = jnp.float32

    def nrm(k, shape, scale):
        return jax.random.normal(k, shape, f32) * scale

    def gain(k, shape):
        return 1.0 + 0.05 * jax.random.normal(k, shape, f32)

    return {
        "x": jax.random.normal(ks[0], (BATCH, SEQ, D_MODEL), f32),
        "ffn1_norm": gain(ks[1], (DEPTH, D_MODEL)),
        "ffn1_w_gu": nrm(ks[2], (DEPTH, D_MODEL, 2 * D_FF), D_MODEL ** -0.5),
        "ffn1_w_down": nrm(ks[3], (DEPTH, D_FF, D_MODEL), D_FF ** -0.5),
        "mix_norm": gain(ks[4], (DEPTH, D_MODEL)),
        "w_in": nrm(ks[5], (DEPTH, D_MODEL, N_IN), D_MODEL ** -0.5),
        "b_gate": nrm(ks[6], (DEPTH, 2 * D_MODEL), 0.02),
        "gmlp_ln_g": gain(ks[7], (DEPTH, A_HALF)),
        "gmlp_ln_b": nrm(ks[8], (DEPTH, A_HALF), 0.02),
        "gmlp_w_s": nrm(ks[9], (DEPTH, A_GROUPS, CHUNK, CHUNK), 0.5 * CHUNK ** -0.5),
        "gmlp_b_s": 1.0 + 0.1 * jax.random.normal(ks[10], (DEPTH, A_GROUPS, CHUNK), f32),
        "w_pa": nrm(ks[11], (DEPTH, A_HALF, D_MODEL), A_HALF ** -0.5),
        "w_pb": nrm(ks[12], (DEPTH, ATT_W, D_MODEL), ATT_W ** -0.5),
        "w_out": nrm(ks[13], (DEPTH, D_MODEL, D_MODEL), D_MODEL ** -0.5),
        "ffn2_norm": gain(ks[14], (DEPTH, D_MODEL)),
        "ffn2_w_gu": nrm(ks[15], (DEPTH, D_MODEL, 2 * D_FF), D_MODEL ** -0.5),
        "ffn2_w_down": nrm(ks[16], (DEPTH, D_FF, D_MODEL), D_FF ** -0.5),
        "final_norm": gain(ks[17], (D_MODEL,)),
    }

def first_block(x, ffn1_norm, ffn1_w_gu, ffn1_w_down, mix_norm, w_in, b_gate, gmlp_ln_g, gmlp_ln_b,
              gmlp_w_s, gmlp_b_s, w_pa, w_pb, w_out, ffn2_norm, ffn2_w_gu, ffn2_w_down, final_norm):
    for l in range(DEPTH):
        x = x + 0.5 * _swiglu(_rms_norm(x, ffn1_norm[l]), ffn1_w_gu[l], ffn1_w_down[l])
        x = x + _hybrid_mixer(_rms_norm(x, mix_norm[l]), w_in[l], b_gate[l], gmlp_ln_g[l], gmlp_ln_b[l],
                              gmlp_w_s[l], gmlp_b_s[l], w_pa[l], w_pb[l], w_out[l])
        x = x + 0.5 * _swiglu(_rms_norm(x, ffn2_norm[l]), ffn2_w_gu[l], ffn2_w_down[l])
    return _rms_norm(x, final_norm)


CTX_LEN = 256
GRID_W = 64
N_MOD = 6
MLP_HIDDEN = 4 * D_MODEL

CONV_CH = D_MODEL // 2
CONV_W = 31
DIFF_HEADS = 4
DIFF_DQK = 64
DIFF_DV = 2 * DIFF_DQK
ROPE_BASE = 10000.0
EV_QK = DIFF_HEADS * 2 * DIFF_DQK
EV_VW = DIFF_HEADS * DIFF_DV
EV_Q0 = 2 * CONV_CH
EV_K0 = EV_Q0 + EV_QK
EV_V0 = EV_K0 + EV_QK
EVEN_IN = EV_V0 + EV_VW
EVEN_MIX = CONV_CH + EV_VW

HY_CH = D_MODEL // 2
HY_ORDER = 2
HY_SHORT_W = 3
HY_EMB = 33
HY_FFN = 64
HY_FAST = 0.3
HY_SLOW = 1.5
HY_TARGET = 1e-2
HY_MAX_DECAY = math.log(HY_TARGET) / HY_FAST
HY_MIN_DECAY = math.log(HY_TARGET) / HY_SLOW
HY_IN = (HY_ORDER + 1) * HY_CH
DN_HEADS = 4
DN_DK = 128
DN_DV = 128
DN_WIDTH = DN_HEADS * DN_DK
DN_CONV_W = 5
DN_CHUNK = 64
OD_G0 = HY_IN
OD_Q0 = OD_G0 + DN_HEADS * DN_DV
OD_K0 = OD_Q0 + DN_WIDTH
ODD_IN = OD_K0 + 2 * DN_WIDTH + 4 * DN_HEADS
ODD_MIX = HY_CH + DN_HEADS * DN_DV

N_EVEN = (DEPTH + 1) // 2
N_ODD = DEPTH // 2


F32 = jnp.float32

def rms_norm(x, g):
    xf = x.astype(F32)
    y = xf * lax.rsqrt(jnp.mean(xf * xf, axis=-1, keepdims=True) + EPS)
    return (y * g.astype(F32)).astype(x.dtype)

def layer_norm(x, g, b):
    xf = x.astype(F32)
    mu = jnp.mean(xf, axis=-1, keepdims=True)
    var = jnp.mean(jnp.square(xf - mu), axis=-1, keepdims=True)
    y = (xf - mu) * lax.rsqrt(var + EPS)
    return (y * g.astype(F32) + b.astype(F32)).astype(x.dtype)

def l2norm(t):
    return t * lax.rsqrt(jnp.sum(t * t, axis=-1, keepdims=True) + 1e-6)

def modulate(h, shift, scale):
    return h * (1.0 + scale) + shift

def squared_relu_mlp(h, w1, w2):
    return jnp.square(jax.nn.relu(h @ w1)) @ w2

def depthwise_conv(x, w, b=None):
    width = w.shape[0]
    left = (width - 1) // 2
    y = lax.conv_general_dilated(x, w[:, None, :].astype(x.dtype), (1,), [(left, width - 1 - left)],
                                 dimension_numbers=('NWC', 'WIO', 'NWC'), feature_group_count=x.shape[-1])
    return y if b is None else y + b

def axial_rope_tables(length):
    rows = length // GRID_W
    row = jnp.repeat(jnp.arange(rows, dtype=F32), GRID_W)
    col = jnp.tile(jnp.arange(GRID_W, dtype=F32), rows)
    n_freq = DIFF_DQK // 4
    inv = ROPE_BASE ** (-jnp.arange(n_freq, dtype=F32) / n_freq)
    ang_r = row[:, None] * inv
    ang_c = col[:, None] * inv
    return (jnp.cos(ang_r), jnp.sin(ang_r), jnp.cos(ang_c), jnp.sin(ang_c))

def rotate(x, cos, sin):
    x1, x2 = jnp.split(x, 2, axis=-1)
    return jnp.concatenate([x1 * cos - x2 * sin, x1 * sin + x2 * cos], axis=-1)

def apply_axial_rope(x, rope):
    cr, sr, cc, sc = rope
    xf = x.astype(F32)
    half = x.shape[-1] // 2
    return jnp.concatenate([rotate(xf[..., :half], cr, sr), rotate(xf[..., half:], cc, sc)], axis=-1).astype(x.dtype)

def conformer_conv(p_glu, conv_w, conv_b, ln_g, ln_b):
    a, gate = jnp.split(p_glu, 2, axis=-1)
    u = depthwise_conv(a * jax.nn.sigmoid(gate), conv_w, conv_b)
    return jax.nn.silu(layer_norm(u, ln_g, ln_b))

def qk_heads(t):
    b, l, _ = t.shape
    return t.reshape(b, l, DIFF_HEADS, 2, DIFF_DQK).transpose(0, 2, 3, 1, 4)

def v_heads(t):
    b, l, _ = t.shape
    return t.reshape(b, l, DIFF_HEADS, DIFF_DV).transpose(0, 2, 1, 3)

def diff_attend(q, k, v, lam):
    s = jnp.einsum('bhmqd,bhmkd->bhmqk', q, k).astype(F32) * (DIFF_DQK ** -0.5)
    p = jax.nn.softmax(s, axis=-1)
    p = p[:, :, 0] - lam * p[:, :, 1]
    return jnp.einsum('bhqk,bhkv->bhqv', p.astype(v.dtype), v)

def diff_merge(o, subln_g, lambda_init):
    b, h, l, dv = o.shape
    o = rms_norm(o, subln_g) * (1.0 - lambda_init)
    return o.transpose(0, 2, 1, 3).reshape(b, l, h * dv)

def even_mixer(h_lat, h_ctx, rope, w_in, conv_w, conv_b, ln_g, ln_b, lq1, lk1, lq2, lk2, subln_g, w_out,
               lambda_init, ctx_out):
    lam = (jnp.exp(jnp.sum(lq1.astype(F32) * lk1.astype(F32)))
           - jnp.exp(jnp.sum(lq2.astype(F32) * lk2.astype(F32))) + lambda_init)
    b, length = h_lat.shape[:2]
    p_lat = h_lat @ w_in
    conv_lat = conformer_conv(p_lat[..., :EV_Q0], conv_w, conv_b, ln_g, ln_b)
    q_lat = apply_axial_rope(qk_heads(p_lat[..., EV_Q0:EV_K0]), rope)
    k_lat = apply_axial_rope(qk_heads(p_lat[..., EV_K0:EV_V0]), rope)
    v_lat = v_heads(p_lat[..., EV_V0:])
    if ctx_out:
        p_ctx = h_ctx @ w_in
        kv_ctx = p_ctx[..., EV_K0:]
    else:
        kv_ctx = h_ctx @ w_in[:, EV_K0:]
    k_ctx = qk_heads(kv_ctx[..., :EV_QK])
    v_ctx = v_heads(kv_ctx[..., EV_QK:])
    k_all = jnp.concatenate([k_lat, k_ctx], axis=3)
    v_all = jnp.concatenate([v_lat, v_ctx], axis=2)
    nb = length // Q_BLOCK
    q_blocks = jnp.moveaxis(q_lat.reshape(b, DIFF_HEADS, 2, nb, Q_BLOCK, DIFF_DQK), 3, 0)
    o = lax.map(lambda qb: diff_attend(qb, k_all, v_all, lam), q_blocks)
    o = jnp.moveaxis(o, 0, 2).reshape(b, DIFF_HEADS, length, DIFF_DV)
    y_lat = jnp.concatenate([conv_lat, diff_merge(o, subln_g, lambda_init)], axis=-1) @ w_out
    if not ctx_out:
        return y_lat, None
    conv_ctx = conformer_conv(p_ctx[..., :EV_Q0], conv_w, conv_b, ln_g, ln_b)
    o_ctx = diff_attend(qk_heads(p_ctx[..., EV_Q0:EV_K0]), k_ctx, v_ctx, lam)
    y_ctx = jnp.concatenate([conv_ctx, diff_merge(o_ctx, subln_g, lambda_init)], axis=-1) @ w_out
    return y_lat, y_ctx

def hyena_filters(length, w1, b1, freq1, w2, b2, freq2, w3):
    t = jnp.linspace(0.0, 1.0, length, dtype=F32)[:, None]
    bands = (HY_EMB - 1) // 2
    omega = 2.0 * math.pi * jnp.arange(length, dtype=F32)[:, None] / length
    ang = omega * jnp.linspace(1e-4, bands - 1, bands, dtype=F32)
    z = jnp.concatenate([t, jnp.cos(ang), -jnp.sin(ang)], axis=-1)
    hid = jnp.sin(freq1 * (z @ w1 + b1))
    hid = jnp.sin(freq2 * (hid @ w2 + b2))
    filt = (hid @ w3).astype(F32).reshape(length, HY_ORDER, 2, HY_CH)
    deltas = jnp.abs(jnp.linspace(HY_MIN_DECAY, HY_MAX_DECAY, HY_CH, dtype=F32))
    filt = filt * jnp.exp(-t * deltas)[:, None, None, :]
    return filt / jnp.sum(jnp.abs(filt), axis=(0, 2), keepdims=True)

def two_sided(h_fwd, h_bwd):
    return jnp.concatenate([h_fwd, jnp.zeros((1, h_fwd.shape[1]), h_fwd.dtype), h_bwd[:0:-1]], axis=0)

def fft_long_conv(u, filt2, skip):
    length = u.shape[1]
    n = 2 * length
    y = jnp.fft.irfft(jnp.fft.rfft(u, n=n, axis=1) * jnp.fft.rfft(filt2, n=n, axis=0), n=n, axis=1)[:, :length]
    return y + u * skip.astype(F32)

def hyena(p_hy, short_w, short_b, w1, b1, freq1, w2, b2, freq2, w3, skip):
    length = p_hy.shape[1]
    u = depthwise_conv(p_hy, short_w, short_b).astype(F32)
    v, x1, x2 = jnp.split(u, 3, axis=-1)
    filt = hyena_filters(length, w1, b1, freq1, w2, b2, freq2, w3)
    z = v
    for order, gate in enumerate((x1, x2)):
        z = gate * fft_long_conv(z, two_sided(filt[:, order, 0], filt[:, order, 1]), skip[order])
    return z.astype(p_hy.dtype)

def delta_features(p, conv_w, a_log_f, a_log_b, dtb_f, dtb_b, with_q):
    n_qkv = (3 if with_q else 2) * DN_WIDTH
    qkv = jax.nn.silu(depthwise_conv(p[..., :n_qkv], conv_w[:, -n_qkv:])).astype(F32)
    b, l = qkv.shape[:2]
    parts = [t.reshape(b, l, DN_HEADS, -1).transpose(0, 2, 1, 3) for t in jnp.split(qkv, n_qkv // DN_WIDTH, axis=-1)]
    if with_q:
        q, k, v = parts
        q = l2norm(q)
    else:
        k, v = parts
        q = None
    k = l2norm(k)
    rest = p[..., n_qkv:].astype(F32).transpose(0, 2, 1)
    h = DN_HEADS
    beta_f = jax.nn.sigmoid(rest[:, 0:h])
    beta_b = jax.nn.sigmoid(rest[:, h:2 * h])
    g_f = -jnp.exp(a_log_f.astype(F32))[None, :, None] * jax.nn.softplus(rest[:, 2 * h:3 * h] + dtb_f.astype(F32)[None, :, None])
    g_b = -jnp.exp(a_log_b.astype(F32))[None, :, None] * jax.nn.softplus(rest[:, 3 * h:4 * h] + dtb_b.astype(F32)[None, :, None])
    return q, k, v, beta_f, beta_b, g_f, g_b

def gated_delta_chunked(q, k, v, beta, g, state):
    b, h, length, dk = k.shape
    n = length // DN_CHUNK
    chunk = lambda t: t.reshape(b, h, n, DN_CHUNK, *t.shape[3:])
    k, v, beta, g = chunk(k), chunk(v), chunk(beta), chunk(g)
    gcum = jnp.cumsum(g, axis=-1)
    pos = jnp.arange(DN_CHUNK)
    incl = pos[:, None] >= pos[None, :]
    strict = pos[:, None] > pos[None, :]
    decay = jnp.exp(jnp.where(incl, gcum[..., :, None] - gcum[..., None, :], -jnp.inf))
    kb = k * beta[..., None]
    lower = jnp.where(strict, jnp.einsum('bhncd,bhnsd->bhncs', kb, k) * decay, 0.0)
    eye = jnp.eye(DN_CHUNK, dtype=F32)
    tmat = lax.linalg.triangular_solve(eye + lower, jnp.broadcast_to(eye, lower.shape),
                                       left_side=True, lower=True, unit_diagonal=True)
    u = tmat @ (v * beta[..., None])
    w = tmat @ (kb * jnp.exp(gcum)[..., None])
    g_last = gcum[..., -1]
    k_dec = k * jnp.exp(g_last[..., None] - gcum)[..., None]
    front = lambda t: jnp.moveaxis(t, 2, 0)
    if q is None:
        def step_state(s, xs):
            u_c, w_c, kd_c, gl_c = xs
            v_new = u_c - w_c @ s
            return s * jnp.exp(gl_c)[..., None, None] + jnp.swapaxes(kd_c, -1, -2) @ v_new, None
        state, _ = lax.scan(step_state, state, (front(u), front(w), front(k_dec), front(g_last)))
        return None, state
    q = chunk(q) * (dk ** -0.5)
    attn = jnp.einsum('bhncd,bhnsd->bhncs', q, k) * decay
    q_dec = q * jnp.exp(gcum)[..., None]

    def step(s, xs):
        u_c, w_c, kd_c, gl_c, a_c, qd_c = xs
        v_new = u_c - w_c @ s
        o = qd_c @ s + a_c @ v_new
        return s * jnp.exp(gl_c)[..., None, None] + jnp.swapaxes(kd_c, -1, -2) @ v_new, o
    state, o = lax.scan(step, state, (front(u), front(w), front(k_dec), front(g_last), front(attn), front(q_dec)))
    o = jnp.moveaxis(o, 0, 2).reshape(b, h, length, -1)
    return o, state

def flip_seq(t):
    return None if t is None else jnp.flip(t, axis=2)

def delta_output(o, gate, norm_g):
    b, h, l, dv = o.shape
    o = rms_norm(o.transpose(0, 2, 1, 3), norm_g)
    return (o * jax.nn.silu(gate.reshape(b, l, h, dv).astype(F32))).reshape(b, l, h * dv).astype(gate.dtype)

def odd_mixer(h_lat, h_ctx, w_in, hy_short_w, hy_short_b, hy_w1, hy_b1, hy_freq1, hy_w2, hy_b2, hy_freq2, hy_w3,
              hy_skip, dn_conv_w, a_log_f, a_log_b, dtb_f, dtb_b, dn_norm_g, w_out, ctx_out):
    hy_args = (hy_short_w, hy_short_b, hy_w1, hy_b1, hy_freq1, hy_w2, hy_b2, hy_freq2, hy_w3, hy_skip)
    dn_args = (a_log_f, a_log_b, dtb_f, dtb_b)
    p_lat = h_lat @ w_in
    hy_lat = hyena(p_lat[..., :HY_IN], *hy_args)
    q_l, k_l, v_l, bf_l, bb_l, gf_l, gb_l = delta_features(p_lat[..., OD_Q0:], dn_conv_w, *dn_args, True)
    if ctx_out:
        p_ctx = h_ctx @ w_in
        feats_ctx = delta_features(p_ctx[..., OD_Q0:], dn_conv_w, *dn_args, True)
    else:
        feats_ctx = delta_features(h_ctx @ w_in[:, OD_K0:], dn_conv_w, *dn_args, False)
    q_c, k_c, v_c, bf_c, bb_c, gf_c, gb_c = feats_ctx
    s0 = jnp.zeros((h_lat.shape[0], DN_HEADS, DN_DK, DN_DV), F32)
    o_cf, s_cf = gated_delta_chunked(q_c, k_c, v_c, bf_c, gf_c, s0)
    o_cb, s_cb = gated_delta_chunked(flip_seq(q_c), flip_seq(k_c), flip_seq(v_c), flip_seq(bb_c), flip_seq(gb_c), s0)
    o_lf, _ = gated_delta_chunked(q_l, k_l, v_l, bf_l, gf_l, s_cf)
    o_lb, _ = gated_delta_chunked(flip_seq(q_l), flip_seq(k_l), flip_seq(v_l), flip_seq(bb_l), flip_seq(gb_l), s_cb)
    dn_lat = delta_output(o_lf + flip_seq(o_lb), p_lat[..., OD_G0:OD_Q0], dn_norm_g)
    y_lat = jnp.concatenate([hy_lat, dn_lat], axis=-1) @ w_out
    if not ctx_out:
        return y_lat, None
    hy_ctx = hyena(p_ctx[..., :HY_IN], *hy_args)
    dn_ctx = delta_output(o_cf + flip_seq(o_cb), p_ctx[..., OD_G0:OD_Q0], dn_norm_g)
    y_ctx = jnp.concatenate([hy_ctx, dn_ctx], axis=-1) @ w_out
    return y_lat, y_ctx

def second_inputs(seed: int = 0) -> dict:
    key = jax.random.key(seed)
    ks = list(jax.random.split(key, 48))
    nrm = lambda shape, scale: scale * jax.random.normal(ks.pop(), shape, F32)
    gain = lambda shape: 1.0 + 0.05 * jax.random.normal(ks.pop(), shape, F32)
    d = D_MODEL
    a_log = lambda: jnp.log(jax.random.uniform(ks.pop(), (N_ODD, DN_HEADS), F32, 1.0, 16.0))

    def dt_bias():
        dt = jnp.exp(jax.random.uniform(ks.pop(), (N_ODD, DN_HEADS), F32, math.log(1e-3), math.log(1e-1)))
        return dt + jnp.log(-jnp.expm1(-dt))
    return {
        'x': nrm((BATCH, SEQ, d), 1.0),
        'c': nrm((BATCH, d), 1.0),
        'ctx': nrm((BATCH, CTX_LEN, d), 1.0),
        'c_ctx': nrm((d,), 1.0),
        'ada_w': nrm((DEPTH, d, N_MOD * d), 0.5 * d ** -0.5),
        'ada_b': nrm((DEPTH, N_MOD * d), 0.02),
        'norm1_g': gain((DEPTH, d)),
        'norm2_g': gain((DEPTH, d)),
        'mlp_w1': nrm((DEPTH, d, MLP_HIDDEN), d ** -0.5),
        'mlp_w2': nrm((DEPTH, MLP_HIDDEN, d), MLP_HIDDEN ** -0.5),
        'ev_w_in': nrm((N_EVEN, d, EVEN_IN), d ** -0.5),
        'ev_conv_w': nrm((N_EVEN, CONV_W, CONV_CH), CONV_W ** -0.5),
        'ev_conv_b': nrm((N_EVEN, CONV_CH), 0.02),
        'ev_ln_g': gain((N_EVEN, CONV_CH)),
        'ev_ln_b': nrm((N_EVEN, CONV_CH), 0.02),
        'ev_lq1': nrm((N_EVEN, DIFF_DQK), 0.1),
        'ev_lk1': nrm((N_EVEN, DIFF_DQK), 0.1),
        'ev_lq2': nrm((N_EVEN, DIFF_DQK), 0.1),
        'ev_lk2': nrm((N_EVEN, DIFF_DQK), 0.1),
        'ev_subln_g': gain((N_EVEN, DIFF_DV)),
        'ev_w_out': nrm((N_EVEN, EVEN_MIX, d), EVEN_MIX ** -0.5),
        'od_w_in': nrm((N_ODD, d, ODD_IN), d ** -0.5),
        'od_hy_short_w': nrm((N_ODD, HY_SHORT_W, HY_IN), HY_SHORT_W ** -0.5),
        'od_hy_short_b': nrm((N_ODD, HY_IN), 0.02),
        'od_hy_w1': nrm((N_ODD, HY_EMB, HY_FFN), HY_EMB ** -0.5),
        'od_hy_b1': nrm((N_ODD, HY_FFN), 0.02),
        'od_hy_freq1': gain((N_ODD, HY_FFN)),
        'od_hy_w2': nrm((N_ODD, HY_FFN, HY_FFN), HY_FFN ** -0.5),
        'od_hy_b2': nrm((N_ODD, HY_FFN), 0.02),
        'od_hy_freq2': gain((N_ODD, HY_FFN)),
        'od_hy_w3': nrm((N_ODD, HY_FFN, HY_ORDER * 2 * HY_CH), HY_FFN ** -0.5),
        'od_hy_skip': nrm((N_ODD, HY_ORDER, HY_CH), 0.5),
        'od_dn_conv_w': nrm((N_ODD, DN_CONV_W, 3 * DN_WIDTH), DN_CONV_W ** -0.5),
        'od_dn_alog_f': a_log(),
        'od_dn_alog_b': a_log(),
        'od_dn_dtb_f': dt_bias(),
        'od_dn_dtb_b': dt_bias(),
        'od_dn_norm_g': gain((N_ODD, DN_DV)),
        'od_w_out': nrm((N_ODD, ODD_MIX, d), ODD_MIX ** -0.5),
        'final_g': gain((d,)),
    }

def second_block(x, c, ctx, c_ctx, ada_w, ada_b, norm1_g, norm2_g, mlp_w1, mlp_w2,
              ev_w_in, ev_conv_w, ev_conv_b, ev_ln_g, ev_ln_b, ev_lq1, ev_lk1, ev_lq2, ev_lk2, ev_subln_g, ev_w_out,
              od_w_in, od_hy_short_w, od_hy_short_b, od_hy_w1, od_hy_b1, od_hy_freq1, od_hy_w2, od_hy_b2, od_hy_freq2,
              od_hy_w3, od_hy_skip, od_dn_conv_w, od_dn_alog_f, od_dn_alog_b, od_dn_dtb_f, od_dn_dtb_b, od_dn_norm_g,
              od_w_out, final_g):
    rope = axial_rope_tables(x.shape[1])
    cond_lat = jax.nn.silu(c)
    cond_ctx = jax.nn.silu(c_ctx)
    for i in range(DEPTH):
        last = i == DEPTH - 1
        mods = jnp.split(cond_lat @ ada_w[i] + ada_b[i], N_MOD, axis=-1)
        sh1, sc1, gt1, sh2, sc2, gt2 = [m[:, None, :] for m in mods]
        n_ctx_mod = 2 if last else N_MOD
        mods_c = jnp.split(cond_ctx @ ada_w[i][:, :n_ctx_mod * D_MODEL] + ada_b[i][:n_ctx_mod * D_MODEL], n_ctx_mod)
        h_lat = modulate(rms_norm(x, norm1_g[i]), sh1, sc1)
        h_ctx = modulate(rms_norm(ctx, norm1_g[i]), mods_c[0], mods_c[1])
        j = i // 2
        if i % 2 == 0:
            y_lat, y_ctx = even_mixer(h_lat, h_ctx, rope, ev_w_in[j], ev_conv_w[j], ev_conv_b[j], ev_ln_g[j], ev_ln_b[j],
                                      ev_lq1[j], ev_lk1[j], ev_lq2[j], ev_lk2[j], ev_subln_g[j], ev_w_out[j],
                                      0.8 - 0.6 * math.exp(-0.3 * i), not last)
        else:
            y_lat, y_ctx = odd_mixer(h_lat, h_ctx, od_w_in[j], od_hy_short_w[j], od_hy_short_b[j], od_hy_w1[j],
                                     od_hy_b1[j], od_hy_freq1[j], od_hy_w2[j], od_hy_b2[j], od_hy_freq2[j], od_hy_w3[j],
                                     od_hy_skip[j], od_dn_conv_w[j], od_dn_alog_f[j], od_dn_alog_b[j], od_dn_dtb_f[j],
                                     od_dn_dtb_b[j], od_dn_norm_g[j], od_w_out[j], not last)
        x = x + gt1 * y_lat
        x = x + gt2 * squared_relu_mlp(modulate(rms_norm(x, norm2_g[i]), sh2, sc2), mlp_w1[i], mlp_w2[i])
        if not last:
            ctx = ctx + mods_c[2] * y_ctx
            ctx = ctx + mods_c[5] * squared_relu_mlp(modulate(rms_norm(ctx, norm2_g[i]), mods_c[3], mods_c[4]),
                                                     mlp_w1[i], mlp_w2[i])
    return rms_norm(x, final_g)


def setup_inputs(seed=0):
    out = dict(first_inputs(seed))
    for name, value in second_inputs(seed + 1).items():
        if name != "x":
            out[name + "_2"] = value
    return out


def reference(
    x, ffn1_norm, ffn1_w_gu, ffn1_w_down, mix_norm, w_in, b_gate, gmlp_ln_g, gmlp_ln_b,
    gmlp_w_s, gmlp_b_s, w_pa, w_pb, w_out, ffn2_norm, ffn2_w_gu, ffn2_w_down, final_norm, c_2,
    ctx_2, c_ctx_2, ada_w_2, ada_b_2, norm1_g_2, norm2_g_2, mlp_w1_2, mlp_w2_2, ev_w_in_2,
    ev_conv_w_2, ev_conv_b_2, ev_ln_g_2, ev_ln_b_2, ev_lq1_2, ev_lk1_2, ev_lq2_2, ev_lk2_2,
    ev_subln_g_2, ev_w_out_2, od_w_in_2, od_hy_short_w_2, od_hy_short_b_2, od_hy_w1_2,
    od_hy_b1_2, od_hy_freq1_2, od_hy_w2_2, od_hy_b2_2, od_hy_freq2_2, od_hy_w3_2, od_hy_skip_2,
    od_dn_conv_w_2, od_dn_alog_f_2, od_dn_alog_b_2, od_dn_dtb_f_2, od_dn_dtb_b_2,
    od_dn_norm_g_2, od_w_out_2, final_g_2,
):
    x = first_block(
        x, ffn1_norm, ffn1_w_gu, ffn1_w_down, mix_norm, w_in, b_gate, gmlp_ln_g, gmlp_ln_b,
        gmlp_w_s, gmlp_b_s, w_pa, w_pb, w_out, ffn2_norm, ffn2_w_gu, ffn2_w_down, final_norm,
    )
    return second_block(
        x, c_2, ctx_2, c_ctx_2, ada_w_2, ada_b_2, norm1_g_2, norm2_g_2, mlp_w1_2, mlp_w2_2,
        ev_w_in_2, ev_conv_w_2, ev_conv_b_2, ev_ln_g_2, ev_ln_b_2, ev_lq1_2, ev_lk1_2, ev_lq2_2,
        ev_lk2_2, ev_subln_g_2, ev_w_out_2, od_w_in_2, od_hy_short_w_2, od_hy_short_b_2,
        od_hy_w1_2, od_hy_b1_2, od_hy_freq1_2, od_hy_w2_2, od_hy_b2_2, od_hy_freq2_2,
        od_hy_w3_2, od_hy_skip_2, od_dn_conv_w_2, od_dn_alog_f_2, od_dn_alog_b_2, od_dn_dtb_f_2,
        od_dn_dtb_b_2, od_dn_norm_g_2, od_w_out_2, final_g_2,
    )


_drawn_inputs = setup_inputs


def setup_inputs(seed=0):
    import zlib

    import numpy as np

    out = dict(_drawn_inputs(seed))
    spreads = {}
    factors = {'b_gate': 8.0,
     'gmlp_ln_g': 5.067,
     'gmlp_ln_b': 8.0,
     'norm1_g_2': 3.652,
     'ev_conv_b_2': 8.0,
     'ev_ln_g_2': 7.392,
     'ev_ln_b_2': 8.0,
     'ev_lq1_2': 6.914,
     'ev_lk1_2': 8.0,
     'ev_lq2_2': 8.0,
     'ev_lk2_2': 8.0,
     'ev_subln_g_2': 6.493,
     'od_hy_short_b_2': 8.0,
     'od_hy_b1_2': 8.0,
     'od_hy_freq1_2': 8.0,
     'od_hy_b2_2': 8.0,
     'od_hy_freq2_2': 8.0,
     'od_dn_alog_f_2': 8.0,
     'od_dn_dtb_f_2': 7.927,
     'od_dn_dtb_b_2': 3.701,
     'od_dn_norm_g_2': 7.498}
    for name, (base, spread) in spreads.items():
        noise = np.random.default_rng([zlib.crc32(name.encode()), seed]).standard_normal(out[name].shape)
        drawn = base * np.exp(spread * noise) if base else spread * noise
        out[name] = jnp.asarray(drawn.astype(out[name].dtype))
    for name, factor in factors.items():
        out[name] = (out[name] * factor).astype(out[name].dtype)
    return out
```

```python
import math
from contextlib import ExitStack, contextmanager

import numpy as np

import concourse.bass as bass
from concourse import mybir

F32 = mybir.dt.float32
ACT = mybir.ActivationFunctionType
ALU = mybir.AluOpType
AX = mybir.AxisListType.X

P = 128
D = 1024
DK = D // P
SEQ = 256
TT = SEQ // P
DEPTH = 2
EPS = 1e-6
BANK = 512

FF = 2816
FK = FF // P
GU = FF // 256
DN = -(-FK // 4)
HEADS, HD = 8, 64
CH = 512
SMALL = 72
TOPK = 64
IDX_SCALE = (64 ** -0.5) * (8 ** -0.5)
ATT_SCALE = 64 ** -0.5
MASKED = -1.0e30
TAKEN = -3.0e38

RING = 4
PANEL = 4096
L1_PANELS = GU + DN + 10 + 4 + GU + DN
assert L1_PANELS % RING == 0
AT_FFN1 = 0
AT_PROJ = GU + DN
AT_FFN2 = AT_PROJ + 14

C_FFN1, C_MIX, C_FFN2, C_BS = 0, 8, 16, 24
C_WS = 28
C_SMALL = C_WS + 4 * P
C_END = C_SMALL + DK * SMALL
R_BGATE, R_LNG, R_LNB, R_END = 0, 2 * D, 2 * D + CH, 2 * D + 2 * CH

K_ID = 0
K_UPPER = K_ID + P
K_CAUSAL = K_UPPER + P
K_COS = K_CAUSAL + TT * SEQ
K_SIN = K_COS + TT * HD
K_END1 = K_SIN + TT * HD


@contextmanager
def stage(nc, *names):
    with ExitStack() as ctx:
        sems = [ctx.enter_context(nc.semaphore(n)) for n in names]
        with nc.Block(no_gpsimd_drain=True) as block:
            yield (block, *sems)
        nums = [s.num for s in sems]
        nc.sync.sem_clear(range(min(nums), max(nums) + 1))
        nc.all_engine_barrier(sem_only=True)


class Panels:

    def __init__(self, c, layer, per_layer, first, total):
        self.c, self.layer, self.per, self.first, self.total = c, layer, per_layer, first, total

    def _base(self, unit):
        b = (self.first // RING) * unit
        return b if self.layer is None else self.layer * (self.per // RING * unit) + b

    def landed(self, eng, m):
        slot = m % RING
        eng.wait_ge(self.c.landed[slot], self._base(16) + 16 * (m // RING + 1))
        return self.c.ring[:, slot]

    def refill(self, sp, m):
        at = self.first + m + RING
        if self.layer is None and at >= self.total:
            return
        src = self.c.panels[at] if self.layer is None else self.c.panels[self.layer * self.per + at]
        sp.dma_start(self.c.ring[:, m % RING], src).then_inc(self.c.landed[m % RING], 16)


def mm(nc, out, lhsT, rhs, start, stop):
    return nc.tensor.matmul(out, lhsT, rhs, start=start, stop=stop)


def norm_stage(nc, c, tiles, scale, shift=None):
    n = len(tiles)
    with stage(nc, "squares", "mean_sq", "root", "inv_root", "normed", "turned", "cols") as (
            block, squares, mean_sq, root, inv_root, normed, turned, cols):
        ps = c.ps[:, :, :].rearrange("p b n -> p (b n)").rearrange("p (k t) -> p k t", k=DK)

        def cols_of(t):
            return ps[:, :, t * P:(t + 1) * P] if n == 4 else \
                c.ps[:, 0:4, :].rearrange("p b (k t) -> p (b k) t", k=2)[:, :, t * P:(t + 1) * P]

        def cols_all(k):
            return ps[:, k, :] if n == 4 else c.ps[:, k // 2, (k % 2) * 256:(k % 2) * 256 + 256]

        @block.scalar
        def _(act):
            for i, t in enumerate(tiles):
                nc.scalar.activation(c.junk[:, :], c.x[:, t], ACT.Square,
                                     accum_out=c.stat[:, i:i + 1]).then_inc(squares, 1)
                act.wait_ge(squares, i + 1)
            act.wait_ge(mean_sq, 1)
            nc.scalar.activation(c.stat[:, 8:8 + n], c.stat[:, 4:4 + n], ACT.Sqrt).then_inc(root, 1)
            act.wait_ge(turned, n)
            for k in (1, 3, 5, 7) if n == 4 else (2, 3, 6, 7):
                for st in range(n // TT):
                    tok = slice(st * SEQ, (st + 1) * SEQ)
                    nc.scalar.activation(c.hT[:, k, tok], cols_all(k)[:, tok], ACT.Identity, scale=scale(k, st),
                                         bias=shift(k, st) if shift else 0.0).then_inc(cols, 1)

        @block.vector
        def _(dve):
            dve.wait_ge(squares, n)
            nc.vector.tensor_scalar(c.stat[:, 4:4 + n], c.stat[:, 0:n], 1.0 / D, EPS,
                                    ALU.mult, ALU.add).then_inc(mean_sq, 1)
            dve.wait_ge(root, 1)
            nc.vector.reciprocal(c.stat[:, 12:12 + n], c.stat[:, 8:8 + n]).then_inc(inv_root, 1)
            dve.wait_ge(inv_root, 1)
            for i, t in enumerate(tiles):
                nc.vector.tensor_scalar(c.tok[:, i], c.x[:, t], c.stat[:, 12 + i:13 + i], None,
                                        ALU.mult).then_inc(normed, 1)
            dve.wait_ge(turned, n)
            for k in (0, 2, 4, 6) if n == 4 else (0, 1, 4, 5):
                for st in range(n // TT):
                    tok = slice(st * SEQ, (st + 1) * SEQ)
                    nc.vector.tensor_scalar(c.hT[:, k, tok], cols_all(k)[:, tok], scale(k, st),
                                            shift(k, st) if shift else None, ALU.mult,
                                            ALU.add if shift else ALU.bypass).then_inc(cols, 1)

        @block.tensor
        def _(pe):
            for i in range(n):
                pe.wait_ge(normed, i + 1)
                dst = cols_of(i)
                for k in range(DK):
                    last = nc.tensor.transpose(dst[:, k], c.tok[:, i, k * P:(k + 1) * P], c.ident)
                last.then_inc(turned, 1)


def ffn_stage(nc, c, w, m0):
    with stage(nc, "gate_ready", "up_ready", "silu_ready", "hidden", "down_ready", "added") as (
            block, gate_ready, up_ready, silu_ready, hidden, down_ready, added):

        @block.sync
        def _(sp):
            for i in range(GU):
                sp.wait_ge(up_ready, i + 1)
                w.refill(sp, m0 + i)
            for i in range(DN):
                sp.wait_ge(down_ready, i + 1)
                w.refill(sp, m0 + GU + i)

        @block.tensor
        def _(pe):
            for i in range(GU):
                wt = w.landed(pe, m0 + i).rearrange("p (k n) -> p k n", k=DK)
                if i >= 2:
                    pe.wait_ge(hidden, i - 1)
                for part, ready in ((0, gate_ready), (1, up_ready)):
                    for f in range(2):
                        for k in range(DK):
                            last = mm(nc, c.ps[:, 2 * (i % 2) + part, f * 256:(f + 1) * 256],
                                      wt[:, k, (2 * part + f) * P:(2 * part + f + 1) * P], c.hT[:, k, 0:SEQ],
                                      k == 0, k == DK - 1)
                    last.then_inc(ready, 1)
            for i in range(DN):
                wt = w.landed(pe, m0 + GU + i).rearrange("p (k n) -> p k n", k=4)
                for kk in range(min(4, FK - 4 * i)):
                    k = 4 * i + kk
                    if k % 2 == 0:
                        pe.wait_ge(hidden, k // 2 + 1)
                    for t in range(TT):
                        for n in range(2):
                            last = mm(nc, c.ps[:, 4 + 2 * t + n], c.hid[:, k, t * P:(t + 1) * P],
                                      wt[:, kk, n * BANK:(n + 1) * BANK], k == 0, k == FK - 1)
                last.then_inc(down_ready, 1)

        @block.scalar
        def _(act):
            for i in range(GU):
                act.wait_ge(gate_ready, i + 1)
                if i >= 2:
                    act.wait_ge(hidden, i - 1)
                nc.scalar.activation(c.tok[:, i % 2, 0:BANK], c.ps[:, 2 * (i % 2)], ACT.Silu).then_inc(silu_ready, 1)

        @block.vector
        def _(dve):
            for i in range(GU):
                dve.wait_ge(silu_ready, i + 1)
                dve.wait_ge(up_ready, i + 1)
                nc.vector.tensor_tensor(c.hid[:, 2 * i:2 * i + 2, :].rearrange("p k t -> p (k t)"),
                                        c.ps[:, 2 * (i % 2) + 1], c.tok[:, i % 2, 0:BANK], ALU.mult).then_inc(hidden, 1)
            dve.wait_ge(down_ready, DN)
            for t in range(TT):
                for n in range(2):
                    xs = c.x[:, t, n * BANK:(n + 1) * BANK]
                    nc.vector.scalar_tensor_tensor(out=xs, in0=c.ps[:, 4 + 2 * t + n], scalar=0.5, in1=xs,
                                                   op0=ALU.mult, op1=ALU.add).then_inc(added, 1)


def mixer1_stage(nc, c, w, m0):
    Q, K, QI, V, U, VA, GATES, PA, PB, WO = 0, 1, 2, 3, 4, 5, 6, 10, 11, 12
    UNITS = [(qb, h) for qb in range(TT) for h in (0, 1, 4, 5)]
    names = ["proj", "proj_read", "small_ready", "small_read", "rope_step", "roped", "kiroped", "q_turned", "q_cols",
             "logits", "relu_done", "score_step", "selected", "s_ready", "s_masked", "negmax", "exp_done", "p_turned",
             "p_cols", "pv", "o_norm", "o_step", "o_turned", "o_cols", "u_gelu", "v_gelu", "ln_step", "v_mean", "v_root",
             "v_norm", "ws_masked", "mixed", "ya", "ya_turned", "ya_cols", "gate_sum", "gate", "pa", "ma", "pb",
             "m_done", "m_turned", "m_cols", "out_ready", "added"]
    with stage(nc, *names) as (block, *sems):
        s = dict(zip(names, sems))
        proj, proj_read = s["proj"], s["proj_read"]
        q, k, qi, v = (c.work[:, a * 1024:(a + 1) * 1024].rearrange("p (t n) -> p t n", t=TT) for a in range(4))
        u, va = (c.work[:, a * 1024:(a + 1) * 1024].rearrange("p (t n) -> p t n", t=TT) for a in (4, 5))
        qT, kT, qiT, yaT = (c.work[:, a * 1024:(a + 1) * 1024].rearrange("p (k t) -> p k t", k=4) for a in (6, 7, 8, 9))
        oT = qiT
        gates = c.work[:, 10 * 1024:14 * 1024].rearrange("p (g t n) -> p g t n", g=2, t=TT)
        o = q
        m = c.work[:, 6 * 1024:8 * 1024].rearrange("p (t n) -> p t n", t=TT)
        mT = c.work[:, 4 * 1024:6 * 1024].rearrange("p (k t) -> p k t", k=DK)
        kiT = c.work[:, 14 * 1024:14 * 1024 + SEQ]
        ki = c.work[:, 14 * 1024 + 256:14 * 1024 + 512].rearrange("p (t a n) -> p t a n", t=TT, a=2)
        wi = c.work[:, 14 * 1024 + 512:14 * 1024 + 528].rearrange("p (t n) -> p t n", t=TT)
        top = c.work[:, 14 * 1024 + 528:14 * 1024 + 536]
        negm = c.work[:, 14 * 1024 + 544:14 * 1024 + 560]
        sums = c.work[:, 14 * 1024 + 560:14 * 1024 + 576]
        rsum = c.work[:, 14 * 1024 + 576:14 * 1024 + 592]
        bn = c.work[:, 14 * 1024 + 592:14 * 1024 + 604].rearrange("p (t n) -> p t n", t=TT)
        mv = c.work[:, 14 * 1024 + 604:14 * 1024 + 608].rearrange("p (t n) -> p t n", t=TT)
        vstd = c.work[:, 14 * 1024 + 608:14 * 1024 + 616]
        mxs = c.work[:, 14 * 1024 + 616:14 * 1024 + 632]
        score = c.work[:, 15 * 1024:15 * 1024 + 512].rearrange("p (t n) -> p t n", t=TT)
        bias = c.work[:, 15 * 1024 + 512:16 * 1024].rearrange("p (t n) -> p t n", t=TT)
        relu = c.tok[:, 0:2, :].rearrange("p a b -> p (a b)")
        ropes = c.tok[:, 2:4, :].rearrange("p a b -> p (a b)")
        sm = c.tok[:, 2, :].rearrange("p (a n) -> p a n", a=2)
        prob = c.tok[:, 0, :].rearrange("p (a n) -> p a n", a=2)
        probT = c.tok[:, 1, :].rearrange("p (a n) -> p a n", a=2)
        ws = c.lay[:, C_WS:C_WS + 4 * P].rearrange("p (g t) -> p g t", g=4)
        small_w = c.lay[:, C_SMALL:C_END].rearrange("p (k n) -> p k n", k=DK)
        cos = c.const[:, K_COS:K_SIN].rearrange("p (t n) -> p t n", t=TT)
        sin = c.const[:, K_SIN:K_END1].rearrange("p (t n) -> p t n", t=TT)
        causal = c.const[:, K_CAUSAL:K_COS].rearrange("p (t n) -> p t n", t=TT)

        @block.sync
        def _(sp):
            for i in range(PA):
                sp.wait_ge(proj, 2 * i + 2)
                w.refill(sp, m0 + i)
            for done, value, i in ((s["pa"], 2, PA), (s["pb"], 2, PB), (s["out_ready"], 1, WO), (s["out_ready"], 2, WO + 1)):
                sp.wait_ge(done, value)
                w.refill(sp, m0 + i)

        @block.tensor
        def _(pe):
            def panel_tile(i, t):
                wt = w.landed(pe, m0 + i).rearrange("p (k n) -> p k n", k=DK) if t == 0 else \
                    c.ring[:, (m0 + i) % RING].rearrange("p (k n) -> p k n", k=DK)
                if i >= 2:
                    pe.wait_ge(proj_read, 2 * (i - 2) + t + 1)
                for kk in range(DK):
                    last = mm(nc, c.ps[:, 2 * (i % 2) + t], c.hT[:, kk, t * P:(t + 1) * P], wt[:, kk, :],
                              kk == 0, kk == DK - 1)
                last.then_inc(proj, 1)

            def turn(src, n_turn):
                for b in range(4):
                    for t in range(TT):
                        last = nc.tensor.transpose(c.ps[:, 4 + b // 2, (b % 2) * 256 + t * P:(b % 2) * 256 + (t + 1) * P],
                                                   src[:, t, b * P:(b + 1) * P], c.ident)
                last.then_inc(s["q_turned"], 1)

            for t in range(TT):
                for kk in range(DK):
                    last = mm(nc, c.ps[:, 6, t * P:t * P + SMALL], c.hT[:, kk, t * P:(t + 1) * P], small_w[:, kk, :],
                              kk == 0, kk == DK - 1)
            last.then_inc(s["small_ready"], 1)
            for t in range(TT):
                panel_tile(Q, t)
            for t in range(TT):
                panel_tile(K, t)
            pe.wait_ge(s["roped"], 1)
            turn(q, 0)
            for t in range(TT):
                panel_tile(QI, t)
            pe.wait_ge(s["roped"], 2)
            pe.wait_ge(s["q_cols"], 1)
            turn(k, 1)
            for t in range(TT):
                panel_tile(V, t)
            pe.wait_ge(s["roped"], 3)
            pe.wait_ge(s["q_cols"], 2)
            turn(qi, 2)
            pe.wait_ge(s["kiroped"], 1)
            for t in range(TT):
                last = nc.tensor.transpose(c.ps[:, 7, t * P:(t + 1) * P], ki[:, t].rearrange("p a n -> p (a n)"), c.ident)
            last.then_inc(s["q_turned"], 1)
            for t in range(TT):
                panel_tile(U, t)
            pe.wait_ge(s["q_cols"], 4)
            n = 0
            for qb in range(TT):
                keys = (qb + 1) * P
                for half in range(2):
                    if n >= 2:
                        pe.wait_ge(s["relu_done"], n - 1)
                    for hh in range(4):
                        h = 4 * half + hh
                        hp = slice(64 * (h % 2), 64 * (h % 2) + 64)
                        last = mm(nc, c.ps[:, 4 + 2 * (n % 2) + hh % 2, (hh // 2) * 256:(hh // 2) * 256 + keys],
                                  qiT[hp, h // 2, qb * P:(qb + 1) * P], kiT[hp, 0:keys], True, True)
                    last.then_inc(s["logits"], 1)
                    n += 1
            for t in range(TT):
                panel_tile(VA, t)

            def scores(j):
                qb, h0 = UNITS[j]
                keys = (qb + 1) * P
                if j == 0:
                    pe.wait_ge(s["relu_done"], 4)
                if j >= 1:
                    pe.wait_ge(s["s_masked"], j)
                for e in range(2):
                    h = h0 + 2 * e
                    hp = slice(64 * (h % 2), 64 * (h % 2) + 64)
                    last = mm(nc, c.ps[:, 4, e * keys:(e + 1) * keys], qT[hp, h // 2, qb * P:(qb + 1) * P],
                              kT[hp, h // 2, 0:keys], True, True)
                last.then_inc(s["s_ready"], 1)

            def turn_probs(j):
                qb, h0 = UNITS[j]
                pe.wait_ge(s["exp_done"], 2 * j + 2)
                if j >= 1:
                    pe.wait_ge(s["p_cols"], j)
                for e in range(2):
                    for kb in range(qb + 1):
                        b = e * (qb + 1) + kb
                        last = nc.tensor.transpose(c.ps[:, 6, b * P:(b + 1) * P], prob[:, j % 2, b * P:(b + 1) * P],
                                                   c.ident)
                last.then_inc(s["p_turned"], 1)

            def weigh(j):
                qb, h0 = UNITS[j]
                pe.wait_ge(s["p_cols"], j + 1)
                if h0 == 0 and qb:
                    pe.wait_ge(s["o_norm"], qb)
                for e in range(2):
                    for kb in range(qb + 1):
                        b = e * (qb + 1) + kb
                        h = h0 + 2 * e
                        last = mm(nc, c.ps[:, 7, h * HD:(h + 1) * HD], probT[:, j % 2, b * P:(b + 1) * P],
                                  v[:, kb, h * HD:(h + 1) * HD], kb == 0, kb == qb)
                last.then_inc(s["pv"], 1)

            def spatial(n):
                if n == 0:
                    pe.wait_ge(s["ws_masked"], 1)
                pe.wait_ge(s["v_norm"], n + 1)
                if n:
                    pe.wait_ge(s["ya"], 4 * n)
                for g in range(4):
                    last = mm(nc, c.ps[:, 5, g * P:(g + 1) * P], ws[:, g, :], va[:, n, g * P:(g + 1) * P], True, True)
                last.then_inc(s["mixed"], 1)

            def turn_ya(n):
                pe.wait_ge(s["ya"], 4 * TT)
                if n:
                    pe.wait_ge(s["ya_cols"], n)
                for g in range(4):
                    last = nc.tensor.transpose(c.ps[:, 5, g * P:(g + 1) * P], u[:, n, g * P:(g + 1) * P], c.ident)
                last.then_inc(s["ya_turned"], 1)

            for j in range(8):
                scores(j)
                panel_tile(GATES + j // 2, j % 2)
                if j >= 1:
                    turn_probs(j - 1)
                if j >= 2:
                    weigh(j - 2)
                if j in (2, 3):
                    spatial(j - 2)
                if j in (5, 6):
                    turn_ya(j - 5)
            wt = w.landed(pe, m0 + PA).rearrange("p (k n) -> p k n", k=4)
            pe.wait_ge(s["ya_cols"], 2)
            pe.wait_ge(proj_read, 20)
            for t in range(TT):
                for kk in range(4):
                    for n in range(2):
                        last = mm(nc, c.ps[:, 2 * t + n], yaT[:, kk, t * P:(t + 1) * P], wt[:, kk, n * BANK:(n + 1) * BANK],
                                  kk == 0, kk == 3)
                last.then_inc(s["pa"], 1)
                if t == 0:
                    turn_probs(7)
                    weigh(6)
            weigh(7)
            pe.wait_ge(s["o_norm"], 2)
            for b in range(4):
                for t in range(TT):
                    last = nc.tensor.transpose(c.ps[:, 4 + b // 2, (b % 2) * 256 + t * P:(b % 2) * 256 + (t + 1) * P],
                                               o[:, t, b * P:(b + 1) * P], c.ident)
            last.then_inc(s["o_turned"], 1)
            wt = w.landed(pe, m0 + PB).rearrange("p (k n) -> p k n", k=4)
            pe.wait_ge(s["o_cols"], 1)
            for t in range(TT):
                for kk in range(4):
                    for n in range(2):
                        last = mm(nc, c.ps[:, 4 + 2 * t + n], oT[:, kk, t * P:(t + 1) * P],
                                  wt[:, kk, n * BANK:(n + 1) * BANK], kk == 0, kk == 3)
                last.then_inc(s["pb"], 1)
            pe.wait_ge(s["ma"], 4)
            for t in range(TT):
                pe.wait_ge(s["m_done"], 2 * t + 2)
                for kk in range(DK):
                    last = nc.tensor.transpose(c.ps[:, kk // 2, (kk % 2) * 256 + t * P:(kk % 2) * 256 + (t + 1) * P],
                                               m[:, t, kk * P:(kk + 1) * P], c.ident)
                last.then_inc(s["m_turned"], 1)
            for half in range(2):
                wt = w.landed(pe, m0 + WO + half).rearrange("p (k n) -> p k n", k=4)
                for kk in range(4):
                    k8 = 4 * half + kk
                    if k8 % 2 == 0:
                        pe.wait_ge(s["m_cols"], k8 // 2 + 1)
                    for t in range(TT):
                        for n in range(2):
                            last = mm(nc, c.ps[:, 4 + 2 * t + n], mT[:, k8, t * P:(t + 1) * P],
                                      wt[:, kk, n * BANK:(n + 1) * BANK], k8 == 0, k8 == DK - 1)
                last.then_inc(s["out_ready"], 1)

        @block.scalar
        def _(act):
            def columns(dst, sem):
                act.wait_ge(s["q_turned"], sem)
                nc.scalar.activation(dst.rearrange("p k t -> p (k t)"), c.ps[:, 4:6, :].rearrange("p b n -> p (b n)"),
                                     ACT.Copy).then_inc(s["q_cols"], 1)

            act.wait_ge(s["kiroped"], 1)
            for t in range(TT):
                nc.scalar.activation(wi[:, t], c.ps[:, 6, t * P + 64:t * P + 72], ACT.Copy,
                                     scale=IDX_SCALE).then_inc(s["small_read"], 1)
            columns(qT, 1)
            columns(kT, 2)
            for t in range(TT):
                act.wait_ge(proj, 2 * V + t + 1)
                act.wait_ge(proj_read, 2 * V + t)
                nc.scalar.activation(v[:, t], c.ps[:, 2 * (V % 2) + t], ACT.Copy).then_inc(proj_read, 1)
            columns(qiT, 3)
            act.wait_ge(s["q_turned"], 4)
            nc.scalar.activation(kiT, c.ps[:, 7, 0:SEQ], ACT.Copy).then_inc(s["q_cols"], 1)
            for t in range(TT):
                act.wait_ge(proj, 2 * U + t + 1)
                nc.scalar.activation(u[:, t], c.ps[:, 2 * (U % 2) + t], ACT.Gelu_apprx_tanh).then_inc(proj_read, 1)
            act.wait_ge(proj_read, 2 * U + 2)
            for n in range(4):
                qb = n // 2
                act.wait_ge(s["logits"], n + 1)
                if n >= 2:
                    act.wait_ge(s["score_step"], 4 * (n - 1))
                keys = (qb + 1) * P
                nc.scalar.activation(
                    relu[:, (n % 2) * 1024:(n % 2 + 1) * 1024].rearrange("p (h n) -> p h n", h=4)[:, :, 0:keys],
                    c.ps[:, 4 + 2 * (n % 2):6 + 2 * (n % 2), :].rearrange("p b (h n) -> p (b h) n", h=2)[:, :, 0:keys],
                    ACT.Relu).then_inc(s["relu_done"], 1)
            for t in range(TT):
                act.wait_ge(proj, 2 * VA + t + 1)
                nc.scalar.activation(va[:, t], c.ps[:, 2 * (VA % 2) + t], ACT.Gelu_apprx_tanh).then_inc(proj_read, 1)
            act.wait_ge(s["v_mean"], 1)
            nc.scalar.activation(vstd[:, 2:4], vstd[:, 0:2], ACT.Sqrt).then_inc(s["v_root"], 1)

            def exps(j):
                qb, h0 = UNITS[j]
                keys = (qb + 1) * P
                act.wait_ge(s["negmax"], j + 1)
                if j >= 2:
                    act.wait_ge(s["p_turned"], j - 1)
                if j == 0:
                    act.wait_ge(s["score_step"], 16)
                for e in range(2):
                    h = 8 * qb + h0 + 2 * e
                    nc.scalar.activation(prob[:, j % 2, e * keys:(e + 1) * keys], sm[:, j % 2, e * keys:(e + 1) * keys],
                                         ACT.Exp, bias=negm[:, h:h + 1],
                                         accum_out=sums[:, h:h + 1]).then_inc(s["exp_done"], 1)

            def prob_columns(j):
                qb, h0 = UNITS[j]
                n = 2 * (qb + 1) * P
                act.wait_ge(s["p_turned"], j + 1)
                if j >= 2:
                    act.wait_ge(s["pv"], j - 1)
                nc.scalar.activation(probT[:, j % 2, 0:n], c.ps[:, 6, 0:n], ACT.Copy).then_inc(s["p_cols"], 1)

            for j in range(8):
                exps(j)
                if j >= 1:
                    prob_columns(j - 1)
                if j in (6, 7):
                    n = j - 6
                    act.wait_ge(s["ya_turned"], n + 1)
                    nc.scalar.activation(yaT[:, :, n * P:(n + 1) * P], c.ps[:, 5, :].rearrange("p (g t) -> p g t", g=4),
                                         ACT.Copy).then_inc(s["ya_cols"], 1)
            prob_columns(7)
            for i in range(4):
                act.wait_ge(s["gate_sum"], 2 * i + 2)
                g = gates[:, i // 2, :, (i % 2) * BANK:(i % 2 + 1) * BANK]
                nc.scalar.activation(g, g, ACT.Sigmoid).then_inc(s["gate"], 1)
            act.wait_ge(s["o_turned"], 1)
            nc.scalar.activation(oT.rearrange("p k t -> p (k t)"), c.ps[:, 4:6, :].rearrange("p b n -> p (b n)"),
                                 ACT.Copy).then_inc(s["o_cols"], 1)
            act.wait_ge(s["m_turned"], 2)
            for b in range(1, 4, 2):
                act.wait_ge(s["m_cols"], b)
                nc.scalar.activation(mT[:, 2 * b:2 * b + 2, :].rearrange("p k t -> p (k t)"), c.ps[:, b],
                                     ACT.Copy).then_inc(s["m_cols"], 1)

        @block.vector
        def _(dve):
            rope_n = [0]

            def rope_tile(src, t, heads, dsts):
                n = heads * HD
                a = ropes[:, 0:n].rearrange("p (h n) -> p h n", h=heads)
                b = ropes[:, 512:512 + n].rearrange("p (h n) -> p h n", h=heads)
                sv = src.rearrange("p (h n) -> p h n", h=heads)
                ct = cos[:, t].unsqueeze(1).broadcast_to([P, heads, HD])
                st = sin[:, t].unsqueeze(1).broadcast_to([P, heads, HD])
                nc.vector.tensor_tensor(a, sv, ct, ALU.mult).then_inc(s["rope_step"], 1)
                nc.vector.tensor_tensor(b[:, :, 0:32], sv[:, :, 32:64], st[:, :, 0:32], ALU.mult).then_inc(s["rope_step"], 1)
                nc.vector.tensor_tensor(b[:, :, 32:64], sv[:, :, 0:32], st[:, :, 32:64], ALU.mult).then_inc(s["rope_step"], 1)
                rope_n[0] += 3
                dve.wait_ge(s["rope_step"], rope_n[0])
                for dst in dsts:
                    nc.vector.tensor_tensor(dst, a, b, ALU.add).then_inc(s["rope_step"], 1)
                    rope_n[0] += 1
                dve.wait_ge(s["rope_step"], rope_n[0])

            nc.vector.tensor_tensor(ws, ws, c.const[:, K_UPPER:K_UPPER + P].unsqueeze(1).broadcast_to([P, 4, P]),
                                    ALU.mult).then_inc(s["ws_masked"], 1)
            dve.wait_ge(s["small_ready"], 1)
            for t in range(TT):
                rope_tile(c.ps[:, 6, t * P:t * P + 64], t, 1, [ki[:, t, e:e + 1, :] for e in range(2)])
            dve.sem_inc(s["kiroped"], 1)
            for i, dst in ((0, q), (1, k), (2, qi)):
                for t in range(TT):
                    dve.wait_ge(proj, 2 * i + t + 1)
                    rope_tile(c.ps[:, 2 * (i % 2) + t], t, HEADS, [dst[:, t].rearrange("p (h n) -> p h n", h=HEADS)])
                    dve.sem_inc(proj_read, 1)
                dve.sem_inc(s["roped"], 1)
            dve.wait_ge(s["small_read"], 2)
            for n in range(4):
                qb = n // 2
                keys = (qb + 1) * P
                dve.wait_ge(s["relu_done"], n + 1)
                for hh in range(4):
                    h = 4 * (n % 2) + hh
                    at = (n % 2) * 1024 + (hh % 2) * 512 + (hh // 2) * 256
                    r = relu[:, at:at + keys]
                    sc = score[:, qb, 0:keys]
                    if h == 0:
                        nc.vector.tensor_scalar(sc, r, wi[:, qb, 0:1], None, ALU.mult).then_inc(s["score_step"], 1)
                    else:
                        dve.wait_ge(s["score_step"], 4 * n + hh)
                        nc.vector.scalar_tensor_tensor(out=sc, in0=r, scalar=wi[:, qb, h:h + 1], in1=sc,
                                                       op0=ALU.mult, op1=ALU.add).then_inc(s["score_step"], 1)
            step = [16]

            def then(ins):
                ins.then_inc(s["score_step"], 1)
                step[0] += 1
                dve.wait_ge(s["score_step"], step[0])

            dve.wait_ge(s["score_step"], 16)
            for qb in range(TT):
                keys = (qb + 1) * P
                sc = score[:, qb, 0:keys]
                bi = bias[:, qb, 0:keys]
                then(nc.vector.tensor_tensor(sc, sc, causal[:, qb, 0:keys], ALU.add))
                for _ in range(TOPK // 8):
                    then(nc.vector.max(top, sc))
                    then(nc.vector.match_replace(sc, top, sc, TAKEN))
                then(nc.vector.tensor_scalar(bi, sc, TAKEN / 2, MASKED, ALU.is_gt, ALU.mult))
                then(nc.vector.tensor_tensor(bi, bi, causal[:, qb, 0:keys], ALU.add))

            def mask(j):
                qb, h0 = UNITS[j]
                keys = (qb + 1) * P
                dve.wait_ge(s["s_ready"], j + 1)
                if j >= 2:
                    dve.wait_ge(s["exp_done"], 2 * (j - 1))
                dst = sm[:, j % 2, 0:2 * keys].rearrange("p (e n) -> p e n", e=2)
                nc.vector.scalar_tensor_tensor(out=dst, in0=c.ps[:, 4, 0:2 * keys].rearrange("p (e n) -> p e n", e=2),
                                               scalar=ATT_SCALE, in1=bias[:, qb, 0:keys].unsqueeze(1).broadcast_to([P, 2, keys]),
                                               op0=ALU.mult, op1=ALU.add).then_inc(s["s_masked"], 1)
                dve.wait_ge(s["s_masked"], j + 1)
                h = 8 * qb + h0
                nc.vector.tensor_reduce(mxs[:, h:h + 3:2], dst, axis=AX, op=ALU.max).then_inc(s["o_step"], 1)
                ostep[0] += 1
                dve.wait_ge(s["o_step"], ostep[0])
                nc.vector.tensor_scalar(negm[:, h:h + 3:2], mxs[:, h:h + 3:2], -1.0, None, ALU.mult).then_inc(s["negmax"], 1)

            ostep = [0]

            def add_gate_bias(i, t):
                dve.wait_ge(proj, 2 * (GATES + i) + t + 1)
                nc.vector.tensor_tensor(gates[:, i // 2, t, (i % 2) * BANK:(i % 2 + 1) * BANK],
                                        c.ps[:, 2 * (i % 2) + t], c.rows[:, R_BGATE + i * BANK:R_BGATE + (i + 1) * BANK],
                                        ALU.add).then_inc(s["gate_sum"], 1)
                dve.wait_ge(s["gate_sum"], 2 * i + t + 1)
                dve.sem_inc(proj_read, 1)

            def norm_out(qb):
                dve.wait_ge(s["pv"], 4 * (qb + 1))
                nc.vector.reciprocal(rsum[:, 8 * qb:8 * qb + 8], sums[:, 8 * qb:8 * qb + 8]).then_inc(s["o_step"], 1)
                ostep[0] += 1
                dve.wait_ge(s["o_step"], ostep[0])
                nc.vector.tensor_tensor(o[:, qb].rearrange("p (h n) -> p h n", h=HEADS),
                                        c.ps[:, 7].rearrange("p (h n) -> p h n", h=HEADS),
                                        rsum[:, 8 * qb:8 * qb + 8].unsqueeze(2).broadcast_to([P, HEADS, HD]),
                                        ALU.mult).then_inc(s["o_norm"], 1)

            ln = [0]

            def ln_then(ins):
                ins.then_inc(s["ln_step"], 1)
                ln[0] += 1
                dve.wait_ge(s["ln_step"], ln[0])

            dve.wait_ge(proj_read, 2 * VA + 2)
            for t in range(TT):
                ln_then(nc.vector.bn_stats(bn[:, t], va[:, t]))
                ln_then(nc.vector.bn_aggr(mv[:, t], bn[:, t]))
            nc.vector.tensor_scalar(vstd[:, 0:2], mv[:, :, 1], EPS, None, ALU.add).then_inc(s["v_mean"], 1)
            dve.wait_ge(s["v_root"], 1)
            ln_then(nc.vector.reciprocal(vstd[:, 4:6], vstd[:, 2:4]))
            for t in range(TT):
                ln_then(nc.vector.tensor_scalar(va[:, t], va[:, t], mv[:, t, 0:1], vstd[:, 4 + t:5 + t],
                                                ALU.subtract, ALU.mult))
                ln_then(nc.vector.tensor_tensor(va[:, t], va[:, t], c.rows[:, R_LNG:R_LNB], ALU.mult))
                nc.vector.tensor_tensor(va[:, t], va[:, t], c.rows[:, R_LNB:R_END], ALU.add).then_inc(s["v_norm"], 1)

            def gate_u(n):
                dve.wait_ge(s["mixed"], n + 1)
                for g in range(4):
                    us = u[:, n, g * P:(g + 1) * P]
                    nc.vector.scalar_tensor_tensor(out=us, in0=c.ps[:, 5, g * P:(g + 1) * P],
                                                   scalar=c.lay[:, C_BS + g:C_BS + g + 1], in1=us,
                                                   op0=ALU.add, op1=ALU.mult).then_inc(s["ya"], 1)

            for j in range(8):
                mask(j)
                add_gate_bias(j // 2, j % 2)
                if j in (2, 3):
                    gate_u(j - 2)
                if j == 6:
                    norm_out(0)
            norm_out(1)
            for t in range(TT):
                dve.wait_ge(s["pa"], t + 1)
                for n in range(2):
                    dve.wait_ge(s["gate"], n + 1)
                    nc.vector.tensor_tensor(m[:, t, n * BANK:(n + 1) * BANK], c.ps[:, 2 * t + n],
                                            gates[:, 0, t, n * BANK:(n + 1) * BANK], ALU.mult).then_inc(s["ma"], 1)
            for t in range(TT):
                dve.wait_ge(s["pb"], t + 1)
                for n in range(2):
                    dve.wait_ge(s["gate"], n + 3)
                    gb = gates[:, 1, t, n * BANK:(n + 1) * BANK]
                    ms = m[:, t, n * BANK:(n + 1) * BANK]
                    ln_then(nc.vector.tensor_tensor(gb, c.ps[:, 4 + 2 * t + n], gb, ALU.mult))
                    nc.vector.tensor_tensor(ms, ms, gb, ALU.add).then_inc(s["m_done"], 1)
            dve.wait_ge(s["m_turned"], 2)
            for b in range(0, 4, 2):
                if b:
                    dve.wait_ge(s["m_cols"], b)
                nc.vector.tensor_copy(mT[:, 2 * b:2 * b + 2, :].rearrange("p k t -> p (k t)"),
                                      c.ps[:, b]).then_inc(s["m_cols"], 1)
            dve.wait_ge(s["out_ready"], 2)
            for t in range(TT):
                for n in range(2):
                    xs = c.x[:, t, n * BANK:(n + 1) * BANK]
                    nc.vector.tensor_tensor(xs, c.ps[:, 4 + 2 * t + n], xs, ALU.add).then_inc(s["added"], 1)
STREAMS = 2
ALL = TT * STREAMS
BOTH = SEQ * STREAMS
MODS = 6
CONV_W = 31
PAD = (CONV_W - 1) // 2
LAMBDA0 = 0.8 - 0.6 * math.exp(-0.3 * 0)
MLP = 4 * D
MK = MLP // P

B_ADA0 = 0
B_EVEN = B_ADA0 + 12
B_MLP0 = B_EVEN + 5 + 2
B_ADA1 = B_MLP0 + 16
B_ODD = B_ADA1 + 12
B_MLP1 = B_ODD + 7 + 2
B_END = B_MLP1 + 16
PANELS = DEPTH * L1_PANELS + B_END

S_COND = 0
S_ADAB = S_COND + DK * 2
S_N1 = S_ADAB + DEPTH * 48
S_N2 = S_N1 + DEPTH * DK
S_CONVW = S_N2 + DEPTH * DK
S_CONVB = S_CONVW + 4 * CONV_W
S_LNG = S_CONVB + 4
S_LNB = S_LNG + 4
S_SUBLN = S_LNB + 4
S_HYSW = S_SUBLN + 1
S_HYSB = S_HYSW + 12 * 3
S_HYSKIP = S_HYSB + 12
S_DNW = S_HYSKIP + 8
S_DNG = S_DNW + 12 * 5
S_FB = S_DNG + 1
S_W1 = S_FB + 4
S_W2 = S_W1 + 64
S_REST = S_W2 + 64
S_END = S_REST + DK * 16

V_ADAG = 0
V_LQK = V_ADAG + DEPTH * 2 * D
V_DN = V_LQK + 4 * 64
V_END = V_DN + 16

K2_COS = 0
K2_SIN = K2_COS + TT * 64
K2_LOWER = K2_SIN + TT * 64
K2_END = K2_LOWER + P


def ada_stage(nc, c, w, m0, layer):
    with stage(nc, "silu_c", "cols_ready", "cols_read", "row_ready", "row_read", "spread", "gates", "scales",
               "bias_in") as (
            block, silu_c, cols_ready, cols_read, row_ready, row_read, spread, gates, scales, bias_in):
        cond = c.par[:, S_COND:S_COND + 2 * DK].rearrange("p (k s) -> p k s", s=2)
        bcol = c.par[:, S_ADAB + 48 * layer:S_ADAB + 48 * layer + 48]
        order = [0, 1, 3, 4]
        brow = c.tok[:, 0:2, :]
        row = c.tok[0:2, 2, :].rearrange("p (a n) -> p a n", a=2)

        @block.sync
        def _(sp):
            sp.dma_start(brow.rearrange("p a n -> p (a n)"),
                         c.vrows[V_ADAG + 2 * D * layer:V_ADAG + 2 * D * (layer + 1)].partition_broadcast(P)).then_inc(bias_in, 16)
            for i in range(8):
                sp.wait_ge(cols_ready, i + 1)
                w.refill(sp, m0 + i)
            for i in range(4):
                sp.wait_ge(row_ready, i + 1)
                w.refill(sp, m0 + 8 + i)

        @block.tensor
        def _(pe):
            pe.wait_ge(silu_c, 1)
            for i in range(8):
                wt = w.landed(pe, m0 + i).rearrange("p (k n) -> p k n", k=DK)
                if i >= 2:
                    pe.wait_ge(cols_read, i - 1)
                for f in range(4):
                    for k in range(DK):
                        last = mm(nc, c.ps[:, i % 2, 2 * f:2 * f + 2], wt[:, k, f * P:(f + 1) * P], c.silu_c[:, k, :],
                                  k == 0, k == DK - 1)
                last.then_inc(cols_ready, 1)

            def spread_row(i):
                pe.wait_ge(row_read, i + 1)
                if i >= 1:
                    pe.wait_ge(gates, 2 * i)
                for s in range(STREAMS):
                    last = mm(nc, c.ps[:, 4 + s], c.ident[0:2, s:s + 1].broadcast_to([2, P]), row[:, i % 2, :],
                              True, True)
                last.then_inc(spread, 1)

            for i in range(4):
                wt = w.landed(pe, m0 + 8 + i).rearrange("p (k n) -> p k n", k=DK)
                if i >= 2:
                    pe.wait_ge(row_read, i - 1)
                for k in range(DK):
                    last = mm(nc, c.ps[0:2, 2 + i % 2], c.silu_c[:, k, :], wt[:, k, :], k == 0, k == DK - 1)
                last.then_inc(row_ready, 1)
                if i >= 1:
                    spread_row(i - 1)
            spread_row(3)

        @block.scalar
        def _(act):
            nc.scalar.activation(c.silu_c, cond, ACT.Silu).then_inc(silu_c, 1)
            for i in range(4):
                act.wait_ge(row_ready, i + 1)
                if i >= 2:
                    act.wait_ge(spread, i - 1)
                nc.scalar.activation(row[:, i % 2, :], c.ps[0:2, 2 + i % 2], ACT.Copy).then_inc(row_read, 1)

        @block.vector
        def _(dve):
            for i in range(8):
                dve.wait_ge(cols_ready, i + 1)
                part = order[i // 2]
                at = part * DK + 4 * (i % 2)
                nc.vector.tensor_tensor(
                    c.mod[:, i // 2, :, 4 * (i % 2):4 * (i % 2) + 4],
                    c.ps[:, i % 2, 0:8].rearrange("p (f s) -> p s f", s=2),
                    bcol[:, at:at + 4].unsqueeze(1).broadcast_to([P, 2, 4]), ALU.add).then_inc(cols_read, 1)
            dve.wait_ge(cols_read, 8)
            for j, at in ((1, S_N1 + DK * layer), (3, S_N2 + DK * layer)):
                for s in range(STREAMS):
                    nc.vector.scalar_tensor_tensor(out=c.mod[:, j, s, :], in0=c.mod[:, j, s, :], scalar=1.0,
                                                   in1=c.par[:, at:at + DK], op0=ALU.add, op1=ALU.mult).then_inc(scales, 1)
            dve.wait_ge(bias_in, 16)
            for i in range(4):
                dve.wait_ge(spread, i + 1)
                for s in range(STREAMS):
                    at = (i % 2) * BANK
                    nc.vector.tensor_tensor(c.gate_rows[:, 2 * (i // 2) + s, at:at + BANK], c.ps[:, 4 + s],
                                            brow[:, i // 2, at:at + BANK], ALU.add).then_inc(gates, 1)


def add_gated(nc, c, prod, tiles, gate):
    for i, t in enumerate(tiles):
        for n in range(2):
            b = 2 * i + n
            nc.vector.tensor_tensor(c.tok[:, i, n * BANK:(n + 1) * BANK], c.ps[:, b],
                                    c.gate_rows[:, 2 * gate + t // TT, n * BANK:(n + 1) * BANK], ALU.mult).then_inc(prod, 1)


def mlp_stage(nc, c, w, m0, tiles):
    nt = len(tiles)
    T = nt * P
    with stage(nc, "hid_ready", "relu_done", "hidden", "down_ready", "product", "added") as (
            block, hid_ready, relu_done, hidden, down_ready, product, added):
        hid = c.work[:, 0:MK * T].rearrange("p (k t) -> p k t", k=MK)

        @block.sync
        def _(sp):
            for i in range(8):
                sp.wait_ge(hid_ready, 4 * i + 4)
                w.refill(sp, m0 + i)
            for i in range(8):
                sp.wait_ge(down_ready, i + 1)
                w.refill(sp, m0 + 8 + i)

        @block.tensor
        def _(pe):
            for i in range(8):
                wt = w.landed(pe, m0 + i).rearrange("p (k n) -> p k n", k=DK)
                for f in range(4):
                    j = 4 * i + f
                    if j >= 8:
                        pe.wait_ge(hidden, j - 7)
                    for k in range(DK):
                        last = mm(nc, c.ps[:, j % 8, 0:T], wt[:, k, f * P:(f + 1) * P], c.hT[:, k, 0:T],
                                  k == 0, k == DK - 1)
                    last.then_inc(hid_ready, 1)
            for i in range(8):
                wt = w.landed(pe, m0 + 8 + i).rearrange("p (k n) -> p k n", k=4)
                for kk in range(4):
                    k = 4 * i + kk
                    if k == 0:
                        pe.wait_ge(hidden, MK)
                    for t in range(nt):
                        for n in range(2):
                            last = mm(nc, c.ps[:, 2 * t + n], hid[:, k, t * P:(t + 1) * P],
                                      wt[:, kk, n * BANK:(n + 1) * BANK], k == 0, k == MK - 1)
                last.then_inc(down_ready, 1)

        @block.scalar
        def _(act):
            for j in range(MK):
                act.wait_ge(hid_ready, j + 1)
                if j >= 4:
                    act.wait_ge(hidden, j - 3)
                nc.scalar.activation(c.tok[:, j % 4, 0:T], c.ps[:, j % 8, 0:T], ACT.Relu).then_inc(relu_done, 1)

        @block.vector
        def _(dve):
            for j in range(MK):
                dve.wait_ge(relu_done, j + 1)
                nc.vector.tensor_tensor(hid[:, j, :], c.ps[:, j % 8, 0:T], c.tok[:, j % 4, 0:T], ALU.mult).then_inc(hidden, 1)
            dve.wait_ge(down_ready, 8)
            add_gated(nc, c, product, tiles, 1)

        @block.gpsimd
        def _(pool):
            for i, t in enumerate(tiles):
                for n in range(2):
                    pool.wait_ge(product, 2 * i + n + 1)
                    xs = c.x[:, t, n * BANK:(n + 1) * BANK]
                    nc.gpsimd.tensor_tensor(xs, xs, c.tok[:, i, n * BANK:(n + 1) * BANK], ALU.add).then_inc(added, 1)
            pool.wait_ge(added, 2 * nt)


def even_mixer_stage(nc, c, w, m0):
    QP, KP, VP, WO = 2, 3, 4, 5
    names = ["glu_ready", "sig_done", "glu_done", "padded", "conv_step", "conv_done", "q_lat", "q_ctx", "k_lat", "k_ctx",
             "v_ready", "q_roped", "k_roped", "rope_step", "q_ctx_read", "k_ctx_read", "v_read", "q_turned", "k_turned",
             "qT_read", "kT_read", "lam_in", "lam_step", "lam_ready", "lam_exp", "s_ready", "max_step", "negmax", "exp_done",
             "mix_step", "mixed", "p_turned", "p_cols", "pv", "o_done", "o_squares", "o_root", "o_step", "o_normed",
             "o_turned", "o_cols", "ln_mean", "centred", "ln_sq", "ln_var", "ln_eps", "ln_root", "ln_inv", "ln_norm",
             "conv_out", "out_ready", "product", "added"]
    UNITS = [(t, h) for t in range(ALL) for h in range(4)]
    with stage(nc, *names) as (block, *sems):
        s = dict(zip(names, sems))

        def area(at, n):
            return c.work[:, at:at + n]

        PW = SEQ + 2 * PAD
        glu = area(0, 4 * 2 * PW).rearrange("p (f s n) -> p f s n", f=4, s=2)
        at = 4 * 2 * PW
        conv = area(at, 2048).rearrange("p (f t) -> p f t", f=4)
        q = area(at + 2048, 2048).rearrange("p (t n) -> p t n", t=ALL)
        k = area(at + 4096, 2048).rearrange("p (t n) -> p t n", t=ALL)
        v = area(at + 6144, 2048).rearrange("p (t n) -> p t n", t=ALL)
        qT = area(at + 8192, 2048).rearrange("p (f t) -> p f t", f=4)
        kT = area(at + 10240, 2048).rearrange("p (f t) -> p f t", f=4)
        sq = area(at + 12288, 1024).rearrange("p (a n) -> p a n", a=2)
        small = area(at + 13312, 128)
        o = q
        oT = area(at + 4096, 2048).rearrange("p (f t) -> p f t", f=4)
        sig = c.tok[:, 0:2, :].rearrange("p a (b n) -> p (a b) n", b=2)
        ropes = c.tok[:, 2:3, :].rearrange("p a n -> p (a n)")
        prob = c.tok[:, 0:2, :].rearrange("p a (b n) -> p a b n", b=2)
        probT = c.tok[:, 2, :].rearrange("p (a n) -> p a n", a=2)
        lqk = c.tok[:, 3, 0:256].rearrange("p (a b n) -> p a b n", a=2, b=2)
        junk = c.tok[:, 3, 256:512]
        lam = small[:, 0:4]
        mx, negm, sums, rs = (small[:, 8 + 4 * a:12 + 4 * a] for a in range(4))
        osq, ostd, oinv = (small[:, 32 + 16 * a:48 + 16 * a] for a in range(3))
        cos = c.const2[:, K2_COS:K2_SIN].rearrange("p (t n) -> p t n", t=TT)
        sin = c.const2[:, K2_SIN:K2_LOWER].rearrange("p (t n) -> p t n", t=TT)

        @block.sync
        def _(sp):
            sp.dma_start(c.tok[:, 3, 0:256], c.vrows[V_LQK:V_DN].partition_broadcast(P)).then_inc(s["lam_in"], 16)
            for i, (done, n) in enumerate([(s["glu_ready"], 2), (s["glu_ready"], 4), (s["q_ctx"], 1), (s["k_ctx"], 1),
                                           (s["v_ready"], 4), (s["out_ready"], 1), (s["out_ready"], 2)]):
                sp.wait_ge(done, n)
                w.refill(sp, m0 + i)

        @block.gpsimd
        def _(pool):
            nc.gpsimd.memset(glu[:, :, :, 0:PAD], 0.0).then_inc(s["padded"], 1)
            nc.gpsimd.memset(glu[:, :, :, PAD + SEQ:PW], 0.0).then_inc(s["padded"], 1)
            for i in range(ALL):
                for n in range(2):
                    pool.wait_ge(s["product"], 2 * i + n + 1)
                    xs = c.x[:, i, n * BANK:(n + 1) * BANK]
                    nc.gpsimd.tensor_tensor(xs, xs, c.tok[:, i, n * BANK:(n + 1) * BANK], ALU.add).then_inc(s["added"], 1)
            pool.wait_ge(s["added"], 2 * ALL)

        @block.tensor
        def _(pe):
            for i in range(2):
                wt = w.landed(pe, m0 + i).rearrange("p (k n) -> p k n", k=DK)
                for half in (1, 0):
                    for f in range(2):
                        for kk in range(DK):
                            last = mm(nc, c.ps[:, 4 * i + 2 * half + f], wt[:, kk, (2 * half + f) * P:(2 * half + f + 1) * P],
                                      c.hT[:, kk, :], kk == 0, kk == DK - 1)
                    last.then_inc(s["glu_ready"], 1)

            def tokens(wt, tiles, bank, sem):
                for i, t in enumerate(tiles):
                    for kk in range(DK):
                        last = mm(nc, c.ps[:, bank + i], c.hT[:, kk, t * P:(t + 1) * P], wt[:, kk, :], kk == 0, kk == DK - 1)
                    last.then_inc(sem, 1)

            def features(wt, bank, sem):
                for f in range(4):
                    for kk in range(DK):
                        last = mm(nc, c.ps[:, bank + f // 2, (f % 2) * SEQ:(f % 2 + 1) * SEQ], wt[:, kk, f * P:(f + 1) * P],
                                  c.hT[:, kk, SEQ:BOTH], kk == 0, kk == DK - 1)
                last.then_inc(sem, 1)

            wt = w.landed(pe, m0 + QP).rearrange("p (k n) -> p k n", k=DK)
            pe.wait_ge(s["glu_done"], 2)
            tokens(wt, (0, 1), 0, s["q_lat"])
            features(wt, 2, s["q_ctx"])
            wt = w.landed(pe, m0 + KP).rearrange("p (k n) -> p k n", k=DK)
            pe.wait_ge(s["glu_done"], 4)
            tokens(wt, (0, 1), 4, s["k_lat"])
            pe.wait_ge(s["q_roped"], 2)
            features(wt, 0, s["k_ctx"])
            wt = w.landed(pe, m0 + VP).rearrange("p (k n) -> p k n", k=DK)
            pe.wait_ge(s["q_ctx_read"], 1)
            tokens(wt, (0, 1), 2, s["v_ready"])
            pe.wait_ge(s["k_roped"], 2)
            tokens(wt, (2, 3), 4, s["v_ready"])
            pe.wait_ge(s["k_ctx_read"], 1)
            for src, bank, sem in ((q, 0, s["q_turned"]), (k, 2, s["k_turned"])):
                if bank == 2:
                    pe.wait_ge(s["v_read"], 2)
                for f in range(4):
                    for t in range(TT):
                        last = nc.tensor.transpose(c.ps[:, bank + f // 2, (f % 2) * SEQ + t * P:(f % 2) * SEQ + (t + 1) * P],
                                                   src[:, t, f * P:(f + 1) * P], c.ident)
                last.then_inc(sem, 1)
            pe.wait_ge(s["qT_read"], 1)
            pe.wait_ge(s["kT_read"], 1)
            pe.wait_ge(s["v_read"], 4)

            def scores(j):
                t, h = UNITS[j]
                k0 = 0 if t < TT else SEQ
                if j >= 2:
                    pe.wait_ge(s["exp_done"], 2 * j - 2)
                for e in range(2):
                    hp = slice(64 * e, 64 * e + 64)
                    last = mm(nc, c.ps[:, 2 * (j % 2) + e, 0:BOTH - k0], qT[hp, h, t * P:(t + 1) * P], kT[hp, h, k0:BOTH],
                              True, True)
                    last.then_inc(s["s_ready"], 1)

            def turn_probs(j):
                t, h = UNITS[j]
                nb = 4 if t < TT else 2
                pe.wait_ge(s["mixed"], j + 1)
                if j >= 1:
                    pe.wait_ge(s["p_cols"], j)
                for b in range(nb):
                    last = nc.tensor.transpose(c.ps[:, 4, b * P:(b + 1) * P], prob[:, j % 2, 0, b * P:(b + 1) * P], c.ident)
                last.then_inc(s["p_turned"], 1)

            def weigh(j):
                t, h = UNITS[j]
                tiles = range(4) if t < TT else range(2, 4)
                pe.wait_ge(s["p_cols"], j + 1)
                if h == 0 and t:
                    pe.wait_ge(s["o_done"], t)
                for b, kt in enumerate(tiles):
                    last = mm(nc, c.ps[:, 5, h * P:(h + 1) * P], probT[:, j % 2, b * P:(b + 1) * P],
                              v[:, kt, h * P:(h + 1) * P], b == 0, b == len(tiles) - 1)
                last.then_inc(s["pv"], 1)

            for j in range(len(UNITS) + 2):
                if j < len(UNITS):
                    scores(j)
                if 1 <= j <= len(UNITS):
                    turn_probs(j - 1)
                if j >= 2:
                    weigh(j - 2)
            pe.wait_ge(s["conv_done"], 4)
            for f in range(4):
                last = mm(nc, c.ps[:, 6], c.mean512, conv[:, f, :], f == 0, f == 3)
            last.then_inc(s["ln_mean"], 1)
            for f in range(4):
                pe.wait_ge(s["ln_sq"], f + 1)
                last = mm(nc, c.ps[:, 7], c.mean512, sq[:, f % 2, :], f == 0, f == 3)
                last.then_inc(s["ln_var"], 1)
            for t in range(ALL):
                pe.wait_ge(s["o_normed"], 4 * t + 4)
                for h in range(4):
                    last = nc.tensor.transpose(c.ps[:, h, t * P:(t + 1) * P], o[:, t, h * P:(h + 1) * P], c.ident)
            last.then_inc(s["o_turned"], 1)
            pe.wait_ge(s["conv_out"], 4)
            pe.wait_ge(s["o_cols"], 4)
            for half in range(2):
                wt = w.landed(pe, m0 + WO + half).rearrange("p (k n) -> p k n", k=4)
                src = oT if half else conv
                for kk in range(4):
                    for t in range(ALL):
                        for n in range(2):
                            last = mm(nc, c.ps[:, 2 * t + n], src[:, kk, t * P:(t + 1) * P],
                                      wt[:, kk, n * BANK:(n + 1) * BANK], half + kk == 0, half == 1 and kk == 3)
                last.then_inc(s["out_ready"], 1)

        @block.scalar
        def _(act):
            for i in range(2):
                act.wait_ge(s["glu_ready"], 2 * i + 1)
                for f in range(2):
                    if i:
                        act.wait_ge(s["glu_done"], f + 1)
                    nc.scalar.activation(sig[:, f, :], c.ps[:, 4 * i + 2 + f], ACT.Sigmoid).then_inc(s["sig_done"], 1)
            act.wait_ge(s["q_ctx"], 1)
            nc.scalar.activation(qT[:, :, SEQ:BOTH], c.ps[:, 2:4, :].rearrange("p b (f t) -> p (b f) t", f=2),
                                 ACT.Copy).then_inc(s["q_ctx_read"], 1)
            act.wait_ge(s["k_ctx"], 1)
            nc.scalar.activation(kT[:, :, SEQ:BOTH], c.ps[:, 0:2, :].rearrange("p b (f t) -> p (b f) t", f=2),
                                 ACT.Copy).then_inc(s["k_ctx_read"], 1)
            for t in range(ALL):
                act.wait_ge(s["v_ready"], t + 1)
                nc.scalar.activation(v[:, t], c.ps[:, 2 + t], ACT.Copy).then_inc(s["v_read"], 1)
            act.wait_ge(s["q_turned"], 1)
            nc.scalar.activation(qT[:, :, 0:SEQ], c.ps[:, 0:2, :].rearrange("p b (f t) -> p (b f) t", f=2),
                                 ACT.Copy).then_inc(s["qT_read"], 1)
            act.wait_ge(s["k_turned"], 1)
            nc.scalar.activation(kT[:, :, 0:SEQ], c.ps[:, 2:4, :].rearrange("p b (f t) -> p (b f) t", f=2),
                                 ACT.Copy).then_inc(s["kT_read"], 1)
            act.wait_ge(s["lam_ready"], 1)
            nc.scalar.activation(lam[:, 2:4], lam[:, 0:2], ACT.Exp).then_inc(s["lam_exp"], 1)

            def exps(j):
                t, h = UNITS[j]
                n = BOTH if t < TT else SEQ
                act.wait_ge(s["negmax"], j + 1)
                if j >= 2:
                    act.wait_ge(s["p_turned"], j - 1)
                for e in range(2):
                    col = 2 * (j % 2) + e
                    nc.scalar.activation(prob[:, j % 2, e, 0:n], c.ps[:, 2 * (j % 2) + e, 0:n], ACT.Exp, scale=ATT_SCALE,
                                         bias=negm[:, col:col + 1], accum_out=sums[:, col:col + 1]).then_inc(s["exp_done"], 1)

            def prob_columns(j):
                t, h = UNITS[j]
                n = BOTH if t < TT else SEQ
                act.wait_ge(s["p_turned"], j + 1)
                if j >= 2:
                    act.wait_ge(s["pv"], j - 1)
                nc.scalar.activation(probT[:, j % 2, 0:n], c.ps[:, 4, 0:n], ACT.Copy).then_inc(s["p_cols"], 1)

            for j in range(len(UNITS) + 1):
                if j < len(UNITS):
                    exps(j)
                if j >= 1:
                    prob_columns(j - 1)
            for f in range(4):
                act.wait_ge(s["centred"], f + 1)
                if f >= 2:
                    act.wait_ge(s["ln_var"], f - 1)
                nc.scalar.activation(sq[:, f % 2, :], conv[:, f, :], ACT.Square).then_inc(s["ln_sq"], 1)
            act.wait_ge(s["o_squares"], 16)
            nc.scalar.activation(ostd, osq, ACT.Sqrt).then_inc(s["o_root"], 1)
            act.wait_ge(s["ln_eps"], 1)
            nc.scalar.activation(sq[:, 0, :], sq[:, 0, :], ACT.Sqrt).then_inc(s["ln_root"], 1)
            for f in range(4):
                act.wait_ge(s["ln_norm"], f + 1)
                nc.scalar.activation(conv[:, f, :], conv[:, f, :], ACT.Silu, scale=c.par[:, S_LNG + f:S_LNG + f + 1],
                                     bias=c.par[:, S_LNB + f:S_LNB + f + 1]).then_inc(s["conv_out"], 1)
            act.wait_ge(s["o_turned"], 1)
            for f in range(4):
                nc.scalar.activation(oT[:, f, :], c.ps[:, f], ACT.Copy, scale=c.subln[:, 0:1]).then_inc(s["o_cols"], 1)

        @block.vector
        def _(dve):
            count = {}

            def then(name, ins):
                ins.then_inc(s[name], 1)
                count[name] = count.get(name, 0) + 1
                dve.wait_ge(s[name], count[name])

            dve.wait_ge(s["lam_in"], 16)
            for a in range(2):
                then("lam_step", nc.vector.tensor_tensor_reduce(
                    out=junk[:, 0:64], in0=lqk[:, a, 0], in1=lqk[:, a, 1], scale=1.0, scalar=0.0, op0=ALU.mult,
                    op1=ALU.add, accum_out=lam[:, a:a + 1]))
            dve.sem_inc(s["lam_ready"], 1)
            then("lam_step", nc.vector.tensor_scalar(c.subln[:, 0:1], c.par[:, S_SUBLN:S_SUBLN + 1], 1.0 - LAMBDA0, None,
                                                     ALU.mult))
            dve.wait_ge(s["padded"], 2)
            for i in range(2):
                dve.wait_ge(s["glu_ready"], 2 * i + 2)
                for f in range(2):
                    dve.wait_ge(s["sig_done"], 2 * i + f + 1)
                    nc.vector.tensor_tensor(glu[:, 2 * i + f, :, PAD:PAD + SEQ],
                                            c.ps[:, 4 * i + f].rearrange("p (s t) -> p s t", s=2),
                                            sig[:, f, :].rearrange("p (s t) -> p s t", s=2), ALU.mult).then_inc(s["glu_done"], 1)

            def convolve(f):
                dve.wait_ge(s["glu_done"], 4)
                for tap in range(CONV_W):
                    src = glu[:, f, :, tap:tap + SEQ]
                    dst = c.ps[:, 6 + tap % 2].rearrange("p (s t) -> p s t", s=2)
                    prev = c.ps[:, 7 - tap % 2].rearrange("p (s t) -> p s t", s=2)
                    wc = c.par[:, S_CONVW + f * CONV_W + tap:S_CONVW + f * CONV_W + tap + 1]
                    if tap == 0:
                        then("conv_step", nc.vector.tensor_scalar(dst, src, wc, c.par[:, S_CONVB + f:S_CONVB + f + 1],
                                                                  ALU.mult, ALU.add))
                    elif tap < CONV_W - 1:
                        then("conv_step", nc.vector.scalar_tensor_tensor(out=dst, in0=src, scalar=wc, in1=prev,
                                                                         op0=ALU.mult, op1=ALU.add))
                    else:
                        nc.vector.scalar_tensor_tensor(out=conv[:, f, :].rearrange("p (s t) -> p s t", s=2), in0=src,
                                                       scalar=wc, in1=prev, op0=ALU.mult, op1=ALU.add).then_inc(s["conv_done"], 1)

            def rope(ready, bank, dst, roped):
                a = ropes[:, 0:512]
                b = ropes[:, 512:1024]
                for t in range(TT):
                    dve.wait_ge(ready, t + 1)
                    sv = c.ps[:, bank + t]
                    ct = cos[:, t].unsqueeze(1).broadcast_to([P, 8, 64])
                    nc.vector.tensor_tensor(a.rearrange("p (h n) -> p h n", h=8), sv.rearrange("p (h n) -> p h n", h=8), ct,
                                            ALU.mult).then_inc(s["rope_step"], 1)
                    count["rope_step"] = count.get("rope_step", 0) + 1
                    for e in range(2):
                        bv = b.rearrange("p (h x y n) -> p h x y n", h=8, x=2, y=2)[:, :, :, e]
                        xv = sv.rearrange("p (h x y n) -> p h x y n", h=8, x=2, y=2)[:, :, :, 1 - e]
                        st = sin[:, t].rearrange("p (x y n) -> p x y n", x=2, y=2)[:, :, e].unsqueeze(1).broadcast_to([P, 8, 2, 16])
                        nc.vector.tensor_tensor(bv, xv, st, ALU.mult).then_inc(s["rope_step"], 1)
                        count["rope_step"] += 1
                    dve.wait_ge(s["rope_step"], count["rope_step"])
                    then("rope_step", nc.vector.tensor_tensor(dst[:, t], a, b, ALU.add))
                    dve.sem_inc(roped, 1)

            convolve(0)
            rope(s["q_lat"], 0, q, s["q_roped"])
            convolve(1)
            rope(s["k_lat"], 4, k, s["k_roped"])
            convolve(2)
            convolve(3)
            dve.wait_ge(s["lam_exp"], 1)
            then("lam_step", nc.vector.tensor_tensor(lam[:, 0:1], lam[:, 2:3], lam[:, 3:4], ALU.subtract))
            then("lam_step", nc.vector.tensor_scalar(lam[:, 1:2], lam[:, 0:1], LAMBDA0, None, ALU.add))

            def maxima(j):
                t, h = UNITS[j]
                n = BOTH if t < TT else SEQ
                for e in range(2):
                    col = 2 * (j % 2) + e
                    dve.wait_ge(s["s_ready"], 2 * j + e + 1)
                    nc.vector.tensor_reduce(mx[:, col:col + 1], c.ps[:, 2 * (j % 2) + e, 0:n], axis=AX,
                                            op=ALU.max).then_inc(s["max_step"], 1)
                dve.wait_ge(s["max_step"], 2 * j + 2)
                cs = slice(2 * (j % 2), 2 * (j % 2) + 2)
                nc.vector.tensor_scalar(negm[:, cs], mx[:, cs], -ATT_SCALE, None, ALU.mult).then_inc(s["negmax"], 1)

            def mix(j):
                t, h = UNITS[j]
                n = BOTH if t < TT else SEQ
                dve.wait_ge(s["exp_done"], 2 * j + 2)
                c0 = 2 * (j % 2)
                then("mix_step", nc.vector.reciprocal(rs[:, c0:c0 + 2], sums[:, c0:c0 + 2]))
                e0, e1 = prob[:, j % 2, 0, 0:n], prob[:, j % 2, 1, 0:n]
                then("mix_step", nc.vector.tensor_scalar(e1, e1, rs[:, c0 + 1:c0 + 2], lam[:, 1:2], ALU.mult, ALU.mult))
                nc.vector.scalar_tensor_tensor(out=e0, in0=e0, scalar=rs[:, c0:c0 + 1], in1=e1, op0=ALU.mult,
                                               op1=ALU.subtract).then_inc(s["mixed"], 1)

            def take_o(t):
                dve.wait_ge(s["pv"], 4 * t + 4)
                then("o_done", nc.vector.tensor_copy(o[:, t], c.ps[:, 5]))
                for h in range(4):
                    oh = o[:, t, h * P:(h + 1) * P]
                    i = 4 * t + h
                    then("o_step", nc.vector.tensor_tensor_reduce(out=junk[:, 0:P], in0=oh, in1=oh, scale=1.0 / P, scalar=EPS,
                                                                  op0=ALU.mult, op1=ALU.add, accum_out=osq[:, i:i + 1]))
                    dve.sem_inc(s["o_squares"], 1)

            for j in range(len(UNITS) + 1):
                if j < len(UNITS):
                    maxima(j)
                if j >= 1:
                    mix(j - 1)
                if j >= 5 and (j - 5) % 4 == 0:
                    take_o((j - 5) // 4)
            dve.wait_ge(s["ln_mean"], 1)
            for f in range(4):
                nc.vector.tensor_tensor(conv[:, f, :], conv[:, f, :], c.ps[:, 6], ALU.subtract).then_inc(s["centred"], 1)
            take_o(3)
            dve.wait_ge(s["ln_var"], 4)
            nc.vector.tensor_scalar(sq[:, 0, :], c.ps[:, 7], EPS, None, ALU.add).then_inc(s["ln_eps"], 1)
            dve.wait_ge(s["o_root"], 1)
            then("o_step", nc.vector.reciprocal(oinv, ostd))
            for i in range(16):
                oh = o[:, i // 4, (i % 4) * P:(i % 4 + 1) * P]
                nc.vector.tensor_scalar(oh, oh, oinv[:, i:i + 1], None, ALU.mult).then_inc(s["o_normed"], 1)
            dve.wait_ge(s["ln_root"], 1)
            nc.vector.reciprocal(c.ps[:, 6], sq[:, 0, :]).then_inc(s["ln_inv"], 1)
            dve.wait_ge(s["ln_inv"], 1)
            for f in range(4):
                nc.vector.tensor_tensor(conv[:, f, :], conv[:, f, :], c.ps[:, 6], ALU.mult).then_inc(s["ln_norm"], 1)
            dve.wait_ge(s["out_ready"], 2)
            add_gated(nc, c, s["product"], range(ALL), 0)
TAPS_HY, TAPS_DN = 3, 5
DNH = 4
O_HY, O_Q, O_K, O_V, O_GATE, O_TEMP = 0, 3072, 4096, 6144, 8192, 9216
TURN = (6.28125, 0.0019350051879882812, 3.019915979507459e-07)
LEVELS = 7

T_FH = 0
T_FU = T_FH + 4 * 640
T_INV = T_FU + 2 * 512
T_WIN = T_INV + 4 * SEQ
T_Z = T_WIN + 2 * 512
T_END = T_Z + SEQ
M_LEVEL = 0
M_BIAS = M_LEVEL + 2 * LEVELS * P
M_END = M_BIAS + 2 * P


def odd_project_stage(nc, c, w, m0):
    names = ["rest_ready", "rest_read", "proj", "padded", "copied", "conv_step", "conv_done", "gate_done", "conv_silu"]
    with stage(nc, *names) as (block, rest_ready, rest_read, proj, padded, copied, conv_step, conv_done, gate_done,
                               conv_silu):
        hy = c.work[:, O_HY:O_HY + 3072].rearrange("p (f t) -> p f t", f=12)
        gs = c.work[:, O_GATE:O_GATE + 1024].rearrange("p (t n) -> p t n", t=TT)
        rest_w = c.par[:, S_REST:S_END].rearrange("p (k n) -> p k n", k=DK)
        convs = [(i, 1, TAPS_HY, S_HYSW + 12 * i, S_HYSB + 4 * i, O_HY + 1024 * i) for i in range(3)]
        convs += [(3, 1, TAPS_DN, S_DNW, None, O_Q), (4, 2, TAPS_DN, S_DNW + 20, None, O_K),
                  (5, 2, TAPS_DN, S_DNW + 40, None, O_V)]

        def padded_buffer(i):
            _, ns, taps, _, _, _ = convs[i]
            n = 4 * ns * (SEQ + taps - 1)
            at = O_TEMP + 2080 * (i % 2)
            return c.work[:, at:at + n].rearrange("p (f s t) -> p f s t", f=4, s=ns)

        @block.sync
        def _(sp):
            for i in range(7):
                sp.wait_ge(proj, i + 1)
                w.refill(sp, m0 + i)

        @block.tensor
        def _(pe):
            for t in range(ALL):
                for k in range(DK):
                    last = mm(nc, c.ps[:, 4, t * 16:t * 16 + 16], c.hT[:, k, t * P:(t + 1) * P], rest_w[:, k, :],
                              k == 0, k == DK - 1)
            last.then_inc(rest_ready, 1)
            for i, ns, taps, _, _, _ in convs:
                wt = w.landed(pe, m0 + i).rearrange("p (k n) -> p k n", k=DK)
                n = ns * SEQ
                if i:
                    pe.wait_ge(copied, i)
                for f in range(4):
                    for k in range(DK):
                        last = mm(nc, c.ps[:, f, 0:n], wt[:, k, f * P:(f + 1) * P], c.hT[:, k, 0:n], k == 0, k == DK - 1)
                last.then_inc(proj, 1)
            wt = w.landed(pe, m0 + 6).rearrange("p (k n) -> p k n", k=DK)
            pe.wait_ge(copied, 6)
            for t in range(TT):
                for k in range(DK):
                    last = mm(nc, c.ps[:, t], c.hT[:, k, t * P:(t + 1) * P], wt[:, k, :], k == 0, k == DK - 1)
            last.then_inc(proj, 1)

        @block.gpsimd
        def _(pool):
            for i, ns, taps, _, _, _ in convs:
                if i >= 2:
                    pool.wait_ge(conv_done, 4 * (i - 1))
                side = (taps - 1) // 2
                buf = padded_buffer(i)
                nc.gpsimd.memset(buf[:, :, :, 0:side], 0.0).then_inc(padded, 1)
                nc.gpsimd.memset(buf[:, :, :, side + SEQ:], 0.0).then_inc(padded, 1)

        @block.scalar
        def _(act):
            act.wait_ge(rest_ready, 1)
            nc.scalar.activation(c.rest, c.ps[:, 4, 0:64], ACT.Copy).then_inc(rest_read, 1)
            for i, ns, taps, _, _, _ in convs:
                side = (taps - 1) // 2
                act.wait_ge(proj, i + 1)
                if i >= 2:
                    act.wait_ge(conv_done, 4 * (i - 1))
                act.wait_ge(padded, 2 * i + 2)
                for f in range(4):
                    ins = nc.scalar.activation(padded_buffer(i)[:, f, :, side:side + SEQ],
                                               c.ps[:, f, 0:ns * SEQ].rearrange("p (s t) -> p s t", s=ns), ACT.Copy)
                    if f == 3:
                        ins.then_inc(copied, 1)
                    else:
                        ins.then_inc(gate_done, 1)
            act.wait_ge(proj, 7)
            for t in range(TT):
                nc.scalar.activation(gs[:, t], c.ps[:, t], ACT.Silu).then_inc(gate_done, 1)
            act.wait_ge(conv_done, 24)
            for at, n in ((O_Q, 1024), (O_K, 2048), (O_V, 2048)):
                nc.scalar.activation(c.work[:, at:at + n], c.work[:, at:at + n], ACT.Silu).then_inc(conv_silu, 1)

        @block.vector
        def _(dve):
            step = 0
            for i, ns, taps, wcol, bcol, at in convs:
                dve.wait_ge(copied, i + 1)
                buf = padded_buffer(i)
                for f in range(4):
                    for tap in range(taps):
                        src = buf[:, f, :, tap:tap + SEQ]
                        wc = c.par[:, wcol + f * taps + tap:wcol + f * taps + tap + 1]
                        dst = c.ps[:, 6 + tap % 2, 0:ns * SEQ].rearrange("p (s t) -> p s t", s=ns)
                        prev = c.ps[:, 7 - tap % 2, 0:ns * SEQ].rearrange("p (s t) -> p s t", s=ns)
                        if tap == 0:
                            nc.vector.tensor_scalar(dst, src, wc, c.par[:, bcol + f:bcol + f + 1] if bcol else None, ALU.mult,
                                                    ALU.add if bcol else ALU.bypass).then_inc(conv_step, 1)
                        elif tap < taps - 1:
                            nc.vector.scalar_tensor_tensor(out=dst, in0=src, scalar=wc, in1=prev, op0=ALU.mult,
                                                           op1=ALU.add).then_inc(conv_step, 1)
                        else:
                            out = c.work[:, at + f * ns * SEQ:at + (f + 1) * ns * SEQ].rearrange("p (s t) -> p s t", s=ns)
                            nc.vector.scalar_tensor_tensor(out=out, in0=src, scalar=wc, in1=prev, op0=ALU.mult,
                                                           op1=ALU.add).then_inc(conv_done, 1)
                            dve.wait_ge(conv_done, 4 * i + f + 1)
                            continue
                        step += 1
                        dve.wait_ge(conv_step, step)


def hyena_stage(nc, c, order):
    names = ["tables_in", "w3_in", "arg", "range_step", "sine", "layer_ready", "filt_ready", "windowed", "absolute",
             "norm_ready", "norm_inv", "filt_done", "spec_ready", "spec_read", "z_turned", "z_read", "sig_ready", "sig_read",
             "prod_step", "prod_done", "y_ready", "gated"]
    with stage(nc, *names) as (block, *sems):
        s = dict(zip(names, sems))
        hy = c.work[:, O_HY:O_HY + 3072].rearrange("p (f t) -> p f t", f=12)
        filt = c.work[:, O_TEMP:O_TEMP + 2048].rearrange("p (d t n) -> p d t n", d=2, t=TT)
        spec = c.work[:, O_TEMP + 2048:O_TEMP + 4608].rearrange("p (f n) -> p f n", f=5)
        sig = c.work[:, O_TEMP + 4608:O_TEMP + 6656].rearrange("p (f n) -> p f n", f=4)
        fh = c.hTf[:, 0:2560].rearrange("p (d t n) -> p d t n", d=2, t=TT)
        fu = c.hTf[:, 2560:3584].rearrange("p (t n) -> p t n", t=TT)
        tokf = c.tok[:, :, :].rearrange("p a n -> p (a n)")
        inv = tokf[:, 0:1024].rearrange("p (f t) -> p f t", f=4)
        win = tokf[:, 1024:2048].rearrange("p (t n) -> p t n", t=TT)
        zT = tokf[0:33, 2048:2304]
        hid = tokf[0:64, 2304:2560]
        turns = c.hTf[0:64, 3584:3840]
        w3 = tokf[0:64, 2816:3840].rearrange("p (d n) -> p d n", d=2)
        mag = c.junk[:, 0:1024].rearrange("p (a n) -> p a n", a=2)
        z = c.junk[:, 0:1024].rearrange("p (t n) -> p t n", t=TT)
        w1 = c.par[0:33, S_W1:S_W1 + 64]
        w2 = c.par[0:64, S_W2:S_W2 + 64]
        fb = c.par[0:64, S_FB:S_FB + 4]
        ma, mb = (c.work[:, O_TEMP + a:O_TEMP + a + 1024].rearrange("p (f n) -> p f n", f=2) for a in (0, 1024))
        MAGIC = 12582912.0

        @block.sync
        def _(sp):
            if order == 0:
                sp.dma_start(c.hTf[:, 0:3584], c.transforms[:, T_FH:T_INV]).then_inc(s["tables_in"], 16)
                sp.dma_start(tokf[:, 0:2304], c.transforms[:, T_INV:T_END]).then_inc(s["tables_in"], 16)
            sp.dma_start(w3.rearrange("p d n -> p (d n)"), c.w3[:, order * 1024:(order + 1) * 1024]).then_inc(s["w3_in"], 16)

        @block.tensor
        def _(pe):
            if order == 0:
                pe.wait_ge(s["tables_in"], 32)
                mm(nc, c.ps[0:64, 0, 0:SEQ], w1, zT, True, True).then_inc(s["layer_ready"], 1)
                pe.wait_ge(s["sine"], 1)
                mm(nc, c.ps[0:64, 1, 0:SEQ], w2, hid, True, True).then_inc(s["layer_ready"], 1)
                pe.wait_ge(s["sine"], 2)
            for t in range(TT):
                for f in range(4):
                    last = nc.tensor.transpose(c.ps[:, 6 + t, f * P:(f + 1) * P], hy[:, f, t * P:(t + 1) * P], c.ident)
            last.then_inc(s["z_turned"], 1)
            pe.wait_ge(s["w3_in"], 16)
            for d in range(2):
                for t in range(TT):
                    mm(nc, c.ps[:, 2 * d + t], c.hidden_z[:, t * P:(t + 1) * P], w3[:, d, :], True, True).then_inc(s["filt_ready"], 1)
            for i in range(4):
                pe.wait_ge(s["absolute"], i + 1)
                last = mm(nc, c.ps[:, 4], c.ones, mag[:, i % 2, :], i == 0, i == 3)
                last.then_inc(s["norm_ready"], 1)
            pe.wait_ge(s["filt_done"], 4)
            for f in range(5):
                if f >= 4:
                    pe.wait_ge(s["spec_read"], f - 3)
                for i in range(4):
                    last = mm(nc, c.ps[:, f % 4], fh[:, i // 2, i % 2, f * P:(f + 1) * P], filt[:, i // 2, i % 2, :],
                              i == 0, i == 3)
                last.then_inc(s["spec_ready"], 1)
            pe.wait_ge(s["z_read"], 2)
            for f in range(4):
                bank = 5 + f if f < 3 else 4
                if f == 3:
                    pe.wait_ge(s["filt_done"], 4)
                for t in range(TT):
                    last = mm(nc, c.ps[:, bank], fu[:, t, f * P:(f + 1) * P], z[:, t, :], t == 0, t == TT - 1)
                last.then_inc(s["sig_ready"], 1)
            pe.wait_ge(s["prod_done"], 4)
            for f in range(4):
                for k in range(4):
                    last = mm(nc, c.ps[:, f, 0:SEQ], sig[:, k, f * P:(f + 1) * P], inv[:, k, :], k == 0, k == 3)
                last.then_inc(s["y_ready"], 1)

        @block.scalar
        def _(act):
            if order == 0:
                for i in range(2):
                    act.wait_ge(s["arg"], i + 1)
                    dst = c.hidden_z if i else hid
                    nc.scalar.activation(dst, turns, ACT.Sin).then_inc(s["sine"], 1)
            for i in range(4):
                act.wait_ge(s["windowed"], i + 1)
                if i >= 2:
                    act.wait_ge(s["norm_ready"], i - 1)
                nc.scalar.activation(mag[:, i % 2, :], filt[:, i // 2, i % 2, :], ACT.Abs).then_inc(s["absolute"], 1)
            act.wait_ge(s["norm_ready"], 4)
            act.wait_ge(s["z_turned"], 1)
            for t in range(TT):
                nc.scalar.activation(z[:, t, :], c.ps[:, 6 + t], ACT.Copy).then_inc(s["z_read"], 1)
            for f in range(5):
                act.wait_ge(s["spec_ready"], f + 1)
                nc.scalar.activation(spec[:, f, :], c.ps[:, f % 4], ACT.Copy).then_inc(s["spec_read"], 1)

        @block.vector
        def _(dve):
            count = {}

            def then(name, ins):
                ins.then_inc(s[name], 1)
                count[name] = count.get(name, 0) + 1
                dve.wait_ge(s[name], count[name])

            if order == 0:
                dve.wait_ge(s["tables_in"], 32)
                whole = c.hTf[0:64, 3840:4096]
                for i in range(2):
                    dve.wait_ge(s["layer_ready"], i + 1)
                    then("range_step", nc.vector.tensor_scalar(turns, c.ps[0:64, i, 0:SEQ], fb[:, 2 * i:2 * i + 1],
                                                               fb[:, 2 * i + 1:2 * i + 2], ALU.add, ALU.mult))
                    then("range_step", nc.vector.tensor_scalar(whole, turns, 1.0 / (2 * math.pi), MAGIC, ALU.mult, ALU.add))
                    then("range_step", nc.vector.tensor_scalar(whole, whole, MAGIC, None, ALU.subtract))
                    for part in TURN:
                        then("range_step", nc.vector.scalar_tensor_tensor(out=turns, in0=whole, scalar=-part, in1=turns,
                                                                          op0=ALU.mult, op1=ALU.add))
                    then("range_step", nc.vector.tensor_scalar(turns, turns, 3.1415925, -3.1415925, ALU.min, ALU.max))
                    dve.sem_inc(s["arg"], 1)
                    dve.wait_ge(s["sine"], i + 1)
            for i in range(4):
                dve.wait_ge(s["filt_ready"], i + 1)
                nc.vector.tensor_tensor(filt[:, i // 2, i % 2, :], c.ps[:, i], win[:, i % 2, :], ALU.mult).then_inc(s["windowed"], 1)
            dve.wait_ge(s["norm_ready"], 4)
            then("norm_inv", nc.vector.reciprocal(c.ps[:, 5], c.ps[:, 4]))
            for i in range(4):
                fl = filt[:, i // 2, i % 2, :]
                nc.vector.tensor_tensor(fl, fl, c.ps[:, 5], ALU.mult).then_inc(s["filt_done"], 1)
            dve.wait_ge(s["spec_read"], 5)
            for f in range(4):
                bank = 5 + f if f < 3 else 4
                dve.wait_ge(s["sig_ready"], f + 1)
                then("sig_read", nc.vector.tensor_copy(sig[:, f, :], c.ps[:, bank]))
            for f in range(2):
                ur, ui, hr, hi = sig[:, f, :], sig[:, 2 + f, :], spec[:, f, :], spec[:, 2 + f, :]
                hr2 = spec[:, 4, :] if f == 0 else hr
                then("prod_step", nc.vector.tensor_tensor(ma[:, 0, :], ui, hi, ALU.mult))
                then("prod_step", nc.vector.tensor_tensor(ma[:, 1, :], ur, hi, ALU.mult))
                then("prod_step", nc.vector.tensor_tensor(mb[:, 0, :], ur, hr, ALU.mult))
                then("prod_step", nc.vector.tensor_tensor(mb[:, 1, :], ui, hr2, ALU.mult))
                then("prod_done", nc.vector.tensor_tensor(ur, mb[:, 0, :], ma[:, 0, :], ALU.subtract))
                then("prod_done", nc.vector.tensor_tensor(ui, mb[:, 1, :], ma[:, 1, :], ALU.add))
            for f in range(4):
                dve.wait_ge(s["y_ready"], f + 1)
                zf = hy[:, f, :]
                skip = c.par[:, S_HYSKIP + 4 * order + f:S_HYSKIP + 4 * order + f + 1]
                then("gated", nc.vector.scalar_tensor_tensor(out=zf, in0=zf, scalar=skip, in1=c.ps[:, f, 0:SEQ],
                                                             op0=ALU.mult, op1=ALU.add))
                then("gated", nc.vector.tensor_tensor(zf, zf, hy[:, 4 * (order + 1) + f, :], ALU.mult))


def delta_features_stage(nc, c):
    names = ["square", "sum_ready", "eps_done", "root", "inv", "unit", "k_turned", "k_tok", "v_turned", "v_tok", "beta",
             "dn_in", "masks_in", "exp_a", "gate_step", "exp_x", "g_ready", "cum_ready", "cum_read", "last_ready",
             "last_read", "exps_in", "exps_done", "turned", "rows_read"]
    with stage(nc, *names) as (block, *sems):
        s = dict(zip(names, sems))
        q, k, v = c.work[:, O_Q:O_Q + 1024], c.work[:, O_K:O_K + 2048], c.work[:, O_V:O_V + 2048]
        parts = [(q, 0), (q, 1), (k, 0), (k, 1), (k, 2), (k, 3)]
        sq = c.tok[:, 0:3, :].rearrange("p a (b n) -> p (a b) n", b=2)
        g = c.gate_small
        dn = c.junk[:, 0:16]

        def seg(i):
            t, n = parts[i]
            return t[:, n * BANK:(n + 1) * BANK]

        @block.sync
        def _(sp):
            sp.dma_start(dn, c.vrows[V_DN:V_END].partition_broadcast(P)).then_inc(s["dn_in"], 16)
            sp.dma_start(c.hTf[:, 0:M_END], c.masks).then_inc(s["masks_in"], 16)
            sp.wait_ge(s["masks_in"], 16)

        @block.tensor
        def _(pe):
            for i in range(6):
                pe.wait_ge(s["square"], i + 1)
                mm(nc, c.ps[:, i], c.ones, sq[:, i, :], True, True).then_inc(s["sum_ready"], 1)
            vv = v.rearrange("p (h t) -> p h t", h=DNH)
            kk = k.rearrange("p (h t) -> p h t", h=DNH)
            for t in range(ALL):
                bank = 6 + t % 2
                if t >= 2:
                    pe.wait_ge(s["v_tok"], t - 1)
                for h in range(DNH):
                    last = nc.tensor.transpose(c.ps[:, bank, h * P:(h + 1) * P], vv[:, h, t * P:(t + 1) * P], c.ident)
                last.then_inc(s["v_turned"], 1)
            pe.wait_ge(s["g_ready"], 1)
            pe.wait_ge(s["v_tok"], 4)
            mm(nc, c.ps[:, 6, 0:16], c.upper, g["g"][:, 0:16], True, True)
            mm(nc, c.ps[:, 6, 16:32], c.lower, g["g"][:, 16:32], True, True).then_inc(s["cum_ready"], 1)
            pe.wait_ge(s["cum_read"], 1)
            mm(nc, c.ps[:, 7, 0:16], c.ident[:, P - 1:P].broadcast_to([P, P]), g["cum"][:, 0:16], True, True)
            mm(nc, c.ps[:, 7, 16:32], c.ident[:, 0:1].broadcast_to([P, P]), g["cum"][:, 16:32], True, True).then_inc(s["last_ready"], 1)
            pe.wait_ge(s["last_read"], 1)
            nc.tensor.transpose(c.ps[0:32, 6, 0:P], g["cum"], c.ident)
            nc.tensor.transpose(c.ps[0:32, 6, P:2 * P], g["beta"], c.ident).then_inc(s["turned"], 1)
            pe.wait_ge(s["rows_read"], 1)
            for t in range(ALL):
                pe.wait_ge(s["unit"], 6)
                bank = 6 + t % 2
                if t >= 2:
                    pe.wait_ge(s["k_tok"], t - 1)
                for h in range(DNH):
                    last = nc.tensor.transpose(c.ps[:, bank, h * P:(h + 1) * P], kk[:, h, t * P:(t + 1) * P], c.ident)
                last.then_inc(s["k_turned"], 1)

        @block.scalar
        def _(act):
            for i in range(6):
                nc.scalar.activation(sq[:, i, :], seg(i), ACT.Square).then_inc(s["square"], 1)
            for t in range(ALL):
                act.wait_ge(s["v_turned"], t + 1)
                nc.scalar.activation(c.v_tok[:, t], c.ps[:, 6 + t % 2], ACT.Copy).then_inc(s["v_tok"], 1)
            nc.scalar.activation(g["beta"].rearrange("p (d t h) -> p t d h", d=2, t=ALL),
                                 c.rest.rearrange("p (t x h) -> p t x h", t=ALL, x=4)[:, :, 0:2, :],
                                 ACT.Sigmoid).then_inc(s["beta"], 1)
            act.wait_ge(s["dn_in"], 16)
            nc.scalar.activation(dn[:, 0:8], dn[:, 0:8], ACT.Exp).then_inc(s["exp_a"], 1)
            act.wait_ge(s["gate_step"], 2)
            nc.scalar.activation(g["e"], g["ax"], ACT.Exp, scale=-1.0).then_inc(s["exp_x"], 1)
            act.wait_ge(s["cum_ready"], 1)
            nc.scalar.activation(g["cum"], c.ps[:, 6, 0:32], ACT.Copy).then_inc(s["cum_read"], 1)
            act.wait_ge(s["last_ready"], 1)
            nc.scalar.activation(g["last"], c.ps[:, 7, 0:32], ACT.Copy).then_inc(s["last_read"], 1)
            act.wait_ge(s["exps_in"], 1)
            nc.scalar.activation(g["ecum"], g["cum"], ACT.Exp).then_inc(s["exps_done"], 1)
            nc.scalar.activation(g["elast"], g["last"], ACT.Exp).then_inc(s["exps_done"], 1)
            nc.scalar.activation(g["erest"], g["ax"], ACT.Exp).then_inc(s["exps_done"], 1)
            act.wait_ge(s["turned"], 1)
            nc.scalar.activation(c.gate_rowsT[:, 0:2 * P], c.ps[0:32, 6, 0:2 * P], ACT.Copy).then_inc(s["rows_read"], 1)
            for i in range(6):
                act.wait_ge(s["eps_done"], i + 1)
                nc.scalar.activation(sq[:, i, :], sq[:, i, :], ACT.Sqrt).then_inc(s["root"], 1)
            for t in range(ALL):
                act.wait_ge(s["k_turned"], t + 1)
                nc.scalar.activation(c.k_tok[:, t], c.ps[:, 6 + t % 2], ACT.Copy).then_inc(s["k_tok"], 1)

        @block.vector
        def _(dve):
            step = [0]

            def then(ins):
                ins.then_inc(s["gate_step"], 1)
                step[0] += 1
                dve.wait_ge(s["gate_step"], step[0])

            dve.wait_ge(s["dn_in"], 16)
            rest = c.rest.rearrange("p (t x h) -> p t x h", t=ALL, x=4)[:, :, 2:4, :]
            bias = dn[:, 8:16].rearrange("p (d h) -> p d h", d=2)
            for d in range(2):
                ins = nc.vector.tensor_tensor(g["x"][:, 16 * d:16 * d + 16].rearrange("p (t h) -> p t h", t=ALL),
                                              rest[:, :, d, :], bias[:, d].unsqueeze(1).broadcast_to([P, ALL, DNH]), ALU.add)
                if d:
                    then(ins)
                else:
                    ins.then_inc(s["inv"], 1)
                    dve.wait_ge(s["inv"], 1)
            then(nc.vector.scalar_tensor_tensor(out=g["ax"], in0=g["x"], scalar=-1.0, in1=g["x"], op0=ALU.mult, op1=ALU.max))
            dve.wait_ge(s["exp_x"], 1)
            then(nc.vector.tensor_scalar(g["t"], g["e"], 2.0, None, ALU.add))
            then(nc.vector.reciprocal(g["t"], g["t"]))
            then(nc.vector.tensor_tensor(g["t"], g["t"], g["e"], ALU.mult))
            then(nc.vector.tensor_tensor(g["t2"], g["t"], g["t"], ALU.mult))
            then(nc.vector.tensor_scalar(g["g"], g["t2"], 1.0 / 17, 1.0 / 15, ALU.mult, ALU.add))
            for n in (13, 11, 9, 7, 5, 3, 1):
                then(nc.vector.tensor_tensor(g["g"], g["g"], g["t2"], ALU.mult))
                then(nc.vector.tensor_scalar(g["g"], g["g"], 1.0 / n, None, ALU.add))
            then(nc.vector.scalar_tensor_tensor(out=g["g"], in0=g["t"], scalar=2.0, in1=g["g"], op0=ALU.mult, op1=ALU.mult))
            then(nc.vector.scalar_tensor_tensor(out=g["g"], in0=g["x"], scalar=0.0, in1=g["g"], op0=ALU.max, op1=ALU.add))
            dve.wait_ge(s["exp_a"], 1)
            ea = dn[:, 0:8].rearrange("p (d h) -> p d h", d=2)
            for d in range(2):
                gd = g["g"][:, 16 * d:16 * d + 16].rearrange("p (t h) -> p t h", t=ALL)
                then(nc.vector.tensor_tensor(gd, gd, ea[:, d].unsqueeze(1).broadcast_to([P, ALL, DNH]), ALU.mult))
            then(nc.vector.tensor_scalar(g["g"], g["g"], -1.0, None, ALU.mult))
            dve.sem_inc(s["g_ready"], 1)
            dve.wait_ge(s["last_read"], 1)
            then(nc.vector.tensor_tensor(g["ax"], g["last"], g["cum"], ALU.subtract))
            dve.sem_inc(s["exps_in"], 1)
            dve.wait_ge(s["exps_done"], 3)
            dve.wait_ge(s["beta"], 1)
            then(nc.vector.scalar_tensor_tensor(out=g["nbe"], in0=g["beta"], scalar=-1.0, in1=g["ecum"], op0=ALU.mult,
                                                op1=ALU.mult))
            for i in range(6):
                dve.wait_ge(s["sum_ready"], i + 1)
                nc.vector.tensor_scalar(sq[:, i, :], c.ps[:, i], 1e-6, None, ALU.add).then_inc(s["eps_done"], 1)
            for i in range(6):
                dve.wait_ge(s["root"], i + 1)
                nc.vector.reciprocal(c.ps[:, i], sq[:, i, :]).then_inc(s["inv"], 1)
                dve.wait_ge(s["inv"], i + 2)
                nc.vector.scalar_tensor_tensor(out=seg(i), in0=seg(i), scalar=float(P) ** -0.5 if i < 2 else 1.0,
                                               in1=c.ps[:, i], op0=ALU.mult, op1=ALU.mult).then_inc(s["unit"], 1)


def delta_inverse_stage(nc, c):
    GROUPS = [(t, d) for t in range(ALL) for d in range(2)]
    names = ["rows0", "rows1", "diff0", "diff1", "decay0", "decay1", "prep_step0", "prep_step1", "start0", "start1",
             "xt0", "xt1", "x0", "x1", "y_ready0", "y_ready1", "y0", "y1", "p_ready0", "p_ready1", "step0", "step1"]
    with stage(nc, *names) as (block, *sems):
        s = dict(zip(names, sems))
        tokf = c.tok[:, :, :].rearrange("p a n -> p (a n)")
        q = c.work[:, O_Q:O_Q + 1024].rearrange("p (h t) -> p h t", h=DNH)
        k = c.work[:, O_K:O_K + 2048].rearrange("p (h t) -> p h t", h=DNH)

        def buf(e, n):
            return tokf[:, 2048 * e + 512 * n:2048 * e + 512 * (n + 1)].rearrange("p (h n) -> p h n", h=DNH)

        X, LT, Y, DT = ([buf(e, n) for e in range(2)] for n in range(4))
        level = c.hTf[:, M_LEVEL:M_BIAS].rearrange("p (d l n) -> p d l n", d=2, l=LEVELS)
        mbias = c.hTf[:, M_BIAS:M_END].rearrange("p (d n) -> p d n", d=2)

        def heads(bank):
            return c.ps[:, bank].rearrange("p (h n) -> p h n", h=DNH)

        def over_heads(m):
            return m.unsqueeze(1).broadcast_to([P, DNH, P])

        @block.tensor
        def _(pe):
            for pair in range(4):
                for e in range(2):
                    i = 2 * pair + e
                    t, d = GROUPS[i]
                    if pair:
                        pe.wait_ge(s[f"step{e}"], pair * (LEVELS - 1))
                    tr = slice(t * P, (t + 1) * P)
                    for h in range(DNH):
                        r = 16 * d + 4 * t + h
                        hs = slice(h * P, (h + 1) * P)
                        sel = c.ident[0:32, r:r + 1].broadcast_to([32, P])
                        mm(nc, c.ps[:, 4 * e, hs], sel, c.gate_rowsT[:, 0:P], True, True)
                        mm(nc, c.ps[:, 4 * e + 1, hs], sel, c.gate_rowsT[:, P:2 * P], True, True)
                        last = mm(nc, c.ps[:, 4 * e + 2, hs], k[:, h, tr], k[:, h, tr], True, True)
                        if t < TT:
                            last = mm(nc, c.ps[:, 4 * e + 3, hs], k[:, h, tr], q[:, h, tr], True, True)
                    last.then_inc(s[f"rows{e}"], 1)
                for e in range(2):
                    i = 2 * pair + e
                    pe.wait_ge(s[f"start{e}"], pair + 1)
                    for h in range(DNH):
                        last = nc.tensor.transpose(heads(4 * e)[:, h], c.invT[i][:, h], c.ident)
                    last.then_inc(s[f"xt{e}"], 1)
                for l in range(1, LEVELS):
                    n = pair * (LEVELS - 1) + l
                    for e in range(2):
                        if l == 1:
                            pe.wait_ge(s[f"x{e}"], pair + 1)
                        else:
                            pe.wait_ge(s[f"step{e}"], n - 1)
                        for h in range(DNH):
                            last = mm(nc, heads(4 * e + 1)[:, h], LT[e][:, h], X[e][:, h], True, True)
                        last.then_inc(s[f"y_ready{e}"], 1)
                    for e in range(2):
                        i = 2 * pair + e
                        pe.wait_ge(s[f"y{e}"], n)
                        for h in range(DNH):
                            last = mm(nc, heads(4 * e + 2)[:, h], Y[e][:, h], c.invT[i][:, h], True, True)
                        if l < LEVELS - 1:
                            for h in range(DNH):
                                last = mm(nc, heads(4 * e + 3)[:, h], c.invT[i][:, h], Y[e][:, h], True, True)
                        last.then_inc(s[f"p_ready{e}"], 1)

        @block.scalar
        def _(act):
            for pair in range(4):
                for e in range(2):
                    act.wait_ge(s[f"diff{e}"], 4 * pair + 4)
                    nc.scalar.activation(DT[e], DT[e], ACT.Exp).then_inc(s[f"decay{e}"], 1)
                for e in range(2):
                    act.wait_ge(s[f"xt{e}"], pair + 1)
                    nc.scalar.activation(X[e], heads(4 * e), ACT.Copy).then_inc(s[f"x{e}"], 1)

        @block.vector
        def _(dve):
            steps = [0, 0]

            def then(e, ins):
                ins.then_inc(s[f"prep_step{e}"], 1)
                steps[e] += 1
                dve.wait_ge(s[f"prep_step{e}"], steps[e])

            for pair in range(4):
                for e in range(2):
                    i = 2 * pair + e
                    t, d = GROUPS[i]
                    dve.wait_ge(s[f"rows{e}"], pair + 1)
                    for h in range(DNH):
                        col = 16 * d + 4 * t + h
                        nc.vector.scalar_tensor_tensor(out=DT[e][:, h], in0=heads(4 * e)[:, h],
                                                       scalar=c.gate_small["cum"][:, col:col + 1], in1=mbias[:, d],
                                                       op0=ALU.subtract, op1=ALU.add).then_inc(s[f"diff{e}"], 1)
                for e in range(2):
                    i = 2 * pair + e
                    t, d = GROUPS[i]
                    dve.wait_ge(s[f"decay{e}"], pair + 1)
                    if t < TT:
                        then(e, nc.vector.tensor_tensor(c.attT[i], heads(4 * e + 3), DT[e], ALU.mult))
                    then(e, nc.vector.tensor_tensor(DT[e], heads(4 * e + 2), DT[e], ALU.mult))
                    then(e, nc.vector.tensor_tensor(LT[e], heads(4 * e + 1), DT[e], ALU.mult))
                    then(e, nc.vector.tensor_tensor(Y[e], LT[e], over_heads(level[:, 1 - d, 0]), ALU.mult))
                    nc.vector.tensor_tensor(c.invT[i], over_heads(c.ident), Y[e], ALU.subtract).then_inc(s[f"start{e}"], 1)
                    dve.wait_ge(s[f"start{e}"], pair + 1)
                for l in range(1, LEVELS):
                    n = pair * (LEVELS - 1) + l
                    for e in range(2):
                        i = 2 * pair + e
                        t, d = GROUPS[i]
                        dve.wait_ge(s[f"y_ready{e}"], n)
                        nc.vector.tensor_tensor(Y[e], heads(4 * e + 1), over_heads(level[:, d, l]), ALU.mult).then_inc(s[f"y{e}"], 1)
                    for e in range(2):
                        i = 2 * pair + e
                        dve.wait_ge(s[f"p_ready{e}"], n)
                        if l < LEVELS - 1:
                            then(e, nc.vector.tensor_tensor(X[e], X[e], heads(4 * e + 3), ALU.subtract))
                        nc.vector.tensor_tensor(c.invT[i], c.invT[i], heads(4 * e + 2), ALU.subtract).then_inc(s[f"step{e}"], 1)


def delta_scan_stage(nc, c):
    ORDER = [(2, 3, 0, 1), (3, 2, 1, 0)]
    names = []
    for d in range(2):
        names += [f"{n}{d}" for n in ("read", "values", "wanted", "fresh", "fresh_read", "vb", "kd", "grow", "state",
                                      "own_out", "out_scaled", "out")]
    with stage(nc, *names) as (block, *sems):
        s = dict(zip(names, sems))
        tokf = c.tok[:, :, :].rearrange("p a n -> p (a n)")
        q = c.work[:, O_Q:O_Q + 1024].rearrange("p (h t) -> p h t", h=DNH)
        k = c.work[:, O_K:O_K + 2048].rearrange("p (h t) -> p h t", h=DNH)
        g = c.gate_small

        def buf(d, n):
            return tokf[:, 2048 * d + 512 * n:2048 * d + 512 * (n + 1)].rearrange("p (h n) -> p h n", h=DNH)

        VB, VN, KD, OT = ([buf(d, n) for d in range(2)] for n in range(4))

        def heads(bank):
            return c.ps[:, bank].rearrange("p (h n) -> p h n", h=DNH)

        def col(name, d, t, h):
            i = 16 * d + 4 * t + h
            return g[name][:, i:i + 1]

        @block.tensor
        def _(pe):
            for i in range(4):
                for d in range(2):
                    t = ORDER[d][i]
                    tr = slice(t * P, (t + 1) * P)
                    if i:
                        pe.wait_ge(s[f"state{d}"], 4 * i)
                        for h in range(DNH):
                            last = mm(nc, heads(4 * d)[:, h], k[:, h, tr], c.state[d][:, h], True, True)
                        last.then_inc(s[f"read{d}"], 1)
                    if t < TT:
                        if i == 3:
                            pe.wait_ge(s[f"out_scaled{d}"], 4)
                        for h in range(DNH):
                            last = mm(nc, heads(4 * d + 2)[:, h], q[:, h, tr], c.state[d][:, h], True, True)
                        last.then_inc(s[f"own_out{d}"], 1)
                for d in range(2):
                    t = ORDER[d][i]
                    if i:
                        pe.wait_ge(s[f"values{d}"], 4 * i)
                    else:
                        pe.wait_ge(s[f"vb{d}"], 4)
                    for h in range(DNH):
                        last = mm(nc, heads(4 * d + 1)[:, h], c.invT[2 * t + d][:, h], VB[d][:, h], True, True)
                    last.then_inc(s[f"fresh{d}"], 1)
                for d in range(2):
                    t = ORDER[d][i]
                    pe.wait_ge(s[f"fresh_read{d}"], i + 1)
                    if i < 3:
                        pe.wait_ge(s[f"kd{d}"], 4 * i + 4)
                        for h in range(DNH):
                            last = mm(nc, heads(4 * d)[:, h], KD[d][:, h], VN[d][:, h], True, True)
                        last.then_inc(s[f"grow{d}"], 1)
                    if t < TT:
                        if i == 3:
                            pe.wait_ge(s[f"out{d}"], 1)
                        for h in range(DNH):
                            last = mm(nc, heads(4 * d + 3)[:, h], c.attT[2 * t + d][:, h], VN[d][:, h], True, True)
                        last.then_inc(s[f"own_out{d}"], 1)

        @block.scalar
        def _(act):
            for i in range(4):
                for d in range(2):
                    t = ORDER[d][i]
                    if i:
                        act.wait_ge(s[f"fresh{d}"], i)
                    for h in range(DNH):
                        nc.scalar.activation(VB[d][:, h], c.v_tok[:, t].rearrange("p (h n) -> p h n", h=DNH)[:, h], ACT.Copy,
                                             scale=col("beta", d, t, h)).then_inc(s[f"vb{d}"], 1)
                    if t < TT:
                        act.wait_ge(s[f"own_out{d}"], 2 * (i - 2) + 1)
                        if i == 3:
                            act.wait_ge(s[f"out{d}"], 1)
                        for h in range(DNH):
                            nc.scalar.activation(OT[d][:, h], heads(4 * d + 2)[:, h], ACT.Copy,
                                                 scale=col("ecum", d, t, h)).then_inc(s[f"out_scaled{d}"], 1)
                for d in range(2):
                    act.wait_ge(s[f"fresh{d}"], i + 1)
                    if i:
                        act.wait_ge(s[f"grow{d}"], i)
                    if i == 3:
                        act.wait_ge(s[f"own_out{d}"], 2)
                    nc.scalar.activation(VN[d], heads(4 * d + 1), ACT.Copy).then_inc(s[f"fresh_read{d}"], 1)

        @block.gpsimd
        def _(pool):
            for i in range(3):
                for d in range(2):
                    t = ORDER[d][i]
                    if i:
                        pool.wait_ge(s[f"grow{d}"], i)
                    for h in range(DNH):
                        nc.gpsimd.tensor_scalar(KD[d][:, h], c.k_tok[:, t].rearrange("p (h n) -> p h n", h=DNH)[:, h],
                                                col("erest", d, t, h), None, ALU.mult).then_inc(s[f"kd{d}"], 1)

        @block.vector
        def _(dve):
            for i in range(4):
                for d in range(2):
                    t = ORDER[d][i]
                    if i:
                        dve.wait_ge(s[f"read{d}"], i)
                        dve.wait_ge(s[f"vb{d}"], 4 * i + 4)
                        for h in range(DNH):
                            nc.vector.scalar_tensor_tensor(out=VB[d][:, h], in0=heads(4 * d)[:, h], scalar=col("nbe", d, t, h),
                                                           in1=VB[d][:, h], op0=ALU.mult, op1=ALU.add).then_inc(s[f"values{d}"], 1)
                for d in range(2):
                    t = ORDER[d][i]
                    if i < 3:
                        dve.wait_ge(s[f"grow{d}"], i + 1)
                        for h in range(DNH):
                            if i == 0:
                                nc.vector.tensor_copy(c.state[d][:, h], heads(4 * d)[:, h]).then_inc(s[f"state{d}"], 1)
                            else:
                                if t < TT:
                                    dve.wait_ge(s[f"own_out{d}"], 2 * (i - 2) + 1)
                                nc.vector.scalar_tensor_tensor(out=c.state[d][:, h], in0=c.state[d][:, h],
                                                               scalar=col("elast", d, t, h), in1=heads(4 * d)[:, h],
                                                               op0=ALU.mult, op1=ALU.add).then_inc(s[f"state{d}"], 1)
                    if t < TT:
                        dve.wait_ge(s[f"own_out{d}"], 2 * (i - 2) + 2)
                        dve.wait_ge(s[f"out_scaled{d}"], 4 * (i - 2) + 4)
                        ot = c.o_tok[:, t].rearrange("p (h n) -> p h n", h=DNH)
                        if i == 2:
                            nc.vector.tensor_tensor(ot, OT[d], heads(4 * d + 3), ALU.add).then_inc(s[f"out{d}"], 1)
                        else:
                            nc.vector.tensor_tensor(OT[d], OT[d], heads(4 * d + 3), ALU.add).then_inc(s[f"out{d}"], 1)
                            dve.wait_ge(s[f"out{d}"], 2)
                            dve.wait_ge(s[f"out{1 - d}"], 1)
                            nc.vector.tensor_tensor(ot, ot, OT[d], ALU.add).then_inc(s[f"out{d}"], 1)


def odd_out_stage(nc, c, w, m0):
    with stage(nc, "squares", "root", "step", "gated", "turned", "cols", "out_ready", "product", "added") as (
            block, squares, root, step, gated, turned, cols, out_ready, product, added):
        o = c.o_tok
        gs = c.work[:, O_GATE:O_GATE + 1024].rearrange("p (t n) -> p t n", t=TT)
        oT = c.work[:, O_Q:O_Q + 1024].rearrange("p (h t) -> p h t", h=DNH)
        hy = c.work[:, O_HY:O_HY + 1024].rearrange("p (f t) -> p f t", f=4)
        junk = c.junk[:, 0:P]
        sm = c.junk[:, P:P + 32]

        @block.sync
        def _(sp):
            for i in range(2):
                sp.wait_ge(out_ready, i + 1)
                w.refill(sp, m0 + i)

        @block.tensor
        def _(pe):
            for half in range(2):
                wt = w.landed(pe, m0 + half).rearrange("p (k n) -> p k n", k=4)
                if half:
                    for t in range(TT):
                        pe.wait_ge(gated, t + 1)
                        for h in range(DNH):
                            last = nc.tensor.transpose(c.ps[:, 4 + h // 2, (h % 2) * SEQ + t * P:(h % 2) * SEQ + (t + 1) * P],
                                                       o[:, t, h * P:(h + 1) * P], c.ident)
                    last.then_inc(turned, 1)
                    pe.wait_ge(cols, 1)
                src = oT if half else hy
                for kk in range(4):
                    for t in range(TT):
                        for n in range(2):
                            last = mm(nc, c.ps[:, 2 * t + n], src[:, kk, t * P:(t + 1) * P], wt[:, kk, n * BANK:(n + 1) * BANK],
                                      half + kk == 0, half == 1 and kk == 3)
                last.then_inc(out_ready, 1)

        @block.scalar
        def _(act):
            act.wait_ge(squares, 8)
            nc.scalar.activation(sm[:, 8:16], sm[:, 0:8], ACT.Sqrt).then_inc(root, 1)
            act.wait_ge(turned, 1)
            nc.scalar.activation(oT.rearrange("p h t -> p (h t)"), c.ps[:, 4:6, :].rearrange("p b n -> p (b n)"), ACT.Copy,
                                 scale=c.par[:, S_DNG:S_DNG + 1]).then_inc(cols, 1)

        @block.vector
        def _(dve):
            for i in range(8):
                oh = o[:, i // 4, (i % 4) * P:(i % 4 + 1) * P]
                nc.vector.tensor_tensor_reduce(out=junk, in0=oh, in1=oh, scale=1.0 / P, scalar=EPS, op0=ALU.mult, op1=ALU.add,
                                               accum_out=sm[:, i:i + 1]).then_inc(squares, 1)
                dve.wait_ge(squares, i + 1)
            dve.wait_ge(root, 1)
            nc.vector.reciprocal(sm[:, 16:24], sm[:, 8:16]).then_inc(step, 1)
            dve.wait_ge(step, 1)
            for i in range(8):
                oh = o[:, i // 4, (i % 4) * P:(i % 4 + 1) * P]
                nc.vector.tensor_scalar(oh, oh, sm[:, 16 + i:17 + i], None, ALU.mult).then_inc(step, 1)
            dve.wait_ge(step, 9)
            for t in range(TT):
                nc.vector.tensor_tensor(o[:, t], o[:, t], gs[:, t], ALU.mult).then_inc(gated, 1)
            dve.wait_ge(out_ready, 2)
            add_gated(nc, c, product, range(TT), 0)

        @block.gpsimd
        def _(pool):
            for t in range(TT):
                for n in range(2):
                    pool.wait_ge(product, 2 * t + n + 1)
                    xs = c.x[:, t, n * BANK:(n + 1) * BANK]
                    nc.gpsimd.tensor_tensor(xs, xs, c.tok[:, t, n * BANK:(n + 1) * BANK], ALU.add).then_inc(added, 1)
            pool.wait_ge(added, 2 * TT)


class Core:
    pass


def first_block(nc, c, layers, rows):
    with nc.Fori(0, DEPTH) as layer:
        w = Panels(c, layer, L1_PANELS, 0, 0)
        with stage(nc, "lay_in", "rows_in") as (block, lay_in, rows_in):
            @block.scalar
            def _(act):
                act.dma_start(c.lay[:, :], layers[layer]).then_inc(lay_in, 16)
                act.dma_start(c.rows[:, :], rows[layer].partition_broadcast(P)).then_inc(rows_in, 16)
                act.wait_ge(lay_in, 16)
                act.wait_ge(rows_in, 16)
        norm_stage(nc, c, [0, 1], lambda k, _: c.lay[:, C_FFN1 + k:C_FFN1 + k + 1])
        ffn_stage(nc, c, w, AT_FFN1)
        norm_stage(nc, c, [0, 1], lambda k, _: c.lay[:, C_MIX + k:C_MIX + k + 1])
        mixer1_stage(nc, c, w, AT_PROJ)
        norm_stage(nc, c, [0, 1], lambda k, _: c.lay[:, C_FFN2 + k:C_FFN2 + k + 1])
        ffn_stage(nc, c, w, AT_FFN2)


def token_norm_stage(nc, c, gain, out=None):
    with stage(nc, "gain_in", "squares", "mean_sq", "root", "step", "normed", "stored") as (
            block, gain_in, squares, mean_sq, root, step, normed, stored):
        @block.sync
        def _(sp):
            sp.dma_start(c.tok[:, 0], gain.partition_broadcast(P)).then_inc(gain_in, 16)
            if out is not None:
                sp.wait_ge(normed, TT)
                sp.dma_start(out.rearrange("(t p) n -> p t n", p=P), c.x[:, 0:TT, :]).then_inc(stored, 16)
                sp.wait_ge(stored, 16)

        @block.scalar
        def _(act):
            for t in range(TT):
                nc.scalar.activation(c.junk[:, :], c.x[:, t], ACT.Square,
                                     accum_out=c.stat[:, t:t + 1]).then_inc(squares, 1)
                act.wait_ge(squares, t + 1)
            act.wait_ge(mean_sq, 1)
            nc.scalar.activation(c.stat[:, 4:6], c.stat[:, 2:4], ACT.Sqrt).then_inc(root, 1)

        @block.vector
        def _(dve):
            dve.wait_ge(squares, TT)
            nc.vector.tensor_scalar(c.stat[:, 2:4], c.stat[:, 0:2], 1.0 / D, EPS, ALU.mult, ALU.add).then_inc(mean_sq, 1)
            dve.wait_ge(root, 1)
            nc.vector.reciprocal(c.stat[:, 6:8], c.stat[:, 4:6]).then_inc(step, 1)
            dve.wait_ge(step, 1)
            dve.wait_ge(gain_in, 16)
            for t in range(TT):
                nc.vector.scalar_tensor_tensor(out=c.x[:, t], in0=c.x[:, t], scalar=c.stat[:, 6 + t:7 + t],
                                               in1=c.tok[:, 0], op0=ALU.mult, op1=ALU.mult).then_inc(normed, 1)


def second_block(nc, c, final_gain, out):
    w = Panels(c, None, 0, DEPTH * L1_PANELS, PANELS)

    def modulated(j):
        return (lambda k, st: c.mod[:, 2 * j + 1, st, k:k + 1], lambda k, st: c.mod[:, 2 * j, st, k:k + 1])

    ada_stage(nc, c, w, B_ADA0, 0)
    norm_stage(nc, c, [0, 1, 2, 3], *modulated(0))
    even_mixer_stage(nc, c, w, B_EVEN)
    norm_stage(nc, c, [0, 1, 2, 3], *modulated(1))
    mlp_stage(nc, c, w, B_MLP0, [0, 1, 2, 3])
    ada_stage(nc, c, w, B_ADA1, 1)
    norm_stage(nc, c, [0, 1, 2, 3], *modulated(0))
    odd_project_stage(nc, c, w, B_ODD)
    for order in range(2):
        hyena_stage(nc, c, order)
    delta_features_stage(nc, c)
    delta_inverse_stage(nc, c)
    delta_scan_stage(nc, c)
    odd_out_stage(nc, c, w, B_ODD + 7)
    norm_stage(nc, c, [0, 1], *modulated(1))
    mlp_stage(nc, c, w, B_MLP1, [0, 1])
    token_norm_stage(nc, c, final_gain, out)
def program(nc, a, out):
    c = Core()
    with ExitStack() as ctx:
        def sb(name, *shape):
            return ctx.enter_context(nc.sbuf_tensor(name, [P, *shape], F32))

        c.ring = sb("ring", RING, PANEL)
        c.x = sb("x", 4, D)
        c.hT = sb("hT", DK, 4 * P)
        c.tok = sb("tok", 4, D)
        c.work = sb("work", 16 * 1024)
        c.hid = c.work[:, 0:FK * SEQ].rearrange("p (k t) -> p k t", k=FK)
        params = sb("params", C_END + R_END)
        c.lay = params[:, 0:C_END]
        c.rows = params[:, C_END:C_END + R_END]
        c.gate_rows = params[:, 0:4 * D].rearrange("p (g n) -> p g n", g=4)
        c.const = sb("const", K_END1)
        c.stat = sb("stat", 16)
        c.junk = sb("junk", D)
        c.par = sb("par", S_END)
        c.const2 = sb("const2", K2_END)
        small = sb("small", 2 * P + 64 + 16 + 64 + 1 + 13 * 32)
        c.ones = small[:, 0:P]
        c.mean512 = small[:, P:2 * P]
        c.mod = small[:, 256:320].rearrange("p (j s k) -> p j s k", j=4, s=2)
        c.silu_c = small[:, 320:336].rearrange("p (k s) -> p k s", s=2)
        c.rest = small[:, 336:400]
        c.subln = small[:, 400:401]
        c.gate_small = {n: small[:, 401 + 32 * j:433 + 32 * j] for j, n in enumerate(
            ("x", "ax", "e", "t", "t2", "g", "cum", "last", "ecum", "elast", "erest", "beta", "nbe"))}
        c.upper = c.const[:, K_UPPER:K_UPPER + P]
        c.lower = c.const2[:, K2_LOWER:K2_END]
        c.hTf = c.hT[:, :, :].rearrange("p k t -> p (k t)")
        tokf = c.tok[:, :, :].rearrange("p a n -> p (a n)")
        c.hidden_z = tokf[0:64, 3840:4096]
        c.gate_rowsT = c.junk[0:32, 256:512]
        c.k_tok = c.work[:, 9216:11264].rearrange("p (t n) -> p t n", t=ALL)
        c.v_tok = c.work[:, 11264:13312].rearrange("p (t n) -> p t n", t=ALL)
        c.invT = [c.work[:, at:at + 512].rearrange("p (h n) -> p h n", h=DNH)
                  for at in (*range(6144, 8192, 512), *range(13312, 15360, 512))]
        c.attT = [c.work[:, at:at + 512].rearrange("p (h n) -> p h n", h=DNH) for at in range(1024, 3072, 512)]
        c.state = [c.work[:, at:at + 512].rearrange("p (h n) -> p h n", h=DNH) for at in (15360, 15872)]
        c.o_tok = c.hTf[:, 2304:3328].rearrange("p (t n) -> p t n", t=TT)
        c.vrows, c.transforms, c.masks, c.w3 = (a[n] for n in ("vrows", "transforms", "masks", "w3"))
        c.ident = c.const[:, K_ID:K_ID + P]
        c.ps = ctx.enter_context(nc.psum_tensor("ps", [P, 8, BANK], F32))
        c.landed = [ctx.enter_context(nc.semaphore(f"panel_landed{i}")) for i in range(RING)]
        c.panels = a["panels"]
        with stage(nc, "x_in", "const_in", "filled") as (block, x_in, const_in, filled):
            @block.sync
            def _(sp):
                sp.dma_start(c.x[:, 0:TT, :], a["x"].rearrange("(t p) n -> p t n", p=P)).then_inc(x_in, 16)
                sp.dma_start(c.x[:, TT:ALL, :], a["ctx"].rearrange("(t p) n -> p t n", p=P)).then_inc(x_in, 16)
                for m in range(RING):
                    sp.dma_start(c.ring[:, m], a["panels"][m]).then_inc(c.landed[m], 16)
                sp.wait_ge(x_in, 32)

            @block.scalar
            def _(act):
                act.dma_start(c.const[:, :], a["const"]).then_inc(const_in, 16)
                act.dma_start(c.par[:, :], a["par"]).then_inc(const_in, 16)
                act.dma_start(c.const2[:, :], a["const2"]).then_inc(const_in, 16)
                act.wait_ge(const_in, 48)

            @block.gpsimd
            def _(pool):
                nc.gpsimd.memset(c.ones, 1.0).then_inc(filled, 1)
                nc.gpsimd.memset(c.mean512, 1.0 / 512).then_inc(filled, 1)
                pool.wait_ge(filled, 2)
        first_block(nc, c, a["layers"], a["rows"])
        token_norm_stage(nc, c, a["final_norm"])
        second_block(nc, c, a["final_g"], out)


def panel(w):
    k = w.shape[0] // P
    w = w.reshape(k, P, w.shape[1]).transpose(1, 0, 2).reshape(P, -1)
    return np.pad(w, ((0, 0), (0, PANEL - w.shape[1]))) if w.shape[1] < PANEL else w


def column_panels(w):
    return [panel(w[:, i:i + BANK]) for i in range(0, w.shape[1], BANK)]


def row_panels(w):
    return [panel(w[i:i + 4 * P]) for i in range(0, w.shape[0], 4 * P)]


def first_panels(i):
    out = []
    for l in range(DEPTH):
        def ffn(gu, down):
            g = gu[l].reshape(D, 2, GU, 256).transpose(0, 2, 1, 3).reshape(D, 2 * FF)
            return column_panels(g) + row_panels(down[l])
        u, va, q, k, v, qi = (i["w_in"][l][:, n * CH:(n + 1) * CH] for n in range(6))
        gates = i["w_in"][l][:, 6 * CH + SMALL:]
        out += ffn(i["ffn1_w_gu"], i["ffn1_w_down"])
        for part in (q, k, qi, v, u, va, gates):
            out += column_panels(part)
        out += row_panels(i["w_pa"][l]) + row_panels(i["w_pb"][l]) + row_panels(i["w_out"][l])
        out += ffn(i["ffn2_w_gu"], i["ffn2_w_down"])
    return out


def columns(v):
    return v.reshape(-1, P).T


def constants():
    out = np.zeros((P, K_END1), np.float32)
    out[:, K_ID:K_ID + P] = np.eye(P)
    out[:, K_UPPER:K_UPPER + P] = np.triu(np.ones((P, P)))
    pos = np.arange(SEQ)
    causal = np.where(pos[None, :] <= pos[:, None], 0.0, MASKED).astype(np.float32)
    out[:, K_CAUSAL:K_COS] = causal.reshape(TT, P, SEQ).transpose(1, 0, 2).reshape(P, -1)
    inv = np.float32(10000.0) ** (-np.arange(0, HD, 2, dtype=np.float32) / np.float32(HD))
    ang = pos.astype(np.float32)[:, None] * inv[None, :].astype(np.float32)
    cos, sin = np.cos(ang.astype(np.float64)), np.sin(ang.astype(np.float64))
    for at, tab in ((K_COS, np.concatenate([cos, cos], 1)), (K_SIN, np.concatenate([-sin, sin], 1))):
        out[:, at:at + TT * HD] = tab.reshape(TT, P, HD).transpose(1, 0, 2).reshape(P, -1)
    return out


def first_arrays(i):
    layers, rows = [], []
    for l in range(DEPTH):
        small = i["w_in"][l][:, 6 * CH:6 * CH + SMALL]
        layers.append(np.concatenate([
            columns(i["ffn1_norm"][l]), columns(i["mix_norm"][l]), columns(i["ffn2_norm"][l]), i["gmlp_b_s"][l].T,
            i["gmlp_w_s"][l].transpose(2, 0, 1).reshape(P, 4 * P),
            small.reshape(DK, P, SMALL).transpose(1, 0, 2).reshape(P, -1)], axis=1))
        rows.append(np.concatenate([i["b_gate"][l], i["gmlp_ln_g"][l], i["gmlp_ln_b"][l]]))
    return {"x": i["x"][0], "layers": np.stack(layers), "rows": np.stack(rows), "final_norm": i["final_norm"]}


def second_panels(i):
    even, odd = i["ev_w_in_2"][0], i["od_w_in_2"][0]

    def ada(l):
        w = i["ada_w_2"][l]
        return [p for part in (0, 1, 3, 4, 2, 5) for p in column_panels(w[:, part * D:(part + 1) * D])]

    def mlp(l):
        return column_panels(i["mlp_w1_2"][l]) + row_panels(i["mlp_w2_2"][l])

    glu = even[:, 0:2 * CH].reshape(D, 2, 2, 256).transpose(0, 2, 1, 3).reshape(D, 2 * CH)
    out = ada(0) + column_panels(glu) + column_panels(even[:, 2 * CH:]) + row_panels(i["ev_w_out_2"][0]) + mlp(0)
    hy, gate, qkv = odd[:, 0:3 * CH], odd[:, 3 * CH:4 * CH], odd[:, 4 * CH:7 * CH]
    return out + ada(1) + column_panels(hy) + column_panels(qkv) + column_panels(gate) + \
        row_panels(i["od_w_out_2"][0]) + mlp(1)


def channel_taps(w):
    return w.reshape(w.shape[0], -1, P).transpose(2, 1, 0).reshape(P, -1)


def on_partitions(w):
    return np.pad(w, ((0, P - w.shape[0]), (0, 0)))


def second_arrays(i):
    cond = np.stack([columns(i["c_2"][0]), columns(i["c_ctx_2"])], axis=2).reshape(P, -1)
    fb = np.stack([i[n][0] for n in ("od_hy_b1_2", "od_hy_freq1_2", "od_hy_b2_2", "od_hy_freq2_2")], axis=1)
    par = np.concatenate([
        cond, *(columns(i["ada_b_2"][l]) for l in range(DEPTH)), *(columns(i["norm1_g_2"][l]) for l in range(DEPTH)),
        *(columns(i["norm2_g_2"][l]) for l in range(DEPTH)), channel_taps(i["ev_conv_w_2"][0]),
        columns(i["ev_conv_b_2"][0]), columns(i["ev_ln_g_2"][0]), columns(i["ev_ln_b_2"][0]),
        i["ev_subln_g_2"][0][:, None], channel_taps(i["od_hy_short_w_2"][0]), columns(i["od_hy_short_b_2"][0]),
        columns(i["od_hy_skip_2"][0].reshape(-1)), channel_taps(i["od_dn_conv_w_2"][0]), i["od_dn_norm_g_2"][0][:, None],
        on_partitions(fb), on_partitions(i["od_hy_w1_2"][0]), on_partitions(i["od_hy_w2_2"][0]),
        i["od_w_in_2"][0][:, 7 * CH:].reshape(DK, P, 16).transpose(1, 0, 2).reshape(P, -1)], axis=1)
    assert par.shape == (P, S_END)
    gates = [i["ada_b_2"][l][part * D:(part + 1) * D] for l in range(DEPTH) for part in (2, 5)]
    vrows = np.concatenate([*gates, *(i[f"ev_{n}_2"][0] for n in ("lq1", "lk1", "lq2", "lk2")),
                            *(i[f"od_dn_{n}_2"][0] for n in ("alog_f", "alog_b", "dtb_f", "dtb_b"))])
    assert vrows.shape == (V_END,)
    return {"ctx": i["ctx_2"][0], "par": par, "vrows": vrows, "w3": i["od_hy_w3_2"][0], "final_g": i["final_g_2"]}


def second_constants():
    out = np.zeros((P, K2_END), np.float32)
    f32 = np.float32
    pos = np.arange(SEQ)
    inv = f32(10000.0) ** (-np.arange(16, dtype=f32) / f32(16))
    ar, ac = ((x.astype(f32)[:, None] * inv).astype(np.float64) for x in (pos // 64, pos % 64))
    cos = np.concatenate([np.cos(ar), np.cos(ar), np.cos(ac), np.cos(ac)], 1)
    sin = np.concatenate([-np.sin(ar), np.sin(ar), -np.sin(ac), np.sin(ac)], 1)
    for at, tab in ((K2_COS, cos), (K2_SIN, sin)):
        out[:, at:at + TT * 64] = tab.reshape(TT, P, 64).transpose(1, 0, 2).reshape(P, -1)
    out[:, K2_LOWER:] = np.tril(np.ones((P, P)))
    return out


def transform_constants():
    n = 2 * SEQ
    t, f = np.arange(SEQ), np.arange(SEQ)
    ang = 2 * np.pi * ((t[:, None] * f[None, :]) % n) / n
    top = (-1.0) ** t
    re, im = np.cos(ang), -np.sin(ang)
    im_top = im.copy()
    im_top[:, 0] = top
    signal = np.concatenate([re, im_top], 1)
    re_top = re[:, 0:P].copy()
    re_top[:, 0] = top
    forward = np.concatenate([re, im, re_top], 1)
    backward = np.concatenate([re, -im, re_top], 1)
    backward[0] = 0.0
    inv_re, inv_im = 2 * re.T / n, 2 * im.T / n
    inv_re[0] = 1.0 / n
    inv_im[0] = top / n
    inverse = np.concatenate([inv_re, inv_im], 0)

    def tiles(m):
        return m.reshape(-1, P, m.shape[1]).transpose(1, 0, 2).reshape(P, -1)

    f32 = np.float32
    lo, hi = math.log(1e-2) / 1.5, math.log(1e-2) / 0.3
    tt = np.linspace(0.0, 1.0, SEQ).astype(f32)
    deltas = np.abs(np.linspace(lo, hi, CH).astype(f32))
    window = np.exp((-tt[:, None] * deltas).astype(np.float64))
    omega = (f32(2.0 * math.pi) * np.arange(SEQ, dtype=f32) / f32(SEQ))[:, None]
    a = (omega * np.linspace(1e-4, 15, 16).astype(f32)).astype(np.float64)
    z = np.concatenate([tt[:, None], np.cos(a), -np.sin(a)], 1).T
    out = np.concatenate([tiles(np.concatenate([forward, backward])), tiles(signal), tiles(inverse), tiles(window),
                          on_partitions(z)], 1).astype(f32)
    assert out.shape == (P, T_END)
    return out


def mask_constants():
    i = np.arange(P)
    r, s = i[:, None], i[None, :]
    levels = [((r >> l) & 1) & ((s >> l) == (r >> l) - 1) for l in range(LEVELS)]
    levels += [m.T for m in levels]
    bias = [np.where(s >= r, 0.0, MASKED), np.where(s <= r, 0.0, MASKED)]
    return np.concatenate(levels + bias, 1).astype(np.float32)


def kernel(**inputs):
    import concourse.bacc as bacc
    from concourse.bass_utils import run_bass_kernel_spmd as run

    i = {k: np.asarray(v) for k, v in inputs.items()}
    arrays = {**first_arrays(i), **second_arrays(i), "const": constants(), "const2": second_constants(),
              "transforms": transform_constants(), "masks": mask_constants(),
              "panels": np.stack(first_panels(i) + second_panels(i))}
    assert arrays["panels"].shape[0] == PANELS
    arrays = {n: np.ascontiguousarray(v) for n, v in arrays.items()}
    nc = bacc.Bacc("TRN2", target_bir_lowering=False, num_devices=1)
    aps = {n: nc.dram_tensor(f"in_{n}", v.shape, F32, kind="ExternalInput").ap() for n, v in arrays.items()}
    out = nc.dram_tensor("out_x", (SEQ, D), F32, kind="ExternalOutput").ap()
    program(nc, aps, out)
    got = run(nc, [{f"in_{n}": v for n, v in arrays.items()}], core_ids=[0])
    return got.results[0]["out_x"][None]
```

```python
import math
from contextlib import ExitStack, contextmanager

import numpy as np

import concourse.bass as bass
from concourse import mybir

F32 = mybir.dt.float32
F32R = mybir.dt.float32r
ACT = mybir.ActivationFunctionType
ALU = mybir.AluOpType
AX = mybir.AxisListType.X

P = 128
D = 1024
DK = D // P
SEQ = 256
TT = SEQ // P
DEPTH = 2
EPS = 1e-6
BANK = 512

FF = 2816
FK = FF // P
GU = FF // 256
DN = -(-FK // 4)
HEADS, HD = 8, 64
CH = 512
SMALL = 72
TOPK = 64
IDX_SCALE = (64 ** -0.5) * (8 ** -0.5)
ATT_SCALE = 64 ** -0.5
MASKED = -1.0e30
TAKEN = -3.0e38

PANEL = 4096
RING = 2
QUART = PANEL // 4
L1_PANELS = GU + DN + 10 + 4 + GU + DN
assert L1_PANELS % RING == 0
AT_FFN1 = 0
AT_PROJ = GU + DN
AT_FFN2 = AT_PROJ + 14

C_FFN1, C_MIX, C_FFN2, C_BS = 0, 8, 16, 24
C_WS = 28
C_SMALL = C_WS + 4 * P
C_END = C_SMALL + DK * SMALL
R_BGATE, R_LNG, R_LNB, R_END = 0, 2 * D, 2 * D + CH, 2 * D + 2 * CH

K_ID = 0
K_UPPER = K_ID + P
K_CAUSAL = K_UPPER + P
K_COS = K_CAUSAL + TT * SEQ
K_SIN = K_COS + TT * HD
K_END1 = K_SIN + TT * HD


@contextmanager
def stage(nc, *names):
    with ExitStack() as ctx:
        sems = [ctx.enter_context(nc.semaphore(n)) for n in names]
        with nc.Block(no_gpsimd_drain=True) as block:
            yield (block, *sems)
        nums = [s.num for s in sems]
        nc.sync.sem_clear(range(min(nums), max(nums) + 1))
        nc.all_engine_barrier(sem_only=True)


class Panels:

    def __init__(self, c, layer, per_layer, first, total):
        self.c, self.layer, self.per, self.first, self.total = c, layer, per_layer, first, total

    def _base(self, unit):
        b = (self.first // RING) * unit
        return b if self.layer is None else self.layer * (self.per // RING * unit) + b

    def landed(self, eng, m):
        slot = m % RING
        eng.wait_ge(self.c.landed[slot], self._base(16) + 16 * (m // RING + 1))
        return self.c.ring[:, slot]

    def refill(self, sp, m):
        at = self.first + m + RING
        if self.layer is None and at >= self.total:
            return
        src = self.c.panels[at] if self.layer is None else self.c.panels[self.layer * self.per + at]
        sp.dma_start(self.c.ring[:, m % RING], src).then_inc(self.c.landed[m % RING], 16)


def mm(nc, out, lhsT, rhs, start, stop):
    return nc.tensor.matmul(out, lhsT, rhs, start=start, stop=stop)


def norm_stage(nc, c, tiles, scale, shift=None, split=False):
    n = len(tiles)
    T = n * P
    with stage(nc, "squares", "mean_sq", "root", "inv_root", "normed", "turned", "cols_act", "cols_dve", "hi", "lo") as (
            block, squares, mean_sq, root, inv_root, normed, turned, cols_act, cols_dve, hi, lo):
        ps = c.ps[:, :, :].rearrange("p b n -> p (b n)").rearrange("p (k t) -> p k t", k=DK)
        flat = c.tok[:, :, :].rearrange("p a n -> p (a n)")
        out = flat[:, 0:DK * T].rearrange("p (k t) -> p k t", k=DK) if split else c.hT[:, :, 0:T]

        def cols_of(t):
            return ps[:, :, t * P:(t + 1) * P] if n == 4 else \
                c.ps[:, 0:4, :].rearrange("p b (k t) -> p (b k) t", k=2)[:, :, t * P:(t + 1) * P]

        def cols_all(k):
            return ps[:, k, :] if n == 4 else c.ps[:, k // 2, (k % 2) * 256:(k % 2) * 256 + 256]

        @block.scalar
        def _(act):
            for i, t in enumerate(tiles):
                nc.scalar.activation(c.ps[:, 2 * i:2 * i + 2, :].rearrange("p b n -> p (b n)"), c.x[:, t], ACT.Square,
                                     accum_out=c.stat[:, i:i + 1]).then_inc(squares, 1)
            act.wait_ge(mean_sq, 1)
            nc.scalar.activation(c.stat[:, 8:8 + n], c.stat[:, 4:4 + n], ACT.Sqrt).then_inc(root, 1)
            act.wait_ge(turned, n)
            for k in (1, 3, 5, 7) if n == 4 else (2, 3, 6, 7):
                for st in range(n // TT):
                    tok = slice(st * SEQ, (st + 1) * SEQ)
                    nc.scalar.activation(out[:, k, tok], cols_all(k)[:, tok], ACT.Identity, scale=scale(k, st),
                                         bias=shift(k, st) if shift else 0.0).then_inc(cols_act, 1)
            if split:
                for half in range(2):
                    act.wait_ge(cols_act, (half + 1) * n)
                    act.wait_ge(cols_dve, (half + 1) * n)
                    nc.scalar.activation(c.hT_hi[:, 4 * half:4 * half + 4, 0:T], out[:, 4 * half:4 * half + 4, :],
                                         ACT.Copy).then_inc(hi, 1)

        @block.vector
        def _(dve):
            dve.wait_ge(squares, n)
            nc.vector.tensor_scalar(c.stat[:, 4:4 + n], c.stat[:, 0:n], 1.0 / D, EPS,
                                    ALU.mult, ALU.add).then_inc(mean_sq, 1)
            dve.wait_ge(root, 1)
            nc.vector.reciprocal(c.stat[:, 12:12 + n], c.stat[:, 8:8 + n]).then_inc(inv_root, 1)
            dve.wait_ge(inv_root, 1)
            for i, t in enumerate(tiles):
                nc.vector.tensor_scalar(c.tok[:, i], c.x[:, t], c.stat[:, 12 + i:13 + i], None,
                                        ALU.mult).then_inc(normed, 1)
            dve.wait_ge(turned, n)
            for k in (0, 2, 4, 6) if n == 4 else (0, 1, 4, 5):
                for st in range(n // TT):
                    tok = slice(st * SEQ, (st + 1) * SEQ)
                    nc.vector.tensor_scalar(out[:, k, tok], cols_all(k)[:, tok], scale(k, st),
                                            shift(k, st) if shift else None, ALU.mult,
                                            ALU.add if shift else ALU.bypass).then_inc(cols_dve, 1)
            if split:
                for half in range(2):
                    ks = slice(4 * half, 4 * half + 4)
                    dve.wait_ge(hi, half + 1)
                    nc.vector.tensor_tensor(c.hT_lo[:, ks, 0:T], out[:, ks, :], c.hT_hi[:, ks, 0:T].bitcast(F32),
                                            ALU.subtract).then_inc(lo, 1)

        @block.tensor
        def _(pe):
            for i in range(n):
                pe.wait_ge(normed, i + 1)
                dst = cols_of(i)
                for k in range(DK):
                    last = nc.tensor.transpose(dst[:, k], c.tok[:, i, k * P:(k + 1) * P], c.ident)
                last.then_inc(turned, 1)


def mm3(nc, out, lhsT, rhs, start, stop):
    nc.tensor.matmul(out, lhsT[0], rhs[0], start=start, stop=False)
    nc.tensor.matmul(out, lhsT[0], rhs[1], start=False, stop=False)
    return nc.tensor.matmul(out, lhsT[1], rhs[0], start=False, stop=stop)


def split_hi(nc, c, act, w, m, q, Q, quart_done, w_hi, dst=None):
    dst = c.w_hi if dst is None else dst
    n = dst.shape[1]
    if q == 0:
        w.landed(act, m)
    if Q >= n:
        act.wait_ge(quart_done, Q - n + 1)
    nc.scalar.activation(dst[:, Q % n], c.ring[:, m % RING, q * QUART:(q + 1) * QUART], ACT.Copy).then_inc(w_hi, 1)


def split_lo(nc, c, dve, m, q, Q, w_hi, w_lo, dst=None):
    hi, lo = dst or (c.w_hi, c.w_lo)
    n = hi.shape[1]
    dve.wait_ge(w_hi, Q + 1)
    nc.vector.tensor_tensor(lo[:, Q % n], c.ring[:, m % RING, q * QUART:(q + 1) * QUART],
                            hi[:, Q % n].bitcast(F32), ALU.subtract).then_inc(w_lo, 1)


def ffn_stage(nc, c, w, m0, loads=()):
    quarts = [(i, q) for i in range(GU + DN) for q in range(4 if i < GU else min(4, FK - 4 * (i - GU)))]
    with stage(nc, "w_hi", "w_lo", "quart_done", "silu_ready", "product", "hid_hi", "hid_lo", "added", "loaded") as (
            block, w_hi, w_lo, quart_done, silu_ready, product, hid_hi, hid_lo, added, loaded):
        hi, lo = (t[:, 0:FK * SEQ].rearrange("p (k t) -> p k t", k=FK) for t in (c.hid_hi, c.hid_lo))

        def last_quart(i):
            return sum(1 for x, _ in quarts if x <= i)

        @block.sync
        def _(sp):
            sp.wait_ge(c.rows_in, 16)
            for to, src in loads:
                sp.dma_start(to, src).then_inc(loaded, 16)
            for i in range(GU + DN):
                sp.wait_ge(w_lo, last_quart(i))
                w.refill(sp, m0 + i)
            if loads:
                sp.wait_ge(loaded, 16 * len(loads))

        @block.tensor
        def _(pe):
            for Q, (i, q) in enumerate(quarts):
                pe.wait_ge(w_lo, Q + 1)
                if i < GU:
                    if q == 0 and i >= 2:
                        pe.wait_ge(product, i - 1)
                    wt = [t[:, Q % 2].rearrange("p (k n) -> p k n", k=2) for t in (c.w_hi, c.w_lo)]
                    for f in range(4):
                        for kk in range(2):
                            k = 2 * q + kk
                            last = mm3(nc, c.ps[:, 4 * (i % 2) + f, 0:SEQ], [t[:, kk, f * P:(f + 1) * P] for t in wt],
                                       [t[:, k, 0:SEQ] for t in (c.hT_hi, c.hT_lo)], k == 0, k == DK - 1)
                    last.then_inc(quart_done, 1)
                else:
                    k = 4 * (i - GU) + q
                    if k % 2 == 0:
                        pe.wait_ge(hid_lo, k // 2 + 1)
                    for t in range(TT):
                        for n in range(2):
                            last = mm3(nc, c.ps[:, 4 + 2 * t + n], [h[:, k, t * P:(t + 1) * P] for h in (hi, lo)],
                                       [u[:, Q % 2, n * BANK:(n + 1) * BANK] for u in (c.w_hi, c.w_lo)],
                                       k == 0, k == FK - 1)
                    last.then_inc(quart_done, 1)

        @block.scalar
        def _(act):
            for Q, (i, q) in enumerate(quarts):
                split_hi(nc, c, act, w, m0 + i, q, Q, quart_done, w_hi)
                if q == 1 and 1 <= i <= GU:
                    b = 4 * ((i - 1) % 2)
                    act.wait_ge(quart_done, 4 * i)
                    if i >= 3:
                        act.wait_ge(hid_lo, i - 2)
                    nc.scalar.activation(c.tok[:, (i - 1) % 2, 0:BANK].rearrange("p (f t) -> p f t", f=2),
                                         c.ps[:, b:b + 2, 0:SEQ], ACT.Silu).then_inc(silu_ready, 1)
                if q == 2 and 1 <= i <= GU:
                    act.wait_ge(product, i)
                    nc.scalar.activation(hi[:, 2 * i - 2:2 * i, :].rearrange("p k t -> p (k t)"),
                                         c.tok[:, (i - 1) % 2, 0:BANK], ACT.Copy).then_inc(hid_hi, 1)

        @block.vector
        def _(dve):
            for Q, (i, q) in enumerate(quarts):
                split_lo(nc, c, dve, m0 + i, q, Q, w_hi, w_lo)
                if q == 1 and 1 <= i <= GU:
                    b = 4 * ((i - 1) % 2)
                    dve.wait_ge(silu_ready, i)
                    p = c.tok[:, (i - 1) % 2, 0:BANK].rearrange("p (f t) -> p f t", f=2)
                    nc.vector.tensor_tensor(p, c.ps[:, b + 2:b + 4, 0:SEQ], p, ALU.mult).then_inc(product, 1)
                if q == 2 and 1 <= i <= GU:
                    dve.wait_ge(hid_hi, i)
                    ks = slice(2 * i - 2, 2 * i)
                    nc.vector.tensor_tensor(lo[:, ks, :].rearrange("p k t -> p (k t)"), c.tok[:, (i - 1) % 2, 0:BANK],
                                            hi[:, ks, :].rearrange("p k t -> p (k t)").bitcast(F32),
                                            ALU.subtract).then_inc(hid_lo, 1)
            dve.wait_ge(quart_done, len(quarts))
            for t in range(TT):
                for n in range(2):
                    xs = c.x[:, t, n * BANK:(n + 1) * BANK]
                    nc.vector.scalar_tensor_tensor(out=xs, in0=c.ps[:, 4 + 2 * t + n], scalar=0.5, in1=xs,
                                                   op0=ALU.mult, op1=ALU.add).then_inc(added, 1)


def mixer1_stage(nc, c, w, m0):
    Q, K, QI, V, U, VA, GATES, PA, PB, WO = 0, 1, 2, 3, 4, 5, 6, 10, 11, 12
    UNITS = [(qb, h) for qb in range(TT) for h in (0, 1, 4, 5)]
    names = ["proj", "proj_read", "small_ready", "small_read", "rope_step", "roped", "kiroped", "q_turned", "q_cols",
             "logits", "relu_done", "score_step", "selected", "s_ready", "s_masked", "negmax", "exp_done", "p_turned",
             "p_cols", "pv", "o_norm", "o_step", "o_turned", "o_cols", "u_gelu", "v_gelu", "ln_step", "v_mean", "v_root",
             "v_norm", "ws_masked", "mixed", "ya", "ya_turned", "ya_cols", "gate_sum", "gate", "pa", "ma", "pb",
             "m_done", "m_turned", "m_cols", "out_ready", "added"]
    with stage(nc, *names) as (block, *sems):
        s = dict(zip(names, sems))
        proj, proj_read = s["proj"], s["proj_read"]
        q, k, qi, v = (c.work[:, a * 1024:(a + 1) * 1024].rearrange("p (t n) -> p t n", t=TT) for a in range(4))
        u, va = (c.work[:, a * 1024:(a + 1) * 1024].rearrange("p (t n) -> p t n", t=TT) for a in (4, 5))
        qT, kT, qiT, yaT = (c.work[:, a * 1024:(a + 1) * 1024].rearrange("p (k t) -> p k t", k=4) for a in (6, 7, 8, 9))
        oT = qiT
        gates = c.work[:, 10 * 1024:14 * 1024].rearrange("p (g t n) -> p g t n", g=2, t=TT)
        o = q
        m = c.work[:, 6 * 1024:8 * 1024].rearrange("p (t n) -> p t n", t=TT)
        mT = c.work[:, 4 * 1024:6 * 1024].rearrange("p (k t) -> p k t", k=DK)
        kiT = c.work[:, 14 * 1024:14 * 1024 + SEQ]
        ki = c.work[:, 14 * 1024 + 256:14 * 1024 + 512].rearrange("p (t a n) -> p t a n", t=TT, a=2)
        wi = c.work[:, 14 * 1024 + 512:14 * 1024 + 528].rearrange("p (t n) -> p t n", t=TT)
        top = c.work[:, 14 * 1024 + 528:14 * 1024 + 536]
        negm = c.work[:, 14 * 1024 + 544:14 * 1024 + 560]
        sums = c.work[:, 14 * 1024 + 560:14 * 1024 + 576]
        rsum = c.work[:, 14 * 1024 + 576:14 * 1024 + 592]
        bn = c.work[:, 14 * 1024 + 592:14 * 1024 + 604].rearrange("p (t n) -> p t n", t=TT)
        mv = c.work[:, 14 * 1024 + 604:14 * 1024 + 608].rearrange("p (t n) -> p t n", t=TT)
        vstd = c.work[:, 14 * 1024 + 608:14 * 1024 + 616]
        mxs = c.work[:, 14 * 1024 + 616:14 * 1024 + 632]
        score = c.work[:, 15 * 1024:15 * 1024 + 512].rearrange("p (t n) -> p t n", t=TT)
        bias = c.work[:, 15 * 1024 + 512:16 * 1024].rearrange("p (t n) -> p t n", t=TT)
        relu = c.tok[:, 0:2, :].rearrange("p a b -> p (a b)")
        ropes = c.tok[:, 2:4, :].rearrange("p a b -> p (a b)")
        sm = c.tok[:, 2, :].rearrange("p (a n) -> p a n", a=2)
        prob = c.tok[:, 0, :].rearrange("p (a n) -> p a n", a=2)
        probT = c.tok[:, 1, :].rearrange("p (a n) -> p a n", a=2)
        ws = c.lay[:, C_WS:C_WS + 4 * P].rearrange("p (g t) -> p g t", g=4)
        small_w = c.lay[:, C_SMALL:C_END].rearrange("p (k n) -> p k n", k=DK)
        cos = c.const[:, K_COS:K_SIN].rearrange("p (t n) -> p t n", t=TT)
        sin = c.const[:, K_SIN:K_END1].rearrange("p (t n) -> p t n", t=TT)
        causal = c.const[:, K_CAUSAL:K_COS].rearrange("p (t n) -> p t n", t=TT)

        @block.sync
        def _(sp):
            for i in range(PA):
                sp.wait_ge(proj, 2 * i + 2)
                w.refill(sp, m0 + i)
            for done, value, i in ((s["pa"], 2, PA), (s["pb"], 2, PB), (s["out_ready"], 1, WO), (s["out_ready"], 2, WO + 1)):
                sp.wait_ge(done, value)
                w.refill(sp, m0 + i)

        @block.tensor
        def _(pe):
            def panel_tile(i, t):
                wt = w.landed(pe, m0 + i).rearrange("p (k n) -> p k n", k=DK) if t == 0 else \
                    c.ring[:, (m0 + i) % RING].rearrange("p (k n) -> p k n", k=DK)
                if i >= 2:
                    pe.wait_ge(proj_read, 2 * (i - 2) + t + 1)
                for kk in range(DK):
                    last = mm(nc, c.ps[:, 2 * (i % 2) + t], c.hT[:, kk, t * P:(t + 1) * P], wt[:, kk, :],
                              kk == 0, kk == DK - 1)
                last.then_inc(proj, 1)

            def turn(src, n_turn):
                for b in range(4):
                    for t in range(TT):
                        last = nc.tensor.transpose(c.ps[:, 4 + b // 2, (b % 2) * 256 + t * P:(b % 2) * 256 + (t + 1) * P],
                                                   src[:, t, b * P:(b + 1) * P], c.ident)
                last.then_inc(s["q_turned"], 1)

            for t in range(TT):
                for kk in range(DK):
                    last = mm(nc, c.ps[:, 6, t * P:t * P + SMALL], c.hT[:, kk, t * P:(t + 1) * P], small_w[:, kk, :],
                              kk == 0, kk == DK - 1)
            last.then_inc(s["small_ready"], 1)
            for t in range(TT):
                panel_tile(Q, t)
            for t in range(TT):
                panel_tile(K, t)
            pe.wait_ge(s["roped"], 1)
            turn(q, 0)
            for t in range(TT):
                panel_tile(QI, t)
            pe.wait_ge(s["roped"], 2)
            pe.wait_ge(s["q_cols"], 1)
            turn(k, 1)
            for t in range(TT):
                panel_tile(V, t)
            pe.wait_ge(s["roped"], 3)
            pe.wait_ge(s["q_cols"], 2)
            turn(qi, 2)
            pe.wait_ge(s["kiroped"], 1)
            for t in range(TT):
                last = nc.tensor.transpose(c.ps[:, 7, t * P:(t + 1) * P], ki[:, t].rearrange("p a n -> p (a n)"), c.ident)
            last.then_inc(s["q_turned"], 1)
            for t in range(TT):
                panel_tile(U, t)
            pe.wait_ge(s["q_cols"], 4)
            n = 0
            for qb in range(TT):
                keys = (qb + 1) * P
                for half in range(2):
                    if n >= 2:
                        pe.wait_ge(s["relu_done"], n - 1)
                    for hh in range(4):
                        h = 4 * half + hh
                        hp = slice(64 * (h % 2), 64 * (h % 2) + 64)
                        last = mm(nc, c.ps[:, 4 + 2 * (n % 2) + hh % 2, (hh // 2) * 256:(hh // 2) * 256 + keys],
                                  qiT[hp, h // 2, qb * P:(qb + 1) * P], kiT[hp, 0:keys], True, True)
                    last.then_inc(s["logits"], 1)
                    n += 1
            for t in range(TT):
                panel_tile(VA, t)

            def scores(j):
                qb, h0 = UNITS[j]
                keys = (qb + 1) * P
                if j == 0:
                    pe.wait_ge(s["relu_done"], 4)
                if j >= 1:
                    pe.wait_ge(s["s_masked"], j)
                for e in range(2):
                    h = h0 + 2 * e
                    hp = slice(64 * (h % 2), 64 * (h % 2) + 64)
                    last = mm(nc, c.ps[:, 4, e * keys:(e + 1) * keys], qT[hp, h // 2, qb * P:(qb + 1) * P],
                              kT[hp, h // 2, 0:keys], True, True)
                last.then_inc(s["s_ready"], 1)

            def turn_probs(j):
                qb, h0 = UNITS[j]
                pe.wait_ge(s["exp_done"], 2 * j + 2)
                if j >= 1:
                    pe.wait_ge(s["p_cols"], j)
                for e in range(2):
                    for kb in range(qb + 1):
                        b = e * (qb + 1) + kb
                        last = nc.tensor.transpose(c.ps[:, 6, b * P:(b + 1) * P], prob[:, j % 2, b * P:(b + 1) * P],
                                                   c.ident)
                last.then_inc(s["p_turned"], 1)

            def weigh(j):
                qb, h0 = UNITS[j]
                pe.wait_ge(s["p_cols"], j + 1)
                if h0 == 0 and qb:
                    pe.wait_ge(s["o_norm"], qb)
                for e in range(2):
                    for kb in range(qb + 1):
                        b = e * (qb + 1) + kb
                        h = h0 + 2 * e
                        last = mm(nc, c.ps[:, 7, h * HD:(h + 1) * HD], probT[:, j % 2, b * P:(b + 1) * P],
                                  v[:, kb, h * HD:(h + 1) * HD], kb == 0, kb == qb)
                last.then_inc(s["pv"], 1)

            def spatial(n):
                if n == 0:
                    pe.wait_ge(s["ws_masked"], 1)
                pe.wait_ge(s["v_norm"], n + 1)
                if n:
                    pe.wait_ge(s["ya"], 4 * n)
                for g in range(4):
                    last = mm(nc, c.ps[:, 5, g * P:(g + 1) * P], ws[:, g, :], va[:, n, g * P:(g + 1) * P], True, True)
                last.then_inc(s["mixed"], 1)

            def turn_ya(n):
                pe.wait_ge(s["ya"], 4 * TT)
                if n:
                    pe.wait_ge(s["ya_cols"], n)
                for g in range(4):
                    last = nc.tensor.transpose(c.ps[:, 5, g * P:(g + 1) * P], u[:, n, g * P:(g + 1) * P], c.ident)
                last.then_inc(s["ya_turned"], 1)

            for j in range(8):
                scores(j)
                panel_tile(GATES + j // 2, j % 2)
                if j >= 1:
                    turn_probs(j - 1)
                if j >= 2:
                    weigh(j - 2)
                if j in (2, 3):
                    spatial(j - 2)
                if j in (5, 6):
                    turn_ya(j - 5)
            wt = w.landed(pe, m0 + PA).rearrange("p (k n) -> p k n", k=4)
            pe.wait_ge(s["ya_cols"], 2)
            pe.wait_ge(proj_read, 20)
            for t in range(TT):
                for kk in range(4):
                    for n in range(2):
                        last = mm(nc, c.ps[:, 2 * t + n], yaT[:, kk, t * P:(t + 1) * P], wt[:, kk, n * BANK:(n + 1) * BANK],
                                  kk == 0, kk == 3)
                last.then_inc(s["pa"], 1)
                if t == 0:
                    turn_probs(7)
                    weigh(6)
            weigh(7)
            pe.wait_ge(s["o_norm"], 2)
            for b in range(4):
                for t in range(TT):
                    last = nc.tensor.transpose(c.ps[:, 4 + b // 2, (b % 2) * 256 + t * P:(b % 2) * 256 + (t + 1) * P],
                                               o[:, t, b * P:(b + 1) * P], c.ident)
            last.then_inc(s["o_turned"], 1)
            wt = w.landed(pe, m0 + PB).rearrange("p (k n) -> p k n", k=4)
            pe.wait_ge(s["o_cols"], 1)
            for t in range(TT):
                for kk in range(4):
                    for n in range(2):
                        last = mm(nc, c.ps[:, 4 + 2 * t + n], oT[:, kk, t * P:(t + 1) * P],
                                  wt[:, kk, n * BANK:(n + 1) * BANK], kk == 0, kk == 3)
                last.then_inc(s["pb"], 1)
            pe.wait_ge(s["ma"], 4)
            for t in range(TT):
                pe.wait_ge(s["m_done"], 2 * t + 2)
                for kk in range(DK):
                    last = nc.tensor.transpose(c.ps[:, kk // 2, (kk % 2) * 256 + t * P:(kk % 2) * 256 + (t + 1) * P],
                                               m[:, t, kk * P:(kk + 1) * P], c.ident)
                last.then_inc(s["m_turned"], 1)
            for half in range(2):
                wt = w.landed(pe, m0 + WO + half).rearrange("p (k n) -> p k n", k=4)
                for kk in range(4):
                    k8 = 4 * half + kk
                    if k8 % 2 == 0:
                        pe.wait_ge(s["m_cols"], k8 // 2 + 1)
                    for t in range(TT):
                        for n in range(2):
                            last = mm(nc, c.ps[:, 4 + 2 * t + n], mT[:, k8, t * P:(t + 1) * P],
                                      wt[:, kk, n * BANK:(n + 1) * BANK], k8 == 0, k8 == DK - 1)
                last.then_inc(s["out_ready"], 1)

        @block.scalar
        def _(act):
            def columns(dst, sem):
                act.wait_ge(s["q_turned"], sem)
                nc.scalar.activation(dst.rearrange("p k t -> p (k t)"), c.ps[:, 4:6, :].rearrange("p b n -> p (b n)"),
                                     ACT.Copy).then_inc(s["q_cols"], 1)

            act.wait_ge(s["kiroped"], 1)
            for t in range(TT):
                nc.scalar.activation(wi[:, t], c.ps[:, 6, t * P + 64:t * P + 72], ACT.Copy,
                                     scale=IDX_SCALE).then_inc(s["small_read"], 1)
            columns(qT, 1)
            columns(kT, 2)
            for t in range(TT):
                act.wait_ge(proj, 2 * V + t + 1)
                act.wait_ge(proj_read, 2 * V + t)
                nc.scalar.activation(v[:, t], c.ps[:, 2 * (V % 2) + t], ACT.Copy).then_inc(proj_read, 1)
            columns(qiT, 3)
            act.wait_ge(s["q_turned"], 4)
            nc.scalar.activation(kiT, c.ps[:, 7, 0:SEQ], ACT.Copy).then_inc(s["q_cols"], 1)
            for t in range(TT):
                act.wait_ge(proj, 2 * U + t + 1)
                nc.scalar.activation(u[:, t], c.ps[:, 2 * (U % 2) + t], ACT.Gelu_apprx_tanh).then_inc(proj_read, 1)
            act.wait_ge(proj_read, 2 * U + 2)
            for n in range(4):
                qb = n // 2
                act.wait_ge(s["logits"], n + 1)
                if n >= 2:
                    act.wait_ge(s["score_step"], 4 * (n - 1))
                keys = (qb + 1) * P
                nc.scalar.activation(
                    relu[:, (n % 2) * 1024:(n % 2 + 1) * 1024].rearrange("p (h n) -> p h n", h=4)[:, :, 0:keys],
                    c.ps[:, 4 + 2 * (n % 2):6 + 2 * (n % 2), :].rearrange("p b (h n) -> p (b h) n", h=2)[:, :, 0:keys],
                    ACT.Relu).then_inc(s["relu_done"], 1)
            for t in range(TT):
                act.wait_ge(proj, 2 * VA + t + 1)
                nc.scalar.activation(va[:, t], c.ps[:, 2 * (VA % 2) + t], ACT.Gelu_apprx_tanh).then_inc(proj_read, 1)
            act.wait_ge(s["v_mean"], 1)
            nc.scalar.activation(vstd[:, 2:4], vstd[:, 0:2], ACT.Sqrt).then_inc(s["v_root"], 1)

            def exps(j):
                qb, h0 = UNITS[j]
                keys = (qb + 1) * P
                act.wait_ge(s["negmax"], j + 1)
                if j >= 2:
                    act.wait_ge(s["p_turned"], j - 1)
                if j == 0:
                    act.wait_ge(s["score_step"], 16)
                for e in range(2):
                    h = 8 * qb + h0 + 2 * e
                    nc.scalar.activation(prob[:, j % 2, e * keys:(e + 1) * keys], sm[:, j % 2, e * keys:(e + 1) * keys],
                                         ACT.Exp, bias=negm[:, h:h + 1],
                                         accum_out=sums[:, h:h + 1]).then_inc(s["exp_done"], 1)

            def prob_columns(j):
                qb, h0 = UNITS[j]
                n = 2 * (qb + 1) * P
                act.wait_ge(s["p_turned"], j + 1)
                if j >= 2:
                    act.wait_ge(s["pv"], j - 1)
                nc.scalar.activation(probT[:, j % 2, 0:n], c.ps[:, 6, 0:n], ACT.Copy).then_inc(s["p_cols"], 1)

            for j in range(8):
                exps(j)
                if j >= 1:
                    prob_columns(j - 1)
                if j in (6, 7):
                    n = j - 6
                    act.wait_ge(s["ya_turned"], n + 1)
                    nc.scalar.activation(yaT[:, :, n * P:(n + 1) * P], c.ps[:, 5, :].rearrange("p (g t) -> p g t", g=4),
                                         ACT.Copy).then_inc(s["ya_cols"], 1)
            prob_columns(7)
            for i in range(4):
                act.wait_ge(s["gate_sum"], 2 * i + 2)
                g = gates[:, i // 2, :, (i % 2) * BANK:(i % 2 + 1) * BANK]
                nc.scalar.activation(g, g, ACT.Sigmoid).then_inc(s["gate"], 1)
            act.wait_ge(s["o_turned"], 1)
            nc.scalar.activation(oT.rearrange("p k t -> p (k t)"), c.ps[:, 4:6, :].rearrange("p b n -> p (b n)"),
                                 ACT.Copy).then_inc(s["o_cols"], 1)
            act.wait_ge(s["m_turned"], 2)
            for b in range(1, 4, 2):
                act.wait_ge(s["m_cols"], b)
                nc.scalar.activation(mT[:, 2 * b:2 * b + 2, :].rearrange("p k t -> p (k t)"), c.ps[:, b],
                                     ACT.Copy).then_inc(s["m_cols"], 1)

        @block.vector
        def _(dve):
            rope_n = [0]

            def rope_tile(src, t, heads, dsts):
                n = heads * HD
                a = ropes[:, 0:n].rearrange("p (h n) -> p h n", h=heads)
                b = ropes[:, 512:512 + n].rearrange("p (h n) -> p h n", h=heads)
                sv = src.rearrange("p (h n) -> p h n", h=heads)
                ct = cos[:, t].unsqueeze(1).broadcast_to([P, heads, HD])
                st = sin[:, t].unsqueeze(1).broadcast_to([P, heads, HD])
                nc.vector.tensor_tensor(a, sv, ct, ALU.mult).then_inc(s["rope_step"], 1)
                nc.vector.tensor_tensor(b[:, :, 0:32], sv[:, :, 32:64], st[:, :, 0:32], ALU.mult).then_inc(s["rope_step"], 1)
                nc.vector.tensor_tensor(b[:, :, 32:64], sv[:, :, 0:32], st[:, :, 32:64], ALU.mult).then_inc(s["rope_step"], 1)
                rope_n[0] += 3
                dve.wait_ge(s["rope_step"], rope_n[0])
                for dst in dsts:
                    nc.vector.tensor_tensor(dst, a, b, ALU.add).then_inc(s["rope_step"], 1)
                    rope_n[0] += 1
                dve.wait_ge(s["rope_step"], rope_n[0])

            nc.vector.tensor_tensor(ws, ws, c.const[:, K_UPPER:K_UPPER + P].unsqueeze(1).broadcast_to([P, 4, P]),
                                    ALU.mult).then_inc(s["ws_masked"], 1)
            dve.wait_ge(s["small_ready"], 1)
            for t in range(TT):
                rope_tile(c.ps[:, 6, t * P:t * P + 64], t, 1, [ki[:, t, e:e + 1, :] for e in range(2)])
            dve.sem_inc(s["kiroped"], 1)
            for i, dst in ((0, q), (1, k), (2, qi)):
                for t in range(TT):
                    dve.wait_ge(proj, 2 * i + t + 1)
                    rope_tile(c.ps[:, 2 * (i % 2) + t], t, HEADS, [dst[:, t].rearrange("p (h n) -> p h n", h=HEADS)])
                    dve.sem_inc(proj_read, 1)
                dve.sem_inc(s["roped"], 1)
            dve.wait_ge(s["small_read"], 2)
            for n in range(4):
                qb = n // 2
                keys = (qb + 1) * P
                dve.wait_ge(s["relu_done"], n + 1)
                for hh in range(4):
                    h = 4 * (n % 2) + hh
                    at = (n % 2) * 1024 + (hh % 2) * 512 + (hh // 2) * 256
                    r = relu[:, at:at + keys]
                    sc = score[:, qb, 0:keys]
                    if h == 0:
                        nc.vector.tensor_scalar(sc, r, wi[:, qb, 0:1], None, ALU.mult).then_inc(s["score_step"], 1)
                    else:
                        dve.wait_ge(s["score_step"], 4 * n + hh)
                        nc.vector.scalar_tensor_tensor(out=sc, in0=r, scalar=wi[:, qb, h:h + 1], in1=sc,
                                                       op0=ALU.mult, op1=ALU.add).then_inc(s["score_step"], 1)
            step = [16]

            def then(ins):
                ins.then_inc(s["score_step"], 1)
                step[0] += 1
                dve.wait_ge(s["score_step"], step[0])

            dve.wait_ge(s["score_step"], 16)
            for qb in range(TT):
                keys = (qb + 1) * P
                sc = score[:, qb, 0:keys]
                bi = bias[:, qb, 0:keys]
                then(nc.vector.tensor_tensor(sc, sc, causal[:, qb, 0:keys], ALU.add))
                for _ in range(TOPK // 8):
                    then(nc.vector.max(top, sc))
                    then(nc.vector.match_replace(sc, top, sc, TAKEN))
                then(nc.vector.tensor_scalar(bi, sc, TAKEN / 2, MASKED, ALU.is_gt, ALU.mult))
                then(nc.vector.tensor_tensor(bi, bi, causal[:, qb, 0:keys], ALU.add))

            def mask(j):
                qb, h0 = UNITS[j]
                keys = (qb + 1) * P
                dve.wait_ge(s["s_ready"], j + 1)
                if j >= 2:
                    dve.wait_ge(s["exp_done"], 2 * (j - 1))
                dst = sm[:, j % 2, 0:2 * keys].rearrange("p (e n) -> p e n", e=2)
                nc.vector.scalar_tensor_tensor(out=dst, in0=c.ps[:, 4, 0:2 * keys].rearrange("p (e n) -> p e n", e=2),
                                               scalar=ATT_SCALE, in1=bias[:, qb, 0:keys].unsqueeze(1).broadcast_to([P, 2, keys]),
                                               op0=ALU.mult, op1=ALU.add).then_inc(s["s_masked"], 1)
                dve.wait_ge(s["s_masked"], j + 1)
                h = 8 * qb + h0
                nc.vector.tensor_reduce(mxs[:, h:h + 3:2], dst, axis=AX, op=ALU.max).then_inc(s["o_step"], 1)
                ostep[0] += 1
                dve.wait_ge(s["o_step"], ostep[0])
                nc.vector.tensor_scalar(negm[:, h:h + 3:2], mxs[:, h:h + 3:2], -1.0, None, ALU.mult).then_inc(s["negmax"], 1)

            ostep = [0]

            def add_gate_bias(i, t):
                dve.wait_ge(proj, 2 * (GATES + i) + t + 1)
                nc.vector.tensor_tensor(gates[:, i // 2, t, (i % 2) * BANK:(i % 2 + 1) * BANK],
                                        c.ps[:, 2 * (i % 2) + t], c.rows[:, R_BGATE + i * BANK:R_BGATE + (i + 1) * BANK],
                                        ALU.add).then_inc(s["gate_sum"], 1)
                dve.wait_ge(s["gate_sum"], 2 * i + t + 1)
                dve.sem_inc(proj_read, 1)

            def norm_out(qb):
                dve.wait_ge(s["pv"], 4 * (qb + 1))
                nc.vector.reciprocal(rsum[:, 8 * qb:8 * qb + 8], sums[:, 8 * qb:8 * qb + 8]).then_inc(s["o_step"], 1)
                ostep[0] += 1
                dve.wait_ge(s["o_step"], ostep[0])
                nc.vector.tensor_tensor(o[:, qb].rearrange("p (h n) -> p h n", h=HEADS),
                                        c.ps[:, 7].rearrange("p (h n) -> p h n", h=HEADS),
                                        rsum[:, 8 * qb:8 * qb + 8].unsqueeze(2).broadcast_to([P, HEADS, HD]),
                                        ALU.mult).then_inc(s["o_norm"], 1)

            ln = [0]

            def ln_then(ins):
                ins.then_inc(s["ln_step"], 1)
                ln[0] += 1
                dve.wait_ge(s["ln_step"], ln[0])

            dve.wait_ge(proj_read, 2 * VA + 2)
            for t in range(TT):
                ln_then(nc.vector.bn_stats(bn[:, t], va[:, t]))
                ln_then(nc.vector.bn_aggr(mv[:, t], bn[:, t]))
            nc.vector.tensor_scalar(vstd[:, 0:2], mv[:, :, 1], EPS, None, ALU.add).then_inc(s["v_mean"], 1)
            dve.wait_ge(s["v_root"], 1)
            ln_then(nc.vector.reciprocal(vstd[:, 4:6], vstd[:, 2:4]))
            for t in range(TT):
                ln_then(nc.vector.tensor_scalar(va[:, t], va[:, t], mv[:, t, 0:1], vstd[:, 4 + t:5 + t],
                                                ALU.subtract, ALU.mult))
                ln_then(nc.vector.tensor_tensor(va[:, t], va[:, t], c.rows[:, R_LNG:R_LNB], ALU.mult))
                nc.vector.tensor_tensor(va[:, t], va[:, t], c.rows[:, R_LNB:R_END], ALU.add).then_inc(s["v_norm"], 1)

            def gate_u(n):
                dve.wait_ge(s["mixed"], n + 1)
                for g in range(4):
                    us = u[:, n, g * P:(g + 1) * P]
                    nc.vector.scalar_tensor_tensor(out=us, in0=c.ps[:, 5, g * P:(g + 1) * P],
                                                   scalar=c.lay[:, C_BS + g:C_BS + g + 1], in1=us,
                                                   op0=ALU.add, op1=ALU.mult).then_inc(s["ya"], 1)

            for j in range(8):
                mask(j)
                add_gate_bias(j // 2, j % 2)
                if j in (2, 3):
                    gate_u(j - 2)
                if j == 6:
                    norm_out(0)
            norm_out(1)
            for t in range(TT):
                dve.wait_ge(s["pa"], t + 1)
                for n in range(2):
                    dve.wait_ge(s["gate"], n + 1)
                    nc.vector.tensor_tensor(m[:, t, n * BANK:(n + 1) * BANK], c.ps[:, 2 * t + n],
                                            gates[:, 0, t, n * BANK:(n + 1) * BANK], ALU.mult).then_inc(s["ma"], 1)
            for t in range(TT):
                dve.wait_ge(s["pb"], t + 1)
                for n in range(2):
                    dve.wait_ge(s["gate"], n + 3)
                    gb = gates[:, 1, t, n * BANK:(n + 1) * BANK]
                    ms = m[:, t, n * BANK:(n + 1) * BANK]
                    ln_then(nc.vector.tensor_tensor(gb, c.ps[:, 4 + 2 * t + n], gb, ALU.mult))
                    nc.vector.tensor_tensor(ms, ms, gb, ALU.add).then_inc(s["m_done"], 1)
            dve.wait_ge(s["m_turned"], 2)
            for b in range(0, 4, 2):
                if b:
                    dve.wait_ge(s["m_cols"], b)
                nc.vector.tensor_copy(mT[:, 2 * b:2 * b + 2, :].rearrange("p k t -> p (k t)"),
                                      c.ps[:, b]).then_inc(s["m_cols"], 1)
            dve.wait_ge(s["out_ready"], 2)
            for t in range(TT):
                for n in range(2):
                    xs = c.x[:, t, n * BANK:(n + 1) * BANK]
                    nc.vector.tensor_tensor(xs, c.ps[:, 4 + 2 * t + n], xs, ALU.add).then_inc(s["added"], 1)
STREAMS = 2
ALL = TT * STREAMS
BOTH = SEQ * STREAMS
MODS = 6
CONV_W = 31
PAD = (CONV_W - 1) // 2
LAMBDA0 = 0.8 - 0.6 * math.exp(-0.3 * 0)
MLP = 4 * D
MK = MLP // P

B_ADA0 = 0
B_EVEN = B_ADA0 + 12
B_MLP0 = B_EVEN + 5 + 2
B_ADA1 = B_MLP0 + 16
B_ODD = B_ADA1 + 12
B_MLP1 = B_ODD + 7 + 2
B_END = B_MLP1 + 16
PANELS = DEPTH * L1_PANELS + B_END

S_COND = 0
S_ADAB = S_COND + DK * 2
S_N1 = S_ADAB + DEPTH * 48
S_N2 = S_N1 + DEPTH * DK
S_CONVW = S_N2 + DEPTH * DK
S_CONVB = S_CONVW + 4 * CONV_W
S_LNG = S_CONVB + 4
S_LNB = S_LNG + 4
S_SUBLN = S_LNB + 4
S_HYSW = S_SUBLN + 1
S_HYSB = S_HYSW + 12 * 3
S_HYSKIP = S_HYSB + 12
S_DNW = S_HYSKIP + 8
S_DNG = S_DNW + 12 * 5
S_FB = S_DNG + 1
S_W1 = S_FB + 4
S_W2 = S_W1 + 64
S_REST = S_W2 + 64
S_END = S_REST + DK * 16

V_ADAG = 0
V_LQK = V_ADAG + DEPTH * 2 * D
V_DN = V_LQK + 4 * 64
V_END = V_DN + 16

K2_COS = 0
K2_SIN = K2_COS + TT * 64
K2_LOWER = K2_SIN + TT * 64
K2_END = K2_LOWER + P


def ada_stage(nc, c, w, m0, layer):
    N = 12
    with stage(nc, "silu_c", "cond_hi", "cond_lo", "fold_made", "w_hi", "w_lo", "quart_done", "row_read", "cols_ready",
               "cols_read", "spread", "gates", "scales", "bias_in") as (
            block, silu_c, cond_hi, cond_lo, fold_made, w_hi, w_lo, quart_done, row_read, cols_ready,
            cols_read, spread, gates, scales, bias_in):
        cond = c.par[:, S_COND:S_COND + 2 * DK].rearrange("p (k s) -> p k s", s=2)
        bcol = c.par[:, S_ADAB + 48 * layer:S_ADAB + 48 * layer + 48]
        order = [0, 1, 3, 4]
        brow = c.tok[:, 0:2, :]
        row = c.tok[0:4, 2, :].rearrange("p (a n) -> p a n", a=2)
        fold = c.stat[0:4, 0:2]
        w_parts = [t[:, :].rearrange("p (b n) -> p b n", n=QUART) for t in (c.hid_hi, c.hid_lo)]
        nb = w_parts[0].shape[1]

        @block.sync
        def _(sp):
            sp.dma_start(brow.rearrange("p a n -> p (a n)"),
                         c.vrows[V_ADAG + 2 * D * layer:V_ADAG + 2 * D * (layer + 1)].partition_broadcast(P)).then_inc(bias_in, 16)
            for i in range(N):
                sp.wait_ge(w_lo, 4 * i + 4)
                w.refill(sp, m0 + i)

        @block.tensor
        def _(pe):
            def deal(i):
                pe.wait_ge(row_read, i + 1)
                r = row[:, i % 2, :]
                if i < 8:
                    if i >= 2:
                        pe.wait_ge(cols_read, i - 1)
                    for f in range(4):
                        last = mm(nc, c.ps[:, i % 2, 2 * f:2 * f + 2], r[:, f * P:(f + 1) * P], fold, True, True)
                    last.then_inc(cols_ready, 1)
                else:
                    if i >= 9:
                        pe.wait_ge(gates, 2 * (i - 8))
                    for s in range(STREAMS):
                        last = mm(nc, c.ps[:, 4 + s], fold[:, s:s + 1].broadcast_to([4, P]), r, True, True)
                    last.then_inc(spread, 1)

            pe.wait_ge(cond_lo, 1)
            pe.wait_ge(fold_made, 1)
            for i in range(N):
                for q in range(4):
                    Q = 4 * i + q
                    pe.wait_ge(w_lo, Q + 1)
                    if q == 0 and i >= 2:
                        pe.wait_ge(row_read, i - 1)
                    for part in w_parts:
                        for kk in range(2):
                            k = 2 * q + kk
                            last = mm(nc, c.ps[0:4, 2 + i % 2], c.cond_parts[:, k, :],
                                      part[:, Q % nb, kk * BANK:(kk + 1) * BANK],
                                      q == 0 and kk == 0 and part is w_parts[0], q == 3 and kk == 1 and part is w_parts[1])
                    last.then_inc(quart_done, 1)
                    if q == 1 and i >= 1:
                        deal(i - 1)
            deal(N - 1)

        @block.scalar
        def _(act):
            nc.scalar.activation(c.silu_c, cond, ACT.Silu).then_inc(silu_c, 1)
            act.wait_ge(silu_c, 1)
            nc.scalar.activation(c.cond_parts[:, :, 0:2], c.silu_c, ACT.Copy).then_inc(cond_hi, 1)

            def read_row(i):
                act.wait_ge(quart_done, 4 * i + 4)
                if i >= 2:
                    act.wait_ge(*((cols_ready, i - 1) if i < 10 else (spread, i - 9)))
                nc.scalar.activation(row[:, i % 2, :], c.ps[0:4, 2 + i % 2], ACT.Copy).then_inc(row_read, 1)

            for i in range(N):
                for q in range(4):
                    split_hi(nc, c, act, w, m0 + i, q, 4 * i + q, quart_done, w_hi, w_parts[0])
                    if q == 1 and i >= 1:
                        read_row(i - 1)
            read_row(N - 1)

        @block.vector
        def _(dve):
            dve.wait_ge(cond_hi, 1)
            nc.vector.tensor_tensor(c.cond_parts[:, :, 2:4], c.silu_c, c.cond_parts[:, :, 0:2].bitcast(F32),
                                    ALU.subtract).then_inc(cond_lo, 1)
            nc.vector.tensor_tensor(fold, c.ident[0:4, 0:2], c.ident[0:4, 2:4], ALU.add).then_inc(fold_made, 1)

            def take(i):
                if i < 8:
                    dve.wait_ge(cols_ready, i + 1)
                    at = order[i // 2] * DK + 4 * (i % 2)
                    nc.vector.tensor_tensor(
                        c.mod[:, i // 2, :, 4 * (i % 2):4 * (i % 2) + 4],
                        c.ps[:, i % 2, 0:8].rearrange("p (f s) -> p s f", s=2),
                        bcol[:, at:at + 4].unsqueeze(1).broadcast_to([P, 2, 4]), ALU.add).then_inc(cols_read, 1)
                else:
                    j = i - 8
                    dve.wait_ge(spread, j + 1)
                    at = (j % 2) * BANK
                    for s in range(STREAMS):
                        nc.vector.tensor_tensor(c.gate_rows[:, 2 * (j // 2) + s, at:at + BANK], c.ps[:, 4 + s],
                                                brow[:, j // 2, at:at + BANK], ALU.add).then_inc(gates, 1)

            for i in range(N):
                for q in range(4):
                    split_lo(nc, c, dve, m0 + i, q, 4 * i + q, w_hi, w_lo, w_parts)
                    if q == 3 and i >= 1:
                        take(i - 1)
                if i == 8:
                    dve.wait_ge(cols_read, 8)
                    for j, at in ((1, S_N1 + DK * layer), (3, S_N2 + DK * layer)):
                        for s in range(STREAMS):
                            nc.vector.scalar_tensor_tensor(out=c.mod[:, j, s, :], in0=c.mod[:, j, s, :], scalar=1.0,
                                                           in1=c.par[:, at:at + DK], op0=ALU.add, op1=ALU.mult).then_inc(scales, 1)
                    dve.wait_ge(bias_in, 16)
            take(N - 1)


def add_gated(nc, c, prod, tiles, gate):
    for i, t in enumerate(tiles):
        for n in range(2):
            b = 2 * i + n
            nc.vector.tensor_tensor(c.tok[:, i, n * BANK:(n + 1) * BANK], c.ps[:, b],
                                    c.gate_rows[:, 2 * gate + t // TT, n * BANK:(n + 1) * BANK], ALU.mult).then_inc(prod, 1)


def mlp_stage(nc, c, w, m0, tiles, parts):
    nt = len(tiles)
    T = nt * P
    PP = 8 // parts
    PK = MK // parts
    quarts = [(i, q) for i in range(2 * PP * parts) for q in range(4)]
    with stage(nc, "w_hi", "w_lo", "quart_done", "relu_done", "square", "hid_hi", "hid_lo", "product", "added") as (
            block, w_hi, w_lo, quart_done, relu_done, square, hid_hi, hid_lo, product, added):
        hi, lo = (t[:, 0:PK * T].rearrange("p (k t) -> p k t", k=PK) for t in (c.hid_hi, c.hid_lo))
        flat = c.tok[:, :, :].rearrange("p a n -> p (a n)")

        def place(i):
            part, j = divmod(i, 2 * PP)
            return part, j >= PP, j % PP, part * PP + min(j, PP)

        def buf(u):
            return flat[:, 2048 * (u % 2):2048 * (u % 2) + 4 * T].rearrange("p (f t) -> p f t", f=4)

        @block.sync
        def _(sp):
            for i in range(2 * PP * parts):
                sp.wait_ge(w_lo, 4 * i + 4)
                w.refill(sp, m0 + i)

        @block.tensor
        def _(pe):
            for Q, (i, q) in enumerate(quarts):
                part, second, j, ups = place(i)
                pe.wait_ge(w_lo, Q + 1)
                if not second:
                    if q == 0 and ups >= 2:
                        pe.wait_ge(square, ups - 1)
                    if q == 0 and j == 0 and part:
                        pe.wait_ge(product, 2 * nt * part)
                        pe.wait_ge(hid_lo, PP * part)
                    wt = [t[:, Q % 2].rearrange("p (k n) -> p k n", k=2) for t in (c.w_hi, c.w_lo)]
                    for f in range(4):
                        for kk in range(2):
                            k = 2 * q + kk
                            last = mm3(nc, c.ps[:, 4 * (j % 2) + f, 0:T], [t[:, kk, f * P:(f + 1) * P] for t in wt],
                                       [t[:, k, 0:T] for t in (c.hT_hi, c.hT_lo)], k == 0, k == DK - 1)
                else:
                    k = 4 * j + q
                    if q == 0:
                        pe.wait_ge(hid_lo, part * PP + j + 1)
                    if k == 0 and 2 * nt == 8:
                        pe.wait_ge(square, ups)
                    for t in range(nt):
                        for n in range(2):
                            last = mm3(nc, c.ps[:, 2 * t + n], [h[:, k, t * P:(t + 1) * P] for h in (hi, lo)],
                                       [u[:, Q % 2, n * BANK:(n + 1) * BANK] for u in (c.w_hi, c.w_lo)],
                                       k == 0, k == PK - 1)
                last.then_inc(quart_done, 1)

        def after(Q):
            i, q = quarts[Q]
            if q != 1 or i == 0:
                return None
            part, second, j, ups = place(i - 1)
            return None if second else (i - 1, ups)

        @block.scalar
        def _(act):
            for Q, (i, q) in enumerate(quarts):
                split_hi(nc, c, act, w, m0 + i, q, Q, quart_done, w_hi)
                done = after(Q)
                if done:
                    made, u = done
                    j = place(made)[2]
                    act.wait_ge(quart_done, 4 * i)
                    if u >= 2:
                        act.wait_ge(hid_lo, u - 1)
                    if j < 2 and u >= PP:
                        act.wait_ge(added, 2 * nt * (u // PP))
                    nc.scalar.activation(buf(u), c.ps[:, 4 * (j % 2):4 * (j % 2) + 4, 0:T], ACT.Relu).then_inc(relu_done, 1)
                    act.wait_ge(square, u + 1)
                    if j == 0 and u >= PP:
                        act.wait_ge(quart_done, 4 * 2 * PP * (u // PP))
                    nc.scalar.activation(hi[:, 4 * j:4 * j + 4, :], buf(u), ACT.Copy).then_inc(hid_hi, 1)

        @block.vector
        def _(dve):
            for Q, (i, q) in enumerate(quarts):
                split_lo(nc, c, dve, m0 + i, q, Q, w_hi, w_lo)
                done = after(Q)
                if done:
                    made, u = done
                    j = place(made)[2]
                    dve.wait_ge(relu_done, u + 1)
                    nc.vector.tensor_tensor(buf(u), c.ps[:, 4 * (j % 2):4 * (j % 2) + 4, 0:T], buf(u), ALU.mult).then_inc(square, 1)
                    dve.wait_ge(hid_hi, u + 1)
                    nc.vector.tensor_tensor(lo[:, 4 * j:4 * j + 4, :], buf(u), hi[:, 4 * j:4 * j + 4, :].bitcast(F32),
                                            ALU.subtract).then_inc(hid_lo, 1)
                if q == 1 and i and i % (2 * PP) == 0:
                    dve.wait_ge(quart_done, 4 * i)
                    add_gated(nc, c, product, tiles, 1)
            dve.wait_ge(quart_done, len(quarts))
            if parts > 1:
                dve.wait_ge(added, 2 * nt * (parts - 1))
            add_gated(nc, c, product, tiles, 1)

        @block.gpsimd
        def _(pool):
            for part in range(parts):
                for i, t in enumerate(tiles):
                    for n in range(2):
                        pool.wait_ge(product, 2 * nt * part + 2 * i + n + 1)
                        xs = c.x[:, t, n * BANK:(n + 1) * BANK]
                        nc.gpsimd.tensor_tensor(xs, xs, c.tok[:, i, n * BANK:(n + 1) * BANK], ALU.add).then_inc(added, 1)
            pool.wait_ge(added, 2 * nt * parts)


def even_mixer_stage(nc, c, w, m0):
    QP, KP, VP, WO = 2, 3, 4, 5
    names = ["glu_ready", "sig_done", "glu_done", "padded", "conv_step", "conv_done", "q_lat", "q_ctx", "k_lat", "k_ctx",
             "v_ready", "q_roped", "k_roped", "rope_step", "q_ctx_read", "k_ctx_read", "v_read", "q_turned", "k_turned",
             "qT_read", "kT_read", "lam_in", "lam_step", "lam_ready", "lam_exp", "s_ready", "max_step", "negmax", "exp_done",
             "mix_step", "mixed", "p_turned", "p_cols", "pv", "o_done", "o_squares", "o_root", "o_step", "o_normed",
             "o_turned", "o_cols", "ln_mean", "centred", "ln_sq", "ln_var", "ln_eps", "ln_root", "ln_inv", "ln_norm",
             "conv_out", "out_ready", "product", "added"]
    UNITS = [(t, h) for t in range(ALL) for h in range(4)]
    with stage(nc, *names) as (block, *sems):
        s = dict(zip(names, sems))

        def area(at, n):
            return c.work[:, at:at + n]

        PW = SEQ + 2 * PAD
        glu = area(0, 4 * 2 * PW).rearrange("p (f s n) -> p f s n", f=4, s=2)
        at = 4 * 2 * PW
        conv = area(at, 2048).rearrange("p (f t) -> p f t", f=4)
        q = area(at + 2048, 2048).rearrange("p (t n) -> p t n", t=ALL)
        k = area(at + 4096, 2048).rearrange("p (t n) -> p t n", t=ALL)
        v = area(at + 6144, 2048).rearrange("p (t n) -> p t n", t=ALL)
        qT = area(at + 8192, 2048).rearrange("p (f t) -> p f t", f=4)
        kT = area(at + 10240, 2048).rearrange("p (f t) -> p f t", f=4)
        sq = area(at + 12288, 1024).rearrange("p (a n) -> p a n", a=2)
        small = area(at + 13312, 128)
        o = q
        oT = area(at + 4096, 2048).rearrange("p (f t) -> p f t", f=4)
        sig = c.tok[:, 0:2, :].rearrange("p a (b n) -> p (a b) n", b=2)
        ropes = c.tok[:, 2:3, :].rearrange("p a n -> p (a n)")
        prob = c.tok[:, 0:2, :].rearrange("p a (b n) -> p a b n", b=2)
        probT = c.tok[:, 2, :].rearrange("p (a n) -> p a n", a=2)
        lqk = c.tok[:, 3, 0:256].rearrange("p (a b n) -> p a b n", a=2, b=2)
        junk = c.tok[:, 3, 256:512]
        lam = small[:, 0:4]
        mx, negm, sums, rs = (small[:, 8 + 4 * a:12 + 4 * a] for a in range(4))
        osq, ostd, oinv = (small[:, 32 + 16 * a:48 + 16 * a] for a in range(3))
        cos = c.const2[:, K2_COS:K2_SIN].rearrange("p (t n) -> p t n", t=TT)
        sin = c.const2[:, K2_SIN:K2_LOWER].rearrange("p (t n) -> p t n", t=TT)

        @block.sync
        def _(sp):
            sp.dma_start(c.tok[:, 3, 0:256], c.vrows[V_LQK:V_DN].partition_broadcast(P)).then_inc(s["lam_in"], 16)
            for i, (done, n) in enumerate([(s["glu_ready"], 2), (s["glu_ready"], 4), (s["q_ctx"], 1), (s["k_ctx"], 1),
                                           (s["v_ready"], 4), (s["out_ready"], 1), (s["out_ready"], 2)]):
                sp.wait_ge(done, n)
                w.refill(sp, m0 + i)

        @block.gpsimd
        def _(pool):
            nc.gpsimd.memset(glu[:, :, :, 0:PAD], 0.0).then_inc(s["padded"], 1)
            nc.gpsimd.memset(glu[:, :, :, PAD + SEQ:PW], 0.0).then_inc(s["padded"], 1)
            for i in range(ALL):
                for n in range(2):
                    pool.wait_ge(s["product"], 2 * i + n + 1)
                    xs = c.x[:, i, n * BANK:(n + 1) * BANK]
                    nc.gpsimd.tensor_tensor(xs, xs, c.tok[:, i, n * BANK:(n + 1) * BANK], ALU.add).then_inc(s["added"], 1)
            pool.wait_ge(s["added"], 2 * ALL)

        @block.tensor
        def _(pe):
            for i in range(2):
                wt = w.landed(pe, m0 + i).rearrange("p (k n) -> p k n", k=DK)
                for half in (1, 0):
                    for f in range(2):
                        for kk in range(DK):
                            last = mm(nc, c.ps[:, 4 * i + 2 * half + f], wt[:, kk, (2 * half + f) * P:(2 * half + f + 1) * P],
                                      c.hT[:, kk, :], kk == 0, kk == DK - 1)
                    last.then_inc(s["glu_ready"], 1)

            def tokens(wt, tiles, bank, sem):
                for i, t in enumerate(tiles):
                    for kk in range(DK):
                        last = mm(nc, c.ps[:, bank + i], c.hT[:, kk, t * P:(t + 1) * P], wt[:, kk, :], kk == 0, kk == DK - 1)
                    last.then_inc(sem, 1)

            def features(wt, bank, sem):
                for f in range(4):
                    for kk in range(DK):
                        last = mm(nc, c.ps[:, bank + f // 2, (f % 2) * SEQ:(f % 2 + 1) * SEQ], wt[:, kk, f * P:(f + 1) * P],
                                  c.hT[:, kk, SEQ:BOTH], kk == 0, kk == DK - 1)
                last.then_inc(sem, 1)

            wt = w.landed(pe, m0 + QP).rearrange("p (k n) -> p k n", k=DK)
            pe.wait_ge(s["glu_done"], 2)
            tokens(wt, (0, 1), 0, s["q_lat"])
            features(wt, 2, s["q_ctx"])
            wt = w.landed(pe, m0 + KP).rearrange("p (k n) -> p k n", k=DK)
            pe.wait_ge(s["glu_done"], 4)
            tokens(wt, (0, 1), 4, s["k_lat"])
            pe.wait_ge(s["q_roped"], 2)
            features(wt, 0, s["k_ctx"])
            wt = w.landed(pe, m0 + VP).rearrange("p (k n) -> p k n", k=DK)
            pe.wait_ge(s["q_ctx_read"], 1)
            tokens(wt, (0, 1), 2, s["v_ready"])
            pe.wait_ge(s["k_roped"], 2)
            tokens(wt, (2, 3), 4, s["v_ready"])
            pe.wait_ge(s["k_ctx_read"], 1)
            for src, bank, sem in ((q, 0, s["q_turned"]), (k, 2, s["k_turned"])):
                if bank == 2:
                    pe.wait_ge(s["v_read"], 2)
                for f in range(4):
                    for t in range(TT):
                        last = nc.tensor.transpose(c.ps[:, bank + f // 2, (f % 2) * SEQ + t * P:(f % 2) * SEQ + (t + 1) * P],
                                                   src[:, t, f * P:(f + 1) * P], c.ident)
                last.then_inc(sem, 1)
            pe.wait_ge(s["qT_read"], 1)
            pe.wait_ge(s["kT_read"], 1)
            pe.wait_ge(s["v_read"], 4)

            def scores(j):
                t, h = UNITS[j]
                k0 = 0 if t < TT else SEQ
                if j >= 2:
                    pe.wait_ge(s["exp_done"], 2 * j - 2)
                for e in range(2):
                    hp = slice(64 * e, 64 * e + 64)
                    last = mm(nc, c.ps[:, 2 * (j % 2) + e, 0:BOTH - k0], qT[hp, h, t * P:(t + 1) * P], kT[hp, h, k0:BOTH],
                              True, True)
                    last.then_inc(s["s_ready"], 1)

            def turn_probs(j):
                t, h = UNITS[j]
                nb = 4 if t < TT else 2
                pe.wait_ge(s["mixed"], j + 1)
                if j >= 1:
                    pe.wait_ge(s["p_cols"], j)
                for b in range(nb):
                    last = nc.tensor.transpose(c.ps[:, 4, b * P:(b + 1) * P], prob[:, j % 2, 0, b * P:(b + 1) * P], c.ident)
                last.then_inc(s["p_turned"], 1)

            def weigh(j):
                t, h = UNITS[j]
                tiles = range(4) if t < TT else range(2, 4)
                pe.wait_ge(s["p_cols"], j + 1)
                if h == 0 and t:
                    pe.wait_ge(s["o_done"], t)
                for b, kt in enumerate(tiles):
                    last = mm(nc, c.ps[:, 5, h * P:(h + 1) * P], probT[:, j % 2, b * P:(b + 1) * P],
                              v[:, kt, h * P:(h + 1) * P], b == 0, b == len(tiles) - 1)
                last.then_inc(s["pv"], 1)

            for j in range(len(UNITS) + 2):
                if j < len(UNITS):
                    scores(j)
                if 1 <= j <= len(UNITS):
                    turn_probs(j - 1)
                if j >= 2:
                    weigh(j - 2)
            pe.wait_ge(s["conv_done"], 4)
            for f in range(4):
                last = mm(nc, c.ps[:, 6], c.mean512, conv[:, f, :], f == 0, f == 3)
            last.then_inc(s["ln_mean"], 1)
            for f in range(4):
                pe.wait_ge(s["ln_sq"], f + 1)
                last = mm(nc, c.ps[:, 7], c.mean512, sq[:, f % 2, :], f == 0, f == 3)
                last.then_inc(s["ln_var"], 1)
            for t in range(ALL):
                pe.wait_ge(s["o_normed"], 4 * t + 4)
                for h in range(4):
                    last = nc.tensor.transpose(c.ps[:, h, t * P:(t + 1) * P], o[:, t, h * P:(h + 1) * P], c.ident)
            last.then_inc(s["o_turned"], 1)
            pe.wait_ge(s["conv_out"], 4)
            pe.wait_ge(s["o_cols"], 4)
            for half in range(2):
                wt = w.landed(pe, m0 + WO + half).rearrange("p (k n) -> p k n", k=4)
                src = oT if half else conv
                for kk in range(4):
                    for t in range(ALL):
                        for n in range(2):
                            last = mm(nc, c.ps[:, 2 * t + n], src[:, kk, t * P:(t + 1) * P],
                                      wt[:, kk, n * BANK:(n + 1) * BANK], half + kk == 0, half == 1 and kk == 3)
                last.then_inc(s["out_ready"], 1)

        @block.scalar
        def _(act):
            for i in range(2):
                act.wait_ge(s["glu_ready"], 2 * i + 1)
                for f in range(2):
                    if i:
                        act.wait_ge(s["glu_done"], f + 1)
                    nc.scalar.activation(sig[:, f, :], c.ps[:, 4 * i + 2 + f], ACT.Sigmoid).then_inc(s["sig_done"], 1)
            act.wait_ge(s["q_ctx"], 1)
            nc.scalar.activation(qT[:, :, SEQ:BOTH], c.ps[:, 2:4, :].rearrange("p b (f t) -> p (b f) t", f=2),
                                 ACT.Copy).then_inc(s["q_ctx_read"], 1)
            act.wait_ge(s["k_ctx"], 1)
            nc.scalar.activation(kT[:, :, SEQ:BOTH], c.ps[:, 0:2, :].rearrange("p b (f t) -> p (b f) t", f=2),
                                 ACT.Copy).then_inc(s["k_ctx_read"], 1)
            for t in range(ALL):
                act.wait_ge(s["v_ready"], t + 1)
                nc.scalar.activation(v[:, t], c.ps[:, 2 + t], ACT.Copy).then_inc(s["v_read"], 1)
            act.wait_ge(s["q_turned"], 1)
            nc.scalar.activation(qT[:, :, 0:SEQ], c.ps[:, 0:2, :].rearrange("p b (f t) -> p (b f) t", f=2),
                                 ACT.Copy).then_inc(s["qT_read"], 1)
            act.wait_ge(s["k_turned"], 1)
            nc.scalar.activation(kT[:, :, 0:SEQ], c.ps[:, 2:4, :].rearrange("p b (f t) -> p (b f) t", f=2),
                                 ACT.Copy).then_inc(s["kT_read"], 1)
            act.wait_ge(s["lam_ready"], 1)
            nc.scalar.activation(lam[:, 2:4], lam[:, 0:2], ACT.Exp).then_inc(s["lam_exp"], 1)

            def exps(j):
                t, h = UNITS[j]
                n = BOTH if t < TT else SEQ
                act.wait_ge(s["negmax"], j + 1)
                if j >= 2:
                    act.wait_ge(s["p_turned"], j - 1)
                for e in range(2):
                    col = 2 * (j % 2) + e
                    nc.scalar.activation(prob[:, j % 2, e, 0:n], c.ps[:, 2 * (j % 2) + e, 0:n], ACT.Exp, scale=ATT_SCALE,
                                         bias=negm[:, col:col + 1], accum_out=sums[:, col:col + 1]).then_inc(s["exp_done"], 1)

            def prob_columns(j):
                t, h = UNITS[j]
                n = BOTH if t < TT else SEQ
                act.wait_ge(s["p_turned"], j + 1)
                if j >= 2:
                    act.wait_ge(s["pv"], j - 1)
                nc.scalar.activation(probT[:, j % 2, 0:n], c.ps[:, 4, 0:n], ACT.Copy).then_inc(s["p_cols"], 1)

            for j in range(len(UNITS) + 1):
                if j < len(UNITS):
                    exps(j)
                if j >= 1:
                    prob_columns(j - 1)
            for f in range(4):
                act.wait_ge(s["centred"], f + 1)
                if f >= 2:
                    act.wait_ge(s["ln_var"], f - 1)
                nc.scalar.activation(sq[:, f % 2, :], conv[:, f, :], ACT.Square).then_inc(s["ln_sq"], 1)
            act.wait_ge(s["o_squares"], 16)
            nc.scalar.activation(ostd, osq, ACT.Sqrt).then_inc(s["o_root"], 1)
            act.wait_ge(s["ln_eps"], 1)
            nc.scalar.activation(sq[:, 0, :], sq[:, 0, :], ACT.Sqrt).then_inc(s["ln_root"], 1)
            for f in range(4):
                act.wait_ge(s["ln_norm"], f + 1)
                nc.scalar.activation(conv[:, f, :], conv[:, f, :], ACT.Silu, scale=c.par[:, S_LNG + f:S_LNG + f + 1],
                                     bias=c.par[:, S_LNB + f:S_LNB + f + 1]).then_inc(s["conv_out"], 1)
            act.wait_ge(s["o_turned"], 1)
            for f in range(4):
                nc.scalar.activation(oT[:, f, :], c.ps[:, f], ACT.Copy, scale=c.subln[:, 0:1]).then_inc(s["o_cols"], 1)

        @block.vector
        def _(dve):
            count = {}

            def then(name, ins):
                ins.then_inc(s[name], 1)
                count[name] = count.get(name, 0) + 1
                dve.wait_ge(s[name], count[name])

            dve.wait_ge(s["lam_in"], 16)
            for a in range(2):
                then("lam_step", nc.vector.tensor_tensor_reduce(
                    out=junk[:, 0:64], in0=lqk[:, a, 0], in1=lqk[:, a, 1], scale=1.0, scalar=0.0, op0=ALU.mult,
                    op1=ALU.add, accum_out=lam[:, a:a + 1]))
            dve.sem_inc(s["lam_ready"], 1)
            then("lam_step", nc.vector.tensor_scalar(c.subln[:, 0:1], c.par[:, S_SUBLN:S_SUBLN + 1], 1.0 - LAMBDA0, None,
                                                     ALU.mult))
            dve.wait_ge(s["padded"], 2)
            for i in range(2):
                dve.wait_ge(s["glu_ready"], 2 * i + 2)
                for f in range(2):
                    dve.wait_ge(s["sig_done"], 2 * i + f + 1)
                    nc.vector.tensor_tensor(glu[:, 2 * i + f, :, PAD:PAD + SEQ],
                                            c.ps[:, 4 * i + f].rearrange("p (s t) -> p s t", s=2),
                                            sig[:, f, :].rearrange("p (s t) -> p s t", s=2), ALU.mult).then_inc(s["glu_done"], 1)

            def convolve(f):
                dve.wait_ge(s["glu_done"], 4)
                for tap in range(CONV_W):
                    src = glu[:, f, :, tap:tap + SEQ]
                    dst = c.ps[:, 6 + tap % 2].rearrange("p (s t) -> p s t", s=2)
                    prev = c.ps[:, 7 - tap % 2].rearrange("p (s t) -> p s t", s=2)
                    wc = c.par[:, S_CONVW + f * CONV_W + tap:S_CONVW + f * CONV_W + tap + 1]
                    if tap == 0:
                        then("conv_step", nc.vector.tensor_scalar(dst, src, wc, c.par[:, S_CONVB + f:S_CONVB + f + 1],
                                                                  ALU.mult, ALU.add))
                    elif tap < CONV_W - 1:
                        then("conv_step", nc.vector.scalar_tensor_tensor(out=dst, in0=src, scalar=wc, in1=prev,
                                                                         op0=ALU.mult, op1=ALU.add))
                    else:
                        nc.vector.scalar_tensor_tensor(out=conv[:, f, :].rearrange("p (s t) -> p s t", s=2), in0=src,
                                                       scalar=wc, in1=prev, op0=ALU.mult, op1=ALU.add).then_inc(s["conv_done"], 1)

            def rope(ready, bank, dst, roped):
                a = ropes[:, 0:512]
                b = ropes[:, 512:1024]
                for t in range(TT):
                    dve.wait_ge(ready, t + 1)
                    sv = c.ps[:, bank + t]
                    ct = cos[:, t].unsqueeze(1).broadcast_to([P, 8, 64])
                    nc.vector.tensor_tensor(a.rearrange("p (h n) -> p h n", h=8), sv.rearrange("p (h n) -> p h n", h=8), ct,
                                            ALU.mult).then_inc(s["rope_step"], 1)
                    count["rope_step"] = count.get("rope_step", 0) + 1
                    for e in range(2):
                        bv = b.rearrange("p (h x y n) -> p h x y n", h=8, x=2, y=2)[:, :, :, e]
                        xv = sv.rearrange("p (h x y n) -> p h x y n", h=8, x=2, y=2)[:, :, :, 1 - e]
                        st = sin[:, t].rearrange("p (x y n) -> p x y n", x=2, y=2)[:, :, e].unsqueeze(1).broadcast_to([P, 8, 2, 16])
                        nc.vector.tensor_tensor(bv, xv, st, ALU.mult).then_inc(s["rope_step"], 1)
                        count["rope_step"] += 1
                    dve.wait_ge(s["rope_step"], count["rope_step"])
                    then("rope_step", nc.vector.tensor_tensor(dst[:, t], a, b, ALU.add))
                    dve.sem_inc(roped, 1)

            convolve(0)
            rope(s["q_lat"], 0, q, s["q_roped"])
            convolve(1)
            rope(s["k_lat"], 4, k, s["k_roped"])
            convolve(2)
            convolve(3)
            dve.wait_ge(s["lam_exp"], 1)
            then("lam_step", nc.vector.tensor_tensor(lam[:, 0:1], lam[:, 2:3], lam[:, 3:4], ALU.subtract))
            then("lam_step", nc.vector.tensor_scalar(lam[:, 1:2], lam[:, 0:1], LAMBDA0, None, ALU.add))

            def maxima(j):
                t, h = UNITS[j]
                n = BOTH if t < TT else SEQ
                for e in range(2):
                    col = 2 * (j % 2) + e
                    dve.wait_ge(s["s_ready"], 2 * j + e + 1)
                    nc.vector.tensor_reduce(mx[:, col:col + 1], c.ps[:, 2 * (j % 2) + e, 0:n], axis=AX,
                                            op=ALU.max).then_inc(s["max_step"], 1)
                dve.wait_ge(s["max_step"], 2 * j + 2)
                cs = slice(2 * (j % 2), 2 * (j % 2) + 2)
                nc.vector.tensor_scalar(negm[:, cs], mx[:, cs], -ATT_SCALE, None, ALU.mult).then_inc(s["negmax"], 1)

            def mix(j):
                t, h = UNITS[j]
                n = BOTH if t < TT else SEQ
                dve.wait_ge(s["exp_done"], 2 * j + 2)
                c0 = 2 * (j % 2)
                then("mix_step", nc.vector.reciprocal(rs[:, c0:c0 + 2], sums[:, c0:c0 + 2]))
                e0, e1 = prob[:, j % 2, 0, 0:n], prob[:, j % 2, 1, 0:n]
                then("mix_step", nc.vector.tensor_scalar(e1, e1, rs[:, c0 + 1:c0 + 2], lam[:, 1:2], ALU.mult, ALU.mult))
                nc.vector.scalar_tensor_tensor(out=e0, in0=e0, scalar=rs[:, c0:c0 + 1], in1=e1, op0=ALU.mult,
                                               op1=ALU.subtract).then_inc(s["mixed"], 1)

            def take_o(t):
                dve.wait_ge(s["pv"], 4 * t + 4)
                then("o_done", nc.vector.tensor_copy(o[:, t], c.ps[:, 5]))
                for h in range(4):
                    oh = o[:, t, h * P:(h + 1) * P]
                    i = 4 * t + h
                    then("o_step", nc.vector.tensor_tensor_reduce(out=junk[:, 0:P], in0=oh, in1=oh, scale=1.0 / P, scalar=EPS,
                                                                  op0=ALU.mult, op1=ALU.add, accum_out=osq[:, i:i + 1]))
                    dve.sem_inc(s["o_squares"], 1)

            for j in range(len(UNITS) + 1):
                if j < len(UNITS):
                    maxima(j)
                if j >= 1:
                    mix(j - 1)
                if j >= 5 and (j - 5) % 4 == 0:
                    take_o((j - 5) // 4)
            dve.wait_ge(s["ln_mean"], 1)
            for f in range(4):
                nc.vector.tensor_tensor(conv[:, f, :], conv[:, f, :], c.ps[:, 6], ALU.subtract).then_inc(s["centred"], 1)
            take_o(3)
            dve.wait_ge(s["ln_var"], 4)
            nc.vector.tensor_scalar(sq[:, 0, :], c.ps[:, 7], EPS, None, ALU.add).then_inc(s["ln_eps"], 1)
            dve.wait_ge(s["o_root"], 1)
            then("o_step", nc.vector.reciprocal(oinv, ostd))
            for i in range(16):
                oh = o[:, i // 4, (i % 4) * P:(i % 4 + 1) * P]
                nc.vector.tensor_scalar(oh, oh, oinv[:, i:i + 1], None, ALU.mult).then_inc(s["o_normed"], 1)
            dve.wait_ge(s["ln_root"], 1)
            nc.vector.reciprocal(c.ps[:, 6], sq[:, 0, :]).then_inc(s["ln_inv"], 1)
            dve.wait_ge(s["ln_inv"], 1)
            for f in range(4):
                nc.vector.tensor_tensor(conv[:, f, :], conv[:, f, :], c.ps[:, 6], ALU.mult).then_inc(s["ln_norm"], 1)
            dve.wait_ge(s["out_ready"], 2)
            add_gated(nc, c, s["product"], range(ALL), 0)
TAPS_HY, TAPS_DN = 3, 5
DNH = 4
O_HY, O_Q, O_K, O_V, O_GATE, O_TEMP = 0, 3072, 4096, 6144, 8192, 9216
TURN = (6.28125, 0.0019350051879882812, 3.019915979507459e-07)
LEVELS = 7

T_FH = 0
T_FU = T_FH + 4 * 640
T_INV = T_FU + 2 * 512
T_WIN = T_INV + 4 * SEQ
T_Z = T_WIN + 2 * 512
T_END = T_Z + SEQ
M_LEVEL = 0
M_BIAS = M_LEVEL + 2 * LEVELS * P
M_END = M_BIAS + 2 * P


def odd_project_stage(nc, c, w, m0):
    names = ["rest_ready", "rest_read", "proj", "padded", "copied", "conv_step", "conv_done", "gate_done", "conv_silu"]
    with stage(nc, *names) as (block, rest_ready, rest_read, proj, padded, copied, conv_step, conv_done, gate_done,
                               conv_silu):
        hy = c.work[:, O_HY:O_HY + 3072].rearrange("p (f t) -> p f t", f=12)
        gs = c.work[:, O_GATE:O_GATE + 1024].rearrange("p (t n) -> p t n", t=TT)
        rest_w = c.par[:, S_REST:S_END].rearrange("p (k n) -> p k n", k=DK)
        convs = [(i, 1, TAPS_HY, S_HYSW + 12 * i, S_HYSB + 4 * i, O_HY + 1024 * i) for i in range(3)]
        convs += [(3, 1, TAPS_DN, S_DNW, None, O_Q), (4, 2, TAPS_DN, S_DNW + 20, None, O_K),
                  (5, 2, TAPS_DN, S_DNW + 40, None, O_V)]

        def padded_buffer(i):
            _, ns, taps, _, _, _ = convs[i]
            n = 4 * ns * (SEQ + taps - 1)
            at = O_TEMP + 2080 * (i % 2)
            return c.work[:, at:at + n].rearrange("p (f s t) -> p f s t", f=4, s=ns)

        @block.sync
        def _(sp):
            for i in range(7):
                sp.wait_ge(proj, i + 1)
                w.refill(sp, m0 + i)

        @block.tensor
        def _(pe):
            for t in range(ALL):
                for k in range(DK):
                    last = mm(nc, c.ps[:, 4, t * 16:t * 16 + 16], c.hT[:, k, t * P:(t + 1) * P], rest_w[:, k, :],
                              k == 0, k == DK - 1)
            last.then_inc(rest_ready, 1)
            for i, ns, taps, _, _, _ in convs:
                wt = w.landed(pe, m0 + i).rearrange("p (k n) -> p k n", k=DK)
                n = ns * SEQ
                if i:
                    pe.wait_ge(copied, i)
                for f in range(4):
                    for k in range(DK):
                        last = mm(nc, c.ps[:, f, 0:n], wt[:, k, f * P:(f + 1) * P], c.hT[:, k, 0:n], k == 0, k == DK - 1)
                last.then_inc(proj, 1)
            wt = w.landed(pe, m0 + 6).rearrange("p (k n) -> p k n", k=DK)
            pe.wait_ge(copied, 6)
            for t in range(TT):
                for k in range(DK):
                    last = mm(nc, c.ps[:, t], c.hT[:, k, t * P:(t + 1) * P], wt[:, k, :], k == 0, k == DK - 1)
            last.then_inc(proj, 1)

        @block.gpsimd
        def _(pool):
            for i, ns, taps, _, _, _ in convs:
                if i >= 2:
                    pool.wait_ge(conv_done, 4 * (i - 1))
                side = (taps - 1) // 2
                buf = padded_buffer(i)
                nc.gpsimd.memset(buf[:, :, :, 0:side], 0.0).then_inc(padded, 1)
                nc.gpsimd.memset(buf[:, :, :, side + SEQ:], 0.0).then_inc(padded, 1)

        @block.scalar
        def _(act):
            act.wait_ge(rest_ready, 1)
            nc.scalar.activation(c.rest, c.ps[:, 4, 0:64], ACT.Copy).then_inc(rest_read, 1)
            for i, ns, taps, _, _, _ in convs:
                side = (taps - 1) // 2
                act.wait_ge(proj, i + 1)
                if i >= 2:
                    act.wait_ge(conv_done, 4 * (i - 1))
                act.wait_ge(padded, 2 * i + 2)
                for f in range(4):
                    ins = nc.scalar.activation(padded_buffer(i)[:, f, :, side:side + SEQ],
                                               c.ps[:, f, 0:ns * SEQ].rearrange("p (s t) -> p s t", s=ns), ACT.Copy)
                    if f == 3:
                        ins.then_inc(copied, 1)
                    else:
                        ins.then_inc(gate_done, 1)
            act.wait_ge(proj, 7)
            for t in range(TT):
                nc.scalar.activation(gs[:, t], c.ps[:, t], ACT.Silu).then_inc(gate_done, 1)
            act.wait_ge(conv_done, 24)
            for at, n in ((O_Q, 1024), (O_K, 2048), (O_V, 2048)):
                nc.scalar.activation(c.work[:, at:at + n], c.work[:, at:at + n], ACT.Silu).then_inc(conv_silu, 1)

        @block.vector
        def _(dve):
            step = 0
            for i, ns, taps, wcol, bcol, at in convs:
                dve.wait_ge(copied, i + 1)
                buf = padded_buffer(i)
                for f in range(4):
                    for tap in range(taps):
                        src = buf[:, f, :, tap:tap + SEQ]
                        wc = c.par[:, wcol + f * taps + tap:wcol + f * taps + tap + 1]
                        dst = c.ps[:, 6 + tap % 2, 0:ns * SEQ].rearrange("p (s t) -> p s t", s=ns)
                        prev = c.ps[:, 7 - tap % 2, 0:ns * SEQ].rearrange("p (s t) -> p s t", s=ns)
                        if tap == 0:
                            nc.vector.tensor_scalar(dst, src, wc, c.par[:, bcol + f:bcol + f + 1] if bcol else None, ALU.mult,
                                                    ALU.add if bcol else ALU.bypass).then_inc(conv_step, 1)
                        elif tap < taps - 1:
                            nc.vector.scalar_tensor_tensor(out=dst, in0=src, scalar=wc, in1=prev, op0=ALU.mult,
                                                           op1=ALU.add).then_inc(conv_step, 1)
                        else:
                            out = c.work[:, at + f * ns * SEQ:at + (f + 1) * ns * SEQ].rearrange("p (s t) -> p s t", s=ns)
                            nc.vector.scalar_tensor_tensor(out=out, in0=src, scalar=wc, in1=prev, op0=ALU.mult,
                                                           op1=ALU.add).then_inc(conv_done, 1)
                            dve.wait_ge(conv_done, 4 * i + f + 1)
                            continue
                        step += 1
                        dve.wait_ge(conv_step, step)


def hyena_stage(nc, c, order):
    names = ["tables_in", "w3_in", "arg", "range_step", "sine", "layer_ready", "filt_ready", "windowed", "absolute",
             "norm_ready", "norm_inv", "filt_done", "spec_ready", "spec_read", "z_turned", "z_read", "sig_ready", "sig_read",
             "prod_step", "prod_done", "y_ready", "gated"]
    with stage(nc, *names) as (block, *sems):
        s = dict(zip(names, sems))
        hy = c.work[:, O_HY:O_HY + 3072].rearrange("p (f t) -> p f t", f=12)
        filt = c.work[:, O_TEMP:O_TEMP + 2048].rearrange("p (d t n) -> p d t n", d=2, t=TT)
        spec = c.work[:, O_TEMP + 2048:O_TEMP + 4608].rearrange("p (f n) -> p f n", f=5)
        sig = c.work[:, O_TEMP + 4608:O_TEMP + 6656].rearrange("p (f n) -> p f n", f=4)
        fh = c.hTf[:, 0:2560].rearrange("p (d t n) -> p d t n", d=2, t=TT)
        fu = c.hTf[:, 2560:3584].rearrange("p (t n) -> p t n", t=TT)
        tokf = c.tok[:, :, :].rearrange("p a n -> p (a n)")
        inv = tokf[:, 0:1024].rearrange("p (f t) -> p f t", f=4)
        win = tokf[:, 1024:2048].rearrange("p (t n) -> p t n", t=TT)
        zT = tokf[0:33, 2048:2304]
        hid = tokf[0:64, 2304:2560]
        turns = c.hTf[0:64, 3584:3840]
        w3 = tokf[0:64, 2816:3840].rearrange("p (d n) -> p d n", d=2)
        mag = c.spare[:, 0:1024].rearrange("p (a n) -> p a n", a=2)
        z = c.spare[:, 0:1024].rearrange("p (t n) -> p t n", t=TT)
        w1 = c.par[0:33, S_W1:S_W1 + 64]
        w2 = c.par[0:64, S_W2:S_W2 + 64]
        fb = c.par[0:64, S_FB:S_FB + 4]
        ma, mb = (c.work[:, O_TEMP + a:O_TEMP + a + 1024].rearrange("p (f n) -> p f n", f=2) for a in (0, 1024))
        MAGIC = 12582912.0

        @block.sync
        def _(sp):
            if order == 0:
                sp.dma_start(c.hTf[:, 0:3584], c.transforms[:, T_FH:T_INV]).then_inc(s["tables_in"], 16)
                sp.dma_start(tokf[:, 0:2304], c.transforms[:, T_INV:T_END]).then_inc(s["tables_in"], 16)
            sp.dma_start(w3.rearrange("p d n -> p (d n)"), c.w3[:, order * 1024:(order + 1) * 1024]).then_inc(s["w3_in"], 16)

        @block.tensor
        def _(pe):
            if order == 0:
                pe.wait_ge(s["tables_in"], 32)
                mm(nc, c.ps[0:64, 0, 0:SEQ], w1, zT, True, True).then_inc(s["layer_ready"], 1)
                pe.wait_ge(s["sine"], 1)
                mm(nc, c.ps[0:64, 1, 0:SEQ], w2, hid, True, True).then_inc(s["layer_ready"], 1)
                pe.wait_ge(s["sine"], 2)
            for t in range(TT):
                for f in range(4):
                    last = nc.tensor.transpose(c.ps[:, 6 + t, f * P:(f + 1) * P], hy[:, f, t * P:(t + 1) * P], c.ident)
            last.then_inc(s["z_turned"], 1)
            pe.wait_ge(s["w3_in"], 16)
            for d in range(2):
                for t in range(TT):
                    mm(nc, c.ps[:, 2 * d + t], c.hidden_z[:, t * P:(t + 1) * P], w3[:, d, :], True, True).then_inc(s["filt_ready"], 1)
            for i in range(4):
                pe.wait_ge(s["absolute"], i + 1)
                last = mm(nc, c.ps[:, 4], c.ones, mag[:, i % 2, :], i == 0, i == 3)
                last.then_inc(s["norm_ready"], 1)
            pe.wait_ge(s["filt_done"], 4)
            for f in range(5):
                if f >= 4:
                    pe.wait_ge(s["spec_read"], f - 3)
                for i in range(4):
                    last = mm(nc, c.ps[:, f % 4], fh[:, i // 2, i % 2, f * P:(f + 1) * P], filt[:, i // 2, i % 2, :],
                              i == 0, i == 3)
                last.then_inc(s["spec_ready"], 1)
            pe.wait_ge(s["z_read"], 2)
            for f in range(4):
                bank = 5 + f if f < 3 else 4
                if f == 3:
                    pe.wait_ge(s["filt_done"], 4)
                for t in range(TT):
                    last = mm(nc, c.ps[:, bank], fu[:, t, f * P:(f + 1) * P], z[:, t, :], t == 0, t == TT - 1)
                last.then_inc(s["sig_ready"], 1)
            pe.wait_ge(s["prod_done"], 4)
            for f in range(4):
                for k in range(4):
                    last = mm(nc, c.ps[:, f, 0:SEQ], sig[:, k, f * P:(f + 1) * P], inv[:, k, :], k == 0, k == 3)
                last.then_inc(s["y_ready"], 1)

        @block.scalar
        def _(act):
            if order == 0:
                for i in range(2):
                    act.wait_ge(s["arg"], i + 1)
                    dst = c.hidden_z if i else hid
                    nc.scalar.activation(dst, turns, ACT.Sin).then_inc(s["sine"], 1)
            for i in range(4):
                act.wait_ge(s["windowed"], i + 1)
                if i >= 2:
                    act.wait_ge(s["norm_ready"], i - 1)
                nc.scalar.activation(mag[:, i % 2, :], filt[:, i // 2, i % 2, :], ACT.Abs).then_inc(s["absolute"], 1)
            act.wait_ge(s["norm_ready"], 4)
            act.wait_ge(s["z_turned"], 1)
            for t in range(TT):
                nc.scalar.activation(z[:, t, :], c.ps[:, 6 + t], ACT.Copy).then_inc(s["z_read"], 1)
            for f in range(5):
                act.wait_ge(s["spec_ready"], f + 1)
                nc.scalar.activation(spec[:, f, :], c.ps[:, f % 4], ACT.Copy).then_inc(s["spec_read"], 1)

        @block.vector
        def _(dve):
            count = {}

            def then(name, ins):
                ins.then_inc(s[name], 1)
                count[name] = count.get(name, 0) + 1
                dve.wait_ge(s[name], count[name])

            if order == 0:
                dve.wait_ge(s["tables_in"], 32)
                whole = c.hTf[0:64, 3840:4096]
                for i in range(2):
                    dve.wait_ge(s["layer_ready"], i + 1)
                    then("range_step", nc.vector.tensor_scalar(turns, c.ps[0:64, i, 0:SEQ], fb[:, 2 * i:2 * i + 1],
                                                               fb[:, 2 * i + 1:2 * i + 2], ALU.add, ALU.mult))
                    then("range_step", nc.vector.tensor_scalar(whole, turns, 1.0 / (2 * math.pi), MAGIC, ALU.mult, ALU.add))
                    then("range_step", nc.vector.tensor_scalar(whole, whole, MAGIC, None, ALU.subtract))
                    for part in TURN:
                        then("range_step", nc.vector.scalar_tensor_tensor(out=turns, in0=whole, scalar=-part, in1=turns,
                                                                          op0=ALU.mult, op1=ALU.add))
                    then("range_step", nc.vector.tensor_scalar(turns, turns, 3.1415925, -3.1415925, ALU.min, ALU.max))
                    dve.sem_inc(s["arg"], 1)
                    dve.wait_ge(s["sine"], i + 1)
            for i in range(4):
                dve.wait_ge(s["filt_ready"], i + 1)
                nc.vector.tensor_tensor(filt[:, i // 2, i % 2, :], c.ps[:, i], win[:, i % 2, :], ALU.mult).then_inc(s["windowed"], 1)
            dve.wait_ge(s["norm_ready"], 4)
            then("norm_inv", nc.vector.reciprocal(c.ps[:, 5], c.ps[:, 4]))
            for i in range(4):
                fl = filt[:, i // 2, i % 2, :]
                nc.vector.tensor_tensor(fl, fl, c.ps[:, 5], ALU.mult).then_inc(s["filt_done"], 1)
            dve.wait_ge(s["spec_read"], 5)
            for f in range(4):
                bank = 5 + f if f < 3 else 4
                dve.wait_ge(s["sig_ready"], f + 1)
                then("sig_read", nc.vector.tensor_copy(sig[:, f, :], c.ps[:, bank]))
            for f in range(2):
                ur, ui, hr, hi = sig[:, f, :], sig[:, 2 + f, :], spec[:, f, :], spec[:, 2 + f, :]
                hr2 = spec[:, 4, :] if f == 0 else hr
                then("prod_step", nc.vector.tensor_tensor(ma[:, 0, :], ui, hi, ALU.mult))
                then("prod_step", nc.vector.tensor_tensor(ma[:, 1, :], ur, hi, ALU.mult))
                then("prod_step", nc.vector.tensor_tensor(mb[:, 0, :], ur, hr, ALU.mult))
                then("prod_step", nc.vector.tensor_tensor(mb[:, 1, :], ui, hr2, ALU.mult))
                then("prod_done", nc.vector.tensor_tensor(ur, mb[:, 0, :], ma[:, 0, :], ALU.subtract))
                then("prod_done", nc.vector.tensor_tensor(ui, mb[:, 1, :], ma[:, 1, :], ALU.add))
            for f in range(4):
                dve.wait_ge(s["y_ready"], f + 1)
                zf = hy[:, f, :]
                skip = c.par[:, S_HYSKIP + 4 * order + f:S_HYSKIP + 4 * order + f + 1]
                then("gated", nc.vector.scalar_tensor_tensor(out=zf, in0=zf, scalar=skip, in1=c.ps[:, f, 0:SEQ],
                                                             op0=ALU.mult, op1=ALU.add))
                then("gated", nc.vector.tensor_tensor(zf, zf, hy[:, 4 * (order + 1) + f, :], ALU.mult))


def delta_features_stage(nc, c):
    names = ["square", "sum_ready", "eps_done", "root", "inv", "unit", "k_turned", "k_tok", "v_turned", "v_tok", "beta",
             "dn_in", "masks_in", "exp_a", "gate_step", "exp_x", "g_ready", "cum_ready", "cum_read", "last_ready",
             "last_read", "exps_in", "exps_done", "turned", "rows_read"]
    with stage(nc, *names) as (block, *sems):
        s = dict(zip(names, sems))
        q, k, v = c.work[:, O_Q:O_Q + 1024], c.work[:, O_K:O_K + 2048], c.work[:, O_V:O_V + 2048]
        parts = [(q, 0), (q, 1), (k, 0), (k, 1), (k, 2), (k, 3)]
        sq = c.tok[:, 0:3, :].rearrange("p a (b n) -> p (a b) n", b=2)
        g = c.gate_small
        dn = c.spare[:, 0:16]

        def seg(i):
            t, n = parts[i]
            return t[:, n * BANK:(n + 1) * BANK]

        @block.sync
        def _(sp):
            sp.dma_start(dn, c.vrows[V_DN:V_END].partition_broadcast(P)).then_inc(s["dn_in"], 16)
            sp.dma_start(c.hTf[:, 0:M_END], c.masks).then_inc(s["masks_in"], 16)
            sp.wait_ge(s["masks_in"], 16)

        @block.tensor
        def _(pe):
            for i in range(6):
                pe.wait_ge(s["square"], i + 1)
                mm(nc, c.ps[:, i], c.ones, sq[:, i, :], True, True).then_inc(s["sum_ready"], 1)
            vv = v.rearrange("p (h t) -> p h t", h=DNH)
            kk = k.rearrange("p (h t) -> p h t", h=DNH)
            for t in range(ALL):
                bank = 6 + t % 2
                if t >= 2:
                    pe.wait_ge(s["v_tok"], t - 1)
                for h in range(DNH):
                    last = nc.tensor.transpose(c.ps[:, bank, h * P:(h + 1) * P], vv[:, h, t * P:(t + 1) * P], c.ident)
                last.then_inc(s["v_turned"], 1)
            pe.wait_ge(s["g_ready"], 1)
            pe.wait_ge(s["v_tok"], 4)
            mm(nc, c.ps[:, 6, 0:16], c.upper, g["g"][:, 0:16], True, True)
            mm(nc, c.ps[:, 6, 16:32], c.lower, g["g"][:, 16:32], True, True).then_inc(s["cum_ready"], 1)
            pe.wait_ge(s["cum_read"], 1)
            mm(nc, c.ps[:, 7, 0:16], c.ident[:, P - 1:P].broadcast_to([P, P]), g["cum"][:, 0:16], True, True)
            mm(nc, c.ps[:, 7, 16:32], c.ident[:, 0:1].broadcast_to([P, P]), g["cum"][:, 16:32], True, True).then_inc(s["last_ready"], 1)
            pe.wait_ge(s["last_read"], 1)
            nc.tensor.transpose(c.ps[0:32, 6, 0:P], g["cum"], c.ident)
            nc.tensor.transpose(c.ps[0:32, 6, P:2 * P], g["beta"], c.ident).then_inc(s["turned"], 1)
            pe.wait_ge(s["rows_read"], 1)
            for t in range(ALL):
                pe.wait_ge(s["unit"], 6)
                bank = 6 + t % 2
                if t >= 2:
                    pe.wait_ge(s["k_tok"], t - 1)
                for h in range(DNH):
                    last = nc.tensor.transpose(c.ps[:, bank, h * P:(h + 1) * P], kk[:, h, t * P:(t + 1) * P], c.ident)
                last.then_inc(s["k_turned"], 1)

        @block.scalar
        def _(act):
            for i in range(6):
                nc.scalar.activation(sq[:, i, :], seg(i), ACT.Square).then_inc(s["square"], 1)
            for t in range(ALL):
                act.wait_ge(s["v_turned"], t + 1)
                nc.scalar.activation(c.v_tok[:, t], c.ps[:, 6 + t % 2], ACT.Copy).then_inc(s["v_tok"], 1)
            nc.scalar.activation(g["beta"].rearrange("p (d t h) -> p t d h", d=2, t=ALL),
                                 c.rest.rearrange("p (t x h) -> p t x h", t=ALL, x=4)[:, :, 0:2, :],
                                 ACT.Sigmoid).then_inc(s["beta"], 1)
            act.wait_ge(s["dn_in"], 16)
            nc.scalar.activation(dn[:, 0:8], dn[:, 0:8], ACT.Exp).then_inc(s["exp_a"], 1)
            act.wait_ge(s["gate_step"], 2)
            nc.scalar.activation(g["e"], g["ax"], ACT.Exp, scale=-1.0).then_inc(s["exp_x"], 1)
            act.wait_ge(s["cum_ready"], 1)
            nc.scalar.activation(g["cum"], c.ps[:, 6, 0:32], ACT.Copy).then_inc(s["cum_read"], 1)
            act.wait_ge(s["last_ready"], 1)
            nc.scalar.activation(g["last"], c.ps[:, 7, 0:32], ACT.Copy).then_inc(s["last_read"], 1)
            act.wait_ge(s["exps_in"], 1)
            nc.scalar.activation(g["ecum"], g["cum"], ACT.Exp).then_inc(s["exps_done"], 1)
            nc.scalar.activation(g["elast"], g["last"], ACT.Exp).then_inc(s["exps_done"], 1)
            nc.scalar.activation(g["erest"], g["ax"], ACT.Exp).then_inc(s["exps_done"], 1)
            act.wait_ge(s["turned"], 1)
            nc.scalar.activation(c.gate_rowsT[:, 0:2 * P], c.ps[0:32, 6, 0:2 * P], ACT.Copy).then_inc(s["rows_read"], 1)
            for i in range(6):
                act.wait_ge(s["eps_done"], i + 1)
                nc.scalar.activation(sq[:, i, :], sq[:, i, :], ACT.Sqrt).then_inc(s["root"], 1)
            for t in range(ALL):
                act.wait_ge(s["k_turned"], t + 1)
                nc.scalar.activation(c.k_tok[:, t], c.ps[:, 6 + t % 2], ACT.Copy).then_inc(s["k_tok"], 1)

        @block.vector
        def _(dve):
            step = [0]

            def then(ins):
                ins.then_inc(s["gate_step"], 1)
                step[0] += 1
                dve.wait_ge(s["gate_step"], step[0])

            dve.wait_ge(s["dn_in"], 16)
            rest = c.rest.rearrange("p (t x h) -> p t x h", t=ALL, x=4)[:, :, 2:4, :]
            bias = dn[:, 8:16].rearrange("p (d h) -> p d h", d=2)
            for d in range(2):
                ins = nc.vector.tensor_tensor(g["x"][:, 16 * d:16 * d + 16].rearrange("p (t h) -> p t h", t=ALL),
                                              rest[:, :, d, :], bias[:, d].unsqueeze(1).broadcast_to([P, ALL, DNH]), ALU.add)
                if d:
                    then(ins)
                else:
                    ins.then_inc(s["inv"], 1)
                    dve.wait_ge(s["inv"], 1)
            then(nc.vector.scalar_tensor_tensor(out=g["ax"], in0=g["x"], scalar=-1.0, in1=g["x"], op0=ALU.mult, op1=ALU.max))
            dve.wait_ge(s["exp_x"], 1)
            then(nc.vector.tensor_scalar(g["t"], g["e"], 2.0, None, ALU.add))
            then(nc.vector.reciprocal(g["t"], g["t"]))
            then(nc.vector.tensor_tensor(g["t"], g["t"], g["e"], ALU.mult))
            then(nc.vector.tensor_tensor(g["t2"], g["t"], g["t"], ALU.mult))
            then(nc.vector.tensor_scalar(g["g"], g["t2"], 1.0 / 17, 1.0 / 15, ALU.mult, ALU.add))
            for n in (13, 11, 9, 7, 5, 3, 1):
                then(nc.vector.tensor_tensor(g["g"], g["g"], g["t2"], ALU.mult))
                then(nc.vector.tensor_scalar(g["g"], g["g"], 1.0 / n, None, ALU.add))
            then(nc.vector.scalar_tensor_tensor(out=g["g"], in0=g["t"], scalar=2.0, in1=g["g"], op0=ALU.mult, op1=ALU.mult))
            then(nc.vector.scalar_tensor_tensor(out=g["g"], in0=g["x"], scalar=0.0, in1=g["g"], op0=ALU.max, op1=ALU.add))
            dve.wait_ge(s["exp_a"], 1)
            ea = dn[:, 0:8].rearrange("p (d h) -> p d h", d=2)
            for d in range(2):
                gd = g["g"][:, 16 * d:16 * d + 16].rearrange("p (t h) -> p t h", t=ALL)
                then(nc.vector.tensor_tensor(gd, gd, ea[:, d].unsqueeze(1).broadcast_to([P, ALL, DNH]), ALU.mult))
            then(nc.vector.tensor_scalar(g["g"], g["g"], -1.0, None, ALU.mult))
            dve.sem_inc(s["g_ready"], 1)
            dve.wait_ge(s["last_read"], 1)
            then(nc.vector.tensor_tensor(g["ax"], g["last"], g["cum"], ALU.subtract))
            dve.sem_inc(s["exps_in"], 1)
            dve.wait_ge(s["exps_done"], 3)
            dve.wait_ge(s["beta"], 1)
            then(nc.vector.scalar_tensor_tensor(out=g["nbe"], in0=g["beta"], scalar=-1.0, in1=g["ecum"], op0=ALU.mult,
                                                op1=ALU.mult))
            for i in range(6):
                dve.wait_ge(s["sum_ready"], i + 1)
                nc.vector.tensor_scalar(sq[:, i, :], c.ps[:, i], 1e-6, None, ALU.add).then_inc(s["eps_done"], 1)
            for i in range(6):
                dve.wait_ge(s["root"], i + 1)
                nc.vector.reciprocal(c.ps[:, i], sq[:, i, :]).then_inc(s["inv"], 1)
                dve.wait_ge(s["inv"], i + 2)
                nc.vector.scalar_tensor_tensor(out=seg(i), in0=seg(i), scalar=float(P) ** -0.5 if i < 2 else 1.0,
                                               in1=c.ps[:, i], op0=ALU.mult, op1=ALU.mult).then_inc(s["unit"], 1)


def delta_inverse_stage(nc, c):
    GROUPS = [(t, d) for t in range(ALL) for d in range(2)]
    names = ["rows0", "rows1", "diff0", "diff1", "decay0", "decay1", "prep_step0", "prep_step1", "start0", "start1",
             "xt0", "xt1", "x0", "x1", "y_ready0", "y_ready1", "y0", "y1", "p_ready0", "p_ready1", "step0", "step1"]
    with stage(nc, *names) as (block, *sems):
        s = dict(zip(names, sems))
        tokf = c.tok[:, :, :].rearrange("p a n -> p (a n)")
        q = c.work[:, O_Q:O_Q + 1024].rearrange("p (h t) -> p h t", h=DNH)
        k = c.work[:, O_K:O_K + 2048].rearrange("p (h t) -> p h t", h=DNH)

        def buf(e, n):
            return tokf[:, 2048 * e + 512 * n:2048 * e + 512 * (n + 1)].rearrange("p (h n) -> p h n", h=DNH)

        X, LT, Y, DT = ([buf(e, n) for e in range(2)] for n in range(4))
        level = c.hTf[:, M_LEVEL:M_BIAS].rearrange("p (d l n) -> p d l n", d=2, l=LEVELS)
        mbias = c.hTf[:, M_BIAS:M_END].rearrange("p (d n) -> p d n", d=2)

        def heads(bank):
            return c.ps[:, bank].rearrange("p (h n) -> p h n", h=DNH)

        def over_heads(m):
            return m.unsqueeze(1).broadcast_to([P, DNH, P])

        @block.tensor
        def _(pe):
            for pair in range(4):
                for e in range(2):
                    i = 2 * pair + e
                    t, d = GROUPS[i]
                    if pair:
                        pe.wait_ge(s[f"step{e}"], pair * (LEVELS - 1))
                    tr = slice(t * P, (t + 1) * P)
                    for h in range(DNH):
                        r = 16 * d + 4 * t + h
                        hs = slice(h * P, (h + 1) * P)
                        sel = c.ident[0:32, r:r + 1].broadcast_to([32, P])
                        mm(nc, c.ps[:, 4 * e, hs], sel, c.gate_rowsT[:, 0:P], True, True)
                        mm(nc, c.ps[:, 4 * e + 1, hs], sel, c.gate_rowsT[:, P:2 * P], True, True)
                        last = mm(nc, c.ps[:, 4 * e + 2, hs], k[:, h, tr], k[:, h, tr], True, True)
                        if t < TT:
                            last = mm(nc, c.ps[:, 4 * e + 3, hs], k[:, h, tr], q[:, h, tr], True, True)
                    last.then_inc(s[f"rows{e}"], 1)
                for e in range(2):
                    i = 2 * pair + e
                    pe.wait_ge(s[f"start{e}"], pair + 1)
                    for h in range(DNH):
                        last = nc.tensor.transpose(heads(4 * e)[:, h], c.invT[i][:, h], c.ident)
                    last.then_inc(s[f"xt{e}"], 1)
                for l in range(1, LEVELS):
                    n = pair * (LEVELS - 1) + l
                    for e in range(2):
                        if l == 1:
                            pe.wait_ge(s[f"x{e}"], pair + 1)
                        else:
                            pe.wait_ge(s[f"step{e}"], n - 1)
                        for h in range(DNH):
                            last = mm(nc, heads(4 * e + 1)[:, h], LT[e][:, h], X[e][:, h], True, True)
                        last.then_inc(s[f"y_ready{e}"], 1)
                    for e in range(2):
                        i = 2 * pair + e
                        pe.wait_ge(s[f"y{e}"], n)
                        for h in range(DNH):
                            last = mm(nc, heads(4 * e + 2)[:, h], Y[e][:, h], c.invT[i][:, h], True, True)
                        if l < LEVELS - 1:
                            for h in range(DNH):
                                last = mm(nc, heads(4 * e + 3)[:, h], c.invT[i][:, h], Y[e][:, h], True, True)
                        last.then_inc(s[f"p_ready{e}"], 1)

        @block.scalar
        def _(act):
            for pair in range(4):
                for e in range(2):
                    act.wait_ge(s[f"diff{e}"], 4 * pair + 4)
                    nc.scalar.activation(DT[e], DT[e], ACT.Exp).then_inc(s[f"decay{e}"], 1)
                for e in range(2):
                    act.wait_ge(s[f"xt{e}"], pair + 1)
                    nc.scalar.activation(X[e], heads(4 * e), ACT.Copy).then_inc(s[f"x{e}"], 1)

        @block.vector
        def _(dve):
            steps = [0, 0]

            def then(e, ins):
                ins.then_inc(s[f"prep_step{e}"], 1)
                steps[e] += 1
                dve.wait_ge(s[f"prep_step{e}"], steps[e])

            for pair in range(4):
                for e in range(2):
                    i = 2 * pair + e
                    t, d = GROUPS[i]
                    dve.wait_ge(s[f"rows{e}"], pair + 1)
                    for h in range(DNH):
                        col = 16 * d + 4 * t + h
                        nc.vector.scalar_tensor_tensor(out=DT[e][:, h], in0=heads(4 * e)[:, h],
                                                       scalar=c.gate_small["cum"][:, col:col + 1], in1=mbias[:, d],
                                                       op0=ALU.subtract, op1=ALU.add).then_inc(s[f"diff{e}"], 1)
                for e in range(2):
                    i = 2 * pair + e
                    t, d = GROUPS[i]
                    dve.wait_ge(s[f"decay{e}"], pair + 1)
                    if t < TT:
                        then(e, nc.vector.tensor_tensor(c.attT[i], heads(4 * e + 3), DT[e], ALU.mult))
                    then(e, nc.vector.tensor_tensor(DT[e], heads(4 * e + 2), DT[e], ALU.mult))
                    then(e, nc.vector.tensor_tensor(LT[e], heads(4 * e + 1), DT[e], ALU.mult))
                    then(e, nc.vector.tensor_tensor(Y[e], LT[e], over_heads(level[:, 1 - d, 0]), ALU.mult))
                    nc.vector.tensor_tensor(c.invT[i], over_heads(c.ident), Y[e], ALU.subtract).then_inc(s[f"start{e}"], 1)
                    dve.wait_ge(s[f"start{e}"], pair + 1)
                for l in range(1, LEVELS):
                    n = pair * (LEVELS - 1) + l
                    for e in range(2):
                        i = 2 * pair + e
                        t, d = GROUPS[i]
                        dve.wait_ge(s[f"y_ready{e}"], n)
                        nc.vector.tensor_tensor(Y[e], heads(4 * e + 1), over_heads(level[:, d, l]), ALU.mult).then_inc(s[f"y{e}"], 1)
                    for e in range(2):
                        i = 2 * pair + e
                        dve.wait_ge(s[f"p_ready{e}"], n)
                        if l < LEVELS - 1:
                            then(e, nc.vector.tensor_tensor(X[e], X[e], heads(4 * e + 3), ALU.subtract))
                        nc.vector.tensor_tensor(c.invT[i], c.invT[i], heads(4 * e + 2), ALU.subtract).then_inc(s[f"step{e}"], 1)


def delta_scan_stage(nc, c):
    ORDER = [(2, 3, 0, 1), (3, 2, 1, 0)]
    names = []
    for d in range(2):
        names += [f"{n}{d}" for n in ("read", "values", "wanted", "fresh", "fresh_read", "vb", "kd", "grow", "state",
                                      "own_out", "out_scaled", "out")]
    with stage(nc, *names) as (block, *sems):
        s = dict(zip(names, sems))
        tokf = c.tok[:, :, :].rearrange("p a n -> p (a n)")
        q = c.work[:, O_Q:O_Q + 1024].rearrange("p (h t) -> p h t", h=DNH)
        k = c.work[:, O_K:O_K + 2048].rearrange("p (h t) -> p h t", h=DNH)
        g = c.gate_small

        def buf(d, n):
            return tokf[:, 2048 * d + 512 * n:2048 * d + 512 * (n + 1)].rearrange("p (h n) -> p h n", h=DNH)

        VB, VN, KD, OT = ([buf(d, n) for d in range(2)] for n in range(4))

        def heads(bank):
            return c.ps[:, bank].rearrange("p (h n) -> p h n", h=DNH)

        def col(name, d, t, h):
            i = 16 * d + 4 * t + h
            return g[name][:, i:i + 1]

        @block.tensor
        def _(pe):
            for i in range(4):
                for d in range(2):
                    t = ORDER[d][i]
                    tr = slice(t * P, (t + 1) * P)
                    if i:
                        pe.wait_ge(s[f"state{d}"], 4 * i)
                        for h in range(DNH):
                            last = mm(nc, heads(4 * d)[:, h], k[:, h, tr], c.state[d][:, h], True, True)
                        last.then_inc(s[f"read{d}"], 1)
                    if t < TT:
                        if i == 3:
                            pe.wait_ge(s[f"out_scaled{d}"], 4)
                        for h in range(DNH):
                            last = mm(nc, heads(4 * d + 2)[:, h], q[:, h, tr], c.state[d][:, h], True, True)
                        last.then_inc(s[f"own_out{d}"], 1)
                for d in range(2):
                    t = ORDER[d][i]
                    if i:
                        pe.wait_ge(s[f"values{d}"], 4 * i)
                    else:
                        pe.wait_ge(s[f"vb{d}"], 4)
                    for h in range(DNH):
                        last = mm(nc, heads(4 * d + 1)[:, h], c.invT[2 * t + d][:, h], VB[d][:, h], True, True)
                    last.then_inc(s[f"fresh{d}"], 1)
                for d in range(2):
                    t = ORDER[d][i]
                    pe.wait_ge(s[f"fresh_read{d}"], i + 1)
                    if i < 3:
                        pe.wait_ge(s[f"kd{d}"], 4 * i + 4)
                        for h in range(DNH):
                            last = mm(nc, heads(4 * d)[:, h], KD[d][:, h], VN[d][:, h], True, True)
                        last.then_inc(s[f"grow{d}"], 1)
                    if t < TT:
                        if i == 3:
                            pe.wait_ge(s[f"out{d}"], 1)
                        for h in range(DNH):
                            last = mm(nc, heads(4 * d + 3)[:, h], c.attT[2 * t + d][:, h], VN[d][:, h], True, True)
                        last.then_inc(s[f"own_out{d}"], 1)

        @block.scalar
        def _(act):
            for i in range(4):
                for d in range(2):
                    t = ORDER[d][i]
                    if i:
                        act.wait_ge(s[f"fresh{d}"], i)
                    for h in range(DNH):
                        nc.scalar.activation(VB[d][:, h], c.v_tok[:, t].rearrange("p (h n) -> p h n", h=DNH)[:, h], ACT.Copy,
                                             scale=col("beta", d, t, h)).then_inc(s[f"vb{d}"], 1)
                    if t < TT:
                        act.wait_ge(s[f"own_out{d}"], 2 * (i - 2) + 1)
                        if i == 3:
                            act.wait_ge(s[f"out{d}"], 1)
                        for h in range(DNH):
                            nc.scalar.activation(OT[d][:, h], heads(4 * d + 2)[:, h], ACT.Copy,
                                                 scale=col("ecum", d, t, h)).then_inc(s[f"out_scaled{d}"], 1)
                for d in range(2):
                    act.wait_ge(s[f"fresh{d}"], i + 1)
                    if i:
                        act.wait_ge(s[f"grow{d}"], i)
                    if i == 3:
                        act.wait_ge(s[f"own_out{d}"], 2)
                    nc.scalar.activation(VN[d], heads(4 * d + 1), ACT.Copy).then_inc(s[f"fresh_read{d}"], 1)

        @block.gpsimd
        def _(pool):
            for i in range(3):
                for d in range(2):
                    t = ORDER[d][i]
                    if i:
                        pool.wait_ge(s[f"grow{d}"], i)
                    for h in range(DNH):
                        nc.gpsimd.tensor_scalar(KD[d][:, h], c.k_tok[:, t].rearrange("p (h n) -> p h n", h=DNH)[:, h],
                                                col("erest", d, t, h), None, ALU.mult).then_inc(s[f"kd{d}"], 1)

        @block.vector
        def _(dve):
            for i in range(4):
                for d in range(2):
                    t = ORDER[d][i]
                    if i:
                        dve.wait_ge(s[f"read{d}"], i)
                        dve.wait_ge(s[f"vb{d}"], 4 * i + 4)
                        for h in range(DNH):
                            nc.vector.scalar_tensor_tensor(out=VB[d][:, h], in0=heads(4 * d)[:, h], scalar=col("nbe", d, t, h),
                                                           in1=VB[d][:, h], op0=ALU.mult, op1=ALU.add).then_inc(s[f"values{d}"], 1)
                for d in range(2):
                    t = ORDER[d][i]
                    if i < 3:
                        dve.wait_ge(s[f"grow{d}"], i + 1)
                        for h in range(DNH):
                            if i == 0:
                                nc.vector.tensor_copy(c.state[d][:, h], heads(4 * d)[:, h]).then_inc(s[f"state{d}"], 1)
                            else:
                                if t < TT:
                                    dve.wait_ge(s[f"own_out{d}"], 2 * (i - 2) + 1)
                                nc.vector.scalar_tensor_tensor(out=c.state[d][:, h], in0=c.state[d][:, h],
                                                               scalar=col("elast", d, t, h), in1=heads(4 * d)[:, h],
                                                               op0=ALU.mult, op1=ALU.add).then_inc(s[f"state{d}"], 1)
                    if t < TT:
                        dve.wait_ge(s[f"own_out{d}"], 2 * (i - 2) + 2)
                        dve.wait_ge(s[f"out_scaled{d}"], 4 * (i - 2) + 4)
                        ot = c.o_tok[:, t].rearrange("p (h n) -> p h n", h=DNH)
                        if i == 2:
                            nc.vector.tensor_tensor(ot, OT[d], heads(4 * d + 3), ALU.add).then_inc(s[f"out{d}"], 1)
                        else:
                            nc.vector.tensor_tensor(OT[d], OT[d], heads(4 * d + 3), ALU.add).then_inc(s[f"out{d}"], 1)
                            dve.wait_ge(s[f"out{d}"], 2)
                            dve.wait_ge(s[f"out{1 - d}"], 1)
                            nc.vector.tensor_tensor(ot, ot, OT[d], ALU.add).then_inc(s[f"out{d}"], 1)


def odd_out_stage(nc, c, w, m0):
    with stage(nc, "squares", "root", "step", "gated", "turned", "cols", "out_ready", "product", "added") as (
            block, squares, root, step, gated, turned, cols, out_ready, product, added):
        o = c.o_tok
        gs = c.work[:, O_GATE:O_GATE + 1024].rearrange("p (t n) -> p t n", t=TT)
        oT = c.work[:, O_Q:O_Q + 1024].rearrange("p (h t) -> p h t", h=DNH)
        hy = c.work[:, O_HY:O_HY + 1024].rearrange("p (f t) -> p f t", f=4)
        junk = c.spare[:, 0:P]
        sm = c.spare[:, P:P + 32]

        @block.sync
        def _(sp):
            for i in range(2):
                sp.wait_ge(out_ready, i + 1)
                w.refill(sp, m0 + i)

        @block.tensor
        def _(pe):
            for half in range(2):
                wt = w.landed(pe, m0 + half).rearrange("p (k n) -> p k n", k=4)
                if half:
                    for t in range(TT):
                        pe.wait_ge(gated, t + 1)
                        for h in range(DNH):
                            last = nc.tensor.transpose(c.ps[:, 4 + h // 2, (h % 2) * SEQ + t * P:(h % 2) * SEQ + (t + 1) * P],
                                                       o[:, t, h * P:(h + 1) * P], c.ident)
                    last.then_inc(turned, 1)
                    pe.wait_ge(cols, 1)
                src = oT if half else hy
                for kk in range(4):
                    for t in range(TT):
                        for n in range(2):
                            last = mm(nc, c.ps[:, 2 * t + n], src[:, kk, t * P:(t + 1) * P], wt[:, kk, n * BANK:(n + 1) * BANK],
                                      half + kk == 0, half == 1 and kk == 3)
                last.then_inc(out_ready, 1)

        @block.scalar
        def _(act):
            act.wait_ge(squares, 8)
            nc.scalar.activation(sm[:, 8:16], sm[:, 0:8], ACT.Sqrt).then_inc(root, 1)
            act.wait_ge(turned, 1)
            nc.scalar.activation(oT.rearrange("p h t -> p (h t)"), c.ps[:, 4:6, :].rearrange("p b n -> p (b n)"), ACT.Copy,
                                 scale=c.par[:, S_DNG:S_DNG + 1]).then_inc(cols, 1)

        @block.vector
        def _(dve):
            for i in range(8):
                oh = o[:, i // 4, (i % 4) * P:(i % 4 + 1) * P]
                nc.vector.tensor_tensor_reduce(out=junk, in0=oh, in1=oh, scale=1.0 / P, scalar=EPS, op0=ALU.mult, op1=ALU.add,
                                               accum_out=sm[:, i:i + 1]).then_inc(squares, 1)
                dve.wait_ge(squares, i + 1)
            dve.wait_ge(root, 1)
            nc.vector.reciprocal(sm[:, 16:24], sm[:, 8:16]).then_inc(step, 1)
            dve.wait_ge(step, 1)
            for i in range(8):
                oh = o[:, i // 4, (i % 4) * P:(i % 4 + 1) * P]
                nc.vector.tensor_scalar(oh, oh, sm[:, 16 + i:17 + i], None, ALU.mult).then_inc(step, 1)
            dve.wait_ge(step, 9)
            for t in range(TT):
                nc.vector.tensor_tensor(o[:, t], o[:, t], gs[:, t], ALU.mult).then_inc(gated, 1)
            dve.wait_ge(out_ready, 2)
            add_gated(nc, c, product, range(TT), 0)

        @block.gpsimd
        def _(pool):
            for t in range(TT):
                for n in range(2):
                    pool.wait_ge(product, 2 * t + n + 1)
                    xs = c.x[:, t, n * BANK:(n + 1) * BANK]
                    nc.gpsimd.tensor_tensor(xs, xs, c.tok[:, t, n * BANK:(n + 1) * BANK], ALU.add).then_inc(added, 1)
            pool.wait_ge(added, 2 * TT)


class Core:
    pass


def first_block(nc, c, layers, rows):
    with nc.Fori(0, DEPTH) as layer:
        w = Panels(c, layer, L1_PANELS, 0, 0)
        norm_stage(nc, c, [0, 1], lambda k, _: c.lay[:, C_FFN1 + k:C_FFN1 + k + 1], split=True)
        ffn_stage(nc, c, w, AT_FFN1)
        norm_stage(nc, c, [0, 1], lambda k, _: c.lay[:, C_MIX + k:C_MIX + k + 1])
        mixer1_stage(nc, c, w, AT_PROJ)
        norm_stage(nc, c, [0, 1], lambda k, _: c.lay[:, C_FFN2 + k:C_FFN2 + k + 1], split=True)
        ffn_stage(nc, c, w, AT_FFN2, [(c.lay[:, :], layers[layer + 1]), (c.rows[:, :], rows[layer + 1].partition_broadcast(P))])


def token_norm_stage(nc, c, gain, out=None):
    with stage(nc, "gain_in", "squares", "mean_sq", "root", "step", "normed", "stored") as (
            block, gain_in, squares, mean_sq, root, step, normed, stored):
        @block.sync
        def _(sp):
            sp.dma_start(c.tok[:, 0], gain.partition_broadcast(P)).then_inc(gain_in, 16)
            sp.wait_ge(c.second_in, 48)
            if out is not None:
                sp.wait_ge(normed, TT)
                sp.dma_start(out.rearrange("(t p) n -> p t n", p=P), c.x[:, 0:TT, :]).then_inc(stored, 16)
                sp.wait_ge(stored, 16)

        @block.scalar
        def _(act):
            for t in range(TT):
                nc.scalar.activation(c.ps[:, 2 * t:2 * t + 2, :].rearrange("p b n -> p (b n)"), c.x[:, t], ACT.Square,
                                     accum_out=c.stat[:, t:t + 1]).then_inc(squares, 1)
            act.wait_ge(mean_sq, 1)
            nc.scalar.activation(c.stat[:, 4:6], c.stat[:, 2:4], ACT.Sqrt).then_inc(root, 1)

        @block.vector
        def _(dve):
            dve.wait_ge(squares, TT)
            nc.vector.tensor_scalar(c.stat[:, 2:4], c.stat[:, 0:2], 1.0 / D, EPS, ALU.mult, ALU.add).then_inc(mean_sq, 1)
            dve.wait_ge(root, 1)
            nc.vector.reciprocal(c.stat[:, 6:8], c.stat[:, 4:6]).then_inc(step, 1)
            dve.wait_ge(step, 1)
            dve.wait_ge(gain_in, 16)
            for t in range(TT):
                nc.vector.scalar_tensor_tensor(out=c.x[:, t], in0=c.x[:, t], scalar=c.stat[:, 6 + t:7 + t],
                                               in1=c.tok[:, 0], op0=ALU.mult, op1=ALU.mult).then_inc(normed, 1)


def second_block(nc, c, final_gain, out):
    w = Panels(c, None, 0, DEPTH * L1_PANELS, PANELS)

    def modulated(j):
        return (lambda k, st: c.mod[:, 2 * j + 1, st, k:k + 1], lambda k, st: c.mod[:, 2 * j, st, k:k + 1])

    ada_stage(nc, c, w, B_ADA0, 0)
    norm_stage(nc, c, [0, 1, 2, 3], *modulated(0))
    even_mixer_stage(nc, c, w, B_EVEN)
    norm_stage(nc, c, [0, 1, 2, 3], *modulated(1), split=True)
    mlp_stage(nc, c, w, B_MLP0, [0, 1, 2, 3], 2)
    ada_stage(nc, c, w, B_ADA1, 1)
    norm_stage(nc, c, [0, 1, 2, 3], *modulated(0))
    odd_project_stage(nc, c, w, B_ODD)
    for order in range(2):
        hyena_stage(nc, c, order)
    delta_features_stage(nc, c)
    delta_inverse_stage(nc, c)
    delta_scan_stage(nc, c)
    odd_out_stage(nc, c, w, B_ODD + 7)
    norm_stage(nc, c, [0, 1], *modulated(1), split=True)
    mlp_stage(nc, c, w, B_MLP1, [0, 1], 1)
    token_norm_stage(nc, c, final_gain, out)
def program(nc, a, out):
    c = Core()
    with ExitStack() as ctx:
        def sb(name, *shape):
            return ctx.enter_context(nc.sbuf_tensor(name, [P, *shape], F32))

        c.ring = sb("ring", RING, PANEL)
        c.x = sb("x", 4, D)
        at_hT = nc.sbuf_base
        c.hT = sb("hT", DK, 4 * P)
        c.tok = sb("tok", 4, D)
        at_work = nc.sbuf_base
        c.work = sb("work", 16 * 1024)
        c.hT_hi = nc.alloc_sbuf_tensor_at("hT_hi", [P, DK, 4 * P], F32R, offset=at_hT)
        c.hT_lo = ctx.enter_context(nc.sbuf_tensor("hT_lo", [P, DK, 4 * P], F32R))
        c.hid_hi = nc.alloc_sbuf_tensor_at("hid_hi", [P, 8 * 1024], F32R, offset=at_work)
        c.hid_lo = nc.alloc_sbuf_tensor_at("hid_lo", [P, 8 * 1024], F32R, offset=at_work + 4 * 8 * 1024)
        c.w_hi = ctx.enter_context(nc.sbuf_tensor("w_hi", [P, 2, QUART], F32R))
        c.w_lo = ctx.enter_context(nc.sbuf_tensor("w_lo", [P, 2, QUART], F32R))
        c.cond_parts = ctx.enter_context(nc.sbuf_tensor("cond_parts", [P, DK, 4], F32R))
        params = sb("params", C_END + R_END)
        c.lay = params[:, 0:C_END]
        c.rows = params[:, C_END:C_END + R_END]
        c.spare = params[:, D:2 * D]
        c.gate_rows = params[:, 0:4 * D].rearrange("p (g n) -> p g n", g=4)
        c.const = sb("const", K_END1)
        c.stat = sb("stat", 16)
        c.par = sb("par", S_END)
        c.const2 = sb("const2", K2_END)
        small = sb("small", 2 * P + 64 + 16 + 64 + 1 + 13 * 32)
        c.ones = small[:, 0:P]
        c.mean512 = small[:, P:2 * P]
        c.mod = small[:, 256:320].rearrange("p (j s k) -> p j s k", j=4, s=2)
        c.silu_c = small[:, 320:336].rearrange("p (k s) -> p k s", s=2)
        c.rest = small[:, 336:400]
        c.subln = small[:, 400:401]
        c.gate_small = {n: small[:, 401 + 32 * j:433 + 32 * j] for j, n in enumerate(
            ("x", "ax", "e", "t", "t2", "g", "cum", "last", "ecum", "elast", "erest", "beta", "nbe"))}
        c.upper = c.const[:, K_UPPER:K_UPPER + P]
        c.lower = c.const2[:, K2_LOWER:K2_END]
        c.hTf = c.hT[:, :, :].rearrange("p k t -> p (k t)")
        tokf = c.tok[:, :, :].rearrange("p a n -> p (a n)")
        c.hidden_z = tokf[0:64, 3840:4096]
        c.gate_rowsT = c.spare[0:32, 256:512]
        c.k_tok = c.work[:, 9216:11264].rearrange("p (t n) -> p t n", t=ALL)
        c.v_tok = c.work[:, 11264:13312].rearrange("p (t n) -> p t n", t=ALL)
        c.invT = [c.work[:, at:at + 512].rearrange("p (h n) -> p h n", h=DNH)
                  for at in (*range(6144, 8192, 512), *range(13312, 15360, 512))]
        c.attT = [c.work[:, at:at + 512].rearrange("p (h n) -> p h n", h=DNH) for at in range(1024, 3072, 512)]
        c.state = [c.work[:, at:at + 512].rearrange("p (h n) -> p h n", h=DNH) for at in (15360, 15872)]
        c.o_tok = c.hTf[:, 2304:3328].rearrange("p (t n) -> p t n", t=TT)
        c.vrows, c.transforms, c.masks, c.w3 = (a[n] for n in ("vrows", "transforms", "masks", "w3"))
        c.ident = c.const[:, K_ID:K_ID + P]
        c.ps = ctx.enter_context(nc.psum_tensor("ps", [P, 8, BANK], F32))
        c.landed = [ctx.enter_context(nc.semaphore(f"panel_landed{i}")) for i in range(RING)]
        c.panels = a["panels"]
        c.second_in = ctx.enter_context(nc.semaphore("second_in"))
        c.rows_in = ctx.enter_context(nc.semaphore("rows_in"))
        with stage(nc, "x_in", "const_in", "filled") as (block, x_in, const_in, filled):
            @block.sync
            def _(sp):
                sp.dma_start(c.x[:, 0:TT, :], a["x"].rearrange("(t p) n -> p t n", p=P)).then_inc(x_in, 16)
                sp.dma_start(c.const[:, :], a["const"]).then_inc(const_in, 16)
                sp.dma_start(c.lay[:, :], a["layers"][0]).then_inc(const_in, 16)
                for m in range(RING):
                    sp.dma_start(c.ring[:, m], a["panels"][m]).then_inc(c.landed[m], 16)
                sp.dma_start(c.rows[:, :], a["rows"][0].partition_broadcast(P)).then_inc(c.rows_in, 16)
                sp.dma_start(c.x[:, TT:ALL, :], a["ctx"].rearrange("(t p) n -> p t n", p=P)).then_inc(c.second_in, 16)
                sp.dma_start(c.par[:, :], a["par"]).then_inc(c.second_in, 16)
                sp.dma_start(c.const2[:, :], a["const2"]).then_inc(c.second_in, 16)
                sp.wait_ge(x_in, 16)
                sp.wait_ge(const_in, 32)

            @block.gpsimd
            def _(pool):
                nc.gpsimd.memset(c.ones, 1.0).then_inc(filled, 1)
                nc.gpsimd.memset(c.mean512, 1.0 / 512).then_inc(filled, 1)
                pool.wait_ge(filled, 2)
        first_block(nc, c, a["layers"], a["rows"])
        token_norm_stage(nc, c, a["final_norm"])
        second_block(nc, c, a["final_g"], out)


def panel(w):
    k = w.shape[0] // P
    w = w.reshape(k, P, w.shape[1]).transpose(1, 0, 2).reshape(P, -1)
    return np.pad(w, ((0, 0), (0, PANEL - w.shape[1]))) if w.shape[1] < PANEL else w


def column_panels(w):
    return [panel(w[:, i:i + BANK]) for i in range(0, w.shape[1], BANK)]


def row_panels(w):
    return [panel(w[i:i + 4 * P]) for i in range(0, w.shape[0], 4 * P)]


def first_panels(i):
    out = []
    for l in range(DEPTH):
        def ffn(gu, down):
            g = gu[l].reshape(D, 2, GU, 256).transpose(0, 2, 1, 3).reshape(D, 2 * FF)
            return column_panels(g) + row_panels(down[l])
        u, va, q, k, v, qi = (i["w_in"][l][:, n * CH:(n + 1) * CH] for n in range(6))
        gates = i["w_in"][l][:, 6 * CH + SMALL:]
        out += ffn(i["ffn1_w_gu"], i["ffn1_w_down"])
        for part in (q, k, qi, v, u, va, gates):
            out += column_panels(part)
        out += row_panels(i["w_pa"][l]) + row_panels(i["w_pb"][l]) + row_panels(i["w_out"][l])
        out += ffn(i["ffn2_w_gu"], i["ffn2_w_down"])
    return out


def columns(v):
    return v.reshape(-1, P).T


def constants():
    out = np.zeros((P, K_END1), np.float32)
    out[:, K_ID:K_ID + P] = np.eye(P)
    out[:, K_UPPER:K_UPPER + P] = np.triu(np.ones((P, P)))
    pos = np.arange(SEQ)
    causal = np.where(pos[None, :] <= pos[:, None], 0.0, MASKED).astype(np.float32)
    out[:, K_CAUSAL:K_COS] = causal.reshape(TT, P, SEQ).transpose(1, 0, 2).reshape(P, -1)
    inv = np.float32(10000.0) ** (-np.arange(0, HD, 2, dtype=np.float32) / np.float32(HD))
    ang = pos.astype(np.float32)[:, None] * inv[None, :].astype(np.float32)
    cos, sin = np.cos(ang.astype(np.float64)), np.sin(ang.astype(np.float64))
    for at, tab in ((K_COS, np.concatenate([cos, cos], 1)), (K_SIN, np.concatenate([-sin, sin], 1))):
        out[:, at:at + TT * HD] = tab.reshape(TT, P, HD).transpose(1, 0, 2).reshape(P, -1)
    return out


def first_arrays(i):
    layers, rows = [], []
    for l in range(DEPTH):
        small = i["w_in"][l][:, 6 * CH:6 * CH + SMALL]
        layers.append(np.concatenate([
            columns(i["ffn1_norm"][l]), columns(i["mix_norm"][l]), columns(i["ffn2_norm"][l]), i["gmlp_b_s"][l].T,
            i["gmlp_w_s"][l].transpose(2, 0, 1).reshape(P, 4 * P),
            small.reshape(DK, P, SMALL).transpose(1, 0, 2).reshape(P, -1)], axis=1))
        rows.append(np.concatenate([i["b_gate"][l], i["gmlp_ln_g"][l], i["gmlp_ln_b"][l]]))
    return {"x": i["x"][0], "layers": np.stack(layers + layers[:1]), "rows": np.stack(rows + rows[:1]),
            "final_norm": i["final_norm"]}


def second_panels(i):
    even, odd = i["ev_w_in_2"][0], i["od_w_in_2"][0]

    def ada(l):
        w = i["ada_w_2"][l]
        return [p for part in (0, 1, 3, 4, 2, 5) for p in column_panels(w[:, part * D:(part + 1) * D])]

    def mlp(l, parts):
        up, down = column_panels(i["mlp_w1_2"][l]), row_panels(i["mlp_w2_2"][l])
        n = len(up) // parts
        return [p for j in range(0, len(up), n) for p in up[j:j + n] + down[j:j + n]]

    glu = even[:, 0:2 * CH].reshape(D, 2, 2, 256).transpose(0, 2, 1, 3).reshape(D, 2 * CH)
    out = ada(0) + column_panels(glu) + column_panels(even[:, 2 * CH:]) + row_panels(i["ev_w_out_2"][0]) + mlp(0, 2)
    hy, gate, qkv = odd[:, 0:3 * CH], odd[:, 3 * CH:4 * CH], odd[:, 4 * CH:7 * CH]
    return out + ada(1) + column_panels(hy) + column_panels(qkv) + column_panels(gate) + \
        row_panels(i["od_w_out_2"][0]) + mlp(1, 1)


def channel_taps(w):
    return w.reshape(w.shape[0], -1, P).transpose(2, 1, 0).reshape(P, -1)


def on_partitions(w):
    return np.pad(w, ((0, P - w.shape[0]), (0, 0)))


def second_arrays(i):
    cond = np.stack([columns(i["c_2"][0]), columns(i["c_ctx_2"])], axis=2).reshape(P, -1)
    fb = np.stack([i[n][0] for n in ("od_hy_b1_2", "od_hy_freq1_2", "od_hy_b2_2", "od_hy_freq2_2")], axis=1)
    par = np.concatenate([
        cond, *(columns(i["ada_b_2"][l]) for l in range(DEPTH)), *(columns(i["norm1_g_2"][l]) for l in range(DEPTH)),
        *(columns(i["norm2_g_2"][l]) for l in range(DEPTH)), channel_taps(i["ev_conv_w_2"][0]),
        columns(i["ev_conv_b_2"][0]), columns(i["ev_ln_g_2"][0]), columns(i["ev_ln_b_2"][0]),
        i["ev_subln_g_2"][0][:, None], channel_taps(i["od_hy_short_w_2"][0]), columns(i["od_hy_short_b_2"][0]),
        columns(i["od_hy_skip_2"][0].reshape(-1)), channel_taps(i["od_dn_conv_w_2"][0]), i["od_dn_norm_g_2"][0][:, None],
        on_partitions(fb), on_partitions(i["od_hy_w1_2"][0]), on_partitions(i["od_hy_w2_2"][0]),
        i["od_w_in_2"][0][:, 7 * CH:].reshape(DK, P, 16).transpose(1, 0, 2).reshape(P, -1)], axis=1)
    assert par.shape == (P, S_END)
    gates = [i["ada_b_2"][l][part * D:(part + 1) * D] for l in range(DEPTH) for part in (2, 5)]
    vrows = np.concatenate([*gates, *(i[f"ev_{n}_2"][0] for n in ("lq1", "lk1", "lq2", "lk2")),
                            *(i[f"od_dn_{n}_2"][0] for n in ("alog_f", "alog_b", "dtb_f", "dtb_b"))])
    assert vrows.shape == (V_END,)
    return {"ctx": i["ctx_2"][0], "par": par, "vrows": vrows, "w3": i["od_hy_w3_2"][0], "final_g": i["final_g_2"]}


def second_constants():
    out = np.zeros((P, K2_END), np.float32)
    f32 = np.float32
    pos = np.arange(SEQ)
    inv = f32(10000.0) ** (-np.arange(16, dtype=f32) / f32(16))
    ar, ac = ((x.astype(f32)[:, None] * inv).astype(np.float64) for x in (pos // 64, pos % 64))
    cos = np.concatenate([np.cos(ar), np.cos(ar), np.cos(ac), np.cos(ac)], 1)
    sin = np.concatenate([-np.sin(ar), np.sin(ar), -np.sin(ac), np.sin(ac)], 1)
    for at, tab in ((K2_COS, cos), (K2_SIN, sin)):
        out[:, at:at + TT * 64] = tab.reshape(TT, P, 64).transpose(1, 0, 2).reshape(P, -1)
    out[:, K2_LOWER:] = np.tril(np.ones((P, P)))
    return out


def transform_constants():
    n = 2 * SEQ
    t, f = np.arange(SEQ), np.arange(SEQ)
    ang = 2 * np.pi * ((t[:, None] * f[None, :]) % n) / n
    top = (-1.0) ** t
    re, im = np.cos(ang), -np.sin(ang)
    im_top = im.copy()
    im_top[:, 0] = top
    signal = np.concatenate([re, im_top], 1)
    re_top = re[:, 0:P].copy()
    re_top[:, 0] = top
    forward = np.concatenate([re, im, re_top], 1)
    backward = np.concatenate([re, -im, re_top], 1)
    backward[0] = 0.0
    inv_re, inv_im = 2 * re.T / n, 2 * im.T / n
    inv_re[0] = 1.0 / n
    inv_im[0] = top / n
    inverse = np.concatenate([inv_re, inv_im], 0)

    def tiles(m):
        return m.reshape(-1, P, m.shape[1]).transpose(1, 0, 2).reshape(P, -1)

    f32 = np.float32
    lo, hi = math.log(1e-2) / 1.5, math.log(1e-2) / 0.3
    tt = np.linspace(0.0, 1.0, SEQ).astype(f32)
    deltas = np.abs(np.linspace(lo, hi, CH).astype(f32))
    window = np.exp((-tt[:, None] * deltas).astype(np.float64))
    omega = (f32(2.0 * math.pi) * np.arange(SEQ, dtype=f32) / f32(SEQ))[:, None]
    a = (omega * np.linspace(1e-4, 15, 16).astype(f32)).astype(np.float64)
    z = np.concatenate([tt[:, None], np.cos(a), -np.sin(a)], 1).T
    out = np.concatenate([tiles(np.concatenate([forward, backward])), tiles(signal), tiles(inverse), tiles(window),
                          on_partitions(z)], 1).astype(f32)
    assert out.shape == (P, T_END)
    return out


def mask_constants():
    i = np.arange(P)
    r, s = i[:, None], i[None, :]
    levels = [((r >> l) & 1) & ((s >> l) == (r >> l) - 1) for l in range(LEVELS)]
    levels += [m.T for m in levels]
    bias = [np.where(s >= r, 0.0, MASKED), np.where(s <= r, 0.0, MASKED)]
    return np.concatenate(levels + bias, 1).astype(np.float32)


def kernel(**inputs):
    import concourse.bacc as bacc
    from concourse.bass_utils import run_bass_kernel_spmd as run

    i = {k: np.asarray(v) for k, v in inputs.items()}
    arrays = {**first_arrays(i), **second_arrays(i), "const": constants(), "const2": second_constants(),
              "transforms": transform_constants(), "masks": mask_constants(),
              "panels": np.stack(first_panels(i) + second_panels(i))}
    assert arrays["panels"].shape[0] == PANELS
    arrays = {n: np.ascontiguousarray(v) for n, v in arrays.items()}
    nc = bacc.Bacc("TRN2", target_bir_lowering=False, num_devices=1)
    aps = {n: nc.dram_tensor(f"in_{n}", v.shape, F32, kind="ExternalInput").ap() for n, v in arrays.items()}
    out = nc.dram_tensor("out_x", (SEQ, D), F32, kind="ExternalOutput").ap()
    program(nc, aps, out)
    got = run(nc, [{f"in_{n}": v for n, v in arrays.items()}], core_ids=[0])
    return got.results[0]["out_x"][None]
```

```python
import math
from contextlib import ExitStack, contextmanager

import numpy as np

import concourse.bass as bass
from concourse import mybir

F32 = mybir.dt.float32
F32R = mybir.dt.float32r
ACT = mybir.ActivationFunctionType
ALU = mybir.AluOpType
AX = mybir.AxisListType.X

P = 128
D = 1024
DK = D // P
SEQ = 256
TT = SEQ // P
DEPTH = 2
EPS = 1e-6
BANK = 512

FF = 2816
FK = FF // P
GU = FF // 256
DN = -(-FK // 4)
HEADS, HD = 8, 64
CH = 512
SMALL = 72
TOPK = 64
IDX_SCALE = (64 ** -0.5) * (8 ** -0.5)
ATT_SCALE = 64 ** -0.5
MASKED = -1.0e30
TAKEN = -3.0e38

PANEL = 4096
RING = 2
QUART = PANEL // 4
L1_PANELS = GU + DN + 10 + 4 + GU + DN
assert L1_PANELS % RING == 0
AT_FFN1 = 0
AT_PROJ = GU + DN
AT_FFN2 = AT_PROJ + 14

C_FFN1, C_MIX, C_FFN2, C_BS = 0, 8, 16, 24
C_WS = 28
C_SMALL = C_WS + 4 * P
C_END = C_SMALL + DK * SMALL
R_BGATE, R_LNG, R_LNB, R_END = 0, 2 * D, 2 * D + CH, 2 * D + 2 * CH

K_ID = 0
K_UPPER = K_ID + P
K_CAUSAL = K_UPPER + P
K_COS = K_CAUSAL + TT * SEQ
K_SIN = K_COS + TT * HD
K_END1 = K_SIN + TT * HD


@contextmanager
def stage(nc, *names):
    with ExitStack() as ctx:
        sems = [ctx.enter_context(nc.semaphore(n)) for n in names]
        with nc.Block(no_gpsimd_drain=True) as block:
            yield (block, *sems)
        nums = [s.num for s in sems]
        nc.sync.sem_clear(range(min(nums), max(nums) + 1))
        nc.all_engine_barrier(sem_only=True)


class Panels:

    def __init__(self, c, layer, per_layer, first, total):
        self.c, self.layer, self.per, self.first, self.total = c, layer, per_layer, first, total

    def _base(self, unit):
        b = (self.first // RING) * unit
        return b if self.layer is None else self.layer * (self.per // RING * unit) + b

    def landed(self, eng, m):
        slot = m % RING
        eng.wait_ge(self.c.landed[slot], self._base(16) + 16 * (m // RING + 1))
        return self.c.ring[:, slot]

    def refill(self, sp, m):
        at = self.first + m + RING
        if self.layer is None and at >= self.total:
            return
        src = self.c.panels[at] if self.layer is None else self.c.panels[self.layer * self.per + at]
        sp.dma_start(self.c.ring[:, m % RING], src).then_inc(self.c.landed[m % RING], 16)


def mm(nc, out, lhsT, rhs, start, stop):
    return nc.tensor.matmul(out, lhsT, rhs, start=start, stop=stop)


def norm_stage(nc, c, tiles, scale, shift=None, ahead=None, keep=False):
    n = len(tiles)
    T = n * P
    whole = keep or shift is not None
    with stage(nc, "squares", "mean_sq", "root", "inv_root", "normed", "turned", "cols_act", "cols_dve", "hi", "lo",
               "ahead_hi", "ahead_lo") as (
            block, squares, mean_sq, root, inv_root, normed, turned, cols_act, cols_dve, hi, lo, ahead_hi, ahead_lo):
        ps = c.ps[:, :, :].rearrange("p b n -> p (b n)").rearrange("p (k t) -> p k t", k=DK)
        flat = c.tok[:, :, :].rearrange("p a n -> p (a n)")
        out = flat[:, 0:DK * T].rearrange("p (k t) -> p k t", k=DK)

        def cols_of(t):
            return ps[:, :, t * P:(t + 1) * P] if n == 4 else \
                c.ps[:, 0:4, :].rearrange("p b (k t) -> p (b k) t", k=2)[:, :, t * P:(t + 1) * P]

        def cols_all(k):
            return ps[:, k, :] if n == 4 else c.ps[:, k // 2, (k % 2) * 256:(k % 2) * 256 + 256]

        @block.scalar
        def _(act):
            for i in range(0, n, 2):
                nc.scalar.activation(c.ps[:, 2 * i:2 * i + 2, :].rearrange("p b n -> p (b n)"), c.x[:, tiles[i]], ACT.Square,
                                     accum_out=c.stat[:, i:i + 1]).then_inc(squares, 1)
            act.wait_ge(mean_sq, 1)
            nc.scalar.activation(c.stat[:, 8:8 + n], c.stat[:, 4:4 + n], ACT.Sqrt).then_inc(root, 1)
            if ahead:
                src = ahead[0].landed(act, ahead[1])
                for q in range(2):
                    nc.scalar.activation(c.w_hi[:, q], src[:, q * QUART:(q + 1) * QUART], ACT.Copy).then_inc(ahead_hi, 1)
            act.wait_ge(turned, n)
            if not whole:
                for k in range(DK):
                    nc.scalar.activation(c.hT_hi[:, k, 0:T], cols_all(k), ACT.Copy, scale=scale(k, 0)).then_inc(hi, 1)
                return
            for k in (1, 3, 5, 7) if n == 4 else (2, 3, 6, 7):
                for st in range(n // TT):
                    tok = slice(st * SEQ, (st + 1) * SEQ)
                    nc.scalar.activation(out[:, k, tok], cols_all(k)[:, tok], ACT.Identity, scale=scale(k, st),
                                         bias=shift(k, st) if shift else 0.0).then_inc(cols_act, 1)
            for half in range(2):
                act.wait_ge(cols_act, (half + 1) * n)
                act.wait_ge(cols_dve, (half + 1) * n)
                nc.scalar.activation(c.hT_hi[:, 4 * half:4 * half + 4, 0:T], out[:, 4 * half:4 * half + 4, :],
                                     ACT.Copy).then_inc(hi, 1)

        @block.vector
        def _(dve):
            for i in range(1, n, 2):
                nc.vector.tensor_tensor_reduce(out=c.tok[:, i], in0=c.x[:, tiles[i]], in1=c.x[:, tiles[i]], scale=1.0,
                                               scalar=0.0, op0=ALU.mult, op1=ALU.add,
                                               accum_out=c.stat[:, i:i + 1]).then_inc(squares, 1)
            dve.wait_ge(squares, n)
            nc.vector.tensor_scalar(c.stat[:, 4:4 + n], c.stat[:, 0:n], 1.0 / D, EPS,
                                    ALU.mult, ALU.add).then_inc(mean_sq, 1)
            dve.wait_ge(root, 1)
            nc.vector.reciprocal(c.stat[:, 12:12 + n], c.stat[:, 8:8 + n]).then_inc(inv_root, 1)
            dve.wait_ge(inv_root, 1)
            for i, t in enumerate(tiles):
                nc.vector.tensor_scalar(c.tok[:, i], c.x[:, t], c.stat[:, 12 + i:13 + i], None,
                                        ALU.mult).then_inc(normed, 1)
            if not whole:
                for k in range(DK):
                    dve.wait_ge(hi, 2 * (k // 2) + 2)
                    nc.vector.scalar_tensor_tensor(out=c.hT_lo[:, k, 0:T], in0=cols_all(k), scalar=scale(k, 0),
                                                   in1=c.hT_hi[:, k, 0:T].bitcast(F32), op0=ALU.mult,
                                                   op1=ALU.subtract).then_inc(lo, 1)
                return
            dve.wait_ge(turned, n)
            for k in (0, 2, 4, 6) if n == 4 else (0, 1, 4, 5):
                for st in range(n // TT):
                    tok = slice(st * SEQ, (st + 1) * SEQ)
                    nc.vector.tensor_scalar(out[:, k, tok], cols_all(k)[:, tok], scale(k, st),
                                            shift(k, st) if shift else None, ALU.mult,
                                            ALU.add if shift else ALU.bypass).then_inc(cols_dve, 1)
            for half in range(2):
                ks = slice(4 * half, 4 * half + 4)
                dve.wait_ge(hi, half + 1)
                nc.vector.tensor_tensor(c.hT_lo[:, ks, 0:T], out[:, ks, :], c.hT_hi[:, ks, 0:T].bitcast(F32),
                                        ALU.subtract).then_inc(lo, 1)

        @block.gpsimd
        def _(pool):
            if ahead:
                src = c.ring[:, ahead[1] % RING]
                for q in range(2):
                    pool.wait_ge(ahead_hi, q + 1)
                    nc.gpsimd.tensor_tensor(c.w_lo[:, q], src[:, q * QUART:(q + 1) * QUART], c.w_hi[:, q].bitcast(F32),
                                            ALU.subtract).then_inc(ahead_lo, 1)
                pool.wait_ge(ahead_lo, 2)

        @block.tensor
        def _(pe):
            for i in range(n):
                pe.wait_ge(normed, i + 1)
                dst = cols_of(i)
                for k in range(DK):
                    last = nc.tensor.transpose(dst[:, k], c.tok[:, i, k * P:(k + 1) * P], c.ident)
                last.then_inc(turned, 1)


def mm3(nc, out, lhsT, rhs, start, stop):
    nc.tensor.matmul(out, lhsT[0], rhs[0], start=start, stop=False)
    nc.tensor.matmul(out, lhsT[0], rhs[1], start=False, stop=False)
    return nc.tensor.matmul(out, lhsT[1], rhs[0], start=False, stop=stop)


def split_hi(nc, c, act, w, m, q, Q, quart_done, w_hi, dst=None):
    dst = c.w_hi if dst is None else dst
    n = dst.shape[1]
    if q == 0:
        w.landed(act, m)
    if dst is c.w_hi and Q < 2:
        act.sem_inc(w_hi, 1)
        return
    if Q >= n:
        act.wait_ge(quart_done, Q - n + 1)
    nc.scalar.activation(dst[:, Q % n], c.ring[:, m % RING, q * QUART:(q + 1) * QUART], ACT.Copy).then_inc(w_hi, 1)


def split_lo(nc, c, dve, m, q, Q, w_hi, w_lo, dst=None, engine=None):
    if dst is None and Q < 2:
        dve.wait_ge(w_hi, Q + 1)
        dve.sem_inc(w_lo, 1)
        return
    hi, lo = dst or (c.w_hi, c.w_lo)
    n = hi.shape[1]
    dve.wait_ge(w_hi, Q + 1)
    (engine or nc.vector).tensor_tensor(lo[:, Q % n], c.ring[:, m % RING, q * QUART:(q + 1) * QUART],
                            hi[:, Q % n].bitcast(F32), ALU.subtract).then_inc(w_lo, 1)


def deep_quarters(c):
    own = [tuple(t[:, b].rearrange("p (a n) -> p a n", a=4) for t in (c.w_hi, c.w_lo)) for b in range(2)]
    return own + [tuple(t[:, 4 * b:4 * b + 4, SEQ:] for t in (c.hT_hi, c.hT_lo)) for b in range(2)]


def ffn_stage(nc, c, w, m0, loads=()):
    quarts = [(i, q) for i in range(GU + DN) for q in range(4 if i < GU else min(4, FK - 4 * (i - GU)))]
    with stage(nc, "w_hi", "w_lo", "quart_done", "silu_ready", "product", "hid_hi", "hid_lo", "added", "loaded") as (
            block, w_hi, w_lo, quart_done, silu_ready, product, hid_hi, hid_lo, added, loaded):
        hi, lo = (t[:, 0:FK * SEQ].rearrange("p (k t) -> p k t", k=FK) for t in (c.hid_hi, c.hid_lo))

        def last_quart(i):
            return sum(1 for x, _ in quarts if x <= i)

        @block.sync
        def _(sp):
            sp.wait_ge(c.rows_in, 16)
            for to, src in loads:
                sp.dma_start(to, src).then_inc(loaded, 16)
            for i in range(GU + DN):
                sp.wait_ge(w_lo, last_quart(i))
                w.refill(sp, m0 + i)
            if loads:
                sp.wait_ge(loaded, 16 * len(loads))

        @block.tensor
        def _(pe):
            for Q, (i, q) in enumerate(quarts):
                pe.wait_ge(w_lo, Q + 1)
                if i < GU:
                    if q == 0 and i >= 2:
                        pe.wait_ge(product, i - 1)
                    wt = [t[:, Q % 2].rearrange("p (k n) -> p k n", k=2) for t in (c.w_hi, c.w_lo)]
                    for f in range(4):
                        for kk in range(2):
                            k = 2 * q + kk
                            last = mm3(nc, c.ps[:, 4 * (i % 2) + f, 0:SEQ], [t[:, kk, f * P:(f + 1) * P] for t in wt],
                                       [t[:, k, 0:SEQ] for t in (c.hT_hi, c.hT_lo)], k == 0, k == DK - 1)
                    last.then_inc(quart_done, 1)
                else:
                    k = 4 * (i - GU) + q
                    if k % 2 == 0:
                        pe.wait_ge(hid_lo, k // 2 + 1)
                    for t in range(TT):
                        for n in range(2):
                            last = mm3(nc, c.ps[:, 4 + 2 * t + n], [h[:, k, t * P:(t + 1) * P] for h in (hi, lo)],
                                       [u[:, Q % 2, n * BANK:(n + 1) * BANK] for u in (c.w_hi, c.w_lo)],
                                       k == 0, k == FK - 1)
                    last.then_inc(quart_done, 1)

        @block.scalar
        def _(act):
            for Q, (i, q) in enumerate(quarts):
                split_hi(nc, c, act, w, m0 + i, q, Q, quart_done, w_hi)
                if q == 1 and 1 <= i <= GU:
                    b = 4 * ((i - 1) % 2)
                    act.wait_ge(quart_done, 4 * i)
                    if i >= 3:
                        act.wait_ge(hid_lo, i - 2)
                    nc.scalar.activation(c.tok[:, (i - 1) % 2, 0:BANK].rearrange("p (f t) -> p f t", f=2),
                                         c.ps[:, b:b + 2, 0:SEQ], ACT.Silu).then_inc(silu_ready, 1)
                if q == 2 and 1 <= i <= GU:
                    act.wait_ge(product, i)
                    nc.scalar.activation(hi[:, 2 * i - 2:2 * i, :].rearrange("p k t -> p (k t)"),
                                         c.tok[:, (i - 1) % 2, 0:BANK], ACT.Copy).then_inc(hid_hi, 1)

        @block.vector
        def _(dve):
            for Q, (i, q) in enumerate(quarts):
                split_lo(nc, c, dve, m0 + i, q, Q, w_hi, w_lo)
                if q == 1 and 1 <= i <= GU:
                    b = 4 * ((i - 1) % 2)
                    dve.wait_ge(silu_ready, i)
                    p = c.tok[:, (i - 1) % 2, 0:BANK].rearrange("p (f t) -> p f t", f=2)
                    nc.vector.tensor_tensor(p, c.ps[:, b + 2:b + 4, 0:SEQ], p, ALU.mult).then_inc(product, 1)
                if q == 2 and 1 <= i <= GU:
                    dve.wait_ge(hid_hi, i)
                    ks = slice(2 * i - 2, 2 * i)
                    nc.vector.tensor_tensor(lo[:, ks, :].rearrange("p k t -> p (k t)"), c.tok[:, (i - 1) % 2, 0:BANK],
                                            hi[:, ks, :].rearrange("p k t -> p (k t)").bitcast(F32),
                                            ALU.subtract).then_inc(hid_lo, 1)
            dve.wait_ge(quart_done, len(quarts))
            for t in range(TT):
                for n in range(2):
                    xs = c.x[:, t, n * BANK:(n + 1) * BANK]
                    nc.vector.scalar_tensor_tensor(out=xs, in0=c.ps[:, 4 + 2 * t + n], scalar=0.5, in1=xs,
                                                   op0=ALU.mult, op1=ALU.add).then_inc(added, 1)


def mixer1_stage(nc, c, w, m0):
    Q, K, QI, V, U, VA, GATES, PA, PB, WO = 0, 1, 2, 3, 4, 5, 6, 10, 11, 12
    UNITS = [(qb, h) for qb in range(TT) for h in (0, 1, 4, 5)]
    names = ["proj", "proj_read", "small_ready", "small_read", "rope_step", "roped", "kiroped", "q_turned", "q_cols",
             "logits", "relu_done", "score_step", "selected", "s_ready", "s_masked", "negmax", "exp_done", "p_turned",
             "p_cols", "pv", "o_norm", "o_step", "o_turned", "o_cols", "u_gelu", "v_gelu", "ln_step", "v_mean", "v_root",
             "v_norm", "ws_masked", "mixed", "ya", "ya_turned", "ya_cols", "gate_sum", "gate", "pa", "ma", "pb",
             "m_done", "m_turned", "m_cols", "out_ready", "added", "w_hi", "w_lo", "quart_done", "ya_lo", "o_lo", "m_lo"]
    with stage(nc, *names) as (block, *sems):
        s = dict(zip(names, sems))
        proj, proj_read = s["proj"], s["proj_read"]
        w_hi, w_lo, quart_done = s["w_hi"], s["w_lo"], s["quart_done"]
        bufs = deep_quarters(c)
        h32 = c.tok[:, 0:2, :].rearrange("p a n -> p (a n)").rearrange("p (k t) -> p k t", k=DK)
        yaT = [t.rearrange("p (k t) -> p k t", k=4) for t in (c.hid_lo[:, 1024:2048], c.hid_hi[:, 1024:2048])]
        oT = [t.rearrange("p (k t) -> p k t", k=4) for t in (c.hid_lo[:, 0:1024], c.hid_hi[:, 2048:3072])]
        mT = [c.hid_hi[:, 4096:6144].rearrange("p (k t) -> p k t", k=DK), c.hT_lo[:, :, 0:SEQ]]
        q, k, qi, v = (c.work[:, a * 1024:(a + 1) * 1024].rearrange("p (t n) -> p t n", t=TT) for a in range(4))
        u, va = (c.work[:, a * 1024:(a + 1) * 1024].rearrange("p (t n) -> p t n", t=TT) for a in (4, 5))
        qT, kT, qiT = (c.work[:, a * 1024:(a + 1) * 1024].rearrange("p (k t) -> p k t", k=4) for a in (6, 7, 8))
        gates = c.work[:, 10 * 1024:14 * 1024].rearrange("p (g t n) -> p g t n", g=2, t=TT)
        o = q
        m = c.work[:, 6 * 1024:8 * 1024].rearrange("p (t n) -> p t n", t=TT)
        kiT = c.work[:, 14 * 1024:14 * 1024 + SEQ]
        ki = c.work[:, 14 * 1024 + 256:14 * 1024 + 512].rearrange("p (t a n) -> p t a n", t=TT, a=2)
        wi = c.work[:, 14 * 1024 + 512:14 * 1024 + 528].rearrange("p (t n) -> p t n", t=TT)
        top = c.work[:, 14 * 1024 + 528:14 * 1024 + 536]
        negm = c.work[:, 14 * 1024 + 544:14 * 1024 + 560]
        sums = c.work[:, 14 * 1024 + 560:14 * 1024 + 576]
        rsum = c.work[:, 14 * 1024 + 576:14 * 1024 + 592]
        bn = c.work[:, 14 * 1024 + 592:14 * 1024 + 604].rearrange("p (t n) -> p t n", t=TT)
        mv = c.work[:, 14 * 1024 + 604:14 * 1024 + 608].rearrange("p (t n) -> p t n", t=TT)
        vstd = c.work[:, 14 * 1024 + 608:14 * 1024 + 616]
        mxs = c.work[:, 14 * 1024 + 616:14 * 1024 + 632]
        score = c.work[:, 15 * 1024:15 * 1024 + 512].rearrange("p (t n) -> p t n", t=TT)
        bias = c.work[:, 15 * 1024 + 512:16 * 1024].rearrange("p (t n) -> p t n", t=TT)
        relu = c.tok[:, 0:2, :].rearrange("p a b -> p (a b)")
        ropes = c.tok[:, 2:4, :].rearrange("p a b -> p (a b)")
        sm = c.tok[:, 2, :].rearrange("p (a n) -> p a n", a=2)
        prob = c.tok[:, 0, :].rearrange("p (a n) -> p a n", a=2)
        probT = c.tok[:, 1, :].rearrange("p (a n) -> p a n", a=2)
        ws = c.lay[:, C_WS:C_WS + 4 * P].rearrange("p (g t) -> p g t", g=4)
        small_w = c.lay[:, C_SMALL:C_END].rearrange("p (k n) -> p k n", k=DK)
        cos = c.const[:, K_COS:K_SIN].rearrange("p (t n) -> p t n", t=TT)
        sin = c.const[:, K_SIN:K_END1].rearrange("p (t n) -> p t n", t=TT)
        causal = c.const[:, K_CAUSAL:K_COS].rearrange("p (t n) -> p t n", t=TT)

        @block.sync
        def _(sp):
            for i in range(WO + 2):
                sp.wait_ge(w_lo, 4 * i + 4)
                w.refill(sp, m0 + i)

        @block.tensor
        def _(pe):
            def half_panel(i, half):
                if i >= 2 and half == 0:
                    pe.wait_ge(proj_read, 2 * (i - 2) + 2)
                for qq in (2 * half, 2 * half + 1):
                    pe.wait_ge(w_lo, 4 * i + qq + 1)
                    hi, lo = bufs[qq]
                    for t in range(TT):
                        for e in range(2):
                            kk = 2 * qq + e
                            last = mm3(nc, c.ps[:, 2 * (i % 2) + t], [h[:, kk, t * P:(t + 1) * P] for h in (c.hT_hi, c.hT_lo)],
                                       [b[:, 2 * e:2 * e + 2, :] for b in (hi, lo)], kk == 0, kk == DK - 1)
                        if qq == 3:
                            last.then_inc(proj, 1)
                    if qq < 3:
                        last.then_inc(quart_done, 1)

            def whole_panel(i):
                half_panel(i, 0)
                half_panel(i, 1)

            def turn(src, n_turn):
                for b in range(4):
                    for t in range(TT):
                        last = nc.tensor.transpose(c.ps[:, 4 + b // 2, (b % 2) * 256 + t * P:(b % 2) * 256 + (t + 1) * P],
                                                   src[:, t, b * P:(b + 1) * P], c.ident)
                last.then_inc(s["q_turned"], 1)

            for t in range(TT):
                for kk in range(DK):
                    last = mm(nc, c.ps[:, 6, t * P:t * P + SMALL], h32[:, kk, t * P:(t + 1) * P], small_w[:, kk, :],
                              kk == 0, kk == DK - 1)
            last.then_inc(s["small_ready"], 1)
            whole_panel(Q)
            whole_panel(K)
            pe.wait_ge(s["roped"], 1)
            turn(q, 0)
            whole_panel(QI)
            pe.wait_ge(s["roped"], 2)
            pe.wait_ge(s["q_cols"], 1)
            turn(k, 1)
            whole_panel(V)
            pe.wait_ge(s["roped"], 3)
            pe.wait_ge(s["q_cols"], 2)
            turn(qi, 2)
            pe.wait_ge(s["kiroped"], 1)
            for t in range(TT):
                last = nc.tensor.transpose(c.ps[:, 7, t * P:(t + 1) * P], ki[:, t].rearrange("p a n -> p (a n)"), c.ident)
            last.then_inc(s["q_turned"], 1)
            whole_panel(U)
            pe.wait_ge(s["q_cols"], 4)
            n = 0
            for qb in range(TT):
                keys = (qb + 1) * P
                for half in range(2):
                    if n >= 2:
                        pe.wait_ge(s["relu_done"], n - 1)
                    for hh in range(4):
                        h = 4 * half + hh
                        hp = slice(64 * (h % 2), 64 * (h % 2) + 64)
                        last = mm(nc, c.ps[:, 4 + 2 * (n % 2) + hh % 2, (hh // 2) * 256:(hh // 2) * 256 + keys],
                                  qiT[hp, h // 2, qb * P:(qb + 1) * P], kiT[hp, 0:keys], True, True)
                    last.then_inc(s["logits"], 1)
                    n += 1
            whole_panel(VA)

            def scores(j):
                qb, h0 = UNITS[j]
                keys = (qb + 1) * P
                if j == 0:
                    pe.wait_ge(s["relu_done"], 4)
                if j >= 1:
                    pe.wait_ge(s["s_masked"], j)
                for e in range(2):
                    h = h0 + 2 * e
                    hp = slice(64 * (h % 2), 64 * (h % 2) + 64)
                    last = mm(nc, c.ps[:, 4, e * keys:(e + 1) * keys], qT[hp, h // 2, qb * P:(qb + 1) * P],
                              kT[hp, h // 2, 0:keys], True, True)
                last.then_inc(s["s_ready"], 1)

            def turn_probs(j):
                qb, h0 = UNITS[j]
                pe.wait_ge(s["exp_done"], 2 * j + 2)
                if j >= 1:
                    pe.wait_ge(s["p_cols"], j)
                for e in range(2):
                    for kb in range(qb + 1):
                        b = e * (qb + 1) + kb
                        last = nc.tensor.transpose(c.ps[:, 6, b * P:(b + 1) * P], prob[:, j % 2, b * P:(b + 1) * P],
                                                   c.ident)
                last.then_inc(s["p_turned"], 1)

            def weigh(j):
                qb, h0 = UNITS[j]
                pe.wait_ge(s["p_cols"], j + 1)
                if h0 == 0 and qb:
                    pe.wait_ge(s["o_norm"], qb)
                for e in range(2):
                    for kb in range(qb + 1):
                        b = e * (qb + 1) + kb
                        h = h0 + 2 * e
                        last = mm(nc, c.ps[:, 7, h * HD:(h + 1) * HD], probT[:, j % 2, b * P:(b + 1) * P],
                                  v[:, kb, h * HD:(h + 1) * HD], kb == 0, kb == qb)
                last.then_inc(s["pv"], 1)

            def spatial(n):
                if n == 0:
                    pe.wait_ge(s["ws_masked"], 1)
                pe.wait_ge(s["v_norm"], n + 1)
                if n:
                    pe.wait_ge(s["ya"], 4 * n)
                for g in range(4):
                    last = mm(nc, c.ps[:, 5, g * P:(g + 1) * P], ws[:, g, :], va[:, n, g * P:(g + 1) * P], True, True)
                last.then_inc(s["mixed"], 1)

            def turn_ya(n):
                pe.wait_ge(s["ya"], 4 * TT)
                if n:
                    pe.wait_ge(s["ya_lo"], n)
                for g in range(4):
                    last = nc.tensor.transpose(c.ps[:, 5, g * P:(g + 1) * P], u[:, n, g * P:(g + 1) * P], c.ident)
                last.then_inc(s["ya_turned"], 1)

            for j in range(8):
                scores(j)
                half_panel(GATES + j // 2, j % 2)
                if j >= 1:
                    turn_probs(j - 1)
                if j >= 2:
                    weigh(j - 2)
                if j in (2, 3):
                    spatial(j - 2)
                if j in (5, 6):
                    turn_ya(j - 5)
            def output_tile(qq, src, bank, k8, t, last_k8):
                for n in range(2):
                    last = mm3(nc, c.ps[:, bank + 2 * t + n], [x[:, k8, t * P:(t + 1) * P] for x in src],
                               [b[:, 2 * n:2 * n + 2, :] for b in bufs[qq]], k8 == 0, k8 == last_k8)
                return last

            def output_quarter(i, qq, src, bank, k8, done, last_k8=3):
                pe.wait_ge(w_lo, 4 * i + qq + 1)
                for t in range(TT):
                    last = output_tile(qq, src, bank, k8, t, last_k8)
                last.then_inc(done if qq == 3 else quart_done, 1)

            pe.wait_ge(s["ya_lo"], 2)
            pe.wait_ge(proj_read, 20)
            for qq in range(4):
                output_quarter(PA, qq, yaT, 0, qq, s["pa"])
                if qq == 0:
                    turn_probs(7)
                    weigh(6)
                if qq == 2:
                    weigh(7)
            pe.wait_ge(s["o_norm"], 2)
            for b in range(4):
                for t in range(TT):
                    last = nc.tensor.transpose(c.ps[:, 4 + b // 2, (b % 2) * 256 + t * P:(b % 2) * 256 + (t + 1) * P],
                                               o[:, t, b * P:(b + 1) * P], c.ident)
            last.then_inc(s["o_turned"], 1)
            pe.wait_ge(s["o_lo"], 1)
            for t in range(TT):
                for qq in range(4):
                    if t == 0:
                        pe.wait_ge(w_lo, 4 * PB + qq + 1)
                    last = output_tile(qq, oT, 4, qq, t, 3)
                    if qq == 3:
                        last.then_inc(s["pb"], 1)
                    elif t:
                        last.then_inc(quart_done, 1)
            pe.wait_ge(s["ma"], 4)
            for t in range(TT):
                pe.wait_ge(s["m_done"], 2 * t + 2)
                for kk in range(DK):
                    last = nc.tensor.transpose(c.ps[:, kk // 2, (kk % 2) * 256 + t * P:(kk % 2) * 256 + (t + 1) * P],
                                               m[:, t, kk * P:(kk + 1) * P], c.ident)
                last.then_inc(s["m_turned"], 1)
            for half in range(2):
                for kk in range(4):
                    k8 = 4 * half + kk
                    if k8 % 2 == 0:
                        pe.wait_ge(s["m_lo"], k8 // 2 + 1)
                    output_quarter(WO + half, kk, mT, 4, k8, s["out_ready"], DK - 1)

        @block.gpsimd
        def _(pool):
            for i in range(WO + 2):
                for qq in range(4):
                    pool.wait_ge(w_hi, 4 * i + qq + 1)
                    if i == 0 and qq < 2:
                        pool.sem_inc(w_lo, 1)
                        continue
                    hi, lo = bufs[qq]
                    nc.gpsimd.tensor_tensor(lo, c.ring[:, (m0 + i) % RING, qq * QUART:(qq + 1) * QUART].rearrange(
                        "p (a n) -> p a n", a=4), hi.bitcast(F32), ALU.subtract).then_inc(w_lo, 1)

        @block.scalar
        def _(act):
            def columns(dst, sem):
                act.wait_ge(s["q_turned"], sem)
                nc.scalar.activation(dst.rearrange("p k t -> p (k t)"), c.ps[:, 4:6, :].rearrange("p b n -> p (b n)"),
                                     ACT.Copy).then_inc(s["q_cols"], 1)

            def split_panel(i, quarters=range(4)):
                last_done = {PB: (s["pa"], 1), WO: (s["pb"], 2), WO + 1: (s["out_ready"], 1)}.get(i, (proj, 2 * i))
                for qq in quarters:
                    if qq == 0:
                        w.landed(act, m0 + i)
                    if i == 0 and qq < 2:
                        act.sem_inc(w_hi, 1)
                        continue
                    if i >= 1:
                        act.wait_ge(*(last_done if qq == 3 else (quart_done, 3 * (i - 1) + qq + 1)))
                    nc.scalar.activation(bufs[qq][0],
                                         c.ring[:, (m0 + i) % RING, qq * QUART:(qq + 1) * QUART].rearrange("p (a n) -> p a n", a=4),
                                         ACT.Copy).then_inc(w_hi, 1)

            split_panel(Q)
            act.wait_ge(s["kiroped"], 1)
            for t in range(TT):
                nc.scalar.activation(wi[:, t], c.ps[:, 6, t * P + 64:t * P + 72], ACT.Copy,
                                     scale=IDX_SCALE).then_inc(s["small_read"], 1)
            split_panel(K)
            split_panel(QI)
            columns(qT, 1)
            split_panel(V)
            columns(kT, 2)
            split_panel(U)
            for t in range(TT):
                act.wait_ge(proj, 2 * V + t + 1)
                act.wait_ge(proj_read, 2 * V + t)
                nc.scalar.activation(v[:, t], c.ps[:, 2 * (V % 2) + t], ACT.Copy).then_inc(proj_read, 1)
            columns(qiT, 3)
            act.wait_ge(s["q_turned"], 4)
            nc.scalar.activation(kiT, c.ps[:, 7, 0:SEQ], ACT.Copy).then_inc(s["q_cols"], 1)
            split_panel(VA)
            for t in range(TT):
                act.wait_ge(proj, 2 * U + t + 1)
                nc.scalar.activation(u[:, t], c.ps[:, 2 * (U % 2) + t], ACT.Gelu_apprx_tanh).then_inc(proj_read, 1)
            act.wait_ge(proj_read, 2 * U + 2)
            for n in range(4):
                qb = n // 2
                act.wait_ge(s["logits"], n + 1)
                if n >= 2:
                    act.wait_ge(s["score_step"], 4 * (n - 1))
                keys = (qb + 1) * P
                nc.scalar.activation(
                    relu[:, (n % 2) * 1024:(n % 2 + 1) * 1024].rearrange("p (h n) -> p h n", h=4)[:, :, 0:keys],
                    c.ps[:, 4 + 2 * (n % 2):6 + 2 * (n % 2), :].rearrange("p b (h n) -> p (b h) n", h=2)[:, :, 0:keys],
                    ACT.Relu).then_inc(s["relu_done"], 1)
            split_panel(GATES)
            for t in range(TT):
                act.wait_ge(proj, 2 * VA + t + 1)
                nc.scalar.activation(va[:, t], c.ps[:, 2 * (VA % 2) + t], ACT.Gelu_apprx_tanh).then_inc(proj_read, 1)
            act.wait_ge(s["v_mean"], 1)
            nc.scalar.activation(vstd[:, 2:4], vstd[:, 0:2], ACT.Sqrt).then_inc(s["v_root"], 1)

            def exps(j):
                qb, h0 = UNITS[j]
                keys = (qb + 1) * P
                act.wait_ge(s["negmax"], j + 1)
                if j >= 2:
                    act.wait_ge(s["p_turned"], j - 1)
                if j == 0:
                    act.wait_ge(s["score_step"], 16)
                for e in range(2):
                    h = 8 * qb + h0 + 2 * e
                    nc.scalar.activation(prob[:, j % 2, e * keys:(e + 1) * keys], sm[:, j % 2, e * keys:(e + 1) * keys],
                                         ACT.Exp, bias=negm[:, h:h + 1],
                                         accum_out=sums[:, h:h + 1]).then_inc(s["exp_done"], 1)

            def prob_columns(j):
                qb, h0 = UNITS[j]
                n = 2 * (qb + 1) * P
                act.wait_ge(s["p_turned"], j + 1)
                if j >= 2:
                    act.wait_ge(s["pv"], j - 1)
                nc.scalar.activation(probT[:, j % 2, 0:n], c.ps[:, 6, 0:n], ACT.Copy).then_inc(s["p_cols"], 1)

            for j in range(8):
                exps(j)
                if j in (6, 7):
                    n = j - 6
                    act.wait_ge(s["ya_turned"], n + 1)
                    nc.scalar.activation(yaT[0][:, :, n * P:(n + 1) * P], c.ps[:, 5, :].rearrange("p (g t) -> p g t", g=4),
                                         ACT.Copy).then_inc(s["ya_cols"], 1)
                split_panel(GATES + 1 + j // 2, (0, 1) if j % 2 == 0 else (2, 3))
                if j >= 1:
                    prob_columns(j - 1)
            prob_columns(7)
            split_panel(PB, (0, 1, 2))
            act.wait_ge(s["o_turned"], 1)
            nc.scalar.activation(oT[0].rearrange("p k t -> p (k t)"), c.ps[:, 4:6, :].rearrange("p b n -> p (b n)"),
                                 ACT.Copy).then_inc(s["o_cols"], 1)
            split_panel(PB, (3,))
            for i in range(4):
                act.wait_ge(s["gate_sum"], 2 * i + 2)
                g = gates[:, i // 2, :, (i % 2) * BANK:(i % 2 + 1) * BANK]
                nc.scalar.activation(g, g, ACT.Sigmoid).then_inc(s["gate"], 1)
            split_panel(WO)
            act.wait_ge(s["m_turned"], 2)
            for b in range(4):
                nc.scalar.activation(mT[0][:, 2 * b:2 * b + 2, :].rearrange("p k t -> p (k t)"), c.ps[:, b],
                                     ACT.Copy).then_inc(s["m_cols"], 1)
            split_panel(WO + 1)

        @block.vector
        def _(dve):
            rope_n = [0]

            def rope_tile(src, t, heads, dsts):
                n = heads * HD
                a = ropes[:, 0:n].rearrange("p (h n) -> p h n", h=heads)
                b = ropes[:, 512:512 + n].rearrange("p (h n) -> p h n", h=heads)
                sv = src.rearrange("p (h n) -> p h n", h=heads)
                ct = cos[:, t].unsqueeze(1).broadcast_to([P, heads, HD])
                st = sin[:, t].unsqueeze(1).broadcast_to([P, heads, HD])
                nc.vector.tensor_tensor(a, sv, ct, ALU.mult).then_inc(s["rope_step"], 1)
                nc.vector.tensor_tensor(b[:, :, 0:32], sv[:, :, 32:64], st[:, :, 0:32], ALU.mult).then_inc(s["rope_step"], 1)
                nc.vector.tensor_tensor(b[:, :, 32:64], sv[:, :, 0:32], st[:, :, 32:64], ALU.mult).then_inc(s["rope_step"], 1)
                rope_n[0] += 3
                dve.wait_ge(s["rope_step"], rope_n[0])
                for dst in dsts:
                    nc.vector.tensor_tensor(dst, a, b, ALU.add).then_inc(s["rope_step"], 1)
                    rope_n[0] += 1
                dve.wait_ge(s["rope_step"], rope_n[0])

            nc.vector.tensor_tensor(ws, ws, c.const[:, K_UPPER:K_UPPER + P].unsqueeze(1).broadcast_to([P, 4, P]),
                                    ALU.mult).then_inc(s["ws_masked"], 1)
            dve.wait_ge(s["small_ready"], 1)
            for t in range(TT):
                rope_tile(c.ps[:, 6, t * P:t * P + 64], t, 1, [ki[:, t, e:e + 1, :] for e in range(2)])
            dve.sem_inc(s["kiroped"], 1)
            for i, dst in ((0, q), (1, k), (2, qi)):
                for t in range(TT):
                    dve.wait_ge(proj, 2 * i + t + 1)
                    rope_tile(c.ps[:, 2 * (i % 2) + t], t, HEADS, [dst[:, t].rearrange("p (h n) -> p h n", h=HEADS)])
                    dve.sem_inc(proj_read, 1)
                dve.sem_inc(s["roped"], 1)
            dve.wait_ge(s["small_read"], 2)
            for n in range(4):
                qb = n // 2
                keys = (qb + 1) * P
                dve.wait_ge(s["relu_done"], n + 1)
                for hh in range(4):
                    h = 4 * (n % 2) + hh
                    at = (n % 2) * 1024 + (hh % 2) * 512 + (hh // 2) * 256
                    r = relu[:, at:at + keys]
                    sc = score[:, qb, 0:keys]
                    if h == 0:
                        nc.vector.tensor_scalar(sc, r, wi[:, qb, 0:1], None, ALU.mult).then_inc(s["score_step"], 1)
                    else:
                        dve.wait_ge(s["score_step"], 4 * n + hh)
                        nc.vector.scalar_tensor_tensor(out=sc, in0=r, scalar=wi[:, qb, h:h + 1], in1=sc,
                                                       op0=ALU.mult, op1=ALU.add).then_inc(s["score_step"], 1)
            step = [16]

            def then(ins):
                ins.then_inc(s["score_step"], 1)
                step[0] += 1
                dve.wait_ge(s["score_step"], step[0])

            dve.wait_ge(s["score_step"], 16)
            for qb in range(TT):
                keys = (qb + 1) * P
                sc = score[:, qb, 0:keys]
                bi = bias[:, qb, 0:keys]
                then(nc.vector.tensor_tensor(sc, sc, causal[:, qb, 0:keys], ALU.add))
                for _ in range(TOPK // 8):
                    then(nc.vector.max(top, sc))
                    then(nc.vector.match_replace(sc, top, sc, TAKEN))
                then(nc.vector.tensor_scalar(bi, sc, TAKEN / 2, MASKED, ALU.is_gt, ALU.mult))
                then(nc.vector.tensor_tensor(bi, bi, causal[:, qb, 0:keys], ALU.add))

            def mask(j):
                qb, h0 = UNITS[j]
                keys = (qb + 1) * P
                dve.wait_ge(s["s_ready"], j + 1)
                if j >= 2:
                    dve.wait_ge(s["exp_done"], 2 * (j - 1))
                dst = sm[:, j % 2, 0:2 * keys].rearrange("p (e n) -> p e n", e=2)
                nc.vector.scalar_tensor_tensor(out=dst, in0=c.ps[:, 4, 0:2 * keys].rearrange("p (e n) -> p e n", e=2),
                                               scalar=ATT_SCALE, in1=bias[:, qb, 0:keys].unsqueeze(1).broadcast_to([P, 2, keys]),
                                               op0=ALU.mult, op1=ALU.add).then_inc(s["s_masked"], 1)
                dve.wait_ge(s["s_masked"], j + 1)
                h = 8 * qb + h0
                nc.vector.tensor_reduce(mxs[:, h:h + 3:2], dst, axis=AX, op=ALU.max).then_inc(s["o_step"], 1)
                ostep[0] += 1
                dve.wait_ge(s["o_step"], ostep[0])
                nc.vector.tensor_scalar(negm[:, h:h + 3:2], mxs[:, h:h + 3:2], -1.0, None, ALU.mult).then_inc(s["negmax"], 1)

            ostep = [0]

            def add_gate_bias(i, t):
                dve.wait_ge(proj, 2 * (GATES + i) + t + 1)
                nc.vector.tensor_tensor(gates[:, i // 2, t, (i % 2) * BANK:(i % 2 + 1) * BANK],
                                        c.ps[:, 2 * (i % 2) + t], c.rows[:, R_BGATE + i * BANK:R_BGATE + (i + 1) * BANK],
                                        ALU.add).then_inc(s["gate_sum"], 1)
                dve.wait_ge(s["gate_sum"], 2 * i + t + 1)
                dve.sem_inc(proj_read, 1)

            def norm_out(qb):
                dve.wait_ge(s["pv"], 4 * (qb + 1))
                nc.vector.reciprocal(rsum[:, 8 * qb:8 * qb + 8], sums[:, 8 * qb:8 * qb + 8]).then_inc(s["o_step"], 1)
                ostep[0] += 1
                dve.wait_ge(s["o_step"], ostep[0])
                nc.vector.tensor_tensor(o[:, qb].rearrange("p (h n) -> p h n", h=HEADS),
                                        c.ps[:, 7].rearrange("p (h n) -> p h n", h=HEADS),
                                        rsum[:, 8 * qb:8 * qb + 8].unsqueeze(2).broadcast_to([P, HEADS, HD]),
                                        ALU.mult).then_inc(s["o_norm"], 1)

            ln = [0]

            def ln_then(ins):
                ins.then_inc(s["ln_step"], 1)
                ln[0] += 1
                dve.wait_ge(s["ln_step"], ln[0])

            dve.wait_ge(proj_read, 2 * VA + 2)
            for t in range(TT):
                ln_then(nc.vector.bn_stats(bn[:, t], va[:, t]))
                ln_then(nc.vector.bn_aggr(mv[:, t], bn[:, t]))
            nc.vector.tensor_scalar(vstd[:, 0:2], mv[:, :, 1], EPS, None, ALU.add).then_inc(s["v_mean"], 1)
            dve.wait_ge(s["v_root"], 1)
            ln_then(nc.vector.reciprocal(vstd[:, 4:6], vstd[:, 2:4]))
            for t in range(TT):
                ln_then(nc.vector.tensor_scalar(va[:, t], va[:, t], mv[:, t, 0:1], vstd[:, 4 + t:5 + t],
                                                ALU.subtract, ALU.mult))
                ln_then(nc.vector.tensor_tensor(va[:, t], va[:, t], c.rows[:, R_LNG:R_LNB], ALU.mult))
                nc.vector.tensor_tensor(va[:, t], va[:, t], c.rows[:, R_LNB:R_END], ALU.add).then_inc(s["v_norm"], 1)

            def gate_u(n):
                dve.wait_ge(s["mixed"], n + 1)
                for g in range(4):
                    us = u[:, n, g * P:(g + 1) * P]
                    nc.vector.scalar_tensor_tensor(out=us, in0=c.ps[:, 5, g * P:(g + 1) * P],
                                                   scalar=c.lay[:, C_BS + g:C_BS + g + 1], in1=us,
                                                   op0=ALU.add, op1=ALU.mult).then_inc(s["ya"], 1)

            for j in range(8):
                mask(j)
                if j % 2 == 0 and j:
                    for t in range(TT):
                        add_gate_bias(j // 2 - 1, t)
                if j in (2, 3):
                    gate_u(j - 2)
                if j >= 6:
                    n = j - 6
                    dve.wait_ge(s["ya_cols"], n + 1)
                    tok = slice(n * P, (n + 1) * P)
                    nc.vector.tensor_tensor(yaT[1][:, :, tok], c.ps[:, 5, :].rearrange("p (g t) -> p g t", g=4),
                                            yaT[0][:, :, tok].bitcast(F32), ALU.subtract).then_inc(s["ya_lo"], 1)
                if j == 6:
                    norm_out(0)
            for t in range(TT):
                add_gate_bias(3, t)
            norm_out(1)
            dve.wait_ge(s["o_cols"], 1)
            nc.vector.tensor_tensor(oT[1].rearrange("p k t -> p (k t)"), c.ps[:, 4:6, :].rearrange("p b n -> p (b n)"),
                                    oT[0].rearrange("p k t -> p (k t)").bitcast(F32), ALU.subtract).then_inc(s["o_lo"], 1)
            for t in range(TT):
                dve.wait_ge(s["pa"], 1)
                for n in range(2):
                    dve.wait_ge(s["gate"], n + 1)
                    nc.vector.tensor_tensor(m[:, t, n * BANK:(n + 1) * BANK], c.ps[:, 2 * t + n],
                                            gates[:, 0, t, n * BANK:(n + 1) * BANK], ALU.mult).then_inc(s["ma"], 1)
            for t in range(TT):
                dve.wait_ge(s["pb"], t + 1)
                for n in range(2):
                    dve.wait_ge(s["gate"], n + 3)
                    gb = gates[:, 1, t, n * BANK:(n + 1) * BANK]
                    ms = m[:, t, n * BANK:(n + 1) * BANK]
                    ln_then(nc.vector.tensor_tensor(gb, c.ps[:, 4 + 2 * t + n], gb, ALU.mult))
                    nc.vector.tensor_tensor(ms, ms, gb, ALU.add).then_inc(s["m_done"], 1)
            for b in range(4):
                dve.wait_ge(s["m_cols"], b + 1)
                nc.vector.tensor_tensor(mT[1][:, 2 * b:2 * b + 2, :], c.ps[:, b].rearrange("p (k t) -> p k t", k=2),
                                        mT[0][:, 2 * b:2 * b + 2, :].bitcast(F32), ALU.subtract).then_inc(s["m_lo"], 1)
            dve.wait_ge(s["out_ready"], 2)
            for t in range(TT):
                for n in range(2):
                    xs = c.x[:, t, n * BANK:(n + 1) * BANK]
                    nc.vector.tensor_tensor(xs, c.ps[:, 4 + 2 * t + n], xs, ALU.add).then_inc(s["added"], 1)
STREAMS = 2
ALL = TT * STREAMS
BOTH = SEQ * STREAMS
MODS = 6
CONV_W = 31
PAD = (CONV_W - 1) // 2
LAMBDA0 = 0.8 - 0.6 * math.exp(-0.3 * 0)
MLP = 4 * D
MK = MLP // P

B_ADA0 = 0
B_EVEN = B_ADA0 + 12
B_MLP0 = B_EVEN + 5 + 2
B_ADA1 = B_MLP0 + 16
B_ODD = B_ADA1 + 12
B_MLP1 = B_ODD + 7 + 2
B_END = B_MLP1 + 16
PANELS = DEPTH * L1_PANELS + B_END

S_COND = 0
S_ADAB = S_COND + DK * 2
S_N1 = S_ADAB + DEPTH * 48
S_N2 = S_N1 + DEPTH * DK
S_CONVW = S_N2 + DEPTH * DK
S_CONVB = S_CONVW + 4 * CONV_W
S_LNG = S_CONVB + 4
S_LNB = S_LNG + 4
S_SUBLN = S_LNB + 4
S_HYSW = S_SUBLN + 1
S_HYSB = S_HYSW + 12 * 3
S_HYSKIP = S_HYSB + 12
S_DNW = S_HYSKIP + 8
S_DNG = S_DNW + 12 * 5
S_FB = S_DNG + 1
S_W1 = S_FB + 4
S_W2 = S_W1 + 64
S_REST = S_W2 + 64
S_END = S_REST + DK * 16

V_ADAG = 0
V_LQK = V_ADAG + DEPTH * 2 * D
V_DN = V_LQK + 4 * 64
V_END = V_DN + 16

K2_COS = 0
K2_SIN = K2_COS + TT * 64
K2_LOWER = K2_SIN + TT * 64
K2_END = K2_LOWER + P


def ada_stage(nc, c, w, m0, layer):
    N = 12
    with stage(nc, "silu_c", "cond_hi", "cond_lo", "fold_made", "w_hi", "w_lo", "quart_done", "row_read", "cols_ready",
               "cols_read", "spread", "gates", "scales", "bias_in") as (
            block, silu_c, cond_hi, cond_lo, fold_made, w_hi, w_lo, quart_done, row_read, cols_ready,
            cols_read, spread, gates, scales, bias_in):
        cond = c.par[:, S_COND:S_COND + 2 * DK].rearrange("p (k s) -> p k s", s=2)
        bcol = c.par[:, S_ADAB + 48 * layer:S_ADAB + 48 * layer + 48]
        order = [0, 1, 3, 4]
        brow = c.tok[:, 0:2, :]
        row = c.tok[0:4, 2, :].rearrange("p (a n) -> p a n", a=2)
        fold = c.stat[0:4, 0:2]
        w_parts = [t[:, :].rearrange("p (b n) -> p b n", n=QUART) for t in (c.hid_hi, c.hid_lo)]
        nb = w_parts[0].shape[1]

        @block.sync
        def _(sp):
            sp.dma_start(brow.rearrange("p a n -> p (a n)"),
                         c.vrows[V_ADAG + 2 * D * layer:V_ADAG + 2 * D * (layer + 1)].partition_broadcast(P)).then_inc(bias_in, 16)
            for i in range(N):
                sp.wait_ge(w_lo, 4 * i + 4)
                w.refill(sp, m0 + i)

        @block.tensor
        def _(pe):
            def deal(i):
                pe.wait_ge(row_read, i + 1)
                r = row[:, i % 2, :]
                if i < 8:
                    if i >= 2:
                        pe.wait_ge(cols_read, i - 1)
                    for f in range(4):
                        last = mm(nc, c.ps[:, i % 2, 2 * f:2 * f + 2], r[:, f * P:(f + 1) * P], fold, True, True)
                    last.then_inc(cols_ready, 1)
                else:
                    if i >= 9:
                        pe.wait_ge(gates, 2 * (i - 8))
                    for s in range(STREAMS):
                        last = mm(nc, c.ps[:, 4 + s], fold[:, s:s + 1].broadcast_to([4, P]), r, True, True)
                    last.then_inc(spread, 1)

            pe.wait_ge(cond_lo, 1)
            pe.wait_ge(fold_made, 1)
            for i in range(N):
                for q in range(4):
                    Q = 4 * i + q
                    pe.wait_ge(w_lo, Q + 1)
                    if q == 0 and i >= 2:
                        pe.wait_ge(row_read, i - 1)
                    for part in w_parts:
                        for kk in range(2):
                            k = 2 * q + kk
                            last = mm(nc, c.ps[0:4, 2 + i % 2], c.cond_parts[:, k, :],
                                      part[:, Q % nb, kk * BANK:(kk + 1) * BANK],
                                      q == 0 and kk == 0 and part is w_parts[0], q == 3 and kk == 1 and part is w_parts[1])
                    last.then_inc(quart_done, 1)
                    if q == 1 and i >= 1:
                        deal(i - 1)
            deal(N - 1)

        @block.scalar
        def _(act):
            nc.scalar.activation(c.silu_c, cond, ACT.Silu).then_inc(silu_c, 1)
            act.wait_ge(silu_c, 1)
            nc.scalar.activation(c.cond_parts[:, :, 0:2], c.silu_c, ACT.Copy).then_inc(cond_hi, 1)

            def read_row(i):
                act.wait_ge(quart_done, 4 * i + 4)
                if i >= 2:
                    act.wait_ge(*((cols_ready, i - 1) if i < 10 else (spread, i - 9)))
                nc.scalar.activation(row[:, i % 2, :], c.ps[0:4, 2 + i % 2], ACT.Copy).then_inc(row_read, 1)

            for i in range(N):
                for q in range(4):
                    split_hi(nc, c, act, w, m0 + i, q, 4 * i + q, quart_done, w_hi, w_parts[0])
                    if q == 1 and i >= 1:
                        read_row(i - 1)
            read_row(N - 1)

        @block.vector
        def _(dve):
            dve.wait_ge(cond_hi, 1)
            nc.vector.tensor_tensor(c.cond_parts[:, :, 2:4], c.silu_c, c.cond_parts[:, :, 0:2].bitcast(F32),
                                    ALU.subtract).then_inc(cond_lo, 1)
            nc.vector.tensor_tensor(fold, c.ident[0:4, 0:2], c.ident[0:4, 2:4], ALU.add).then_inc(fold_made, 1)

            def take(i):
                if i < 8:
                    dve.wait_ge(cols_ready, i + 1)
                    at = order[i // 2] * DK + 4 * (i % 2)
                    nc.vector.tensor_tensor(
                        c.mod[:, i // 2, :, 4 * (i % 2):4 * (i % 2) + 4],
                        c.ps[:, i % 2, 0:8].rearrange("p (f s) -> p s f", s=2),
                        bcol[:, at:at + 4].unsqueeze(1).broadcast_to([P, 2, 4]), ALU.add).then_inc(cols_read, 1)
                else:
                    j = i - 8
                    dve.wait_ge(spread, j + 1)
                    at = (j % 2) * BANK
                    for s in range(STREAMS):
                        nc.vector.tensor_tensor(c.gate_rows[:, 2 * (j // 2) + s, at:at + BANK], c.ps[:, 4 + s],
                                                brow[:, j // 2, at:at + BANK], ALU.add).then_inc(gates, 1)

            for i in range(N):
                for q in range(4):
                    split_lo(nc, c, dve, m0 + i, q, 4 * i + q, w_hi, w_lo, w_parts)
                    if q == 3 and i >= 1:
                        take(i - 1)
                if i == 8:
                    dve.wait_ge(cols_read, 8)
                    for j, at in ((1, S_N1 + DK * layer), (3, S_N2 + DK * layer)):
                        for s in range(STREAMS):
                            nc.vector.scalar_tensor_tensor(out=c.mod[:, j, s, :], in0=c.mod[:, j, s, :], scalar=1.0,
                                                           in1=c.par[:, at:at + DK], op0=ALU.add, op1=ALU.mult).then_inc(scales, 1)
                    dve.wait_ge(bias_in, 16)
            take(N - 1)


def add_gated(nc, c, prod, tiles, gate):
    for i, t in enumerate(tiles):
        for n in range(2):
            b = 2 * i + n
            nc.vector.tensor_tensor(c.tok[:, i, n * BANK:(n + 1) * BANK], c.ps[:, b],
                                    c.gate_rows[:, 2 * gate + t // TT, n * BANK:(n + 1) * BANK], ALU.mult).then_inc(prod, 1)


def mlp_stage(nc, c, w, m0, tiles, parts):
    nt = len(tiles)
    T = nt * P
    PP = 8 // parts
    PK = MK // parts
    quarts = [(i, q) for i in range(2 * PP * parts) for q in range(4)]
    with stage(nc, "w_hi", "w_lo", "quart_done", "relu_done", "square", "hid_hi", "hid_lo", "product", "added") as (
            block, w_hi, w_lo, quart_done, relu_done, square, hid_hi, hid_lo, product, added):
        hi, lo = (t[:, 0:PK * T].rearrange("p (k t) -> p k t", k=PK) for t in (c.hid_hi, c.hid_lo))
        flat = c.tok[:, :, :].rearrange("p a n -> p (a n)")

        def place(i):
            part, j = divmod(i, 2 * PP)
            return part, j >= PP, j % PP, part * PP + min(j, PP)

        def buf(u):
            return flat[:, 2048 * (u % 2):2048 * (u % 2) + 4 * T].rearrange("p (f t) -> p f t", f=4)

        @block.sync
        def _(sp):
            for i in range(2 * PP * parts):
                sp.wait_ge(w_lo, 4 * i + 4)
                w.refill(sp, m0 + i)

        @block.tensor
        def _(pe):
            for Q, (i, q) in enumerate(quarts):
                part, second, j, ups = place(i)
                pe.wait_ge(w_lo, Q + 1)
                if not second:
                    if q == 0 and ups >= 2:
                        pe.wait_ge(square, ups - 1)
                    if q == 0 and j == 0 and part:
                        pe.wait_ge(product, 2 * nt * part)
                        pe.wait_ge(hid_lo, PP * part)
                    wt = [t[:, Q % 2].rearrange("p (k n) -> p k n", k=2) for t in (c.w_hi, c.w_lo)]
                    for f in range(4):
                        for kk in range(2):
                            k = 2 * q + kk
                            last = mm3(nc, c.ps[:, 4 * (j % 2) + f, 0:T], [t[:, kk, f * P:(f + 1) * P] for t in wt],
                                       [t[:, k, 0:T] for t in (c.hT_hi, c.hT_lo)], k == 0, k == DK - 1)
                else:
                    k = 4 * j + q
                    if q == 0:
                        pe.wait_ge(hid_lo, part * PP + j + 1)
                    if k == 0 and 2 * nt == 8:
                        pe.wait_ge(square, ups)
                    for t in range(nt):
                        for n in range(2):
                            last = mm3(nc, c.ps[:, 2 * t + n], [h[:, k, t * P:(t + 1) * P] for h in (hi, lo)],
                                       [u[:, Q % 2, n * BANK:(n + 1) * BANK] for u in (c.w_hi, c.w_lo)],
                                       k == 0, k == PK - 1)
                last.then_inc(quart_done, 1)

        def after(Q):
            i, q = quarts[Q]
            if q != 1 or i == 0:
                return None
            part, second, j, ups = place(i - 1)
            return None if second else (i - 1, ups)

        @block.scalar
        def _(act):
            for Q, (i, q) in enumerate(quarts):
                split_hi(nc, c, act, w, m0 + i, q, Q, quart_done, w_hi)
                done = after(Q)
                if done:
                    made, u = done
                    j = place(made)[2]
                    act.wait_ge(quart_done, 4 * i)
                    if u >= 2:
                        act.wait_ge(hid_lo, u - 1)
                    if j < 2 and u >= PP:
                        act.wait_ge(added, 2 * nt * (u // PP))
                    nc.scalar.activation(buf(u), c.ps[:, 4 * (j % 2):4 * (j % 2) + 4, 0:T], ACT.Relu).then_inc(relu_done, 1)
                    act.wait_ge(square, u + 1)
                    if j == 0 and u >= PP:
                        act.wait_ge(quart_done, 4 * 2 * PP * (u // PP))
                    nc.scalar.activation(hi[:, 4 * j:4 * j + 4, :], buf(u), ACT.Copy).then_inc(hid_hi, 1)

        @block.vector
        def _(dve):
            for Q, (i, q) in enumerate(quarts):
                split_lo(nc, c, dve, m0 + i, q, Q, w_hi, w_lo)
                done = after(Q)
                if done:
                    made, u = done
                    j = place(made)[2]
                    dve.wait_ge(relu_done, u + 1)
                    nc.vector.tensor_tensor(buf(u), c.ps[:, 4 * (j % 2):4 * (j % 2) + 4, 0:T], buf(u), ALU.mult).then_inc(square, 1)
                    dve.wait_ge(hid_hi, u + 1)
                    nc.vector.tensor_tensor(lo[:, 4 * j:4 * j + 4, :], buf(u), hi[:, 4 * j:4 * j + 4, :].bitcast(F32),
                                            ALU.subtract).then_inc(hid_lo, 1)
                if q == 1 and i and i % (2 * PP) == 0:
                    dve.wait_ge(quart_done, 4 * i)
                    add_gated(nc, c, product, tiles, 1)
            dve.wait_ge(quart_done, len(quarts))
            if parts > 1:
                dve.wait_ge(added, 2 * nt * (parts - 1))
            add_gated(nc, c, product, tiles, 1)

        @block.gpsimd
        def _(pool):
            for part in range(parts):
                for i, t in enumerate(tiles):
                    for n in range(2):
                        pool.wait_ge(product, 2 * nt * part + 2 * i + n + 1)
                        xs = c.x[:, t, n * BANK:(n + 1) * BANK]
                        nc.gpsimd.tensor_tensor(xs, xs, c.tok[:, i, n * BANK:(n + 1) * BANK], ALU.add).then_inc(added, 1)
            pool.wait_ge(added, 2 * nt * parts)


def even_mixer_stage(nc, c, w, m0):
    QP, KP, VP, WO = 2, 3, 4, 5
    names = ["sig_done", "glu_done", "padded", "conv_step", "conv_done", "w_hi", "w_lo", "quart_done", "parts_hi", "parts_lo",
             "q_roped", "k_roped", "rope_step", "q_ctx_read", "k_ctx_read", "v_read", "q_turned", "k_turned",
             "qT_read", "kT_read", "lam_in", "lam_step", "lam_ready", "lam_exp", "s_ready", "max_step", "negmax", "exp_done",
             "mix_step", "mixed", "p_turned", "p_cols", "pv", "o_done", "o_squares", "o_root", "o_step", "o_normed",
             "o_turned", "term", "term_added", "ln_mean", "centred", "ln_sq", "ln_var", "ln_eps", "ln_root", "ln_inv", "ln_norm",
             "conv_out", "product", "added"]
    UNITS = [(t, h) for t in range(ALL) for h in range(4)]
    with stage(nc, *names) as (block, *sems):
        s = dict(zip(names, sems))

        def area(at, n):
            return c.work[:, at:at + n]

        PW = SEQ + 2 * PAD
        glu = area(0, 4 * 2 * PW).rearrange("p (f s n) -> p f s n", f=4, s=2)
        at = 4 * 2 * PW
        conv = area(at, 2048).rearrange("p (f t) -> p f t", f=4)
        q = area(at + 2048, 2048).rearrange("p (t n) -> p t n", t=ALL)
        k = area(at + 4096, 2048).rearrange("p (t n) -> p t n", t=ALL)
        v = area(at + 6144, 2048).rearrange("p (t n) -> p t n", t=ALL)
        qT = area(at + 8192, 2048).rearrange("p (f t) -> p f t", f=4)
        kT = area(at + 10240, 2048).rearrange("p (f t) -> p f t", f=4)
        sq = area(at + 12288, 1024).rearrange("p (a n) -> p a n", a=2)
        small = area(at + 13312, 128)
        o = q
        w_hi, w_lo, quart_done = s["w_hi"], s["w_lo"], s["quart_done"]

        def panel_done(i):
            return quart_done, 4 * i + 4

        rest = at + 6144 - 8192
        parts = [(c.hid_hi[:, 0:2048], c.hid_lo[:, rest:rest + 2048]),
                 (c.hid_lo[:, rest + 2048:rest + 4096], c.hid_lo[:, rest + 4096:rest + 6144])]
        parts = [tuple(t.rearrange("p (f t) -> p f t", f=4) for t in pair) for pair in parts]
        sig = c.tok[:, 0:2, :].rearrange("p a (b n) -> p (a b) n", b=2)
        ropes = c.tok[:, 2:3, :].rearrange("p a n -> p (a n)")
        prob = c.tok[:, 0:2, :].rearrange("p a (b n) -> p a b n", b=2)
        probT = c.tok[:, 2, :].rearrange("p (a n) -> p a n", a=2)
        lqk = c.tok[:, 3, 0:256].rearrange("p (a b n) -> p a b n", a=2, b=2)
        junk = c.tok[:, 3, 256:512]
        lam = small[:, 0:4]
        mx, negm, sums, rs = (small[:, 8 + 4 * a:12 + 4 * a] for a in range(4))
        osq, ostd, oinv = (small[:, 32 + 16 * a:48 + 16 * a] for a in range(3))
        cos = c.const2[:, K2_COS:K2_SIN].rearrange("p (t n) -> p t n", t=TT)
        sin = c.const2[:, K2_SIN:K2_LOWER].rearrange("p (t n) -> p t n", t=TT)

        @block.sync
        def _(sp):
            sp.dma_start(c.tok[:, 3, 0:256], c.vrows[V_LQK:V_DN].partition_broadcast(P)).then_inc(s["lam_in"], 16)
            for i in range(WO + 2):
                sp.wait_ge(w_lo, 4 * i + 4)
                w.refill(sp, m0 + i)

        @block.gpsimd
        def _(pool):
            nc.gpsimd.memset(glu[:, :, :, 0:PAD], 0.0).then_inc(s["padded"], 1)
            nc.gpsimd.memset(glu[:, :, :, PAD + SEQ:PW], 0.0).then_inc(s["padded"], 1)
            for Q in range(4 * WO + 2):
                split_lo(nc, c, pool, m0 + Q // 4, Q % 4, Q, w_hi, w_lo, engine=nc.gpsimd)
            total = conv[:, 3, :]
            for tap in range(1, CONV_W):
                pool.wait_ge(s["term"], tap + 1)
                if tap >= 2:
                    pool.wait_ge(s["term_added"], tap - 1)
                nc.gpsimd.tensor_tensor(total, total, sq[:, tap % 2, :], ALU.add).then_inc(s["term_added"], 1)
            for Q in range(4 * WO + 2, 4 * (WO + 2)):
                split_lo(nc, c, pool, m0 + Q // 4, Q % 4, Q, w_hi, w_lo, engine=nc.gpsimd)
            for i in range(ALL):
                for n in range(2):
                    pool.wait_ge(s["product"], 2 * i + n + 1)
                    xs = c.x[:, i, n * BANK:(n + 1) * BANK]
                    nc.gpsimd.tensor_tensor(xs, xs, c.tok[:, i, n * BANK:(n + 1) * BANK], ALU.add).then_inc(s["added"], 1)
            pool.wait_ge(s["added"], 2 * ALL)

        @block.tensor
        def _(pe):
            def take(i, banks, token_rows):
                for qq in range(4):
                    Q = 4 * i + qq
                    pe.wait_ge(w_lo, Q + 1)
                    wt = [t[:, Q % 2].rearrange("p (k n) -> p k n", k=2) for t in (c.w_hi, c.w_lo)]
                    for j, bank in enumerate(banks):
                        cols = slice(j * P, (j + 1) * P)
                        for e in range(2):
                            kk = 2 * qq + e
                            h = [t[:, kk] for t in (c.hT_hi, c.hT_lo)]
                            u = [t[:, e] for t in wt]
                            if token_rows:
                                last = mm3(nc, c.ps[:, bank], [t[:, cols] for t in h], u, kk == 0, kk == DK - 1)
                            else:
                                last = mm3(nc, c.ps[:, bank], [t[:, cols] for t in u], h, kk == 0, kk == DK - 1)
                    last.then_inc(quart_done, 1)

            take(0, range(0, 4), False)
            take(1, range(4, 8), False)
            pe.wait_ge(s["glu_done"], 2)
            take(QP, (0, 1, 2, 3), True)
            pe.wait_ge(s["glu_done"], 4)
            pe.wait_ge(s["q_ctx_read"], 2)
            take(KP, (4, 5, 2, 3), True)
            pe.wait_ge(s["q_roped"], 2)
            pe.wait_ge(s["k_ctx_read"], 2)
            take(VP, (0, 1, 2, 3), True)

            def turn(src, f0, bank, sem):
                for f in (f0, f0 + 1):
                    for t in range(ALL):
                        last = nc.tensor.transpose(c.ps[:, bank + f - f0, t * P:(t + 1) * P],
                                                   src[:, t, f * P:(f + 1) * P], c.ident)
                last.then_inc(sem, 1)

            pe.wait_ge(s["k_roped"], 2)
            turn(q, 0, 4, s["q_turned"])
            pe.wait_ge(s["v_read"], 2)
            turn(q, 2, 0, s["q_turned"])
            pe.wait_ge(s["v_read"], 4)
            turn(k, 0, 2, s["k_turned"])
            pe.wait_ge(s["qT_read"], 1)
            turn(k, 2, 4, s["k_turned"])
            pe.wait_ge(s["qT_read"], 2)
            pe.wait_ge(s["kT_read"], 2)

            def scores(j):
                t, h = UNITS[j]
                k0 = 0 if t < TT else SEQ
                if j >= 2:
                    pe.wait_ge(s["exp_done"], 2 * j - 2)
                for e in range(2):
                    hp = slice(64 * e, 64 * e + 64)
                    last = mm(nc, c.ps[:, 2 * (j % 2) + e, 0:BOTH - k0], qT[hp, h, t * P:(t + 1) * P], kT[hp, h, k0:BOTH],
                              True, True)
                    last.then_inc(s["s_ready"], 1)

            def turn_probs(j):
                t, h = UNITS[j]
                nb = 4 if t < TT else 2
                pe.wait_ge(s["mixed"], j + 1)
                if j >= 1:
                    pe.wait_ge(s["p_cols"], j)
                for b in range(nb):
                    last = nc.tensor.transpose(c.ps[:, 4, b * P:(b + 1) * P], prob[:, j % 2, 0, b * P:(b + 1) * P], c.ident)
                last.then_inc(s["p_turned"], 1)

            def weigh(j):
                t, h = UNITS[j]
                tiles = range(4) if t < TT else range(2, 4)
                pe.wait_ge(s["p_cols"], j + 1)
                if h == 0 and t:
                    pe.wait_ge(s["o_done"], t)
                for b, kt in enumerate(tiles):
                    last = mm(nc, c.ps[:, 5, h * P:(h + 1) * P], probT[:, j % 2, b * P:(b + 1) * P],
                              v[:, kt, h * P:(h + 1) * P], b == 0, b == len(tiles) - 1)
                last.then_inc(s["pv"], 1)

            for j in range(len(UNITS) + 3):
                if j < len(UNITS):
                    scores(j)
                if 2 <= j < len(UNITS) + 2:
                    turn_probs(j - 2)
                if j >= 3:
                    weigh(j - 3)
            pe.wait_ge(s["conv_done"], 3)
            pe.wait_ge(s["term_added"], CONV_W - 1)
            for f in range(4):
                last = mm(nc, c.ps[:, 6], c.mean512, conv[:, f, :], f == 0, f == 3)
            last.then_inc(s["ln_mean"], 1)
            for f in range(4):
                pe.wait_ge(s["ln_sq"], f + 1)
                last = mm(nc, c.ps[:, 7], c.mean512, sq[:, f % 2, :], f == 0, f == 3)
                last.then_inc(s["ln_var"], 1)
            for t in range(ALL):
                pe.wait_ge(s["o_normed"], 4 * t + 4)
                for h in range(4):
                    last = nc.tensor.transpose(c.ps[:, h, t * P:(t + 1) * P], o[:, t, h * P:(h + 1) * P], c.ident)
            last.then_inc(s["o_turned"], 1)
            for half in range(2):
                pe.wait_ge(s["parts_lo"], 8)
                for kk in range(4):
                    Q = 4 * (WO + half) + kk
                    pe.wait_ge(w_lo, Q + 1)
                    for t in range(ALL):
                        for n in range(2):
                            last = mm3(nc, c.ps[:, 2 * t + n], [x[:, kk, t * P:(t + 1) * P] for x in parts[half]],
                                       [u[:, Q % 2, n * BANK:(n + 1) * BANK] for u in (c.w_hi, c.w_lo)],
                                       half + kk == 0, half == 1 and kk == 3)
                    last.then_inc(quart_done, 1)

        @block.scalar
        def _(act):
            def split(*quarters):
                for Q in quarters:
                    split_hi(nc, c, act, w, m0 + Q // 4, Q % 4, Q, quart_done, w_hi)

            split(*range(6))
            for i in range(2):
                act.wait_ge(*panel_done(i))
                for f in range(2):
                    if i:
                        act.wait_ge(s["glu_done"], f + 1)
                    nc.scalar.activation(sig[:, f, :], c.ps[:, 4 * i + 2 + f], ACT.Sigmoid).then_inc(s["sig_done"], 1)
                split(*range(4 * i + 6, 4 * i + 10))
            act.wait_ge(*panel_done(QP))
            for t in range(TT, ALL):
                nc.scalar.activation(q[:, t], c.ps[:, t], ACT.Copy).then_inc(s["q_ctx_read"], 1)
            split(*range(14, 18))
            act.wait_ge(*panel_done(KP))
            for t in range(TT, ALL):
                nc.scalar.activation(k[:, t], c.ps[:, t], ACT.Copy).then_inc(s["k_ctx_read"], 1)
            split(*range(18, 22))
            act.wait_ge(*panel_done(VP))
            for t in range(ALL):
                nc.scalar.activation(v[:, t], c.ps[:, t], ACT.Copy).then_inc(s["v_read"], 1)
            for src, dst, n, f0, bank, sem in ((s["q_turned"], qT, 1, 0, 4, s["qT_read"]), (s["q_turned"], qT, 2, 2, 0, s["qT_read"]),
                                               (s["k_turned"], kT, 1, 0, 2, s["kT_read"]), (s["k_turned"], kT, 2, 2, 4, s["kT_read"])):
                act.wait_ge(src, n)
                nc.scalar.activation(dst[:, f0:f0 + 2, :], c.ps[:, bank:bank + 2, :], ACT.Copy).then_inc(sem, 1)
            act.wait_ge(s["lam_ready"], 1)
            nc.scalar.activation(lam[:, 2:4], lam[:, 0:2], ACT.Exp).then_inc(s["lam_exp"], 1)

            def exps(j):
                t, h = UNITS[j]
                n = BOTH if t < TT else SEQ
                act.wait_ge(s["negmax"], j + 1)
                if j >= 2:
                    act.wait_ge(s["p_turned"], j - 1)
                for e in range(2):
                    col = 2 * (j % 2) + e
                    nc.scalar.activation(prob[:, j % 2, e, 0:n], c.ps[:, 2 * (j % 2) + e, 0:n], ACT.Exp, scale=ATT_SCALE,
                                         bias=negm[:, col:col + 1], accum_out=sums[:, col:col + 1]).then_inc(s["exp_done"], 1)

            def prob_columns(j):
                t, h = UNITS[j]
                n = BOTH if t < TT else SEQ
                act.wait_ge(s["p_turned"], j + 1)
                if j >= 2:
                    act.wait_ge(s["pv"], j - 1)
                nc.scalar.activation(probT[:, j % 2, 0:n], c.ps[:, 4, 0:n], ACT.Copy).then_inc(s["p_cols"], 1)

            def conv_term(tap):
                if tap >= 3:
                    act.wait_ge(s["term_added"], tap - 2)
                dst = sq[:, tap % 2, :] if tap else conv[:, 3, :]
                nc.scalar.activation(dst.rearrange("p (s t) -> p s t", s=2), glu[:, 3, :, tap:tap + SEQ], ACT.Identity,
                                     scale=c.par[:, S_CONVW + 3 * CONV_W + tap:S_CONVW + 3 * CONV_W + tap + 1],
                                     bias=0.0 if tap else c.par[:, S_CONVB + 3:S_CONVB + 4]).then_inc(s["term"], 1)

            for j in range(len(UNITS) + 2):
                for tap in range(2 * j, min(2 * j + 2, CONV_W)):
                    conv_term(tap)
                if j >= 2:
                    prob_columns(j - 2)
                if j < len(UNITS):
                    exps(j)
            for f in range(4):
                act.wait_ge(s["centred"], f + 1)
                if f >= 2:
                    act.wait_ge(s["ln_var"], f - 1)
                nc.scalar.activation(sq[:, f % 2, :], conv[:, f, :], ACT.Square).then_inc(s["ln_sq"], 1)
            act.wait_ge(s["o_squares"], 16)
            nc.scalar.activation(ostd, osq, ACT.Sqrt).then_inc(s["o_root"], 1)
            act.wait_ge(s["ln_eps"], 1)
            nc.scalar.activation(sq[:, 0, :], sq[:, 0, :], ACT.Sqrt).then_inc(s["ln_root"], 1)
            for f in range(4):
                act.wait_ge(s["ln_norm"], f + 1)
                nc.scalar.activation(conv[:, f, :], conv[:, f, :], ACT.Silu, scale=c.par[:, S_LNG + f:S_LNG + f + 1],
                                     bias=c.par[:, S_LNB + f:S_LNB + f + 1]).then_inc(s["conv_out"], 1)
            for f in range(4):
                act.wait_ge(s["conv_out"], f + 1)
                nc.scalar.activation(parts[0][0][:, f, :], conv[:, f, :], ACT.Copy).then_inc(s["parts_hi"], 1)
            act.wait_ge(s["o_turned"], 1)
            for f in range(4):
                nc.scalar.activation(parts[1][0][:, f, :], c.ps[:, f], ACT.Copy, scale=c.subln[:, 0:1]).then_inc(s["parts_hi"], 1)
            split(*range(22, 4 * (WO + 2)))

        @block.vector
        def _(dve):
            count = {}

            def then(name, ins):
                ins.then_inc(s[name], 1)
                count[name] = count.get(name, 0) + 1
                dve.wait_ge(s[name], count[name])

            dve.wait_ge(s["lam_in"], 16)
            for a in range(2):
                then("lam_step", nc.vector.tensor_tensor_reduce(
                    out=junk[:, 0:64], in0=lqk[:, a, 0], in1=lqk[:, a, 1], scale=1.0, scalar=0.0, op0=ALU.mult,
                    op1=ALU.add, accum_out=lam[:, a:a + 1]))
            dve.sem_inc(s["lam_ready"], 1)
            then("lam_step", nc.vector.tensor_scalar(c.subln[:, 0:1], c.par[:, S_SUBLN:S_SUBLN + 1], 1.0 - LAMBDA0, None,
                                                     ALU.mult))
            dve.wait_ge(s["padded"], 2)
            for i in range(2):
                dve.wait_ge(*panel_done(i))
                for f in range(2):
                    dve.wait_ge(s["sig_done"], 2 * i + f + 1)
                    nc.vector.tensor_tensor(glu[:, 2 * i + f, :, PAD:PAD + SEQ],
                                            c.ps[:, 4 * i + f].rearrange("p (s t) -> p s t", s=2),
                                            sig[:, f, :].rearrange("p (s t) -> p s t", s=2), ALU.mult).then_inc(s["glu_done"], 1)

            def convolve(f, taps=range(CONV_W)):
                dve.wait_ge(s["glu_done"], 4)
                for tap in taps:
                    src = glu[:, f, :, tap:tap + SEQ]
                    dst = c.ps[:, 6 + tap % 2].rearrange("p (s t) -> p s t", s=2)
                    prev = c.ps[:, 7 - tap % 2].rearrange("p (s t) -> p s t", s=2)
                    wc = c.par[:, S_CONVW + f * CONV_W + tap:S_CONVW + f * CONV_W + tap + 1]
                    if tap == 0:
                        then("conv_step", nc.vector.tensor_scalar(dst, src, wc, c.par[:, S_CONVB + f:S_CONVB + f + 1],
                                                                  ALU.mult, ALU.add))
                    elif tap < CONV_W - 1:
                        then("conv_step", nc.vector.scalar_tensor_tensor(out=dst, in0=src, scalar=wc, in1=prev,
                                                                         op0=ALU.mult, op1=ALU.add))
                    else:
                        nc.vector.scalar_tensor_tensor(out=conv[:, f, :].rearrange("p (s t) -> p s t", s=2), in0=src,
                                                       scalar=wc, in1=prev, op0=ALU.mult, op1=ALU.add).then_inc(s["conv_done"], 1)

            def rope(panel, bank, dst, roped):
                a = ropes[:, 0:512]
                b = ropes[:, 512:1024]
                dve.wait_ge(*panel_done(panel))
                for t in range(TT):
                    sv = c.ps[:, bank + t]
                    ct = cos[:, t].unsqueeze(1).broadcast_to([P, 8, 64])
                    nc.vector.tensor_tensor(a.rearrange("p (h n) -> p h n", h=8), sv.rearrange("p (h n) -> p h n", h=8), ct,
                                            ALU.mult).then_inc(s["rope_step"], 1)
                    count["rope_step"] = count.get("rope_step", 0) + 1
                    for e in range(2):
                        bv = b.rearrange("p (h x y n) -> p h x y n", h=8, x=2, y=2)[:, :, :, e]
                        xv = sv.rearrange("p (h x y n) -> p h x y n", h=8, x=2, y=2)[:, :, :, 1 - e]
                        st = sin[:, t].rearrange("p (x y n) -> p x y n", x=2, y=2)[:, :, e].unsqueeze(1).broadcast_to([P, 8, 2, 16])
                        nc.vector.tensor_tensor(bv, xv, st, ALU.mult).then_inc(s["rope_step"], 1)
                        count["rope_step"] += 1
                    dve.wait_ge(s["rope_step"], count["rope_step"])
                    then("rope_step", nc.vector.tensor_tensor(dst[:, t], a, b, ALU.add))
                    dve.sem_inc(roped, 1)

            convolve(0)
            rope(QP, 0, q, s["q_roped"])
            convolve(1)
            rope(KP, 4, k, s["k_roped"])
            convolve(2, range(8))
            dve.wait_ge(s["lam_exp"], 1)
            then("lam_step", nc.vector.tensor_tensor(lam[:, 0:1], lam[:, 2:3], lam[:, 3:4], ALU.subtract))
            then("lam_step", nc.vector.tensor_scalar(lam[:, 1:2], lam[:, 0:1], LAMBDA0, None, ALU.add))

            def maxima(j):
                t, h = UNITS[j]
                n = BOTH if t < TT else SEQ
                for e in range(2):
                    col = 2 * (j % 2) + e
                    dve.wait_ge(s["s_ready"], 2 * j + e + 1)
                    nc.vector.tensor_reduce(mx[:, col:col + 1], c.ps[:, 2 * (j % 2) + e, 0:n], axis=AX,
                                            op=ALU.max).then_inc(s["max_step"], 1)
                dve.wait_ge(s["max_step"], 2 * j + 2)
                cs = slice(2 * (j % 2), 2 * (j % 2) + 2)
                nc.vector.tensor_scalar(negm[:, cs], mx[:, cs], -ATT_SCALE, None, ALU.mult).then_inc(s["negmax"], 1)

            def mix(j):
                t, h = UNITS[j]
                n = BOTH if t < TT else SEQ
                dve.wait_ge(s["exp_done"], 2 * j + 2)
                c0 = 2 * (j % 2)
                then("mix_step", nc.vector.reciprocal(rs[:, c0:c0 + 2], sums[:, c0:c0 + 2]))
                e0, e1 = prob[:, j % 2, 0, 0:n], prob[:, j % 2, 1, 0:n]
                then("mix_step", nc.vector.tensor_scalar(e1, e1, rs[:, c0 + 1:c0 + 2], lam[:, 1:2], ALU.mult, ALU.mult))
                nc.vector.scalar_tensor_tensor(out=e0, in0=e0, scalar=rs[:, c0:c0 + 1], in1=e1, op0=ALU.mult,
                                               op1=ALU.subtract).then_inc(s["mixed"], 1)

            def take_o(t):
                dve.wait_ge(s["pv"], 4 * t + 4)
                then("o_done", nc.vector.tensor_copy(o[:, t], c.ps[:, 5]))
                for h in range(4):
                    oh = o[:, t, h * P:(h + 1) * P]
                    i = 4 * t + h
                    then("o_step", nc.vector.tensor_tensor_reduce(out=junk[:, 0:P], in0=oh, in1=oh, scale=1.0 / P, scalar=EPS,
                                                                  op0=ALU.mult, op1=ALU.add, accum_out=osq[:, i:i + 1]))
                    dve.sem_inc(s["o_squares"], 1)

            for j in range(len(UNITS) + 1):
                if j >= 7 and (j - 7) % 4 == 0:
                    take_o((j - 7) // 4)
                if j < len(UNITS):
                    maxima(j)
                for tap in range(8 + 2 * j, min(10 + 2 * j, CONV_W)):
                    convolve(2, [tap])
                if j >= 1:
                    mix(j - 1)
            dve.wait_ge(s["ln_mean"], 1)
            for f in range(4):
                nc.vector.tensor_tensor(conv[:, f, :], conv[:, f, :], c.ps[:, 6], ALU.subtract).then_inc(s["centred"], 1)
            take_o(3)
            dve.wait_ge(s["ln_var"], 4)
            nc.vector.tensor_scalar(sq[:, 0, :], c.ps[:, 7], EPS, None, ALU.add).then_inc(s["ln_eps"], 1)
            dve.wait_ge(s["o_root"], 1)
            then("o_step", nc.vector.reciprocal(oinv, ostd))
            for i in range(16):
                oh = o[:, i // 4, (i % 4) * P:(i % 4 + 1) * P]
                nc.vector.tensor_scalar(oh, oh, oinv[:, i:i + 1], None, ALU.mult).then_inc(s["o_normed"], 1)
            dve.wait_ge(s["ln_root"], 1)
            nc.vector.reciprocal(c.ps[:, 6], sq[:, 0, :]).then_inc(s["ln_inv"], 1)
            dve.wait_ge(s["ln_inv"], 1)
            for f in range(4):
                nc.vector.tensor_tensor(conv[:, f, :], conv[:, f, :], c.ps[:, 6], ALU.mult).then_inc(s["ln_norm"], 1)
            for f in range(4):
                dve.wait_ge(s["parts_hi"], f + 1)
                nc.vector.tensor_tensor(parts[0][1][:, f, :], conv[:, f, :], parts[0][0][:, f, :].bitcast(F32),
                                        ALU.subtract).then_inc(s["parts_lo"], 1)
            for f in range(4):
                dve.wait_ge(s["parts_hi"], f + 5)
                nc.vector.scalar_tensor_tensor(out=parts[1][1][:, f, :], in0=c.ps[:, f], scalar=c.subln[:, 0:1],
                                               in1=parts[1][0][:, f, :].bitcast(F32), op0=ALU.mult,
                                               op1=ALU.subtract).then_inc(s["parts_lo"], 1)
            dve.wait_ge(*panel_done(WO + 1))
            add_gated(nc, c, s["product"], range(ALL), 0)
TAPS_HY, TAPS_DN = 3, 5
DNH = 4
O_HY, O_Q, O_K, O_V, O_GATE, O_TEMP = 0, 3072, 4096, 6144, 8192, 9216
TURN = (6.28125, 0.0019350051879882812, 3.019915979507459e-07)
LEVELS = 7

T_FH = 0
T_FU = T_FH + 4 * 640
T_INV = T_FU + 2 * 512
T_WIN = T_INV + 4 * SEQ
T_Z = T_WIN + 2 * 512
T_END = T_Z + SEQ
M_LEVEL = 0
M_BIAS = M_LEVEL + 2 * LEVELS * P
M_END = M_BIAS + 2 * P


def odd_project_stage(nc, c, w, m0):
    names = ["rest_ready", "rest_read", "padded", "copied", "conv_step", "conv_done", "gate_done", "conv_silu",
             "w_hi", "w_lo", "quart_done", "w3_in", "tables_in", "layer_ready", "range_step", "arg", "sine"]
    with stage(nc, *names) as (block, rest_ready, rest_read, padded, copied, conv_step, conv_done, gate_done,
                               conv_silu, w_hi, w_lo, quart_done, w3_in, tables_in, layer_ready, range_step, arg, sine):
        bufs = [tuple(t[:, b].rearrange("p (k n) -> p k n", k=2) for t in (c.w_hi, c.w_lo)) for b in range(2)]
        tokf = c.tok[:, :, :].rearrange("p a n -> p (a n)")
        h32 = tokf.rearrange("p (k t) -> p k t", k=DK)
        zT = tokf[0:33, 2048:2304]
        hid = tokf[0:64, 2304:2560]
        turns, whole = tokf[0:64, 2560:2816], c.spare[0:64, 0:256]
        w1 = c.par[0:33, S_W1:S_W1 + 64]
        w2 = c.par[0:64, S_W2:S_W2 + 64]
        fb = c.par[0:64, S_FB:S_FB + 4]
        hy = c.work[:, O_HY:O_HY + 3072].rearrange("p (f t) -> p f t", f=12)
        gs = c.work[:, O_GATE:O_GATE + 1024].rearrange("p (t n) -> p t n", t=TT)
        rest_w = c.par[:, S_REST:S_END].rearrange("p (k n) -> p k n", k=DK)
        convs = [(i, 1, TAPS_HY, S_HYSW + 12 * i, S_HYSB + 4 * i, O_HY + 1024 * i) for i in range(3)]
        convs += [(3, 1, TAPS_DN, S_DNW, None, O_Q), (4, 2, TAPS_DN, S_DNW + 20, None, O_K),
                  (5, 2, TAPS_DN, S_DNW + 40, None, O_V)]

        def padded_buffer(i):
            _, ns, taps, _, _, _ = convs[i]
            n = 4 * ns * (SEQ + taps - 1)
            at = O_TEMP + 2080 * (i % 2)
            return c.work[:, at:at + n].rearrange("p (f s t) -> p f s t", f=4, s=ns)

        @block.sync
        def _(sp):
            sp.wait_ge(rest_ready, 1)
            sp.dma_start(tokf[:, 0:2304], c.transforms[:, T_INV:T_END]).then_inc(tables_in, 16)
            sp.dma_start(tokf[0:64, 2816:3840], c.w3[:, 0:1024]).then_inc(w3_in, 16)
            for i in range(7):
                sp.wait_ge(w_lo, 4 * i + 4)
                w.refill(sp, m0 + i)
            sp.wait_ge(w3_in, 16)

        @block.tensor
        def _(pe):
            for t in range(ALL):
                for k in range(DK):
                    last = mm(nc, c.ps[:, 4, t * 16:t * 16 + 16], h32[:, k, t * P:(t + 1) * P], rest_w[:, k, :],
                              k == 0, k == DK - 1)
            last.then_inc(rest_ready, 1)
            for i in range(7):
                n = convs[i][1] * SEQ if i < 6 else None
                for qq in range(4):
                    Q = 4 * i + qq
                    pe.wait_ge(w_lo, Q + 1)
                    u = bufs[Q % 2]
                    for f in range(4 if n else TT):
                        if qq == 0 and i:
                            pe.wait_ge(copied, 4 * (i - 1) + f + 1 if n else 24)
                        fs = slice(f * P, (f + 1) * P)
                        for e in range(2):
                            k = 2 * qq + e
                            h = [t[:, k] for t in (c.hT_hi, c.hT_lo)]
                            if n:
                                last = mm3(nc, c.ps[:, f, 0:n], [x[:, e, fs] for x in u], [x[:, 0:n] for x in h], k == 0, k == DK - 1)
                            else:
                                last = mm3(nc, c.ps[:, f], [x[:, fs] for x in h], [x[:, e] for x in u], k == 0, k == DK - 1)
                    last.then_inc(quart_done, 1)
                if i == 0:
                    pe.wait_ge(tables_in, 16)
                    mm(nc, c.ps[0:64, 5, 0:SEQ], w1, zT, True, True).then_inc(layer_ready, 1)
                if i == 2:
                    pe.wait_ge(sine, 1)
                    mm(nc, c.ps[0:64, 5, 0:SEQ], w2, hid, True, True).then_inc(layer_ready, 1)

        @block.gpsimd
        def _(pool):
            for i in range(7):
                for qq in range(4):
                    split_lo(nc, c, pool, m0 + i, qq, 4 * i + qq, w_hi, w_lo, engine=nc.gpsimd)
                if i == 6:
                    continue
                _, ns, taps, _, _, _ = convs[i]
                if i >= 2:
                    pool.wait_ge(conv_done, 4 * (i - 1))
                side = (taps - 1) // 2
                buf = padded_buffer(i)
                nc.gpsimd.memset(buf[:, :, :, 0:side], 0.0).then_inc(padded, 1)
                nc.gpsimd.memset(buf[:, :, :, side + SEQ:], 0.0).then_inc(padded, 1)

        @block.scalar
        def _(act):
            def split(*quarters):
                for Q in quarters:
                    split_hi(nc, c, act, w, m0 + Q // 4, Q % 4, Q, quart_done, w_hi)

            split(0, 1)
            act.wait_ge(rest_ready, 1)
            nc.scalar.activation(c.rest, c.ps[:, 4, 0:64], ACT.Copy).then_inc(rest_read, 1)
            for i, ns, taps, _, _, _ in convs:
                side = (taps - 1) // 2
                split(*range(4 * i + 2, 4 * i + 6))
                if i in (1, 3):
                    act.wait_ge(arg, i // 2 + 1)
                    nc.scalar.activation(c.hidden_z if i == 3 else hid, turns, ACT.Sin).then_inc(sine, 1)
                act.wait_ge(quart_done, 4 * i + 4)
                if i >= 2:
                    act.wait_ge(conv_done, 4 * (i - 1))
                act.wait_ge(padded, 2 * i + 2)
                for f in range(4):
                    nc.scalar.activation(padded_buffer(i)[:, f, :, side:side + SEQ],
                                               c.ps[:, f, 0:ns * SEQ].rearrange("p (s t) -> p s t", s=ns), ACT.Copy).then_inc(copied, 1)
            split(26, 27)
            act.wait_ge(quart_done, 28)
            for t in range(TT):
                nc.scalar.activation(gs[:, t], c.ps[:, t], ACT.Silu).then_inc(gate_done, 1)
            act.wait_ge(conv_done, 24)
            for at, n in ((O_Q, 1024), (O_K, 2048), (O_V, 2048)):
                nc.scalar.activation(c.work[:, at:at + n], c.work[:, at:at + n], ACT.Silu).then_inc(conv_silu, 1)

        @block.vector
        def _(dve):
            step = 0
            turn_steps = [0]

            def range_then(ins):
                ins.then_inc(range_step, 1)
                turn_steps[0] += 1
                dve.wait_ge(range_step, turn_steps[0])

            def reduce(i):
                MAGIC = 12582912.0
                dve.wait_ge(layer_ready, i + 1)
                range_then(nc.vector.tensor_scalar(turns, c.ps[0:64, 5, 0:SEQ], fb[:, 2 * i:2 * i + 1],
                                                   fb[:, 2 * i + 1:2 * i + 2], ALU.add, ALU.mult))
                range_then(nc.vector.tensor_scalar(whole, turns, 1.0 / (2 * math.pi), MAGIC, ALU.mult, ALU.add))
                range_then(nc.vector.tensor_scalar(whole, whole, MAGIC, None, ALU.subtract))
                for part in TURN:
                    range_then(nc.vector.scalar_tensor_tensor(out=turns, in0=whole, scalar=-part, in1=turns,
                                                              op0=ALU.mult, op1=ALU.add))
                range_then(nc.vector.tensor_scalar(turns, turns, 3.1415925, -3.1415925, ALU.min, ALU.max))
                dve.sem_inc(arg, 1)

            for i, ns, taps, wcol, bcol, at in convs:
                if i == 1 or i == 3:
                    reduce(i // 2)
                buf = padded_buffer(i)
                for f in range(4):
                    dve.wait_ge(copied, 4 * i + f + 1)
                    for tap in range(taps):
                        src = buf[:, f, :, tap:tap + SEQ]
                        wc = c.par[:, wcol + f * taps + tap:wcol + f * taps + tap + 1]
                        dst = c.ps[:, 6 + tap % 2, 0:ns * SEQ].rearrange("p (s t) -> p s t", s=ns)
                        prev = c.ps[:, 7 - tap % 2, 0:ns * SEQ].rearrange("p (s t) -> p s t", s=ns)
                        if tap == 0:
                            nc.vector.tensor_scalar(dst, src, wc, c.par[:, bcol + f:bcol + f + 1] if bcol else None, ALU.mult,
                                                    ALU.add if bcol else ALU.bypass).then_inc(conv_step, 1)
                        elif tap < taps - 1:
                            nc.vector.scalar_tensor_tensor(out=dst, in0=src, scalar=wc, in1=prev, op0=ALU.mult,
                                                           op1=ALU.add).then_inc(conv_step, 1)
                        else:
                            out = c.work[:, at + f * ns * SEQ:at + (f + 1) * ns * SEQ].rearrange("p (s t) -> p s t", s=ns)
                            nc.vector.scalar_tensor_tensor(out=out, in0=src, scalar=wc, in1=prev, op0=ALU.mult,
                                                           op1=ALU.add).then_inc(conv_done, 1)
                            dve.wait_ge(conv_done, 4 * i + f + 1)
                            continue
                        step += 1
                        dve.wait_ge(conv_step, step)


def hyena_stage(nc, c, order):
    names = ["tables_in", "w3_in", "filt_ready", "windowed", "absolute",
             "norm_ready", "norm_inv", "filt_done", "spec_ready", "spec_read", "z_turned", "z_read", "sig_ready", "sig_read",
             "prod_step", "prod_done", "y_ready", "gated"]
    with stage(nc, *names) as (block, *sems):
        s = dict(zip(names, sems))
        hy = c.work[:, O_HY:O_HY + 3072].rearrange("p (f t) -> p f t", f=12)
        filt = c.work[:, O_TEMP:O_TEMP + 2048].rearrange("p (d t n) -> p d t n", d=2, t=TT)
        spec = c.work[:, O_TEMP + 2048:O_TEMP + 4608].rearrange("p (f n) -> p f n", f=5)
        sig = c.work[:, O_TEMP + 4608:O_TEMP + 6656].rearrange("p (f n) -> p f n", f=4)
        fh = c.hTf[:, 0:2560].rearrange("p (d t n) -> p d t n", d=2, t=TT)
        fu = c.hTf[:, 2560:3584].rearrange("p (t n) -> p t n", t=TT)
        tokf = c.tok[:, :, :].rearrange("p a n -> p (a n)")
        inv = tokf[:, 0:1024].rearrange("p (f t) -> p f t", f=4)
        win = tokf[:, 1024:2048].rearrange("p (t n) -> p t n", t=TT)
        w3 = tokf[0:64, 2816:3840].rearrange("p (d n) -> p d n", d=2)
        mag = c.spare[:, 0:1024].rearrange("p (a n) -> p a n", a=2)
        z = c.spare[:, 0:1024].rearrange("p (t n) -> p t n", t=TT)
        ma, mb = (c.work[:, O_TEMP + a:O_TEMP + a + 1024].rearrange("p (f n) -> p f n", f=2) for a in (0, 1024))

        @block.sync
        def _(sp):
            if order == 0:
                sp.dma_start(c.hTf[:, 0:3584], c.transforms[:, T_FH:T_INV]).then_inc(s["tables_in"], 16)
            else:
                sp.dma_start(w3.rearrange("p d n -> p (d n)"), c.w3[:, order * 1024:(order + 1) * 1024]).then_inc(s["w3_in"], 16)

        @block.tensor
        def _(pe):
            for t in range(TT):
                for f in range(4):
                    last = nc.tensor.transpose(c.ps[:, 6 + t, f * P:(f + 1) * P], hy[:, f, t * P:(t + 1) * P], c.ident)
            last.then_inc(s["z_turned"], 1)
            if order:
                pe.wait_ge(s["w3_in"], 16)
            for d in range(2):
                for t in range(TT):
                    mm(nc, c.ps[:, 2 * d + t], c.hidden_z[:, t * P:(t + 1) * P], w3[:, d, :], True, True).then_inc(s["filt_ready"], 1)
            for i in range(4):
                pe.wait_ge(s["absolute"], i + 1)
                last = mm(nc, c.ps[:, 4], c.ones, mag[:, i % 2, :], i == 0, i == 3)
                last.then_inc(s["norm_ready"], 1)
            pe.wait_ge(s["filt_done"], 4)
            if order == 0:
                pe.wait_ge(s["tables_in"], 16)
            for f in range(5):
                if f >= 4:
                    pe.wait_ge(s["spec_read"], f - 3)
                for i in range(4):
                    last = mm(nc, c.ps[:, f % 4], fh[:, i // 2, i % 2, f * P:(f + 1) * P], filt[:, i // 2, i % 2, :],
                              i == 0, i == 3)
                last.then_inc(s["spec_ready"], 1)
            pe.wait_ge(s["z_read"], 2)
            for f in range(4):
                bank = 5 + f if f < 3 else 4
                if f == 3:
                    pe.wait_ge(s["filt_done"], 4)
                for t in range(TT):
                    last = mm(nc, c.ps[:, bank], fu[:, t, f * P:(f + 1) * P], z[:, t, :], t == 0, t == TT - 1)
                last.then_inc(s["sig_ready"], 1)
            pe.wait_ge(s["prod_done"], 4)
            for f in range(4):
                for k in range(4):
                    last = mm(nc, c.ps[:, f, 0:SEQ], sig[:, k, f * P:(f + 1) * P], inv[:, k, :], k == 0, k == 3)
                last.then_inc(s["y_ready"], 1)

        @block.scalar
        def _(act):
            for i in range(4):
                act.wait_ge(s["windowed"], i + 1)
                if i >= 2:
                    act.wait_ge(s["norm_ready"], i - 1)
                nc.scalar.activation(mag[:, i % 2, :], filt[:, i // 2, i % 2, :], ACT.Abs).then_inc(s["absolute"], 1)
            act.wait_ge(s["norm_ready"], 4)
            act.wait_ge(s["z_turned"], 1)
            for t in range(TT):
                nc.scalar.activation(z[:, t, :], c.ps[:, 6 + t], ACT.Copy).then_inc(s["z_read"], 1)
            for f in range(5):
                act.wait_ge(s["spec_ready"], f + 1)
                nc.scalar.activation(spec[:, f, :], c.ps[:, f % 4], ACT.Copy).then_inc(s["spec_read"], 1)

        @block.vector
        def _(dve):
            count = {}

            def then(name, ins):
                ins.then_inc(s[name], 1)
                count[name] = count.get(name, 0) + 1
                dve.wait_ge(s[name], count[name])

            for i in range(4):
                dve.wait_ge(s["filt_ready"], i + 1)
                nc.vector.tensor_tensor(filt[:, i // 2, i % 2, :], c.ps[:, i], win[:, i % 2, :], ALU.mult).then_inc(s["windowed"], 1)
            dve.wait_ge(s["norm_ready"], 4)
            then("norm_inv", nc.vector.reciprocal(c.ps[:, 5], c.ps[:, 4]))
            for i in range(4):
                fl = filt[:, i // 2, i % 2, :]
                nc.vector.tensor_tensor(fl, fl, c.ps[:, 5], ALU.mult).then_inc(s["filt_done"], 1)
            dve.wait_ge(s["spec_read"], 5)
            for f in range(4):
                bank = 5 + f if f < 3 else 4
                dve.wait_ge(s["sig_ready"], f + 1)
                then("sig_read", nc.vector.tensor_copy(sig[:, f, :], c.ps[:, bank]))
            for f in range(2):
                ur, ui, hr, hi = sig[:, f, :], sig[:, 2 + f, :], spec[:, f, :], spec[:, 2 + f, :]
                hr2 = spec[:, 4, :] if f == 0 else hr
                then("prod_step", nc.vector.tensor_tensor(ma[:, 0, :], ui, hi, ALU.mult))
                then("prod_step", nc.vector.tensor_tensor(ma[:, 1, :], ur, hi, ALU.mult))
                then("prod_step", nc.vector.tensor_tensor(mb[:, 0, :], ur, hr, ALU.mult))
                then("prod_step", nc.vector.tensor_tensor(mb[:, 1, :], ui, hr2, ALU.mult))
                then("prod_done", nc.vector.tensor_tensor(ur, mb[:, 0, :], ma[:, 0, :], ALU.subtract))
                then("prod_done", nc.vector.tensor_tensor(ui, mb[:, 1, :], ma[:, 1, :], ALU.add))
            for f in range(4):
                dve.wait_ge(s["y_ready"], f + 1)
                zf = hy[:, f, :]
                skip = c.par[:, S_HYSKIP + 4 * order + f:S_HYSKIP + 4 * order + f + 1]
                then("gated", nc.vector.scalar_tensor_tensor(out=zf, in0=zf, scalar=skip, in1=c.ps[:, f, 0:SEQ],
                                                             op0=ALU.mult, op1=ALU.add))
                then("gated", nc.vector.tensor_tensor(zf, zf, hy[:, 4 * (order + 1) + f, :], ALU.mult))


def delta_features_stage(nc, c):
    names = ["square", "sum_ready", "eps_done", "root", "inv", "unit", "k_turned", "k_tok", "v_turned", "v_tok", "beta",
             "dn_in", "masks_in", "exp_a", "gate_step", "exp_x", "g_ready", "cum_ready", "cum_read", "last_ready",
             "last_read", "exps_in", "exps_done", "turned", "rows_read"]
    with stage(nc, *names) as (block, *sems):
        s = dict(zip(names, sems))
        q, k, v = c.work[:, O_Q:O_Q + 1024], c.work[:, O_K:O_K + 2048], c.work[:, O_V:O_V + 2048]
        parts = [(q, 0), (q, 1), (k, 0), (k, 1), (k, 2), (k, 3)]
        sq = c.tok[:, 0:3, :].rearrange("p a (b n) -> p (a b) n", b=2)
        g = c.gate_small
        dn = c.spare[:, 0:16]

        def seg(i):
            t, n = parts[i]
            return t[:, n * BANK:(n + 1) * BANK]

        @block.sync
        def _(sp):
            sp.dma_start(dn, c.vrows[V_DN:V_END].partition_broadcast(P)).then_inc(s["dn_in"], 16)
            sp.dma_start(c.hTf[:, 0:M_END], c.masks).then_inc(s["masks_in"], 16)
            sp.wait_ge(s["masks_in"], 16)

        @block.tensor
        def _(pe):
            for i in range(6):
                pe.wait_ge(s["square"], i + 1)
                mm(nc, c.ps[:, i], c.ones, sq[:, i, :], True, True).then_inc(s["sum_ready"], 1)
            vv = v.rearrange("p (h t) -> p h t", h=DNH)
            kk = k.rearrange("p (h t) -> p h t", h=DNH)
            for t in range(ALL):
                bank = 6 + t % 2
                if t >= 2:
                    pe.wait_ge(s["v_tok"], t - 1)
                for h in range(DNH):
                    last = nc.tensor.transpose(c.ps[:, bank, h * P:(h + 1) * P], vv[:, h, t * P:(t + 1) * P], c.ident)
                last.then_inc(s["v_turned"], 1)
            pe.wait_ge(s["g_ready"], 1)
            pe.wait_ge(s["v_tok"], 4)
            mm(nc, c.ps[:, 6, 0:16], c.upper, g["g"][:, 0:16], True, True)
            mm(nc, c.ps[:, 6, 16:32], c.lower, g["g"][:, 16:32], True, True).then_inc(s["cum_ready"], 1)
            pe.wait_ge(s["cum_read"], 1)
            mm(nc, c.ps[:, 7, 0:16], c.ident[:, P - 1:P].broadcast_to([P, P]), g["cum"][:, 0:16], True, True)
            mm(nc, c.ps[:, 7, 16:32], c.ident[:, 0:1].broadcast_to([P, P]), g["cum"][:, 16:32], True, True).then_inc(s["last_ready"], 1)
            pe.wait_ge(s["last_read"], 1)
            nc.tensor.transpose(c.ps[0:32, 6, 0:P], g["cum"], c.ident)
            nc.tensor.transpose(c.ps[0:32, 6, P:2 * P], g["beta"], c.ident).then_inc(s["turned"], 1)
            pe.wait_ge(s["rows_read"], 1)
            for t in range(ALL):
                pe.wait_ge(s["unit"], 6)
                bank = 6 + t % 2
                if t >= 2:
                    pe.wait_ge(s["k_tok"], t - 1)
                for h in range(DNH):
                    last = nc.tensor.transpose(c.ps[:, bank, h * P:(h + 1) * P], kk[:, h, t * P:(t + 1) * P], c.ident)
                last.then_inc(s["k_turned"], 1)

        @block.scalar
        def _(act):
            for i in range(6):
                nc.scalar.activation(sq[:, i, :], seg(i), ACT.Square).then_inc(s["square"], 1)
            for t in range(ALL):
                act.wait_ge(s["v_turned"], t + 1)
                nc.scalar.activation(c.v_tok[:, t], c.ps[:, 6 + t % 2], ACT.Copy).then_inc(s["v_tok"], 1)
            for i in range(6):
                act.wait_ge(s["eps_done"], i + 1)
                nc.scalar.activation(sq[:, i, :], sq[:, i, :], ACT.Sqrt).then_inc(s["root"], 1)
            nc.scalar.activation(g["beta"].rearrange("p (d t h) -> p t d h", d=2, t=ALL),
                                 c.rest.rearrange("p (t x h) -> p t x h", t=ALL, x=4)[:, :, 0:2, :],
                                 ACT.Sigmoid).then_inc(s["beta"], 1)
            act.wait_ge(s["dn_in"], 16)
            nc.scalar.activation(dn[:, 0:8], dn[:, 0:8], ACT.Exp).then_inc(s["exp_a"], 1)
            act.wait_ge(s["gate_step"], 3)
            nc.scalar.activation(g["e"], g["ax"], ACT.Exp, scale=-1.0).then_inc(s["exp_x"], 1)
            act.wait_ge(s["cum_ready"], 1)
            nc.scalar.activation(g["cum"], c.ps[:, 6, 0:32], ACT.Copy).then_inc(s["cum_read"], 1)
            act.wait_ge(s["last_ready"], 1)
            nc.scalar.activation(g["last"], c.ps[:, 7, 0:32], ACT.Copy).then_inc(s["last_read"], 1)
            act.wait_ge(s["exps_in"], 1)
            nc.scalar.activation(g["ecum"], g["cum"], ACT.Exp).then_inc(s["exps_done"], 1)
            nc.scalar.activation(g["elast"], g["last"], ACT.Exp).then_inc(s["exps_done"], 1)
            nc.scalar.activation(g["erest"], g["ax"], ACT.Exp).then_inc(s["exps_done"], 1)
            act.wait_ge(s["turned"], 1)
            nc.scalar.activation(c.gate_rowsT[:, 0:2 * P], c.ps[0:32, 6, 0:2 * P], ACT.Copy).then_inc(s["rows_read"], 1)
            for t in range(ALL):
                act.wait_ge(s["k_turned"], t + 1)
                nc.scalar.activation(c.k_tok[:, t], c.ps[:, 6 + t % 2], ACT.Copy).then_inc(s["k_tok"], 1)

        @block.vector
        def _(dve):
            step = [0]

            def then(ins):
                ins.then_inc(s["gate_step"], 1)
                step[0] += 1
                dve.wait_ge(s["gate_step"], step[0])

            for i in range(6):
                dve.wait_ge(s["sum_ready"], i + 1)
                nc.vector.tensor_scalar(sq[:, i, :], c.ps[:, i], 1e-6, None, ALU.add).then_inc(s["eps_done"], 1)

            def normalise(i):
                dve.wait_ge(s["root"], i + 1)
                nc.vector.reciprocal(c.ps[:, i], sq[:, i, :]).then_inc(s["inv"], 1)
                dve.wait_ge(s["inv"], i + 1)
                nc.vector.scalar_tensor_tensor(out=seg(i), in0=seg(i), scalar=float(P) ** -0.5 if i < 2 else 1.0,
                                               in1=c.ps[:, i], op0=ALU.mult, op1=ALU.mult).then_inc(s["unit"], 1)

            dve.wait_ge(s["dn_in"], 16)
            rest = c.rest.rearrange("p (t x h) -> p t x h", t=ALL, x=4)[:, :, 2:4, :]
            bias = dn[:, 8:16].rearrange("p (d h) -> p d h", d=2)
            for d in range(2):
                ins = nc.vector.tensor_tensor(g["x"][:, 16 * d:16 * d + 16].rearrange("p (t h) -> p t h", t=ALL),
                                              rest[:, :, d, :], bias[:, d].unsqueeze(1).broadcast_to([P, ALL, DNH]), ALU.add)
                then(ins)
            then(nc.vector.scalar_tensor_tensor(out=g["ax"], in0=g["x"], scalar=-1.0, in1=g["x"], op0=ALU.mult, op1=ALU.max))
            normalise(0)
            dve.wait_ge(s["exp_x"], 1)
            then(nc.vector.tensor_scalar(g["t"], g["e"], 2.0, None, ALU.add))
            then(nc.vector.reciprocal(g["t"], g["t"]))
            then(nc.vector.tensor_tensor(g["t"], g["t"], g["e"], ALU.mult))
            then(nc.vector.tensor_tensor(g["t2"], g["t"], g["t"], ALU.mult))
            then(nc.vector.tensor_scalar(g["g"], g["t2"], 1.0 / 17, 1.0 / 15, ALU.mult, ALU.add))
            for n in (13, 11, 9, 7, 5, 3, 1):
                then(nc.vector.tensor_tensor(g["g"], g["g"], g["t2"], ALU.mult))
                then(nc.vector.tensor_scalar(g["g"], g["g"], 1.0 / n, None, ALU.add))
            then(nc.vector.scalar_tensor_tensor(out=g["g"], in0=g["t"], scalar=2.0, in1=g["g"], op0=ALU.mult, op1=ALU.mult))
            then(nc.vector.scalar_tensor_tensor(out=g["g"], in0=g["x"], scalar=0.0, in1=g["g"], op0=ALU.max, op1=ALU.add))
            dve.wait_ge(s["exp_a"], 1)
            ea = dn[:, 0:8].rearrange("p (d h) -> p d h", d=2)
            for d in range(2):
                gd = g["g"][:, 16 * d:16 * d + 16].rearrange("p (t h) -> p t h", t=ALL)
                then(nc.vector.tensor_tensor(gd, gd, ea[:, d].unsqueeze(1).broadcast_to([P, ALL, DNH]), ALU.mult))
            then(nc.vector.tensor_scalar(g["g"], g["g"], -1.0, None, ALU.mult))
            dve.sem_inc(s["g_ready"], 1)
            normalise(1)
            normalise(2)
            dve.wait_ge(s["last_read"], 1)
            then(nc.vector.tensor_tensor(g["ax"], g["last"], g["cum"], ALU.subtract))
            dve.sem_inc(s["exps_in"], 1)
            normalise(3)
            dve.wait_ge(s["exps_done"], 3)
            dve.wait_ge(s["beta"], 1)
            then(nc.vector.scalar_tensor_tensor(out=g["nbe"], in0=g["beta"], scalar=-1.0, in1=g["ecum"], op0=ALU.mult,
                                                op1=ALU.mult))
            normalise(4)
            normalise(5)


def delta_inverse_stage(nc, c):
    GROUPS = [(t, d) for t in range(ALL) for d in range(2)]
    names = ["sums0", "sums1", "rows0", "rows1", "diff0", "diff1", "decay0", "decay1", "prep_step0", "prep_step1", "start0", "start1",
             "xt0", "xt1", "x0", "x1", "y_ready0", "y_ready1", "y0", "y1", "p_ready0", "p_ready1", "step0", "step1"]
    with stage(nc, *names) as (block, *sems):
        s = dict(zip(names, sems))
        tokf = c.tok[:, :, :].rearrange("p a n -> p (a n)")
        q = c.work[:, O_Q:O_Q + 1024].rearrange("p (h t) -> p h t", h=DNH)
        k = c.work[:, O_K:O_K + 2048].rearrange("p (h t) -> p h t", h=DNH)

        def buf(e, n):
            return tokf[:, 2048 * e + 512 * n:2048 * e + 512 * (n + 1)].rearrange("p (h n) -> p h n", h=DNH)

        X, LT, Y, DT = ([buf(e, n) for e in range(2)] for n in range(4))
        level = c.hTf[:, M_LEVEL:M_BIAS].rearrange("p (d l n) -> p d l n", d=2, l=LEVELS)
        mbias = c.hTf[:, M_BIAS:M_END].rearrange("p (d n) -> p d n", d=2)

        def heads(bank):
            return c.ps[:, bank].rearrange("p (h n) -> p h n", h=DNH)

        def over_heads(m):
            return m.unsqueeze(1).broadcast_to([P, DNH, P])

        @block.tensor
        def _(pe):
            def selector(pair, e, h):
                t, d = GROUPS[2 * pair + e]
                r = 16 * d + 4 * t + h
                return c.ident[0:32, r:r + 1].broadcast_to([32, P])

            def spread_sums(pair, e):
                for h in range(DNH):
                    last = mm(nc, heads(4 * e)[:, h], selector(pair, e, h), c.gate_rowsT[:, 0:P], True, True)
                last.then_inc(s[f"sums{e}"], 1)

            for e in range(2):
                spread_sums(0, e)
            for pair in range(4):
                for e in range(2):
                    i = 2 * pair + e
                    t, d = GROUPS[i]
                    if pair:
                        pe.wait_ge(s[f"step{e}"], pair * (LEVELS - 1))
                    tr = slice(t * P, (t + 1) * P)
                    for h in range(DNH):
                        hs = slice(h * P, (h + 1) * P)
                        last = mm(nc, c.ps[:, 4 * e + 1, hs], selector(pair, e, h), c.gate_rowsT[:, P:2 * P], True, True)
                        if e == 0:
                            last = mm(nc, c.ps[:, 2, hs], k[:, h, tr], k[:, h, tr], True, True)
                            if t < TT:
                                last = mm(nc, c.ps[:, 3, hs], k[:, h, tr], q[:, h, tr], True, True)
                    last.then_inc(s[f"rows{e}"], 1)
                for e in range(2):
                    i = 2 * pair + e
                    pe.wait_ge(s[f"start{e}"], pair + 1)
                    for h in range(DNH):
                        last = nc.tensor.transpose(heads(4 * e)[:, h], c.invT[i][:, h], c.ident)
                    last.then_inc(s[f"xt{e}"], 1)
                for l in range(1, LEVELS):
                    n = pair * (LEVELS - 1) + l
                    for e in range(2):
                        if l == 1:
                            pe.wait_ge(s[f"x{e}"], pair + 1)
                        else:
                            pe.wait_ge(s[f"step{e}"], n - 1)
                        for h in range(DNH):
                            last = mm(nc, heads(4 * e + 1)[:, h], LT[e][:, h], X[e][:, h], True, True)
                        last.then_inc(s[f"y_ready{e}"], 1)
                    if l == 3 and pair < 3:
                        for e in range(2):
                            pe.wait_ge(s[f"x{e}"], pair + 1)
                            spread_sums(pair + 1, e)
                    for e in range(2):
                        i = 2 * pair + e
                        pe.wait_ge(s[f"y{e}"], n)
                        for h in range(DNH):
                            last = mm(nc, heads(4 * e + 2)[:, h], Y[e][:, h], c.invT[i][:, h], True, True)
                        if l < LEVELS - 1:
                            for h in range(DNH):
                                last = mm(nc, heads(4 * e + 3)[:, h], c.invT[i][:, h], Y[e][:, h], True, True)
                        last.then_inc(s[f"p_ready{e}"], 1)

        @block.scalar
        def _(act):
            for pair in range(4):
                for e in range(2):
                    act.wait_ge(s[f"diff{e}"], 4 * pair + 4)
                    nc.scalar.activation(DT[e], DT[e], ACT.Exp).then_inc(s[f"decay{e}"], 1)
                for e in range(2):
                    act.wait_ge(s[f"xt{e}"], pair + 1)
                    nc.scalar.activation(X[e], heads(4 * e), ACT.Copy).then_inc(s[f"x{e}"], 1)

        @block.vector
        def _(dve):
            steps = [0, 0]

            def then(e, ins):
                ins.then_inc(s[f"prep_step{e}"], 1)
                steps[e] += 1
                dve.wait_ge(s[f"prep_step{e}"], steps[e])

            def decays(pair):
                for e in range(2):
                    t, d = GROUPS[2 * pair + e]
                    dve.wait_ge(s[f"sums{e}"], pair + 1)
                    for h in range(DNH):
                        col = 16 * d + 4 * t + h
                        nc.vector.scalar_tensor_tensor(out=DT[e][:, h], in0=heads(4 * e)[:, h],
                                                       scalar=c.gate_small["cum"][:, col:col + 1], in1=mbias[:, d],
                                                       op0=ALU.subtract, op1=ALU.add).then_inc(s[f"diff{e}"], 1)

            decays(0)
            for pair in range(4):
                for e in range(2):
                    i = 2 * pair + e
                    t, d = GROUPS[i]
                    dve.wait_ge(s[f"decay{e}"], pair + 1)
                    dve.wait_ge(s[f"rows{e}"], pair + 1)
                    if t < TT:
                        then(e, nc.vector.tensor_tensor(c.attT[i], heads(3), DT[e], ALU.mult))
                    then(e, nc.vector.tensor_tensor(DT[e], heads(2), DT[e], ALU.mult))
                    then(e, nc.vector.tensor_tensor(LT[e], heads(4 * e + 1), DT[e], ALU.mult))
                    then(e, nc.vector.tensor_tensor(Y[e], LT[e], over_heads(level[:, 1 - d, 0]), ALU.mult))
                    nc.vector.tensor_tensor(c.invT[i], over_heads(c.ident), Y[e], ALU.subtract).then_inc(s[f"start{e}"], 1)
                    dve.wait_ge(s[f"start{e}"], pair + 1)
                for l in range(1, LEVELS):
                    n = pair * (LEVELS - 1) + l
                    for e in range(2):
                        i = 2 * pair + e
                        t, d = GROUPS[i]
                        dve.wait_ge(s[f"y_ready{e}"], n)
                        nc.vector.tensor_tensor(Y[e], heads(4 * e + 1), over_heads(level[:, d, l]), ALU.mult).then_inc(s[f"y{e}"], 1)
                    if l == 4 and pair < 3:
                        decays(pair + 1)
                    for e in range(2):
                        i = 2 * pair + e
                        dve.wait_ge(s[f"p_ready{e}"], n)
                        if l < LEVELS - 1:
                            then(e, nc.vector.tensor_tensor(X[e], X[e], heads(4 * e + 3), ALU.subtract))
                        nc.vector.tensor_tensor(c.invT[i], c.invT[i], heads(4 * e + 2), ALU.subtract).then_inc(s[f"step{e}"], 1)


def delta_scan_stage(nc, c):
    ORDER = [(2, 3, 0, 1), (3, 2, 1, 0)]
    names = []
    for d in range(2):
        names += [f"{n}{d}" for n in ("read", "values", "wanted", "fresh", "fresh_read", "vb", "kd", "grow", "state",
                                      "own_out", "out_scaled", "out")]
    with stage(nc, *names) as (block, *sems):
        s = dict(zip(names, sems))
        tokf = c.tok[:, :, :].rearrange("p a n -> p (a n)")
        q = c.work[:, O_Q:O_Q + 1024].rearrange("p (h t) -> p h t", h=DNH)
        k = c.work[:, O_K:O_K + 2048].rearrange("p (h t) -> p h t", h=DNH)
        g = c.gate_small

        def buf(d, n):
            return tokf[:, 2048 * d + 512 * n:2048 * d + 512 * (n + 1)].rearrange("p (h n) -> p h n", h=DNH)

        VB, VN, KD, OT = ([buf(d, n) for d in range(2)] for n in range(4))

        def heads(bank):
            return c.ps[:, bank].rearrange("p (h n) -> p h n", h=DNH)

        def col(name, d, t, h):
            i = 16 * d + 4 * t + h
            return g[name][:, i:i + 1]

        @block.tensor
        def _(pe):
            for i in range(4):
                for d in range(2):
                    t = ORDER[d][i]
                    tr = slice(t * P, (t + 1) * P)
                    if i:
                        pe.wait_ge(s[f"state{d}"], 4 * i)
                        for h in range(DNH):
                            last = mm(nc, heads(4 * d)[:, h], k[:, h, tr], c.state[d][:, h], True, True)
                        last.then_inc(s[f"read{d}"], 1)
                    if t < TT:
                        if i == 3:
                            pe.wait_ge(s[f"out_scaled{d}"], 4)
                        for h in range(DNH):
                            last = mm(nc, heads(4 * d + 2)[:, h], q[:, h, tr], c.state[d][:, h], True, True)
                        last.then_inc(s[f"own_out{d}"], 1)
                for d in range(2):
                    t = ORDER[d][i]
                    if i:
                        pe.wait_ge(s[f"values{d}"], 4 * i)
                    else:
                        pe.wait_ge(s[f"vb{d}"], 4)
                    for h in range(DNH):
                        last = mm(nc, heads(4 * d + 1)[:, h], c.invT[2 * t + d][:, h], VB[d][:, h], True, True)
                    last.then_inc(s[f"fresh{d}"], 1)
                for d in range(2):
                    t = ORDER[d][i]
                    pe.wait_ge(s[f"fresh_read{d}"], i + 1)
                    if i < 3:
                        pe.wait_ge(s[f"kd{d}"], 4 * i + 4)
                        for h in range(DNH):
                            last = mm(nc, heads(4 * d)[:, h], KD[d][:, h], VN[d][:, h], True, True)
                        last.then_inc(s[f"grow{d}"], 1)
                    if t < TT:
                        if i == 3:
                            pe.wait_ge(s[f"out{d}"], 1)
                        for h in range(DNH):
                            last = mm(nc, heads(4 * d + 3)[:, h], c.attT[2 * t + d][:, h], VN[d][:, h], True, True)
                        last.then_inc(s[f"own_out{d}"], 1)

        @block.scalar
        def _(act):
            for i in range(4):
                for d in range(2):
                    t = ORDER[d][i]
                    if i:
                        act.wait_ge(s[f"fresh{d}"], i)
                    for h in range(DNH):
                        nc.scalar.activation(VB[d][:, h], c.v_tok[:, t].rearrange("p (h n) -> p h n", h=DNH)[:, h], ACT.Copy,
                                             scale=col("beta", d, t, h)).then_inc(s[f"vb{d}"], 1)
                    if t < TT:
                        act.wait_ge(s[f"own_out{d}"], 2 * (i - 2) + 1)
                        if i == 3:
                            act.wait_ge(s[f"out{d}"], 1)
                        for h in range(DNH):
                            nc.scalar.activation(OT[d][:, h], heads(4 * d + 2)[:, h], ACT.Copy,
                                                 scale=col("ecum", d, t, h)).then_inc(s[f"out_scaled{d}"], 1)
                for d in range(2):
                    act.wait_ge(s[f"fresh{d}"], i + 1)
                    if i:
                        act.wait_ge(s[f"grow{d}"], i)
                    if i == 3:
                        act.wait_ge(s[f"own_out{d}"], 2)
                    nc.scalar.activation(VN[d], heads(4 * d + 1), ACT.Copy).then_inc(s[f"fresh_read{d}"], 1)

        @block.gpsimd
        def _(pool):
            for i in range(3):
                for d in range(2):
                    t = ORDER[d][i]
                    if i:
                        pool.wait_ge(s[f"grow{d}"], i)
                    for h in range(DNH):
                        nc.gpsimd.tensor_scalar(KD[d][:, h], c.k_tok[:, t].rearrange("p (h n) -> p h n", h=DNH)[:, h],
                                                col("erest", d, t, h), None, ALU.mult).then_inc(s[f"kd{d}"], 1)

        @block.vector
        def _(dve):
            for i in range(4):
                for d in range(2):
                    t = ORDER[d][i]
                    if i:
                        dve.wait_ge(s[f"read{d}"], i)
                        dve.wait_ge(s[f"vb{d}"], 4 * i + 4)
                        for h in range(DNH):
                            nc.vector.scalar_tensor_tensor(out=VB[d][:, h], in0=heads(4 * d)[:, h], scalar=col("nbe", d, t, h),
                                                           in1=VB[d][:, h], op0=ALU.mult, op1=ALU.add).then_inc(s[f"values{d}"], 1)
                for d in range(2):
                    t = ORDER[d][i]
                    if i < 3:
                        dve.wait_ge(s[f"grow{d}"], i + 1)
                        for h in range(DNH):
                            if i == 0:
                                nc.vector.tensor_copy(c.state[d][:, h], heads(4 * d)[:, h]).then_inc(s[f"state{d}"], 1)
                            else:
                                if t < TT:
                                    dve.wait_ge(s[f"own_out{d}"], 2 * (i - 2) + 1)
                                nc.vector.scalar_tensor_tensor(out=c.state[d][:, h], in0=c.state[d][:, h],
                                                               scalar=col("elast", d, t, h), in1=heads(4 * d)[:, h],
                                                               op0=ALU.mult, op1=ALU.add).then_inc(s[f"state{d}"], 1)
                    if t < TT:
                        dve.wait_ge(s[f"own_out{d}"], 2 * (i - 2) + 2)
                        dve.wait_ge(s[f"out_scaled{d}"], 4 * (i - 2) + 4)
                        ot = c.o_tok[:, t].rearrange("p (h n) -> p h n", h=DNH)
                        if i == 2:
                            nc.vector.tensor_tensor(ot, OT[d], heads(4 * d + 3), ALU.add).then_inc(s[f"out{d}"], 1)
                        else:
                            nc.vector.tensor_tensor(OT[d], OT[d], heads(4 * d + 3), ALU.add).then_inc(s[f"out{d}"], 1)
                            dve.wait_ge(s[f"out{d}"], 2)
                            dve.wait_ge(s[f"out{1 - d}"], 1)
                            nc.vector.tensor_tensor(ot, ot, OT[d], ALU.add).then_inc(s[f"out{d}"], 1)


def odd_out_stage(nc, c, w, m0):
    with stage(nc, "squares", "root", "step", "gated", "turned", "cols", "out_ready", "product", "added") as (
            block, squares, root, step, gated, turned, cols, out_ready, product, added):
        o = c.o_tok
        gs = c.work[:, O_GATE:O_GATE + 1024].rearrange("p (t n) -> p t n", t=TT)
        oT = c.work[:, O_Q:O_Q + 1024].rearrange("p (h t) -> p h t", h=DNH)
        hy = c.work[:, O_HY:O_HY + 1024].rearrange("p (f t) -> p f t", f=4)
        junk = c.spare[:, 0:P]
        sm = c.spare[:, P:P + 32]

        @block.sync
        def _(sp):
            for i in range(2):
                sp.wait_ge(out_ready, i + 1)
                w.refill(sp, m0 + i)

        @block.tensor
        def _(pe):
            for half in range(2):
                wt = w.landed(pe, m0 + half).rearrange("p (k n) -> p k n", k=4)
                if half:
                    for t in range(TT):
                        pe.wait_ge(gated, t + 1)
                        for h in range(DNH):
                            last = nc.tensor.transpose(c.ps[:, 4 + h // 2, (h % 2) * SEQ + t * P:(h % 2) * SEQ + (t + 1) * P],
                                                       o[:, t, h * P:(h + 1) * P], c.ident)
                    last.then_inc(turned, 1)
                    pe.wait_ge(cols, 1)
                src = oT if half else hy
                for kk in range(4):
                    for t in range(TT):
                        for n in range(2):
                            last = mm(nc, c.ps[:, 2 * t + n], src[:, kk, t * P:(t + 1) * P], wt[:, kk, n * BANK:(n + 1) * BANK],
                                      half + kk == 0, half == 1 and kk == 3)
                last.then_inc(out_ready, 1)

        @block.scalar
        def _(act):
            act.wait_ge(squares, 8)
            nc.scalar.activation(sm[:, 8:16], sm[:, 0:8], ACT.Sqrt).then_inc(root, 1)
            act.wait_ge(turned, 1)
            nc.scalar.activation(oT.rearrange("p h t -> p (h t)"), c.ps[:, 4:6, :].rearrange("p b n -> p (b n)"), ACT.Copy,
                                 scale=c.par[:, S_DNG:S_DNG + 1]).then_inc(cols, 1)

        @block.vector
        def _(dve):
            for i in range(8):
                oh = o[:, i // 4, (i % 4) * P:(i % 4 + 1) * P]
                nc.vector.tensor_tensor_reduce(out=junk, in0=oh, in1=oh, scale=1.0 / P, scalar=EPS, op0=ALU.mult, op1=ALU.add,
                                               accum_out=sm[:, i:i + 1]).then_inc(squares, 1)
                dve.wait_ge(squares, i + 1)
            dve.wait_ge(root, 1)
            nc.vector.reciprocal(sm[:, 16:24], sm[:, 8:16]).then_inc(step, 1)
            dve.wait_ge(step, 1)
            for i in range(8):
                oh = o[:, i // 4, (i % 4) * P:(i % 4 + 1) * P]
                nc.vector.tensor_scalar(oh, oh, sm[:, 16 + i:17 + i], None, ALU.mult).then_inc(step, 1)
            dve.wait_ge(step, 9)
            for t in range(TT):
                nc.vector.tensor_tensor(o[:, t], o[:, t], gs[:, t], ALU.mult).then_inc(gated, 1)
            dve.wait_ge(out_ready, 2)
            add_gated(nc, c, product, range(TT), 0)

        @block.gpsimd
        def _(pool):
            for t in range(TT):
                for n in range(2):
                    pool.wait_ge(product, 2 * t + n + 1)
                    xs = c.x[:, t, n * BANK:(n + 1) * BANK]
                    nc.gpsimd.tensor_tensor(xs, xs, c.tok[:, t, n * BANK:(n + 1) * BANK], ALU.add).then_inc(added, 1)
            pool.wait_ge(added, 2 * TT)


class Core:
    pass


def first_block(nc, c, layers, rows):
    with nc.Fori(0, DEPTH) as layer:
        w = Panels(c, layer, L1_PANELS, 0, 0)
        norm_stage(nc, c, [0, 1], lambda k, _: c.lay[:, C_FFN1 + k:C_FFN1 + k + 1], ahead=(w, AT_FFN1))
        ffn_stage(nc, c, w, AT_FFN1)
        norm_stage(nc, c, [0, 1], lambda k, _: c.lay[:, C_MIX + k:C_MIX + k + 1], ahead=(w, AT_PROJ), keep=True)
        mixer1_stage(nc, c, w, AT_PROJ)
        norm_stage(nc, c, [0, 1], lambda k, _: c.lay[:, C_FFN2 + k:C_FFN2 + k + 1], ahead=(w, AT_FFN2))
        ffn_stage(nc, c, w, AT_FFN2, [(c.lay[:, :], layers[layer + 1]), (c.rows[:, :], rows[layer + 1].partition_broadcast(P))])


def token_norm_stage(nc, c, gain, out=None):
    with stage(nc, "gain_in", "squares", "mean_sq", "root", "step", "normed", "stored") as (
            block, gain_in, squares, mean_sq, root, step, normed, stored):
        @block.sync
        def _(sp):
            sp.dma_start(c.tok[:, 0], gain.partition_broadcast(P)).then_inc(gain_in, 16)
            sp.wait_ge(c.second_in, 48)
            if out is not None:
                for t in range(TT):
                    sp.wait_ge(normed, t + 1)
                    sp.dma_start(out[t * P:(t + 1) * P], c.x[:, t, :]).then_inc(stored, 16)
                sp.wait_ge(stored, 16 * TT)

        @block.scalar
        def _(act):
            nc.scalar.activation(c.ps[:, 0:2, :].rearrange("p b n -> p (b n)"), c.x[:, 0], ACT.Square,
                                 accum_out=c.stat[:, 0:1]).then_inc(squares, 1)
            act.wait_ge(mean_sq, 1)
            nc.scalar.activation(c.stat[:, 4:6], c.stat[:, 2:4], ACT.Sqrt).then_inc(root, 1)

        @block.vector
        def _(dve):
            nc.vector.tensor_tensor_reduce(out=c.tok[:, 1], in0=c.x[:, 1], in1=c.x[:, 1], scale=1.0, scalar=0.0,
                                           op0=ALU.mult, op1=ALU.add, accum_out=c.stat[:, 1:2]).then_inc(squares, 1)
            dve.wait_ge(squares, TT)
            nc.vector.tensor_scalar(c.stat[:, 2:4], c.stat[:, 0:2], 1.0 / D, EPS, ALU.mult, ALU.add).then_inc(mean_sq, 1)
            dve.wait_ge(root, 1)
            nc.vector.reciprocal(c.stat[:, 6:8], c.stat[:, 4:6]).then_inc(step, 1)
            dve.wait_ge(step, 1)
            dve.wait_ge(gain_in, 16)
            for t in range(TT):
                nc.vector.scalar_tensor_tensor(out=c.x[:, t], in0=c.x[:, t], scalar=c.stat[:, 6 + t:7 + t],
                                               in1=c.tok[:, 0], op0=ALU.mult, op1=ALU.mult).then_inc(normed, 1)


def second_block(nc, c, final_gain, out):
    w = Panels(c, None, 0, DEPTH * L1_PANELS, PANELS)

    def modulated(j):
        return (lambda k, st: c.mod[:, 2 * j + 1, st, k:k + 1], lambda k, st: c.mod[:, 2 * j, st, k:k + 1])

    ada_stage(nc, c, w, B_ADA0, 0)
    norm_stage(nc, c, [0, 1, 2, 3], *modulated(0), ahead=(w, B_EVEN))
    even_mixer_stage(nc, c, w, B_EVEN)
    norm_stage(nc, c, [0, 1, 2, 3], *modulated(1), ahead=(w, B_MLP0))
    mlp_stage(nc, c, w, B_MLP0, [0, 1, 2, 3], 2)
    ada_stage(nc, c, w, B_ADA1, 1)
    norm_stage(nc, c, [0, 1, 2, 3], *modulated(0), ahead=(w, B_ODD))
    odd_project_stage(nc, c, w, B_ODD)
    for order in range(2):
        hyena_stage(nc, c, order)
    delta_features_stage(nc, c)
    delta_inverse_stage(nc, c)
    delta_scan_stage(nc, c)
    odd_out_stage(nc, c, w, B_ODD + 7)
    norm_stage(nc, c, [0, 1], *modulated(1), ahead=(w, B_MLP1))
    mlp_stage(nc, c, w, B_MLP1, [0, 1], 1)
    token_norm_stage(nc, c, final_gain, out)
def program(nc, a, out):
    c = Core()
    with ExitStack() as ctx:
        def sb(name, *shape):
            return ctx.enter_context(nc.sbuf_tensor(name, [P, *shape], F32))

        c.ring = sb("ring", RING, PANEL)
        c.x = sb("x", 4, D)
        at_hT = nc.sbuf_base
        c.hT = sb("hT", DK, 4 * P)
        c.tok = sb("tok", 4, D)
        at_work = nc.sbuf_base
        c.work = sb("work", 16 * 1024)
        c.hT_hi = nc.alloc_sbuf_tensor_at("hT_hi", [P, DK, 4 * P], F32R, offset=at_hT)
        c.hT_lo = ctx.enter_context(nc.sbuf_tensor("hT_lo", [P, DK, 4 * P], F32R))
        c.hid_hi = nc.alloc_sbuf_tensor_at("hid_hi", [P, 8 * 1024], F32R, offset=at_work)
        c.hid_lo = nc.alloc_sbuf_tensor_at("hid_lo", [P, 8 * 1024], F32R, offset=at_work + 4 * 8 * 1024)
        c.w_hi = ctx.enter_context(nc.sbuf_tensor("w_hi", [P, 2, QUART], F32R))
        c.w_lo = ctx.enter_context(nc.sbuf_tensor("w_lo", [P, 2, QUART], F32R))
        c.cond_parts = ctx.enter_context(nc.sbuf_tensor("cond_parts", [P, DK, 4], F32R))
        params = sb("params", C_END + R_END)
        c.lay = params[:, 0:C_END]
        c.rows = params[:, C_END:C_END + R_END]
        c.spare = params[:, D:2 * D]
        c.gate_rows = params[:, 0:4 * D].rearrange("p (g n) -> p g n", g=4)
        c.const = sb("const", K_END1)
        c.stat = sb("stat", 16)
        c.par = sb("par", S_END)
        c.const2 = sb("const2", K2_END)
        small = sb("small", 2 * P + 64 + 16 + 64 + 1 + 13 * 32)
        c.ones = small[:, 0:P]
        c.mean512 = small[:, P:2 * P]
        c.mod = small[:, 256:320].rearrange("p (j s k) -> p j s k", j=4, s=2)
        c.silu_c = small[:, 320:336].rearrange("p (k s) -> p k s", s=2)
        c.rest = small[:, 336:400]
        c.subln = small[:, 400:401]
        c.gate_small = {n: small[:, 401 + 32 * j:433 + 32 * j] for j, n in enumerate(
            ("x", "ax", "e", "t", "t2", "g", "cum", "last", "ecum", "elast", "erest", "beta", "nbe"))}
        c.upper = c.const[:, K_UPPER:K_UPPER + P]
        c.lower = c.const2[:, K2_LOWER:K2_END]
        c.hTf = c.hT[:, :, :].rearrange("p k t -> p (k t)")
        tokf = c.tok[:, :, :].rearrange("p a n -> p (a n)")
        c.hidden_z = tokf[0:64, 3840:4096]
        c.gate_rowsT = c.spare[0:32, 256:512]
        c.k_tok = c.work[:, 9216:11264].rearrange("p (t n) -> p t n", t=ALL)
        c.v_tok = c.work[:, 11264:13312].rearrange("p (t n) -> p t n", t=ALL)
        c.invT = [c.work[:, at:at + 512].rearrange("p (h n) -> p h n", h=DNH)
                  for at in (*range(6144, 8192, 512), *range(13312, 15360, 512))]
        c.attT = [c.work[:, at:at + 512].rearrange("p (h n) -> p h n", h=DNH) for at in range(1024, 3072, 512)]
        c.state = [c.work[:, at:at + 512].rearrange("p (h n) -> p h n", h=DNH) for at in (15360, 15872)]
        c.o_tok = c.hTf[:, 2304:3328].rearrange("p (t n) -> p t n", t=TT)
        c.vrows, c.transforms, c.masks, c.w3 = (a[n] for n in ("vrows", "transforms", "masks", "w3"))
        c.ident = c.const[:, K_ID:K_ID + P]
        c.ps = ctx.enter_context(nc.psum_tensor("ps", [P, 8, BANK], F32))
        c.landed = [ctx.enter_context(nc.semaphore(f"panel_landed{i}")) for i in range(RING)]
        c.panels = a["panels"]
        c.second_in = ctx.enter_context(nc.semaphore("second_in"))
        c.rows_in = ctx.enter_context(nc.semaphore("rows_in"))
        with stage(nc, "x_in", "const_in", "filled") as (block, x_in, const_in, filled):
            @block.sync
            def _(sp):
                sp.dma_start(c.x[:, 0:TT, :], a["x"].rearrange("(t p) n -> p t n", p=P)).then_inc(x_in, 16)
                sp.dma_start(c.const[:, :], a["const"]).then_inc(const_in, 16)
                sp.dma_start(c.lay[:, :], a["layers"][0]).then_inc(const_in, 16)
                for m in range(RING):
                    sp.dma_start(c.ring[:, m], a["panels"][m]).then_inc(c.landed[m], 16)
                sp.dma_start(c.rows[:, :], a["rows"][0].partition_broadcast(P)).then_inc(c.rows_in, 16)
                sp.dma_start(c.x[:, TT:ALL, :], a["ctx"].rearrange("(t p) n -> p t n", p=P)).then_inc(c.second_in, 16)
                sp.dma_start(c.par[:, :], a["par"]).then_inc(c.second_in, 16)
                sp.dma_start(c.const2[:, :], a["const2"]).then_inc(c.second_in, 16)
                sp.wait_ge(x_in, 16)
                sp.wait_ge(const_in, 32)

            @block.gpsimd
            def _(pool):
                nc.gpsimd.memset(c.ones, 1.0).then_inc(filled, 1)
                nc.gpsimd.memset(c.mean512, 1.0 / 512).then_inc(filled, 1)
                pool.wait_ge(filled, 2)
        first_block(nc, c, a["layers"], a["rows"])
        token_norm_stage(nc, c, a["final_norm"])
        second_block(nc, c, a["final_g"], out)


def panel(w):
    k = w.shape[0] // P
    w = w.reshape(k, P, w.shape[1]).transpose(1, 0, 2).reshape(P, -1)
    return np.pad(w, ((0, 0), (0, PANEL - w.shape[1]))) if w.shape[1] < PANEL else w


def column_panels(w):
    return [panel(w[:, i:i + BANK]) for i in range(0, w.shape[1], BANK)]


def row_panels(w):
    return [panel(w[i:i + 4 * P]) for i in range(0, w.shape[0], 4 * P)]


def first_panels(i):
    out = []
    for l in range(DEPTH):
        def ffn(gu, down):
            g = gu[l].reshape(D, 2, GU, 256).transpose(0, 2, 1, 3).reshape(D, 2 * FF)
            return column_panels(g) + row_panels(down[l])
        u, va, q, k, v, qi = (i["w_in"][l][:, n * CH:(n + 1) * CH] for n in range(6))
        gates = i["w_in"][l][:, 6 * CH + SMALL:]
        out += ffn(i["ffn1_w_gu"], i["ffn1_w_down"])
        for part in (q, k, qi, v, u, va, gates):
            out += column_panels(part)
        out += row_panels(i["w_pa"][l]) + row_panels(i["w_pb"][l]) + row_panels(i["w_out"][l])
        out += ffn(i["ffn2_w_gu"], i["ffn2_w_down"])
    return out


def columns(v):
    return v.reshape(-1, P).T


def constants():
    out = np.zeros((P, K_END1), np.float32)
    out[:, K_ID:K_ID + P] = np.eye(P)
    out[:, K_UPPER:K_UPPER + P] = np.triu(np.ones((P, P)))
    pos = np.arange(SEQ)
    causal = np.where(pos[None, :] <= pos[:, None], 0.0, MASKED).astype(np.float32)
    out[:, K_CAUSAL:K_COS] = causal.reshape(TT, P, SEQ).transpose(1, 0, 2).reshape(P, -1)
    inv = np.float32(10000.0) ** (-np.arange(0, HD, 2, dtype=np.float32) / np.float32(HD))
    ang = pos.astype(np.float32)[:, None] * inv[None, :].astype(np.float32)
    cos, sin = np.cos(ang.astype(np.float64)), np.sin(ang.astype(np.float64))
    for at, tab in ((K_COS, np.concatenate([cos, cos], 1)), (K_SIN, np.concatenate([-sin, sin], 1))):
        out[:, at:at + TT * HD] = tab.reshape(TT, P, HD).transpose(1, 0, 2).reshape(P, -1)
    return out


def first_arrays(i):
    layers, rows = [], []
    for l in range(DEPTH):
        small = i["w_in"][l][:, 6 * CH:6 * CH + SMALL]
        layers.append(np.concatenate([
            columns(i["ffn1_norm"][l]), columns(i["mix_norm"][l]), columns(i["ffn2_norm"][l]), i["gmlp_b_s"][l].T,
            i["gmlp_w_s"][l].transpose(2, 0, 1).reshape(P, 4 * P),
            small.reshape(DK, P, SMALL).transpose(1, 0, 2).reshape(P, -1)], axis=1))
        rows.append(np.concatenate([i["b_gate"][l], i["gmlp_ln_g"][l], i["gmlp_ln_b"][l]]))
    return {"x": i["x"][0], "layers": np.stack(layers + layers[:1]), "rows": np.stack(rows + rows[:1]),
            "final_norm": i["final_norm"]}


def second_panels(i):
    even, odd = i["ev_w_in_2"][0], i["od_w_in_2"][0]

    def ada(l):
        w = i["ada_w_2"][l]
        return [p for part in (0, 1, 3, 4, 2, 5) for p in column_panels(w[:, part * D:(part + 1) * D])]

    def mlp(l, parts):
        up, down = column_panels(i["mlp_w1_2"][l]), row_panels(i["mlp_w2_2"][l])
        n = len(up) // parts
        return [p for j in range(0, len(up), n) for p in up[j:j + n] + down[j:j + n]]

    glu = even[:, 0:2 * CH].reshape(D, 2, 2, 256).transpose(0, 2, 1, 3).reshape(D, 2 * CH)
    out = ada(0) + column_panels(glu) + column_panels(even[:, 2 * CH:]) + row_panels(i["ev_w_out_2"][0]) + mlp(0, 2)
    hy, gate, qkv = odd[:, 0:3 * CH], odd[:, 3 * CH:4 * CH], odd[:, 4 * CH:7 * CH]
    return out + ada(1) + column_panels(hy) + column_panels(qkv) + column_panels(gate) + \
        row_panels(i["od_w_out_2"][0]) + mlp(1, 1)


def channel_taps(w):
    return w.reshape(w.shape[0], -1, P).transpose(2, 1, 0).reshape(P, -1)


def on_partitions(w):
    return np.pad(w, ((0, P - w.shape[0]), (0, 0)))


def second_arrays(i):
    cond = np.stack([columns(i["c_2"][0]), columns(i["c_ctx_2"])], axis=2).reshape(P, -1)
    fb = np.stack([i[n][0] for n in ("od_hy_b1_2", "od_hy_freq1_2", "od_hy_b2_2", "od_hy_freq2_2")], axis=1)
    par = np.concatenate([
        cond, *(columns(i["ada_b_2"][l]) for l in range(DEPTH)), *(columns(i["norm1_g_2"][l]) for l in range(DEPTH)),
        *(columns(i["norm2_g_2"][l]) for l in range(DEPTH)), channel_taps(i["ev_conv_w_2"][0]),
        columns(i["ev_conv_b_2"][0]), columns(i["ev_ln_g_2"][0]), columns(i["ev_ln_b_2"][0]),
        i["ev_subln_g_2"][0][:, None], channel_taps(i["od_hy_short_w_2"][0]), columns(i["od_hy_short_b_2"][0]),
        columns(i["od_hy_skip_2"][0].reshape(-1)), channel_taps(i["od_dn_conv_w_2"][0]), i["od_dn_norm_g_2"][0][:, None],
        on_partitions(fb), on_partitions(i["od_hy_w1_2"][0]), on_partitions(i["od_hy_w2_2"][0]),
        i["od_w_in_2"][0][:, 7 * CH:].reshape(DK, P, 16).transpose(1, 0, 2).reshape(P, -1)], axis=1)
    assert par.shape == (P, S_END)
    gates = [i["ada_b_2"][l][part * D:(part + 1) * D] for l in range(DEPTH) for part in (2, 5)]
    vrows = np.concatenate([*gates, *(i[f"ev_{n}_2"][0] for n in ("lq1", "lk1", "lq2", "lk2")),
                            *(i[f"od_dn_{n}_2"][0] for n in ("alog_f", "alog_b", "dtb_f", "dtb_b"))])
    assert vrows.shape == (V_END,)
    return {"ctx": i["ctx_2"][0], "par": par, "vrows": vrows, "w3": i["od_hy_w3_2"][0], "final_g": i["final_g_2"]}


def second_constants():
    out = np.zeros((P, K2_END), np.float32)
    f32 = np.float32
    pos = np.arange(SEQ)
    inv = f32(10000.0) ** (-np.arange(16, dtype=f32) / f32(16))
    ar, ac = ((x.astype(f32)[:, None] * inv).astype(np.float64) for x in (pos // 64, pos % 64))
    cos = np.concatenate([np.cos(ar), np.cos(ar), np.cos(ac), np.cos(ac)], 1)
    sin = np.concatenate([-np.sin(ar), np.sin(ar), -np.sin(ac), np.sin(ac)], 1)
    for at, tab in ((K2_COS, cos), (K2_SIN, sin)):
        out[:, at:at + TT * 64] = tab.reshape(TT, P, 64).transpose(1, 0, 2).reshape(P, -1)
    out[:, K2_LOWER:] = np.tril(np.ones((P, P)))
    return out


def transform_constants():
    n = 2 * SEQ
    t, f = np.arange(SEQ), np.arange(SEQ)
    ang = 2 * np.pi * ((t[:, None] * f[None, :]) % n) / n
    top = (-1.0) ** t
    re, im = np.cos(ang), -np.sin(ang)
    im_top = im.copy()
    im_top[:, 0] = top
    signal = np.concatenate([re, im_top], 1)
    re_top = re[:, 0:P].copy()
    re_top[:, 0] = top
    forward = np.concatenate([re, im, re_top], 1)
    backward = np.concatenate([re, -im, re_top], 1)
    backward[0] = 0.0
    inv_re, inv_im = 2 * re.T / n, 2 * im.T / n
    inv_re[0] = 1.0 / n
    inv_im[0] = top / n
    inverse = np.concatenate([inv_re, inv_im], 0)

    def tiles(m):
        return m.reshape(-1, P, m.shape[1]).transpose(1, 0, 2).reshape(P, -1)

    f32 = np.float32
    lo, hi = math.log(1e-2) / 1.5, math.log(1e-2) / 0.3
    tt = np.linspace(0.0, 1.0, SEQ).astype(f32)
    deltas = np.abs(np.linspace(lo, hi, CH).astype(f32))
    window = np.exp((-tt[:, None] * deltas).astype(np.float64))
    omega = (f32(2.0 * math.pi) * np.arange(SEQ, dtype=f32) / f32(SEQ))[:, None]
    a = (omega * np.linspace(1e-4, 15, 16).astype(f32)).astype(np.float64)
    z = np.concatenate([tt[:, None], np.cos(a), -np.sin(a)], 1).T
    out = np.concatenate([tiles(np.concatenate([forward, backward])), tiles(signal), tiles(inverse), tiles(window),
                          on_partitions(z)], 1).astype(f32)
    assert out.shape == (P, T_END)
    return out


def mask_constants():
    i = np.arange(P)
    r, s = i[:, None], i[None, :]
    levels = [((r >> l) & 1) & ((s >> l) == (r >> l) - 1) for l in range(LEVELS)]
    levels += [m.T for m in levels]
    bias = [np.where(s >= r, 0.0, MASKED), np.where(s <= r, 0.0, MASKED)]
    return np.concatenate(levels + bias, 1).astype(np.float32)


def kernel(**inputs):
    import concourse.bacc as bacc
    from concourse.bass_utils import run_bass_kernel_spmd as run

    i = {k: np.asarray(v) for k, v in inputs.items()}
    arrays = {**first_arrays(i), **second_arrays(i), "const": constants(), "const2": second_constants(),
              "transforms": transform_constants(), "masks": mask_constants(),
              "panels": np.stack(first_panels(i) + second_panels(i))}
    assert arrays["panels"].shape[0] == PANELS
    arrays = {n: np.ascontiguousarray(v) for n, v in arrays.items()}
    nc = bacc.Bacc("TRN2", target_bir_lowering=False, num_devices=1)
    aps = {n: nc.dram_tensor(f"in_{n}", v.shape, F32, kind="ExternalInput").ap() for n, v in arrays.items()}
    out = nc.dram_tensor("out_x", (SEQ, D), F32, kind="ExternalOutput").ap()
    program(nc, aps, out)
    got = run(nc, [{f"in_{n}": v for n, v in arrays.items()}], core_ids=[0])
    return got.results[0]["out_x"][None]
```
